# Optimizing a Trainium2 kernel written in Bass

```python
import math
import jax
import jax.numpy as jnp
from jax import lax
import numpy as np
import jax, jax.numpy as jnp

D_MODEL = 1024
BATCH = 1
SEQ = 256
DEPTH = 1

ATT_PATTERNS = ((128, 1), (512, 4), (2048, 16))
N_ATT_GROUPS = 3
HEADS_PER_GROUP = 4
ATT_HEADS = N_ATT_GROUPS * HEADS_PER_GROUP
HEAD_DIM = 64
ATT_WIDTH = ATT_HEADS * HEAD_DIM
ATT_OUT_WIDTH = HEADS_PER_GROUP * HEAD_DIM
REL_BUCKETS = 32
REL_MAX_DIST = 2048
RWKV_HEADS = 8
RWKV_HEAD_DIM = 64
RWKV_WIDTH = RWKV_HEADS * RWKV_HEAD_DIM
DECAY_LORA = 64
ICLR_LORA = 64
GATE_LORA = 160
RWKV_SHIFT_WIDTH = 3 * RWKV_WIDTH + DECAY_LORA + ICLR_LORA + GATE_LORA
GN_EPS = 64e-5
N_BRANCHES = 2
IN_WIDTH = 3 * ATT_WIDTH + RWKV_SHIFT_WIDTH + N_BRANCHES * D_MODEL
N_EXPERT_GROUPS = 4
EXPERTS_PER_GROUP = 8
N_EXPERTS = N_EXPERT_GROUPS * EXPERTS_PER_GROUP
TOP_K = 2
D_EXPERT = 512
ROW_BLOCK = 256
NORM_EPS = 1e-6
NEG_INF = -1e30


def rms_norm(x, gain, eps=NORM_EPS):
    xf = x.astype(jnp.float32)
    y = xf * lax.rsqrt(jnp.mean(xf * xf, axis=-1, keepdims=True) + eps)
    return (y * gain.astype(jnp.float32)).astype(x.dtype)

def t5_causal_bucket(dist):
    max_exact = REL_BUCKETS // 2
    d = jnp.maximum(dist.astype(jnp.float32), 1.0)
    large = max_exact + (jnp.log(d / max_exact) / math.log(REL_MAX_DIST / max_exact)
                         * (REL_BUCKETS - max_exact)).astype(jnp.int32)
    large = jnp.minimum(large, REL_BUCKETS - 1)
    return jnp.where(dist < max_exact, dist, large)

def dilated_window_attention(q, k, v, bias_table, window, dilation):
    B, S, H, E = q.shape
    L = S // dilation
    W = window // dilation
    n_blk = -(-L // W)
    Lp = n_blk * W

    def to_sub(t):
        return t.reshape(B, L, dilation, H, E).transpose(0, 2, 3, 1, 4)

    qb = jnp.pad(to_sub(q), ((0, 0),) * 3 + ((0, Lp - L), (0, 0))).reshape(B, dilation, H, n_blk, W, E)
    kv_pad = ((0, 0),) * 3 + ((W, Lp - L), (0, 0))

    def band(t):
        t = jnp.pad(to_sub(t), kv_pad)
        prev = t[:, :, :, :Lp].reshape(B, dilation, H, n_blk, W, E)
        cur = t[:, :, :, W:].reshape(B, dilation, H, n_blk, W, E)
        return jnp.concatenate([prev, cur], axis=4)

    kb, vb = band(k), band(v)
    qi = jnp.arange(W)[:, None]
    kj = jnp.arange(2 * W)[None, :]
    rel = qi + W - kj
    key_pos = (jnp.arange(n_blk) * W - W)[:, None, None] + kj[None]
    valid = (rel >= 0)[None] & (rel <= W)[None] & (key_pos >= 0)
    bias = bias_table[t5_causal_bucket(jnp.clip(rel, 0, W) * dilation)]
    bias = jnp.transpose(bias, (2, 0, 1)).astype(jnp.float32)[:, None]
    s = jnp.einsum('bdhnqe,bdhnke->bdhnqk', qb, kb).astype(jnp.float32) * (E ** -0.5) + bias
    s = jnp.where(valid, s, NEG_INF)
    lse = jax.nn.logsumexp(s, axis=-1)
    p = jnp.exp(s - lse[..., None])
    o = jnp.einsum('bdhnqk,bdhnke->bdhnqe', p.astype(v.dtype), vb)

    def from_sub(t):
        t = t.reshape((B, dilation, H, Lp) + t.shape[5:])[:, :, :, :L]
        t = jnp.moveaxis(t, 3, 1)
        return t.reshape((B, S, H) + t.shape[4:])

    return from_sub(o), from_sub(lse)

def wkv7_scan(r, decay, k, v, kk, a):
    B, S, H, N = r.shape

    def step(state, inp):
        r_t, w_t, k_t, v_t, kk_t, b_t = inp
        sa = jnp.einsum('bhvk,bhk->bhv', state, -kk_t)
        state = (state * w_t[:, :, None, :] + sa[..., None] * b_t[:, :, None, :]
                 + v_t[..., None] * k_t[:, :, None, :])
        return state, jnp.einsum('bhvk,bhk->bhv', state, r_t)

    xs = tuple(jnp.moveaxis(t, 1, 0) for t in (r, decay, k, v, kk, kk * a))
    _, out = lax.scan(step, jnp.zeros((B, H, N, N), jnp.float32), xs)
    return jnp.moveaxis(out, 0, 1)

def rwkv7_time_mix(p, shift_mu, w0, w_up, a0, a_up, g_up, k_k, k_a, r_k, ln_w, ln_b, w_rwkv_out):
    B, S, _ = p.shape
    H, N, C = RWKV_HEADS, RWKV_HEAD_DIM, RWKV_WIDTH
    pf = p.astype(jnp.float32)
    prev = jnp.pad(pf, ((0, 0), (1, 0), (0, 0)))[:, :-1]
    pm = pf + (prev - pf) * shift_mu
    r, k, v, xw, xa, xg = jnp.split(pm, [C, 2 * C, 3 * C, 3 * C + DECAY_LORA,
                                          3 * C + DECAY_LORA + ICLR_LORA], axis=-1)
    w_log = -jax.nn.softplus(-(w0 + jnp.tanh(xw) @ w_up)) - 0.5
    decay = jnp.exp(-jnp.exp(w_log))
    a = jax.nn.sigmoid(a0 + xa @ a_up)
    g = jax.nn.sigmoid(xg) @ g_up
    hd = lambda t: t.reshape(B, S, H, N)
    kk = hd(k * k_k)
    kk = kk / jnp.maximum(jnp.sqrt(jnp.sum(kk * kk, axis=-1, keepdims=True)), 1e-12)
    k = k * (1.0 + (a - 1.0) * k_a)
    o = wkv7_scan(hd(r), hd(decay), hd(k), hd(v), kk, hd(a))
    mu = jnp.mean(o, axis=-1, keepdims=True)
    var = jnp.mean(jnp.square(o - mu), axis=-1, keepdims=True)
    o = ((o - mu) * lax.rsqrt(var + GN_EPS)).reshape(B, S, C) * ln_w + ln_b
    bonus = jnp.sum(hd(r) * hd(k) * r_k, axis=-1, keepdims=True) * hd(v)
    o = (o + bonus.reshape(B, S, C)) * g
    return o.astype(p.dtype) @ w_rwkv_out

def hierarchical_moe(h, w_group_router, b_group_router, w_expert_router, b_expert_router,
                     w_expert_gate, w_expert_up, w_expert_down):
    B, S, D = h.shape
    T = B * S
    hf = h.reshape(T, D)
    grp_prob = jax.nn.softmax((hf @ w_group_router).astype(jnp.float32) + b_group_router, axis=-1)
    grp_p, grp_idx = lax.top_k(grp_prob, 1)
    exp_logits = ((hf @ w_expert_router).astype(jnp.float32) + b_expert_router).reshape(
        T, N_EXPERT_GROUPS, EXPERTS_PER_GROUP)
    sel_logits = jnp.take_along_axis(exp_logits, grp_idx[:, :, None], axis=1)[:, 0]
    top_p, top_i = lax.top_k(jax.nn.softmax(sel_logits, axis=-1), TOP_K)
    gates = grp_p * top_p / jnp.sum(top_p, axis=-1, keepdims=True)
    expert_id = grp_idx * EXPERTS_PER_GROUP + top_i

    A = T * TOP_K
    eid = expert_id.reshape(A).astype(jnp.int32)
    tok = jnp.arange(A, dtype=jnp.int32) // TOP_K
    gate = gates.reshape(A)
    order = jnp.argsort(eid)
    se = eid[order]
    counts = jnp.bincount(eid, length=N_EXPERTS)
    starts = jnp.cumsum(counts) - counts
    pcounts = (counts + ROW_BLOCK - 1) // ROW_BLOCK * ROW_BLOCK
    pends = jnp.cumsum(pcounts)
    pstarts = pends - pcounts
    dest = pstarts[se] + jnp.arange(A, dtype=jnp.int32) - starts[se]
    n_blocks = -(-A // ROW_BLOCK) + N_EXPERTS
    n_rows = n_blocks * ROW_BLOCK
    row_tok = jnp.full((n_rows,), T, jnp.int32).at[dest].set(tok[order])
    row_gate = jnp.zeros((n_rows,), jnp.float32).at[dest].set(gate[order])
    blk_expert = jnp.minimum(jnp.searchsorted(pends, jnp.arange(n_blocks) * ROW_BLOCK, side='right'),
                             N_EXPERTS - 1)
    h_pad = jnp.concatenate([hf, jnp.zeros((1, D), hf.dtype)], axis=0)
    xin = h_pad[row_tok].reshape(n_blocks, ROW_BLOCK, D)

    def expert_block(args):
        xb, e = args
        hid = jax.nn.silu(xb @ w_expert_gate[e]) * (xb @ w_expert_up[e])
        return hid @ w_expert_down[e]

    yb = lax.map(expert_block, (xin, blk_expert)).reshape(n_rows, D)
    y = jax.ops.segment_sum(yb.astype(jnp.float32) * row_gate[:, None], row_tok, num_segments=T + 1)[:T]
    return y.reshape(B, S, D).astype(h.dtype)

def hybrid_layer(x, norm1_gain, w_in, q_norm_gain, k_norm_gain, rel_bias_table, w_att_out,
                 shift_mu, w0, w_up, a0, a_up, g_up, k_k, k_a, r_k, ln_w, ln_b, w_rwkv_out,
                 w_out, norm2_gain, w_group_router, b_group_router, w_expert_router,
                 b_expert_router, w_expert_gate, w_expert_up, w_expert_down):
    B, S, D = x.shape
    h = rms_norm(x, norm1_gain)
    p = h @ w_in
    q, k, v, p_rwkv, p_gate = jnp.split(
        p, [ATT_WIDTH, 2 * ATT_WIDTH, 3 * ATT_WIDTH, 3 * ATT_WIDTH + RWKV_SHIFT_WIDTH], axis=-1)

    heads = lambda t: t.reshape(B, S, N_ATT_GROUPS, HEADS_PER_GROUP, HEAD_DIM)
    q = rms_norm(heads(q), q_norm_gain[:, None, :])
    k = rms_norm(heads(k), k_norm_gain[:, None, :])
    v = heads(v)
    outs, lses = [], []
    for g, (win, dil) in enumerate(ATT_PATTERNS):
        o_g, l_g = dilated_window_attention(
            q[:, :, g], k[:, :, g], v[:, :, g],
            rel_bias_table[:, g * HEADS_PER_GROUP:(g + 1) * HEADS_PER_GROUP], win, dil)
        outs.append(o_g)
        lses.append(l_g)
    wts = jax.nn.softmax(jnp.stack(lses, axis=0), axis=0)
    att = jnp.einsum('gbsh,gbshe->bshe', wts, jnp.stack(outs, axis=0).astype(jnp.float32))
    y_att = att.reshape(B, S, ATT_OUT_WIDTH).astype(x.dtype) @ w_att_out

    y_rwkv = rwkv7_time_mix(p_rwkv, shift_mu, w0, w_up, a0, a_up, g_up, k_k, k_a, r_k,
                            ln_w, ln_b, w_rwkv_out)

    gates = jax.nn.sigmoid(p_gate.astype(jnp.float32)).astype(x.dtype)
    mixed = gates[..., :D] * y_att + gates[..., D:] * y_rwkv
    x = x + mixed @ w_out

    x = x + hierarchical_moe(rms_norm(x, norm2_gain), w_group_router, b_group_router,
                             w_expert_router, b_expert_router, w_expert_gate, w_expert_up,
                             w_expert_down)
    return x

def first_inputs(seed: int = 0) -> dict:
    key = jax.random.key(seed)
    ks = jax.random.split(key, 28)
    f32 = jnp.float32
    L, D = DEPTH, D_MODEL
    nrm = lambda k, shape, scale: scale * jax.random.normal(k, shape, f32)
    return {
        'x': nrm(ks[0], (BATCH, SEQ, D), 1.0),
        'norm1_gain': 1.0 + nrm(ks[1], (L, D), 0.05),
        'w_in': nrm(ks[2], (L, D, IN_WIDTH), D ** -0.5),
        'q_norm_gain': 1.0 + nrm(ks[3], (L, N_ATT_GROUPS, HEAD_DIM), 0.05),
        'k_norm_gain': 1.0 + nrm(ks[4], (L, N_ATT_GROUPS, HEAD_DIM), 0.05),
        'rel_bias_table': nrm(ks[5], (REL_BUCKETS, ATT_HEADS), 0.5),
        'w_att_out': nrm(ks[6], (L, ATT_OUT_WIDTH, D), ATT_OUT_WIDTH ** -0.5),
        'rwkv_shift_mu': jax.random.uniform(ks[7], (L, RWKV_SHIFT_WIDTH), f32),
        'rwkv_w0': jax.random.uniform(ks[8], (L, RWKV_WIDTH), f32, -6.0, 1.0),
        'rwkv_w_up': nrm(ks[9], (L, DECAY_LORA, RWKV_WIDTH), 0.5 * DECAY_LORA ** -0.5),
        'rwkv_a0': nrm(ks[10], (L, RWKV_WIDTH), 0.1),
        'rwkv_a_up': nrm(ks[11], (L, ICLR_LORA, RWKV_WIDTH), ICLR_LORA ** -0.5),
        'rwkv_g_up': nrm(ks[12], (L, GATE_LORA, RWKV_WIDTH), GATE_LORA ** -0.5),
        'rwkv_k_k': 0.85 + nrm(ks[13], (L, RWKV_WIDTH), 0.05),
        'rwkv_k_a': 1.0 + nrm(ks[14], (L, RWKV_WIDTH), 0.05),
        'rwkv_r_k': nrm(ks[15], (L, RWKV_HEADS, RWKV_HEAD_DIM), 0.1),
        'rwkv_ln_w': 1.0 + nrm(ks[16], (L, RWKV_WIDTH), 0.05),
        'rwkv_ln_b': nrm(ks[17], (L, RWKV_WIDTH), 0.01),
        'w_rwkv_out': nrm(ks[18], (L, RWKV_WIDTH, D), RWKV_WIDTH ** -0.5),
        'w_out': nrm(ks[19], (L, D, D), D ** -0.5),
        'norm2_gain': 1.0 + nrm(ks[20], (L, D), 0.05),
        'w_group_router': nrm(ks[21], (L, D, N_EXPERT_GROUPS), D ** -0.5),
        'b_group_router': nrm(ks[22], (L, N_EXPERT_GROUPS), 0.01),
        'w_expert_router': nrm(ks[23], (L, D, N_EXPERTS), D ** -0.5),
        'b_expert_router': nrm(ks[24], (L, N_EXPERTS), 0.01),
        'w_expert_gate': nrm(ks[25], (L, N_EXPERTS, D, D_EXPERT), D ** -0.5),
        'w_expert_up': nrm(ks[26], (L, N_EXPERTS, D, D_EXPERT), D ** -0.5),
        'w_expert_down': nrm(ks[27], (L, N_EXPERTS, D_EXPERT, D), D_EXPERT ** -0.5),
    }

def first_block(x, norm1_gain, w_in, q_norm_gain, k_norm_gain, rel_bias_table, w_att_out,
              rwkv_shift_mu, rwkv_w0, rwkv_w_up, rwkv_a0, rwkv_a_up, rwkv_g_up, rwkv_k_k,
              rwkv_k_a, rwkv_r_k, rwkv_ln_w, rwkv_ln_b, w_rwkv_out, w_out, norm2_gain,
              w_group_router, b_group_router, w_expert_router, b_expert_router,
              w_expert_gate, w_expert_up, w_expert_down):
    for l in range(DEPTH):
        x = hybrid_layer(x, norm1_gain[l], w_in[l], q_norm_gain[l], k_norm_gain[l], rel_bias_table,
                         w_att_out[l], rwkv_shift_mu[l], rwkv_w0[l], rwkv_w_up[l], rwkv_a0[l],
                         rwkv_a_up[l], rwkv_g_up[l], rwkv_k_k[l], rwkv_k_a[l], rwkv_r_k[l],
                         rwkv_ln_w[l], rwkv_ln_b[l], w_rwkv_out[l], w_out[l], norm2_gain[l],
                         w_group_router[l], b_group_router[l], w_expert_router[l],
                         b_expert_router[l], w_expert_gate[l], w_expert_up[l], w_expert_down[l])
    return x


DEPTH_2 = 2

D_MIX = D_MODEL
N_GROUPS = 4
GROUP_WIDTH = D_MIX // N_GROUPS
N_HEADS_GROUP = GROUP_WIDTH // HEAD_DIM
CONF_KERNEL = 31
SHORT_KERNEL = 3
FFN_KERNEL = 3
D_FF = 2816
BLOCK_Q = 128
RET_CHUNK = 128
ROPE_BASE = 10000.0
N_IN_SLICES = 12
D_IN = N_IN_SLICES * GROUP_WIDTH


def rms_norm_2(x, g):
    xf = x.astype(jnp.float32)
    y = xf * lax.rsqrt(jnp.mean(xf * xf, axis=-1, keepdims=True) + NORM_EPS)
    return (y * g.astype(jnp.float32)).astype(x.dtype)

def layer_norm(x, g, b):
    xf = x.astype(jnp.float32)
    mu = jnp.mean(xf, axis=-1, keepdims=True)
    xc = xf - mu
    y = xc * lax.rsqrt(jnp.mean(xc * xc, axis=-1, keepdims=True) + NORM_EPS)
    return (y * g.astype(jnp.float32) + b.astype(jnp.float32)).astype(x.dtype)

def causal_dwconv(x, w):
    k_w, c = w.shape
    return lax.conv_general_dilated(
        x, w[:, None, :].astype(x.dtype), window_strides=(1,), padding=[(k_w - 1, 0)],
        dimension_numbers=('NWC', 'WIO', 'NWC'), feature_group_count=c)

def split_heads(x):
    b, t, _ = x.shape
    return x.reshape(b, t, -1, HEAD_DIM).transpose(0, 2, 1, 3)

def merge_heads(x):
    b, h, t, d = x.shape
    return x.transpose(0, 2, 1, 3).reshape(b, t, h * d)

def rotary(x, pos):
    d = x.shape[-1]
    half = d // 2
    inv_freq = ROPE_BASE ** (-jnp.arange(0, d, 2, dtype=jnp.float32) / d)
    ang = pos.astype(jnp.float32)[:, None] * inv_freq[None, :]
    cos, sin = jnp.cos(ang), jnp.sin(ang)
    xf = x.astype(jnp.float32)
    x1, x2 = xf[..., :half], xf[..., half:]
    return jnp.concatenate([x1 * cos - x2 * sin, x2 * cos + x1 * sin], axis=-1)

def conformer_conv(a, gate, dw_w, dw_b, ln_g, ln_b):
    h = a * jax.nn.sigmoid(gate)
    h = causal_dwconv(h, dw_w) + dw_b.astype(h.dtype)
    return jax.nn.silu(layer_norm(h, ln_g, ln_b))

def stick_breaking_attention(q, k, v):
    b, h, t, d = q.shape
    n_blocks = t // BLOCK_Q
    scale = d ** -0.5
    kf = k.astype(jnp.float32)
    key_pos = jnp.arange(t)
    qb = q.reshape(b, h, n_blocks, BLOCK_Q, d).transpose(2, 0, 1, 3, 4)

    def block(args):
        qi, i = args
        z = jnp.einsum('bhqd,bhkd->bhqk', qi.astype(jnp.float32), kf) * scale
        q_pos = i * BLOCK_Q + jnp.arange(BLOCK_Q)
        mask = key_pos[None, :] < q_pos[:, None]
        log_1m_beta = jnp.where(mask, -jax.nn.softplus(z), 0.0)
        tail = lax.cumsum(log_1m_beta, axis=3, reverse=True) - log_1m_beta
        attn = jnp.where(mask, jnp.exp(jax.nn.log_sigmoid(z) + tail), 0.0)
        return jnp.einsum('bhqk,bhkd->bhqd', attn.astype(v.dtype), v)

    out = lax.map(block, (qb, jnp.arange(n_blocks)))
    return out.transpose(1, 2, 0, 3, 4).reshape(b, h, t, d)

def retention_chunkwise(q, k, v):
    b, h, t, d = q.shape
    n_chunks = t // RET_CHUNK
    log_gamma = jnp.log1p(-jnp.exp2(-5.0 - jnp.arange(h, dtype=jnp.float32)))
    idx = jnp.arange(RET_CHUNK, dtype=jnp.float32)
    diff = idx[:, None] - idx[None, :]
    causal = diff >= 0
    d_intra = jnp.where(causal[None], jnp.exp(jnp.where(causal, diff, 0.0)[None] * log_gamma[:, None, None]), 0.0)
    q_decay = jnp.exp((idx[None, :] + 1.0) * log_gamma[:, None])
    k_decay = jnp.exp((RET_CHUNK - 1.0 - idx[None, :]) * log_gamma[:, None])
    chunk_decay = jnp.exp(RET_CHUNK * log_gamma)
    k = k * (d ** -0.5)

    def to_chunks(z):
        return z.reshape(b, h, n_chunks, RET_CHUNK, d).transpose(2, 0, 1, 3, 4)

    def step(state, inp):
        qc, kc, vc = inp
        inner = jnp.einsum('bhqd,bhkd->bhqk', qc, kc) * d_intra
        o = jnp.einsum('bhqk,bhkd->bhqd', inner, vc) + jnp.einsum('bhqd,bhde->bhqe', qc, state) * q_decay[..., None]
        state = state * chunk_decay[:, None, None] + jnp.einsum('bhkd,bhke->bhde', kc * k_decay[..., None], vc)
        return state, o

    state0 = jnp.zeros((b, h, d, d), jnp.float32)
    _, out = lax.scan(step, state0, (to_chunks(q), to_chunks(k), to_chunks(v)))
    return out.transpose(1, 2, 0, 3, 4).reshape(b, h, t, d)

def retention_mixer(q, k, v, g, norm_g):
    t = q.shape[1]
    pos = jnp.arange(t)
    qh = rotary(split_heads(q), pos)
    kh = rotary(split_heads(k), pos)
    vh = split_heads(v).astype(jnp.float32)
    o = retention_chunkwise(qh, kh, vh)
    mu = jnp.mean(o, axis=-1, keepdims=True)
    oc = o - mu
    o = oc * lax.rsqrt(jnp.mean(oc * oc, axis=-1, keepdims=True) + NORM_EPS)
    y = merge_heads(o) * norm_g.astype(jnp.float32)
    return (jax.nn.silu(g.astype(jnp.float32)) * y).astype(q.dtype)

def short_gated_conv(b_gate, c_gate, h, conv_w):
    return b_gate * causal_dwconv(c_gate * h, conv_w)

def conv_ffn(x, w_up, w_conv, w_down):
    h = causal_dwconv(x @ w_up, w_conv)
    gate, up = jnp.split(h, 2, axis=-1)
    return (jax.nn.silu(gate) * up) @ w_down

def second_inputs(seed: int = 0) -> dict:
    key = jax.random.key(seed)
    ks = jax.random.split(key, 16)
    f32 = jnp.float32

    def nrm(k, shape, scale):
        return jax.random.normal(k, shape, f32) * scale

    def gain(k, shape):
        return 1.0 + 0.05 * jax.random.normal(k, shape, f32)

    return {
        'x': nrm(ks[0], (BATCH, SEQ, D_MODEL), 1.0),
        'norm_mix_pre': gain(ks[1], (DEPTH_2, D_MODEL)),
        'norm_mix_post': gain(ks[2], (DEPTH_2, D_MODEL)),
        'norm_ffn_pre': gain(ks[3], (DEPTH_2, D_MODEL)),
        'norm_ffn_post': gain(ks[4], (DEPTH_2, D_MODEL)),
        'w_in': nrm(ks[5], (DEPTH_2, D_MODEL, D_IN), D_MODEL ** -0.5),
        'conf_dw_w': nrm(ks[6], (DEPTH_2, CONF_KERNEL, GROUP_WIDTH), CONF_KERNEL ** -0.5),
        'conf_dw_b': nrm(ks[7], (DEPTH_2, GROUP_WIDTH), 0.02),
        'conf_ln_g': gain(ks[8], (DEPTH_2, GROUP_WIDTH)),
        'conf_ln_b': nrm(ks[9], (DEPTH_2, GROUP_WIDTH), 0.02),
        'ret_norm_g': gain(ks[10], (DEPTH_2, GROUP_WIDTH)),
        'sc_conv_w': nrm(ks[11], (DEPTH_2, SHORT_KERNEL, GROUP_WIDTH), SHORT_KERNEL ** -0.5),
        'w_out': nrm(ks[12], (DEPTH_2, D_MIX, D_MODEL), D_MIX ** -0.5),
        'ffn_up': nrm(ks[13], (DEPTH_2, D_MODEL, 2 * D_FF), D_MODEL ** -0.5),
        'ffn_conv_w': nrm(ks[14], (DEPTH_2, FFN_KERNEL, 2 * D_FF), FFN_KERNEL ** -0.5),
        'ffn_down': nrm(ks[15], (DEPTH_2, D_FF, D_MODEL), D_FF ** -0.5),
    }

def second_block(x, norm_mix_pre, norm_mix_post, norm_ffn_pre, norm_ffn_post, w_in,
              conf_dw_w, conf_dw_b, conf_ln_g, conf_ln_b, ret_norm_g, sc_conv_w,
              w_out, ffn_up, ffn_conv_w, ffn_down):
    for l in range(DEPTH_2):
        h = rms_norm_2(x, norm_mix_pre[l])
        proj = h @ w_in[l]
        (c_a, c_gate, sb_q, sb_k, sb_v, r_q, r_k, r_v, r_g,
         sc_b, sc_c, sc_h) = jnp.split(proj, N_IN_SLICES, axis=-1)
        y_conf = conformer_conv(c_a, c_gate, conf_dw_w[l], conf_dw_b[l], conf_ln_g[l], conf_ln_b[l])
        y_sb = merge_heads(stick_breaking_attention(split_heads(sb_q), split_heads(sb_k), split_heads(sb_v)))
        y_ret = retention_mixer(r_q, r_k, r_v, r_g, ret_norm_g[l])
        y_sc = short_gated_conv(sc_b, sc_c, sc_h, sc_conv_w[l])
        mix = jnp.concatenate([y_conf, y_sb, y_ret, y_sc], axis=-1) @ w_out[l]
        x = x + rms_norm_2(mix, norm_mix_post[l])
        f = conv_ffn(rms_norm_2(x, norm_ffn_pre[l]), ffn_up[l], ffn_conv_w[l], ffn_down[l])
        x = x + rms_norm_2(f, norm_ffn_post[l])
    return x


def setup_inputs(seed=0):
    out = dict(first_inputs(seed))
    for name, value in second_inputs(seed + 1).items():
        if name != "x":
            out[name + "_2"] = value
    return out


def reference(
    x, norm1_gain, w_in, q_norm_gain, k_norm_gain, rel_bias_table, w_att_out, rwkv_shift_mu,
    rwkv_w0, rwkv_w_up, rwkv_a0, rwkv_a_up, rwkv_g_up, rwkv_k_k, rwkv_k_a, rwkv_r_k, rwkv_ln_w,
    rwkv_ln_b, w_rwkv_out, w_out, norm2_gain, w_group_router, b_group_router, w_expert_router,
    b_expert_router, w_expert_gate, w_expert_up, w_expert_down, norm_mix_pre_2, norm_mix_post_2,
    norm_ffn_pre_2, norm_ffn_post_2, w_in_2, conf_dw_w_2, conf_dw_b_2, conf_ln_g_2, conf_ln_b_2,
    ret_norm_g_2, sc_conv_w_2, w_out_2, ffn_up_2, ffn_conv_w_2, ffn_down_2,
):
    x = first_block(
        x, norm1_gain, w_in, q_norm_gain, k_norm_gain, rel_bias_table, w_att_out, rwkv_shift_mu,
        rwkv_w0, rwkv_w_up, rwkv_a0, rwkv_a_up, rwkv_g_up, rwkv_k_k, rwkv_k_a, rwkv_r_k,
        rwkv_ln_w, rwkv_ln_b, w_rwkv_out, w_out, norm2_gain, w_group_router, b_group_router,
        w_expert_router, b_expert_router, w_expert_gate, w_expert_up, w_expert_down,
    )
    return second_block(
        x, norm_mix_pre_2, norm_mix_post_2, norm_ffn_pre_2, norm_ffn_post_2, w_in_2,
        conf_dw_w_2, conf_dw_b_2, conf_ln_g_2, conf_ln_b_2, ret_norm_g_2, sc_conv_w_2, w_out_2,
        ffn_up_2, ffn_conv_w_2, ffn_down_2,
    )


_drawn_inputs = setup_inputs


def setup_inputs(seed=0):
    import zlib

    import numpy as np

    out = dict(_drawn_inputs(seed))
    spreads = {}
    factors = {'rwkv_ln_b': 3.449, 'b_expert_router': 2.835, 'conf_dw_b_2': 2.773, 'conf_ln_b_2': 6.32}
    for name, (base, spread) in spreads.items():
        noise = np.random.default_rng([zlib.crc32(name.encode()), seed]).standard_normal(out[name].shape)
        drawn = base * np.exp(spread * noise) if base else spread * noise
        out[name] = jnp.asarray(drawn.astype(out[name].dtype))
    for name, factor in factors.items():
        out[name] = (out[name] * factor).astype(out[name].dtype)
    return out
```

```python
import math
from contextlib import ExitStack


import numpy as np

import concourse.bass as bass
from concourse import mybir



class Shared:
    pass


ALU = mybir.AluOpType
ACT = mybir.ActivationFunctionType
AX = mybir.AxisListType.X
F32 = mybir.dt.float32
I32 = mybir.dt.int32

P = 128
SEQ = 256
TT = SEQ // P
D = 1024
KC = D // P
NEG = -1e30
EPS = 1e-6
GN_EPS = 64e-5
HEAD = 64
ATT_HEADS = 12
DILATIONS = (1, 4, 16)
WINDOW = 128
LORA_CHUNK = 12
RW = 512
N_EXP = 32
D_EXP = 512
SLOTS = 64
OVER = 8
SUB = 64
LEAF = 8
BIAS_W = 384
DFF = 2816
GATE_COL = 3 * 768 + 1824
BANKS = 8



def bucket_of(dist):
    d = np.maximum(dist.astype(np.float32), np.float32(1.0))
    large = 16 + (np.log(d / np.float32(16)) / np.float32(math.log(2048 / 16)) * np.float32(16)).astype(np.int32)
    return np.where(dist < 16, dist, np.minimum(large, 31))


def constants():
    s, t = np.arange(P)[:, None], np.arange(P)[None, :]
    same = s // SUB == t // SUB
    leaf = s // LEAF == t // LEAF
    f = {}
    f["ident"] = (s == t)
    f["ones"] = np.ones((P, P))
    f["pair_ones"] = (s // HEAD == t // HEAD)
    strict, incl = same & (s < t), same & (s <= t)
    f["quad_mask"] = np.concatenate([leaf & (s < t), incl, strict, incl], axis=1)
    f["leaf_low"] = leaf & (s > t)
    f["rest_low"] = same & ~leaf & (s > t)
    decay = -math.exp(-0.5)
    f["cumulate"] = decay * np.concatenate([incl, strict], axis=1)
    f["half_rows"] = np.concatenate([s < SUB, s >= SUB], axis=1)
    f["before"] = (s < t)
    f["slot_iota"] = np.broadcast_to(np.arange(SLOTS)[None, :], (P, SLOTS))
    f["first_pick"] = np.broadcast_to(N_EXP - np.arange(N_EXP)[None, :], (P, N_EXP))
    f["over_iota"] = np.broadcast_to(np.arange(OVER)[None, :], (P, OVER))
    f["over_slots"] = np.broadcast_to(np.arange(OVER * SLOTS)[None, :], (P, OVER * SLOTS))
    f["eps"] = np.full((P, 1), EPS)
    f["gn_eps"] = np.full((P, 1), GN_EPS)
    swap = np.zeros((P, P))
    for m in range(P):
        r = m % HEAD
        if r < 32:
            swap[m + 32, m] = -1.0
        else:
            swap[m - 32, m] = 1.0
    f["swap"] = swap
    inv = (10000.0 ** (-np.arange(0, HEAD, 2, dtype=np.float32) / np.float32(HEAD))).astype(np.float32)
    ang = (np.arange(SEQ, dtype=np.float32)[None, :] * inv[np.arange(P) % 32][:, None]).astype(np.float32)
    f["cos"] = np.cos(ang)
    f["sin"] = np.sin(ang)
    j, i = np.arange(P)[:, None], np.arange(SEQ)[None, :]
    ret = []
    for h in range(4):
        lg = math.log1p(-(2.0 ** (-5.0 - h)))
        ret.append(np.where(i >= j, np.exp(np.where(i >= j, i - j, 0) * lg), 0.0) * HEAD ** -0.5)
    f["retain"] = np.concatenate(ret, axis=1)
    f["past"] = np.concatenate([j < i, (j < i)[:, 0:P]], axis=1)
    f["past_neg"] = np.where(f["past"], 0.0, NEG)
    f["down"] = (s >= t)
    at, cols, w = {}, [], 0
    for name, a in f.items():
        at[name] = (w, a.shape[1])
        cols.append(np.asarray(a, np.float32))
        w += a.shape[1]
    return np.ascontiguousarray(np.concatenate(cols, axis=1)), at


def bias_rows():
    out = np.zeros((35, BIAS_W + ATT_HEADS), np.float32)
    u = np.arange(BIAS_W)
    dist = 255 - u
    b = bucket_of(np.maximum(dist, 0))
    for row in range(32):
        out[row, :BIAS_W] = (b == row) & (dist >= 0)
    for g, dil in enumerate(DILATIONS):
        ok = (dist >= 0) & (dist % dil == 0) & (dist // dil <= WINDOW)
        out[32 + g, :BIAS_W] = np.where(ok, 0.0, NEG)
        out[32 + g, BIAS_W + 4 * g:BIAS_W + 4 * g + 4] = 1.0
    return out


CONST, CONST_AT = constants()
BIAS_ROWS = bias_rows()

VEC = {}
_row = 0
for _name, _n in (("norm1_gain", 8), ("norm2_gain", 8), ("rwkv_shift_mu", 15), ("rwkv_a0", 4), ("rwkv_k_k", 4),
                  ("rwkv_k_a", 4), ("rwkv_r_k", 4), ("rwkv_ln_w", 4), ("rwkv_ln_b", 4),
                  ("q_norm_gain", 3), ("k_norm_gain", 3)):
    VEC[_name] = _row
    _row += _n
VEC_ROWS = _row
VEC2 = {}
_row = 0
for _name, _n in (("norm_mix_pre_2", 8), ("norm_mix_post_2", 8), ("norm_ffn_pre_2", 8), ("norm_ffn_post_2", 8),
                  ("conf_dw_b_2", 2), ("conf_ln_g_2", 2), ("conf_ln_b_2", 2), ("ret_norm_g_2", 2),
                  ("sc_conv_w_2", 6), ("conf_dw_w_2", 62)):
    VEC2[_name] = _row
    _row += _n
VEC2_ROWS = _row


def clear_bank_semaphores(nc, m):
    ids = sorted(s.num for s in m.filled + m.drained)
    assert ids == list(range(ids[0], ids[0] + len(ids)))
    with nc.Block() as block:
        @block.gpsimd
        def _(pool):
            pool.sem_clear(range(ids[0], ids[-1] + 1))


def project_part(nc, m, a):
    UNITS = 17
    RING = 6
    with ExitStack() as ctx:
        def sem(n):
            return ctx.enter_context(nc.semaphore(n))
        w_ring = ctx.enter_context(nc.sbuf_tensor("w_ring", [P, RING, KC, 256], F32))
        x_tok = ctx.enter_context(nc.sbuf_tensor("x_tok", [P, TT, D], F32))
        square = ctx.enter_context(nc.sbuf_tensor("square", [P, KC, SEQ], F32))
        log_ms = ctx.enter_context(nc.sbuf_tensor("log_ms", [P, SEQ], F32))
        rstd = ctx.enter_context(nc.sbuf_tensor("rstd", [P, SEQ], F32))
        vec_rows = ctx.enter_context(nc.sbuf_tensor("vec_rows", [P, P], F32))
        table = ctx.enter_context(nc.sbuf_tensor("table", [35, ATT_HEADS], F32))
        bucket_rows = ctx.enter_context(nc.sbuf_tensor("bucket_rows", [35, BIAS_W], F32))
        table_wide = ctx.enter_context(nc.sbuf_tensor("table_wide", [35, ATT_HEADS, P], F32))
        strip = ctx.enter_context(nc.sbuf_tensor("strip", [P, ATT_HEADS, BIAS_W], F32))

        x_in, const_in, vec_in, table_in = sem("x_in"), sem("const_in"), sem("vec_in"), sem("table_in")
        w_landed = [sem(f"w_landed{i}") for i in range(RING)]
        filled, drained = m.filled, m.drained
        rows_zero, square_done, norm_log, rstd_done, h_done = (
            sem("rows_zero"), sem("square_done"), sem("norm_log"), sem("rstd_done"), sem("h_done"))
        pads_zero, wide_done, strip_out, bias_in = sem("pads_zero"), sem("wide_done"), sem("strip_out"), sem("bias_in")

        U_VEC, U_X, U_SS, U_W = 0, 1, 5, 6
        U_B = U_W + UNITS
        block = ctx.enter_context(nc.Block())

        @block.sync
        def _(sp):
            sp.dma_start(m.const[:, :], a["const"]).then_inc(const_in, 16)
            for t in range(TT):
                sp.dma_start(x_tok[:, t, :], a["x"][0, t * P:(t + 1) * P, :]).then_inc(x_in, 16)
            sp.dma_start(table[0:32, :], a["rel_bias_table"]).then_inc(table_in, 16)
            sp.dma_start(table[32:35, :], a["bias_rows"][32:35, BIAS_W:]).then_inc(table_in, 16)
            sp.dma_start(bucket_rows[:, :], a["bias_rows"][:, 0:BIAS_W]).then_inc(table_in, 16)
            for u in range(UNITS):
                n = 256 if u < 16 else 32
                if u >= RING:
                    q = U_W + u - RING
                    sp.wait_ge(filled[q % BANKS], q // BANKS + 1)
                sp.dma_start(w_ring[:, u % RING, :, 0:n],
                             a["w_in"][0].rearrange("(c p) n -> p c n", p=P)[:, :, 256 * u:256 * u + n]
                             ).then_inc(w_landed[u % RING], 16)
            for h in range(ATT_HEADS):
                q = U_B + h
                sp.wait_ge(drained[q % BANKS], q // BANKS + 1)
            sp.dma_start(m.strip_dram[:, :, :], strip[:, :, :]).then_inc(strip_out, 16)
            sp.wait_ge(strip_out, 16)
            sp.dma_start(m.bias[:, :, :], bass.AP(m.strip_dram, P - 1, [[ATT_HEADS * BIAS_W - 1, P],
                                                                        [BIAS_W, ATT_HEADS], [1, SEQ]])
                         ).then_inc(bias_in, 16)
            sp.wait_ge(bias_in, 16)

        @block.gpsimd
        def _(pool):
            pool.memset(m.w_up[:, :], 0.0)
            pool.memset(m.a_up[:, :], 0.0)
            pool.memset(m.g_up[:, :, :], 0.0)
            pool.memset(m.p_rwkv[:, 0:14, 0:1], 0.0)
            pool.memset(m.p_rwkv[:, 14, :], 0.0).then_inc(pads_zero, 1)

        @block.scalar
        def _(act):
            act.wait_ge(rows_zero, 1)
            n_vec = 0
            def row(name, dst_row, src, c0=0, c1=P):
                act.dma_start(vec_rows[dst_row:dst_row + src.shape[0], c0:c1], src).then_inc(vec_in, 16)
                return 1
            for name in ("norm1_gain", "norm2_gain", "rwkv_a0", "rwkv_k_k", "rwkv_k_a", "rwkv_ln_w", "rwkv_ln_b"):
                n_vec += row(name, VEC[name], a[name][0].rearrange("(c p) -> c p", p=P))
            n_vec += row("", VEC["rwkv_r_k"], a["rwkv_r_k"][0].rearrange("(c h) n -> c (h n)", h=2))
            mu = a["rwkv_shift_mu"]
            n_vec += row("", VEC["rwkv_shift_mu"], mu[0, 0:14 * P].rearrange("(c p) -> c p", p=P))
            n_vec += row("", VEC["rwkv_shift_mu"] + 14, mu[:, 14 * P:1824], 0, 32)
            for name in ("q_norm_gain", "k_norm_gain"):
                for half in range(2):
                    n_vec += row("", VEC[name], a[name][0], half * HEAD, half * HEAD + HEAD)
            assert n_vec == m.n_vec
            act.wait_ge(pads_zero, 1)
            act.dma_start(m.w_up[0:64, :], a["rwkv_w_up"][0]).then_inc(m.lora_in, 16)
            act.dma_start(m.w_up[64:65, :], a["rwkv_w0"]).then_inc(m.lora_in, 16)
            act.dma_start(m.a_up[64:128, :], a["rwkv_a_up"][0]).then_inc(m.lora_in, 16)
            act.dma_start(m.g_up[:, 0, :], a["rwkv_g_up"][0, 0:P, :]).then_inc(m.lora_in, 16)
            act.dma_start(m.g_up[0:32, 1, :], a["rwkv_g_up"][0, P:160, :]).then_inc(m.lora_in, 16)
            for b in range(4):
                act.wait_ge(drained[(U_X + b) % BANKS], (U_X + b) // BANKS + 1)
                act.activation(square[:, 2 * b:2 * b + 2, :], m.xT[:, 2 * b:2 * b + 2, :], ACT.Square
                               ).then_inc(square_done, 1)
            act.wait_ge(filled[U_SS], 1)
            act.activation(log_ms[:, :], m.ps[:, U_SS, 0:SEQ], ACT.Ln, bias=m.c("eps"), scale=1.0 / D
                           ).then_inc(drained[U_SS], 1)
            act.drain()
            act.activation(rstd[:, :], log_ms[:, :], ACT.Exp, scale=-0.5).then_inc(rstd_done, 1)
            for h in range(ATT_HEADS):
                q = U_B + h
                act.wait_ge(filled[q % BANKS], q // BANKS + 1)
                act.activation(strip[:, h, :], m.ps[:, q % BANKS, 0:BIAS_W], ACT.Copy).then_inc(drained[q % BANKS], 1)
            act.wait_ge(m.lora_in, 5 * 16)

        @block.tensor
        def _(pe):
            pe.wait_ge(const_in, 16)
            pe.wait_ge(vec_in, 16 * m.n_vec)
            pe.transpose(m.ps[:, U_VEC, 0:P], vec_rows[:, :], m.c("ident")).then_inc(filled[U_VEC], 1)
            pe.wait_ge(x_in, 32)
            for b in range(4):
                for c in (2 * b, 2 * b + 1):
                    for t in range(TT):
                        at = (c % 2) * SEQ + t * P
                        mm = pe.transpose(m.ps[:, U_X + b, at:at + P], x_tok[:, t, c * P:(c + 1) * P], m.c("ident"))
                mm.then_inc(filled[U_X + b], 1)
            for c in range(KC):
                if c % 2 == 0:
                    pe.wait_ge(square_done, c // 2 + 1)
                mm = pe.matmul(m.ps[:, U_SS, 0:SEQ], m.c("ones"), square[:, c, :], start=(c == 0), stop=(c == KC - 1))
            mm.then_inc(filled[U_SS], 1)
            for u in range(UNITS):
                q = U_W + u
                b = q % BANKS
                if q >= BANKS:
                    pe.wait_ge(drained[b], q // BANKS)
                pe.wait_ge(w_landed[u % RING], 16 * (u // RING + 1))
                w = w_ring[:, u % RING, :, :]
                if 6 <= u < 9:
                    for t in range(TT):
                        for k in range(KC):
                            if u == 6:
                                pe.wait_ge(h_done, KC)
                            mm = pe.matmul(m.ps[:, b, t * 256:t * 256 + 256], m.hT[:, k, t * P:(t + 1) * P],
                                           w[:, k, :], start=(k == 0), stop=(k == KC - 1))
                else:
                    halves = ((0, P), (P, P)) if u < 16 else ((0, 32),)
                    for j, (c0, n) in enumerate(halves):
                        for k in range(KC):
                            if u == 0 and j == 0:
                                pe.wait_ge(h_done, k + 1)
                            mm = pe.matmul(m.ps[0:n, b, j * SEQ:(j + 1) * SEQ], w[:, k, c0:c0 + n],
                                           m.hT[:, k, :], start=(k == 0), stop=(k == KC - 1))
                mm.then_inc(filled[b], 1)
            pe.wait_ge(wide_done, 1)
            for h in range(ATT_HEADS):
                q = U_B + h
                pe.wait_ge(drained[q % BANKS], q // BANKS)
                pe.matmul(m.ps[:, q % BANKS, 0:BIAS_W], table_wide[:, h, :], bucket_rows[:, :],
                          start=True, stop=True).then_inc(filled[q % BANKS], 1)

        @block.vector
        def _(dve):
            dve.memset(vec_rows[:, :], 0.0).then_inc(rows_zero, 1)
            dve.wait_ge(table_in, 48)
            dve.tensor_copy(table_wide[:, :, :],
                            table[:, :].rearrange("p (h o) -> p h o", o=1).to_broadcast([35, ATT_HEADS, P])
                            ).then_inc(wide_done, 1)
            dve.wait_ge(filled[U_VEC], 1)
            dve.tensor_copy(m.vec[:, :], m.ps[:, U_VEC, 0:P]).then_inc(drained[U_VEC], 1)
            for b in range(4):
                dve.wait_ge(filled[U_X + b], 1)
                dve.tensor_copy(m.xT[:, 2 * b:2 * b + 2, :],
                                m.ps[:, U_X + b, :].rearrange("p (c t) -> p c t", c=2)).then_inc(drained[U_X + b], 1)
            dve.wait_ge(rstd_done, 1)
            dve.wait_ge(drained[U_VEC], 1)
            dve.wait_ge(drained[U_X + 3], 1)
            for c in range(KC):
                dve.scalar_tensor_tensor(m.hT[:, c, :], m.xT[:, c, :], m.v("norm1_gain", c), rstd[:, :],
                                         ALU.mult, ALU.mult).then_inc(h_done, 1)
            dve.wait_ge(pads_zero, 1)
            for u in range(UNITS):
                q = U_W + u
                b = q % BANKS
                dve.wait_ge(filled[b], q // BANKS + 1)
                src = m.ps[:, b, :].rearrange("p (c t) -> p c t", c=2)
                if u < 6:
                    ins = dve.tensor_copy(m.qk[:, 2 * u:2 * u + 2, :], src)
                elif u < 9:
                    ins = dve.tensor_copy(m.v_att[:, :, (u - 6) * 256:(u - 5) * 256], src)
                elif u < 16:
                    c = 2 * (u - 9)
                    ins = dve.tensor_copy(m.p_rwkv[:, c:c + 2, 1:SEQ + 1], src)
                else:
                    ins = dve.tensor_copy(m.p_rwkv[0:32, 14, 1:SEQ + 1], m.ps[0:32, b, 0:SEQ])
                ins.then_inc(drained[b], 1)


def attention_part(nc, m, a):
    H = 4
    with ExitStack() as ctx:
        def sem(n):
            return ctx.enter_context(nc.semaphore(n))

        def sb(n, s):
            return ctx.enter_context(nc.sbuf_tensor(n, s, F32))
        square = sb("att_square", [P, 12, SEQ])
        log_ms = sb("att_log", [P, 12, SEQ])
        rstd = sb("att_rstd", [P, 12, SEQ])
        prob = sb("prob", [P, 2, 9 * P])
        neg_max = sb("neg_max", [P, 8])
        row_sum = sb("row_sum", [P, 8])
        row_inv = sb("row_inv", [P, 8])
        prob_T = sb("prob_T", [P, 2, 9 * P])
        filled, drained = m.filled, m.drained
        square_done, log_done, rstd_done, normed = sem("a_square"), sem("a_log"), sem("a_rstd"), sem("a_normed")
        scored, maxed, exped, inv_done, probs_done = (
            sem("a_scored"), sem("a_maxed"), sem("a_exped"), sem("a_inv"), sem("a_probs"))
        U_SS, U_H = 0, 6

        def score_unit(h, j):
            return U_H + (0 if h == 0 else 3 + 8 * (h - 1)) + j

        def turn_unit(h, j):
            return U_H + 3 + 8 * h + (3 if h < H - 1 else 0) + j

        block = ctx.enter_context(nc.Block())

        @block.scalar
        def _(act):
            for u in range(6):
                act.activation(square[:, 2 * u:2 * u + 2, :], m.qk[:, 2 * u:2 * u + 2, :], ACT.Square
                               ).then_inc(square_done, 1)
            for u in range(6):
                act.wait_ge(filled[u], 1)
                act.activation(log_ms[:, 2 * u:2 * u + 2, :], m.ps[:, u, :].rearrange("p (c t) -> p c t", c=2),
                               ACT.Ln, bias=m.c("eps"), scale=1.0 / HEAD).then_inc(drained[u], 1)
            for u in range(6):
                act.wait_ge(drained[u], 1)
                act.activation(rstd[:, 2 * u:2 * u + 2, :], log_ms[:, 2 * u:2 * u + 2, :], ACT.Exp, scale=-0.5
                               ).then_inc(rstd_done, 1)
            for h in range(H):
                for t, (c0, n) in enumerate(((0, 3 * P), (3 * P, 6 * P))):
                    i = 2 * h + t
                    act.wait_ge(maxed, i + 1)
                    act.activation(prob[:, h % 2, c0:c0 + n], prob[:, h % 2, c0:c0 + n], ACT.Exp,
                                   bias=neg_max[:, i:i + 1], accum_out=row_sum[:, i:i + 1]).then_inc(exped, 1)
                for j in range(3):
                    q = turn_unit(h, j)
                    act.wait_ge(filled[q % BANKS], q // BANKS + 1)
                    at, n = ((0, 3 * P), (3 * P, 4 * P), (7 * P, 2 * P))[j]
                    act.activation(prob_T[:, h % 2, at:at + n], m.ps[:, q % BANKS, 0:n], ACT.Copy
                                   ).then_inc(drained[q % BANKS], 1)
                for t in range(2):
                    q = turn_unit(h, 3 + t)
                    r = (h % 2) * HEAD
                    act.wait_ge(filled[q % BANKS], q // BANKS + 1)
                    act.activation(m.att_T[r:r + HEAD, h // 2, t * P:(t + 1) * P], m.ps[r:r + HEAD, q % BANKS, 0:P],
                                   ACT.Copy).then_inc(drained[q % BANKS], 1)

        @block.tensor
        def _(pe):
            for u in range(6):
                pe.wait_ge(square_done, u + 1)
                pe.matmul(m.ps[:, u, :], m.c("pair_ones"), square[:, 2 * u:2 * u + 2, :], start=True, stop=True
                          ).then_inc(filled[u], 1)
            pe.wait_ge(normed, 12)

            def scores(h):
                r = (h % 2) * HEAD
                for j, (t, groups, keys) in enumerate(((0, (0, 1, 2), P), (1, (0, 1), SEQ), (1, (2,), SEQ))):
                    q = score_unit(h, j)
                    if q >= BANKS:
                        pe.wait_ge(drained[q % BANKS], q // BANKS)
                    for g in groups:
                        c = 2 * g + h // 2
                        at = (g - groups[0]) * keys
                        mm = pe.matmul(m.ps[:, q % BANKS, at:at + keys], m.qk[r:r + HEAD, c, t * P:(t + 1) * P],
                                       m.qk[r:r + HEAD, 6 + c, 0:keys], start=True, stop=True)
                    mm.then_inc(filled[q % BANKS], 1)

            def outputs(h):
                for j, (first, n) in enumerate(((0, 3), (3, 4), (7, 2))):
                    q = turn_unit(h, j)
                    pe.wait_ge(probs_done, 2 * h + (1 if j == 0 else 2))
                    pe.wait_ge(drained[q % BANKS], q // BANKS)
                    for i in range(n):
                        c = (first + i) * P
                        mm = pe.transpose(m.ps[:, q % BANKS, i * P:(i + 1) * P], prob[:, h % 2, c:c + P], m.c("ident"))
                    mm.then_inc(filled[q % BANKS], 1)
                r = (h % 2) * HEAD
                for t in range(2):
                    q = turn_unit(h, 3 + t)
                    for j in ((0,), (1, 2))[t]:
                        w = turn_unit(h, j)
                        pe.wait_ge(drained[w % BANKS], w // BANKS + 1)
                    pe.wait_ge(drained[q % BANKS], q // BANKS)
                    tiles = [(g, 0, g) for g in range(3)] if t == 0 else [(3 + 2 * g + k, k, g) for g in range(3) for k in range(2)]
                    for n, (tile, k, g) in enumerate(tiles):
                        col = (4 * g + h) * HEAD
                        mm = pe.matmul(m.ps[r:r + HEAD, q % BANKS, 0:P], m.v_att[:, k, col:col + HEAD],
                                       prob_T[:, h % 2, tile * P:(tile + 1) * P],
                                       start=(n == 0), stop=(n == len(tiles) - 1))
                    mm.then_inc(filled[q % BANKS], 1)

            scores(0)
            for h in range(H):
                if h + 1 < H:
                    scores(h + 1)
                outputs(h)

        @block.vector
        def _(dve):
            for c in range(12):
                dve.wait_ge(rstd_done, c // 2 + 1)
                gain = m.v("q_norm_gain", c // 2) if c < 6 else m.v("k_norm_gain", (c - 6) // 2)
                dve.scalar_tensor_tensor(m.qk[:, c, :], m.qk[:, c, :], gain, rstd[:, c, :], ALU.mult, ALU.mult
                                         ).then_inc(normed, 1)
            bias = m.bias[:, :, :].rearrange("p (g h) k -> p g h k", g=3)
            for h in range(H):
                for t in range(2):
                    i = 2 * h + t
                    c0, n = ((0, 3 * P), (3 * P, 6 * P))[t]
                    if h >= 2 and t == 0:
                        w = turn_unit(h - 2, 2)
                        dve.wait_ge(filled[w % BANKS], w // BANKS + 1)
                    for j in ((0,), (1, 2))[t]:
                        q = score_unit(h, j)
                        g0, ng = ((0, 3), (0, 2), (2, 1))[j]
                        keys = P if t == 0 else SEQ
                        at = (0, 3 * P, 7 * P)[j]
                        dve.wait_ge(filled[q % BANKS], q // BANKS + 1)
                        dve.scalar_tensor_tensor(
                            prob[:, h % 2, at:at + ng * keys].rearrange("p (g k) -> p g k", g=ng),
                            m.ps[:, q % BANKS, 0:ng * keys].rearrange("p (g k) -> p g k", g=ng), HEAD ** -0.5,
                            bias[:, g0:g0 + ng, h, SEQ - keys:SEQ], ALU.mult, ALU.add
                        ).then_inc(drained[q % BANKS], 1)
                    dve.drain()
                    dve.tensor_reduce(neg_max[:, i:i + 1], prob[:, h % 2, c0:c0 + n], AX, ALU.max, negate=True
                                      ).then_inc(maxed, 1)
                for t in range(2):
                    i = 2 * h + t
                    c0, n = ((0, 3 * P), (3 * P, 6 * P))[t]
                    dve.wait_ge(exped, i + 1)
                    dve.reciprocal(row_inv[:, i:i + 1], row_sum[:, i:i + 1])
                    dve.drain()
                    dve.tensor_scalar(prob[:, h % 2, c0:c0 + n], prob[:, h % 2, c0:c0 + n], row_inv[:, i:i + 1],
                                      None, ALU.mult).then_inc(probs_done, 1)


def recurrence_part(nc, m, a):
    PAIRS = 4
    with ExitStack() as ctx:
        def sem(n):
            return ctx.enter_context(nc.semaphore(n))

        def sb(n, s):
            return ctx.enter_context(nc.sbuf_tensor(n, s, F32))

        w_upto = sb("w_upto", [P, 8, P])
        rate = sb("rate", [P, 8, P])
        gate = sb("gate", [P, 8, P])
        alpha_rho = sb("alpha_rho", [P, 8, 2, P])
        beta = sb("beta", [P, 8, P])
        kappa = sb("kappa", [P, 8, P])
        key = sb("key", [P, 8, P])
        quad = sb("quad", [P, 16, 4 * P])
        work = [sb(f"work{i}", [P, 16, P]) for i in range(8)]
        LEAF_, REST, SQ, SQ_T, Q4_T, X, X_T, N = work

        shift = [work[0], work[1]]
        w_before, w_inv = work[7][:, 0:8, :], work[7][:, 8:16, :]
        kk, kk_sq = work[6][:, 0:8, :], work[6][:, 8:16, :]
        kk_inv = work[5][:, 0:8, :]
        sig_w = work[5][:, 8:16, :].rearrange("p (t f) n -> p t (f n)", t=TT)
        tanh_w = work[4][:, 0:2, :].rearrange("p a b -> p (a b)")
        sig_g = work[4][:, 2:6, :].rearrange("p (c t) n -> p c (t n)", c=2)
        beta_z = work[0][:, :, :].rearrange("p (t c f) n -> p t c (f n)", t=TT, c=2)
        kappa_z = work[1][:, :, :].rearrange("p (t c f) n -> p t c (f n)", t=TT, c=2)
        mu_tok = work[2][:, :, :].rearrange("p (t k f) n -> p t k (f n)", t=TT, k=2)
        q_T = work[3][:, 0:8, :].rearrange("p (t f) n -> p t f n", t=TT)
        v_tok = work[3][:, 8:16, :].rearrange("p (t f) n -> p t (f n)", t=TT)
        g_bd = work[4][:, 0:8, :].rearrange("p (c f) n -> p c f n", c=2)
        state = work[5][:, 0:8, :].rearrange("p (c f) n -> p c f n", c=2)
        o_raw = work[5][:, 8:16, :]
        ab_tok = work[7][:, :, :].rearrange("p (t k f) n -> p t k (f n)", t=TT, k=2)
        M_T = X_T

        def rows(c0, c1):
            return m.p_rwkv[:, c0:c1, 1:SEQ + 1]

        def by_chunk(x):
            return x.rearrange("p (c t) n -> p c (t n)", t=TT)

        filled, drained = m.filled, m.drained
        ones_set, mixed, lora_act, kk_raw, kk_squared = (
            sem("ones_set"), sem("mixed"), sem("lora_act"), sem("kk_raw"), sem("kk_squared"))
        clamped, rooted, operands, start_x, start_n = (
            sem("clamped"), sem("rooted"), sem("operands"), sem("start_x"), sem("start_n"))
        centred, o_squared, o_log, o_rstd, bonus_in = (
            sem("centred"), sem("o_squared"), sem("o_log"), sem("o_rstd"), sem("bonus_in"))

        U_Z, U_RATE, U_GATE, U_CUM, U_KK = 0, 2, 4, 6, 10
        U_QUAD, U_LOW, U_INV = 12, 28, 32
        STEPS = 15
        U_TOK = U_INV + 4 * STEPS
        U_BV, U_MU, U_Q, U_O, U_G = U_TOK + 8, U_TOK + 10, U_TOK + 14, U_TOK + 16, U_TOK + 18
        U_S = U_G + 2
        U_MEAN, U_BONUS, U_VAR = U_S + 6, U_S + 8, U_S + 10

        DT = quad
        steps = [
            (DT, LEAF_, SQ, False, ()),
            (LEAF_, DT, SQ_T, False, ()),
            (SQ, SQ_T, Q4_T, False, (0, 1)),
            (SQ_T, X, X, True, (1,)),
            (SQ, X_T, X_T, True, (0,)),
            (X, Q4_T, X_T, True, (2, 3, 4)),
            (Q4_T, X, X, True, (2, 3)),
            (X_T, REST, LEAF_, False, (5,)),
            (REST, X_T, SQ, False, (5,)),
            (SQ, LEAF_, SQ_T, False, (7, 8)),
            (LEAF_, SQ, Q4_T, False, (7, 8)),
            (Q4_T, SQ_T, REST, False, (9, 10)),
            (SQ_T, N, N, True, (9,)),
            (REST, N, N, True, (11, 12)),
            (X, N, M_T, False, (6, 13)),
        ]
        instances = [(tt, par, f) for tt in range(TT) for par in range(2) for f in range(PAIRS)]
        block = ctx.enter_context(nc.Block())

        @block.gpsimd
        def _(pool):
            pool.memset(tanh_w[:, :], 1.0).then_inc(ones_set, 1)

        @block.scalar
        def _(act):
            act.wait_ge(mixed, 3)
            act.wait_ge(ones_set, 1)
            act.activation(tanh_w[0:64, :], m.p_rwkv[0:64, LORA_CHUNK, 1:SEQ + 1], ACT.Tanh).then_inc(lora_act, 1)
            act.activation(sig_g[:, :, :], rows(13, 15), ACT.Sigmoid).then_inc(lora_act, 1)
            for t in range(TT):
                act.wait_ge(filled[U_Z + t], 1)
                act.activation(sig_w[:, t, :], m.ps[:, U_Z + t, :], ACT.Sigmoid).then_inc(drained[U_Z + t], 1)
            for f in range(PAIRS):
                b = U_RATE + f // 2
                act.wait_ge(filled[b], 1)
                ins = act.activation(by_chunk(rate[:, :, :])[:, f, :], m.ps[:, b, (f % 2) * SEQ:(f % 2 + 1) * SEQ],
                                     ACT.Sigmoid, bias=m.v("rwkv_a0", f))
                if f % 2:
                    ins.then_inc(drained[b], 1)
            for f in range(PAIRS):
                act.wait_ge(kk_raw, f + 1)
                act.activation(kk_sq[:, 2 * f:2 * f + 2, :], kk[:, 2 * f:2 * f + 2, :], ACT.Square).then_inc(kk_squared, 1)
            for f in range(PAIRS):
                q = U_CUM + f
                act.wait_ge(filled[q % BANKS], q // BANKS + 1)
                src = m.ps[:, q % BANKS, :].rearrange("p (t k n) -> p t k n", t=TT, k=2)
                act.activation(w_upto[:, 2 * f:2 * f + 2, :], src[:, :, 0, :], ACT.Exp)
                act.activation(w_before[:, 2 * f:2 * f + 2, :], src[:, :, 1, :], ACT.Exp)
                act.activation(w_inv[:, 2 * f:2 * f + 2, :], src[:, :, 0, :], ACT.Exp, scale=-1.0
                               ).then_inc(drained[q % BANKS], 1)
            act.wait_ge(clamped, 2)
            act.activation(kk_inv, kk_inv, ACT.Sqrt).then_inc(rooted, 1)
            for s, (_, _, out, adds, _) in enumerate(steps):
                if adds:
                    continue
                for g in range(4):
                    q = U_INV + 4 * s + g
                    act.wait_ge(filled[q % BANKS], q // BANKS + 1)
                    act.activation(out[:, 4 * g:4 * g + 4, :], m.ps[:, q % BANKS, :].rearrange("p (i n) -> p i n", i=4),
                                   ACT.Copy).then_inc(drained[q % BANKS], 1)
            for q, dst in ((U_TOK, v_tok[:, 0, :]), (U_TOK + 1, v_tok[:, 1, :]),
                           (U_TOK + 6, ab_tok[:, 0, 0, :]), (U_TOK + 7, ab_tok[:, 1, 0, :]),
                           (U_BV, ab_tok[:, 0, 1, :]), (U_BV + 1, ab_tok[:, 1, 1, :])):
                act.wait_ge(filled[q % BANKS], q // BANKS + 1)
                act.activation(dst, m.ps[:, q % BANKS, :], ACT.Copy).then_inc(drained[q % BANKS], 1)
            for n in range(4):
                q = U_MU + n
                t, hq = n // 2, n % 2
                act.wait_ge(filled[q % BANKS], q // BANKS + 1)
                for k in range(2):
                    ins = act.activation(
                        mu_tok[:, t, k, hq * 256:hq * 256 + 256].rearrange("p (h d) -> p h d", h=4),
                        m.ps[:, q % BANKS, :].rearrange("p (h k d) -> p h k d", h=4, k=2)[:, :, k, :], ACT.Copy)
                ins.then_inc(drained[q % BANKS], 1)
            for t in range(TT):
                q = U_O + t
                act.wait_ge(filled[q % BANKS], q // BANKS + 1)
                act.activation(o_raw.rearrange("p (f t) n -> p f t n", t=TT)[:, :, t, :],
                               m.ps[:, q % BANKS, :].rearrange("p (f n) -> p f n", f=PAIRS), ACT.Copy
                               ).then_inc(drained[q % BANKS], 1)
            for j in range(2):
                act.wait_ge(centred, j + 1)
                act.activation(work[0][:, 4 * j:4 * j + 4, :], o_raw[:, 4 * j:4 * j + 4, :], ACT.Square
                               ).then_inc(o_squared, 1)
            for j in range(2):
                q = U_VAR + j
                act.wait_ge(filled[q % BANKS], q // BANKS + 1)
                act.activation(work[1][:, 4 * j:4 * j + 4, :], m.ps[:, q % BANKS, :].rearrange("p (c n) -> p c n", c=4),
                               ACT.Ln, bias=m.c("gn_eps"), scale=1.0 / HEAD).then_inc(drained[q % BANKS], 1)
                act.drain()
                act.activation(work[1][:, 4 * j:4 * j + 4, :], work[1][:, 4 * j:4 * j + 4, :], ACT.Exp, scale=-0.5
                               ).then_inc(o_rstd, 1)

        @block.tensor
        def _(pe):
            def free(q):
                if q >= BANKS:
                    pe.wait_ge(drained[q % BANKS], q // BANKS)
                return q % BANKS

            def drained_of(q):
                pe.wait_ge(drained[q % BANKS], q // BANKS + 1)

            pe.wait_ge(mixed, 3)
            for f in range(PAIRS):
                b = free(U_RATE + f // 2)
                mm = pe.matmul(m.ps[:, b, (f % 2) * SEQ:(f % 2 + 1) * SEQ], m.a_up[:, f * P:(f + 1) * P],
                               m.p_rwkv[:, LORA_CHUNK, 1:SEQ + 1], start=True, stop=True)
                if f % 2:
                    mm.then_inc(filled[b], 1)
            pe.wait_ge(lora_act, 1)
            for t in range(TT):
                b = free(U_Z + t)
                pe.matmul(m.ps[:, b, :], tanh_w[:, t * P:(t + 1) * P], m.w_up[:, :], start=True, stop=True
                          ).then_inc(filled[b], 1)
            pe.wait_ge(lora_act, 2)
            for f in range(PAIRS):
                b = free(U_GATE + f // 2)
                for k in range(2):
                    mm = pe.matmul(m.ps[:, b, (f % 2) * SEQ:(f % 2 + 1) * SEQ], m.g_up[:, k, f * P:(f + 1) * P],
                                   sig_g[:, k, :], start=(k == 0), stop=(k == 1))
                if f % 2:
                    mm.then_inc(filled[b], 1)
            for t in range(TT):
                drained_of(U_Z + t)
            for f in range(PAIRS):
                b = free(U_CUM + f)
                for t in range(TT):
                    mm = pe.matmul(m.ps[:, b, t * 256:(t + 1) * 256], sig_w[:, t, f * P:(f + 1) * P], m.c("cumulate"),
                                   start=True, stop=True)
                mm.then_inc(filled[b], 1)
            for j in range(2):
                pe.wait_ge(kk_squared, 2 * j + 2)
                b = free(U_KK + j)
                pe.matmul(m.ps[:, b, :], m.c("pair_ones"), kk_sq[:, 4 * j:4 * j + 4, :], start=True, stop=True
                          ).then_inc(filled[b], 1)
            pe.wait_ge(operands, 4)
            for i, (tt, par, f) in enumerate(instances):
                b = free(U_QUAD + i)
                r = slice(par * HEAD, par * HEAD + HEAD)
                both = alpha_rho[r, 2 * f + tt, :, :]
                pe.matmul(m.ps[:, b, 0:256], beta[r, 2 * f + tt, :], both, start=True, stop=True)
                pe.matmul(m.ps[:, b, 256:512], kappa[r, 2 * f + tt, :], both, start=True, stop=True
                          ).then_inc(filled[b], 1)
            for g in range(4):
                b = free(U_LOW + g)
                for f in range(PAIRS):
                    tt, par, _ = instances[4 * g]
                    r = slice(par * HEAD, par * HEAD + HEAD)
                    mm = pe.matmul(m.ps[:, b, f * P:(f + 1) * P], alpha_rho[r, 2 * f + tt, 0, :],
                                   beta[r, 2 * f + tt, :], start=True, stop=True)
                mm.then_inc(filled[b], 1)
            for s, (lhs, rhs, _, _, needs) in enumerate(steps):
                for g in range(4):
                    b = free(U_INV + 4 * s + g)
                    if s <= 1:
                        drained_of(U_LOW + g)
                        drained_of(U_QUAD + 4 * g + 3)
                    if s in (3, 4):
                        pe.wait_ge(start_x, g + 1)
                    if s == 12:
                        pe.wait_ge(start_n, g + 1)
                    for n in needs:
                        drained_of(U_INV + 4 * n + g)
                    for i in range(4 * g, 4 * g + 4):
                        mm = pe.matmul(m.ps[:, b, (i % 4) * P:(i % 4 + 1) * P], lhs[:, i, 0:P], rhs[:, i, 0:P],
                                       start=True, stop=True)
                    mm.then_inc(filled[b], 1)
            for n, src in enumerate((rows(8, 12), beta, kappa, None)):
                for t in range(TT):
                    b = free(U_TOK + 2 * n + t)
                    for f in range(PAIRS):
                        if n == 0:
                            x = m.p_rwkv[:, 8 + f, 1 + t * P:1 + (t + 1) * P]
                        elif n == 3:
                            x = alpha_rho[:, 2 * f + t, 0, :]
                        else:
                            x = src[:, 2 * f + t, :]
                        mm = pe.transpose(m.ps[:, b, f * P:(f + 1) * P], x, m.c("ident"))
                    mm.then_inc(filled[b], 1)
            for t in range(TT):
                drained_of(U_TOK + t)
                b = free(U_BV + t)
                for h in range(8):
                    i = (2 * t + h % 2) * 4 + h // 2
                    mm = pe.matmul(m.ps[:, b, h * HEAD:(h + 1) * HEAD], quad[:, i, 256:384],
                                   v_tok[:, t, h * HEAD:(h + 1) * HEAD], start=True, stop=True)
                mm.then_inc(filled[b], 1)
            for g in range(4):
                drained_of(U_INV + 4 * (STEPS - 1) + g)
            for n in range(4):
                t, hq = n // 2, n % 2
                drained_of(U_TOK + 6 + t)
                drained_of(U_BV + t)
                b = free(U_MU + n)
                for h in range(4 * hq, 4 * hq + 4):
                    i = (2 * t + h % 2) * 4 + h // 2
                    mm = pe.matmul(m.ps[:, b, (h % 4) * P:(h % 4 + 1) * P], M_T[:, i, :],
                                   ab_tok[:, t, :, h * HEAD:(h + 1) * HEAD], start=True, stop=True)
                mm.then_inc(filled[b], 1)
            for t in range(TT):
                for n in range(2):
                    drained_of(U_MU + 2 * t + n)
                b = free(U_Q + t)
                for f in range(PAIRS):
                    for par in range(2):
                        h, i = 2 * f + par, (2 * t + par) * 4 + f
                        mm = pe.matmul(m.ps[par * HEAD:par * HEAD + HEAD, b, f * P:(f + 1) * P],
                                       mu_tok[:, t, 0, h * HEAD:(h + 1) * HEAD], quad[:, i, P:2 * P],
                                       start=True, stop=True)
                mm.then_inc(filled[b], 1)
            for t in range(TT):
                b = free(U_O + t)
                for f in range(PAIRS):
                    for par in range(2):
                        h, i = 2 * f + par, (2 * t + par) * 4 + f
                        out = m.ps[par * HEAD:par * HEAD + HEAD, b, f * P:(f + 1) * P]
                        pe.matmul(out, mu_tok[:, t, 1, h * HEAD:(h + 1) * HEAD], quad[:, i, P:2 * P],
                                  start=True, stop=False)
                        mm = pe.matmul(out, v_tok[:, t, h * HEAD:(h + 1) * HEAD], quad[:, i, 3 * P:4 * P],
                                       start=False, stop=True)
                mm.then_inc(filled[b], 1)
            for c in (1, 2):
                t, cb = c // 2, c % 2
                drained_of(U_TOK + 2 + t)
                b = free(U_G + c - 1)
                for f in range(PAIRS):
                    mm = pe.matmul(m.ps[:, b, f * P:(f + 1) * P], mu_tok[:, t, 0, f * P:(f + 1) * P],
                                   beta_z[:, t, cb, f * P:(f + 1) * P], start=True, stop=True)
                mm.then_inc(filled[b], 1)
            for t in range(TT):
                drained_of(U_TOK + 4 + t)
                drained_of(U_Q + t)
            for c in range(4):
                t, cb = c // 2, c % 2
                if c > 0:
                    drained_of(U_S + 2 * (c - 1))
                    b = free(U_S + 2 * c - 1)
                    for f in range(PAIRS):
                        mm = pe.matmul(m.ps[:, b, f * SUB:(f + 1) * SUB], state[:, (c - 1) % 2, f, :],
                                       q_T[:, t, f, cb * SUB:(cb + 1) * SUB], start=True, stop=True)
                    mm.then_inc(filled[b], 1)
                if c < 3:
                    b = free(U_S + 2 * c)
                    if c > 0:
                        drained_of(U_G + c - 1)
                    for f in range(PAIRS):
                        out = m.ps[:, b, f * P:(f + 1) * P]
                        cols = slice(f * P, (f + 1) * P)
                        pe.matmul(out, beta_z[:, t, cb, cols], mu_tok[:, t, 1, cols], start=True, stop=False)
                        mm = pe.matmul(out, kappa_z[:, t, cb, cols], v_tok[:, t, cols], start=False, stop=(c == 0))
                        if c > 0:
                            mm = pe.matmul(out, g_bd[:, c - 1, f, :], state[:, (c - 1) % 2, f, :],
                                           start=False, stop=True)
                    mm.then_inc(filled[b], 1)
            drained_of(U_S + 5)
            for t in range(TT):
                drained_of(U_O + t)
            for j in range(2):
                b = free(U_MEAN + j)
                pe.matmul(m.ps[:, b, :], m.c("pair_ones"), o_raw[:, 4 * j:4 * j + 4, :], start=True, stop=True
                          ).then_inc(filled[b], 1)
            for j in range(2):
                pe.wait_ge(bonus_in, 4)
                b = free(U_BONUS + j)
                pe.matmul(m.ps[:, b, :], m.c("pair_ones"), work[6][:, 4 * j:4 * j + 4, :], start=True, stop=True
                          ).then_inc(filled[b], 1)
            for j in range(2):
                pe.wait_ge(o_squared, j + 1)
                b = free(U_VAR + j)
                pe.matmul(m.ps[:, b, :], m.c("pair_ones"), work[0][:, 4 * j:4 * j + 4, :], start=True, stop=True
                          ).then_inc(filled[b], 1)

        @block.vector
        def _(dve):
            def await_filled(q):
                dve.wait_ge(filled[q % BANKS], q // BANKS + 1)
                return q % BANKS

            for c0, c1, dst in ((12, 15, work[3]), (0, 8, work[0]), (8, 12, work[1])):
                d = by_chunk(dst[:, 0:2 * (c1 - c0), :])
                dve.tensor_tensor(d, m.p_rwkv[:, c0:c1, 0:SEQ], rows(c0, c1), ALU.subtract)
                dve.drain()
                for c in range(c0, c1):
                    dve.scalar_tensor_tensor(m.p_rwkv[:, c, 1:SEQ + 1], d[:, c - c0, :], m.v("rwkv_shift_mu", c),
                                             m.p_rwkv[:, c, 1:SEQ + 1], ALU.mult, ALU.add).then_inc(mixed, 1)
            dve.drain()
            for f in range(PAIRS):
                dve.tensor_scalar(by_chunk(kk)[:, f, :], m.p_rwkv[:, 4 + f, 1:SEQ + 1], m.v("rwkv_k_k", f), None,
                                  ALU.mult).then_inc(kk_raw, 1)
            for j in range(2):
                b = await_filled(U_GATE + j)
                dve.tensor_copy(gate[:, 4 * j:4 * j + 4, :], m.ps[:, b, :].rearrange("p (c n) -> p c n", c=4)
                                ).then_inc(drained[b], 1)
            for j in range(2):
                q = U_RATE + j
                dve.wait_ge(drained[q % BANKS], q // BANKS + 1)
            for f in range(PAIRS):
                dve.tensor_scalar(by_chunk(key[:, :, :])[:, f, :], by_chunk(rate[:, :, :])[:, f, :], -1.0,
                                  m.v("rwkv_k_a", f), ALU.add, ALU.mult)
            dve.drain()
            dve.scalar_tensor_tensor(by_chunk(key[:, :, :]), by_chunk(key[:, :, :]), 1.0, rows(4, 8),
                                     ALU.add, ALU.mult)
            for j in range(2):
                b = await_filled(U_KK + j)
                dve.tensor_scalar(kk_inv[:, 4 * j:4 * j + 4, :], m.ps[:, b, :].rearrange("p (c n) -> p c n", c=4),
                                  1e-24, None, ALU.max).then_inc(drained[b], 1)
                dve.drain().then_inc(clamped, 1)
            for f in range(PAIRS):
                q = U_CUM + f
                dve.wait_ge(drained[q % BANKS], q // BANKS + 1)
            dve.tensor_tensor(kappa[:, :, :], key[:, :, :], w_inv, ALU.mult).then_inc(operands, 1)
            dve.tensor_tensor(alpha_rho[:, :, 1, :], m.p_rwkv[:, 0:4, 1:SEQ + 1].rearrange("p c (t n) -> p c t n", t=2),
                              w_upto[:, :, :].rearrange("p (c t) n -> p c t n", t=2), ALU.mult).then_inc(operands, 1)
            dve.wait_ge(rooted, 1)
            dve.reciprocal(kk_inv, kk_inv)
            dve.drain()
            dve.tensor_tensor(kk, kk, kk_inv, ALU.mult)
            dve.drain()
            dve.scalar_tensor_tensor(alpha_rho[:, :, 0, :], w_before, -1.0, kk, ALU.mult, ALU.mult
                                     ).then_inc(operands, 1)
            dve.tensor_tensor(beta[:, :, :], kk, rate[:, :, :], ALU.mult)
            dve.drain()
            dve.tensor_tensor(beta[:, :, :], beta[:, :, :], w_inv, ALU.mult).then_inc(operands, 1)
            for i in range(16):
                b = await_filled(U_QUAD + i)
                dve.tensor_tensor(quad[:, i, :], m.ps[:, b, :], m.c("quad_mask"), ALU.mult).then_inc(drained[b], 1)

            def wide(name):
                return m.c(name).rearrange("p (o n) -> p o n", o=1).to_broadcast([P, 4, P])
            for g in range(4):
                b = await_filled(U_LOW + g)
                i = slice(4 * g, 4 * g + 4)
                src = m.ps[:, b, :].rearrange("p (i n) -> p i n", i=4)
                dve.tensor_tensor(LEAF_[:, i, :], src, wide("leaf_low"), ALU.mult)
                dve.tensor_tensor(REST[:, i, :], src, wide("rest_low"), ALU.mult).then_inc(drained[b], 1)
                dve.drain()
                dve.tensor_tensor(X[:, i, :], LEAF_[:, i, :], wide("ident"), ALU.add)
                dve.tensor_tensor(X_T[:, i, :], quad[:, i, 0:P], wide("ident"), ALU.add)
                dve.drain().then_inc(start_x, 1)
            for s, (_, _, out, adds, needs) in enumerate(steps):
                if s == 12:
                    for g in range(4):
                        i = slice(4 * g, 4 * g + 4)
                        q = U_INV + 4 * 8 + g
                        dve.wait_ge(drained[q % BANKS], q // BANKS + 1)
                        dve.tensor_tensor(N[:, i, :], SQ[:, i, :], wide("ident"), ALU.add)
                        dve.drain().then_inc(start_n, 1)
                if not adds:
                    continue
                for g in range(4):
                    i = slice(4 * g, 4 * g + 4)
                    b = await_filled(U_INV + 4 * s + g)
                    dve.tensor_tensor(out[:, i, :], m.ps[:, b, :].rearrange("p (i n) -> p i n", i=4), out[:, i, :],
                                      ALU.add).then_inc(drained[b], 1)
                dve.drain()
            for n, dst in ((1, beta_z), (2, kappa_z)):
                for t in range(TT):
                    b = await_filled(U_TOK + 2 * n + t)
                    dve.tensor_scalar(dst[:, t, 0, :], m.ps[:, b, :], m.c("half_rows")[:, 0:1], None, ALU.mult)
                    dve.tensor_scalar(dst[:, t, 1, :], m.ps[:, b, :], m.c("half_rows")[:, 1:2], None, ALU.mult
                                      ).then_inc(drained[b], 1)
            for f in range(PAIRS):
                if f == 0:
                    for n in range(4):
                        q = U_MU + n
                        dve.wait_ge(drained[q % BANKS], q // BANKS + 1)
                dve.scalar_tensor_tensor(by_chunk(work[6][:, 0:8, :])[:, f, :], m.p_rwkv[:, f, 1:SEQ + 1],
                                         m.v("rwkv_r_k", f), by_chunk(key[:, :, :])[:, f, :], ALU.mult, ALU.mult
                                         ).then_inc(bonus_in, 1)
            for t in range(TT):
                b = await_filled(U_Q + t)
                rho = alpha_rho[:, :, 1, :].rearrange("p (f t) n -> p f t n", t=TT)[:, :, t, :]
                dve.tensor_tensor(q_T[:, t, :, :], m.ps[:, b, :].rearrange("p (f n) -> p f n", f=PAIRS), rho, ALU.add
                                  ).then_inc(drained[b], 1)
            for c in (1, 2):
                b = await_filled(U_G + c - 1)
                g = g_bd[:, c - 1, :, :]
                dve.tensor_tensor(g, m.ps[:, b, :].rearrange("p (f n) -> p f n", f=PAIRS), wide("pair_ones"), ALU.mult)
                dve.drain()
                dve.tensor_tensor(g, g, wide("ident"), ALU.add).then_inc(drained[b], 1)
            for t in range(TT):
                q = U_O + t
                dve.wait_ge(drained[q % BANKS], q // BANKS + 1)
            o_rows = by_chunk(o_raw)
            for c in range(4):
                t, cb = c // 2, c % 2
                if c > 0:
                    b = await_filled(U_S + 2 * c - 1)
                    o = o_rows[:, :, c * SUB:(c + 1) * SUB]
                    dve.tensor_tensor(o, m.ps[:, b, 0:256].rearrange("p (f n) -> p f n", f=PAIRS), o, ALU.add
                                      ).then_inc(drained[b], 1)
                if c < 3:
                    b = await_filled(U_S + 2 * c)
                    for f in range(PAIRS):
                        end = cb * SUB + SUB - 1
                        ins = dve.scalar_tensor_tensor(
                            state[:, c % 2, f, :], m.ps[:, b, f * P:(f + 1) * P], w_upto[:, 2 * f + t, end:end + 1],
                            m.c("pair_ones"), ALU.mult, ALU.mult)
                    ins.then_inc(drained[b], 1)
            dve.drain()
            for j in range(2):
                b = await_filled(U_MEAN + j)
                o = o_raw[:, 4 * j:4 * j + 4, :]
                dve.scalar_tensor_tensor(o, m.ps[:, b, :].rearrange("p (c n) -> p c n", c=4), -1.0 / HEAD, o,
                                         ALU.mult, ALU.add).then_inc(drained[b], 1)
                dve.drain().then_inc(centred, 1)
            bonus = by_chunk(work[6][:, 8:16, :])
            for j in range(2):
                b = await_filled(U_BONUS + j)
                dve.tensor_tensor(bonus[:, 2 * j:2 * j + 2, :], m.ps[:, b, :].rearrange("p (c n) -> p c n", c=2),
                                  rows(8 + 2 * j, 10 + 2 * j), ALU.mult).then_inc(drained[b], 1)
            for j in range(2):
                o = o_raw[:, 4 * j:4 * j + 4, :]
                dve.wait_ge(o_rstd, j + 1)
                dve.tensor_tensor(o, o, work[1][:, 4 * j:4 * j + 4, :], ALU.mult)
            dve.drain()
            for f in range(PAIRS):
                dve.tensor_scalar(o_rows[:, f, :], o_rows[:, f, :], m.v("rwkv_ln_w", f), m.v("rwkv_ln_b", f),
                                  ALU.mult, ALU.add)
            dve.drain()
            dve.tensor_tensor(o_rows, o_rows, bonus, ALU.add)
            dve.drain()
            dve.tensor_tensor(m.o_T[:, :, :], o_rows, by_chunk(gate[:, :, :]), ALU.mult)


def mix_part(nc, m, a):
    with ExitStack() as ctx:
        def sem(n):
            return ctx.enter_context(nc.semaphore(n))

        def sb(n, s):
            return ctx.enter_context(nc.sbuf_tensor(n, s, F32))
        gate_w = sb("gate_w", [P, 8, KC, 256])
        att_w = sb("att_w", [P, 2, D])
        rec_w = sb("rec_w", [P, 4, D])
        out_w = sb("out_w", [P, KC, D])
        sig = sb("gate_sig", [P, 2, 2, SEQ])
        part = sb("gate_part", [P, 2, SEQ])
        mixed = sb("gate_mixed", [P, KC, SEQ])
        square = sb("mix_square", [P, KC, SEQ])
        log_ms = sb("mix_log", [P, SEQ])
        rstd = sb("mix_rstd", [P, SEQ])
        gate_landed = [sem(f"gate_landed{i}") for i in range(8)]
        att_landed, rec_landed, out_landed = sem("att_landed"), sem("rec_landed"), sem("out_landed")
        filled, drained = m.filled, m.drained
        gated, squared, rstd_done, h_done = sem("gated"), sem("m_squared"), sem("m_rstd"), sem("m_h")
        U_OUT, U_SS, U_TOK = 16, 20, 21
        block = ctx.enter_context(nc.Block())

        @block.sync
        def _(sp):
            w_in = a["w_in"][0].rearrange("(c p) n -> p c n", p=P)
            sp.dma_start(att_w[:, :, :], a["w_att_out"][0].rearrange("(c p) n -> p c n", p=P)).then_inc(att_landed, 16)
            sp.dma_start(rec_w[:, :, :], a["w_rwkv_out"][0].rearrange("(c p) n -> p c n", p=P)).then_inc(rec_landed, 16)
            for j in range(4):
                for k in range(2):
                    col = GATE_COL + k * D + 256 * j
                    sp.dma_start(gate_w[:, 4 * k + j, :, :], w_in[:, :, col:col + 256]).then_inc(gate_landed[4 * k + j], 16)
            sp.dma_start(out_w[:, :, :], a["w_out"][0].rearrange("(c p) n -> p c n", p=P)).then_inc(out_landed, 16)

        @block.tensor
        def _(pe):
            def free(q):
                if q >= BANKS:
                    pe.wait_ge(drained[q % BANKS], q // BANKS)
                return q % BANKS

            for j in range(4):
                for k, (w, x, n, landed) in enumerate(((att_w, m.att_T, 2, att_landed), (rec_w, m.o_T, 4, rec_landed))):
                    b = free(4 * j + k)
                    pe.wait_ge(landed, 16)
                    for c in range(2):
                        for f in range(n):
                            col = (2 * j + c) * P
                            mm = pe.matmul(m.ps[:, b, c * SEQ:(c + 1) * SEQ], w[:, f, col:col + P], x[:, f, :],
                                           start=(f == 0), stop=(f == n - 1))
                    mm.then_inc(filled[b], 1)
                for k in range(2):
                    b = free(4 * j + 2 + k)
                    pe.wait_ge(gate_landed[4 * k + j], 16)
                    for c in range(2):
                        for f in range(KC):
                            mm = pe.matmul(m.ps[:, b, c * SEQ:(c + 1) * SEQ], gate_w[:, 4 * k + j, f, c * P:(c + 1) * P],
                                           m.hT[:, f, :], start=(f == 0), stop=(f == KC - 1))
                    mm.then_inc(filled[b], 1)
            pe.wait_ge(out_landed, 16)
            for j in range(4):
                b = free(U_OUT + j)
                for c in range(2):
                    for f in range(KC):
                        if j == 0 and c == 0:
                            pe.wait_ge(gated, f // 2 + 1)
                        col = (2 * j + c) * P
                        mm = pe.matmul(m.ps[:, b, c * SEQ:(c + 1) * SEQ], out_w[:, f, col:col + P], mixed[:, f, :],
                                       start=(f == 0), stop=(f == KC - 1))
                mm.then_inc(filled[b], 1)
            b = free(U_SS)
            for c in range(KC):
                pe.wait_ge(squared, c // 2 + 1)
                mm = pe.matmul(m.ps[:, b, 0:SEQ], m.c("ones"), square[:, c, :], start=(c == 0), stop=(c == KC - 1))
            mm.then_inc(filled[b], 1)
            for n in range(4):
                t, c0 = n // 2, 4 * (n % 2)
                b = free(U_TOK + n)
                for c in range(c0, c0 + 4):
                    pe.wait_ge(h_done, KC)
                    mm = pe.transpose(m.ps[:, b, (c - c0) * P:(c - c0 + 1) * P], m.hT[:, c, t * P:(t + 1) * P], m.c("ident"))
                mm.then_inc(filled[b], 1)

        @block.scalar
        def _(act):
            for j in range(4):
                for k in range(2):
                    q = 4 * j + 2 + k
                    act.wait_ge(filled[q % BANKS], q // BANKS + 1)
                    if j >= 1:
                        act.wait_ge(gated, j)
                    act.activation(sig[:, k, :, :], m.ps[:, q % BANKS, :].rearrange("p (c t) -> p c t", c=2), ACT.Sigmoid
                                   ).then_inc(drained[q % BANKS], 1)
            for j in range(4):
                q = U_OUT + j
                act.wait_ge(drained[q % BANKS], q // BANKS + 1)
                act.activation(square[:, 2 * j:2 * j + 2, :], m.xT[:, 2 * j:2 * j + 2, :], ACT.Square).then_inc(squared, 1)
            q = U_SS
            act.wait_ge(filled[q % BANKS], q // BANKS + 1)
            act.activation(log_ms[:, :], m.ps[:, q % BANKS, 0:SEQ], ACT.Ln, bias=m.c("eps"), scale=1.0 / D
                           ).then_inc(drained[q % BANKS], 1)
            act.drain()
            act.activation(rstd[:, :], log_ms[:, :], ACT.Exp, scale=-0.5).then_inc(rstd_done, 1)
            for n in range(4):
                q = U_TOK + n
                act.wait_ge(filled[q % BANKS], q // BANKS + 1)
                act.activation(m.h_tok[:, n // 2, (n % 2) * 512:(n % 2 + 1) * 512], m.ps[:, q % BANKS, :], ACT.Copy
                               ).then_inc(drained[q % BANKS], 1)

        @block.vector
        def _(dve):
            for j in range(4):
                for k, dst in enumerate((mixed[:, 2 * j:2 * j + 2, :], part[:, :, :])):
                    q, s = 4 * j + k, 4 * j + 2 + k
                    dve.wait_ge(filled[q % BANKS], q // BANKS + 1)
                    dve.wait_ge(drained[s % BANKS], s // BANKS + 1)
                    dve.tensor_tensor(dst, m.ps[:, q % BANKS, :].rearrange("p (c t) -> p c t", c=2), sig[:, k, :, :],
                                      ALU.mult).then_inc(drained[q % BANKS], 1)
                dve.drain()
                dve.tensor_tensor(mixed[:, 2 * j:2 * j + 2, :], mixed[:, 2 * j:2 * j + 2, :], part[:, :, :], ALU.add)
                dve.drain().then_inc(gated, 1)
            for j in range(4):
                q = U_OUT + j
                dve.wait_ge(filled[q % BANKS], q // BANKS + 1)
                x = m.xT[:, 2 * j:2 * j + 2, :]
                dve.tensor_tensor(x, m.ps[:, q % BANKS, :].rearrange("p (c t) -> p c t", c=2), x, ALU.add
                                  ).then_inc(drained[q % BANKS], 1)
            dve.wait_ge(rstd_done, 1)
            for c in range(KC):
                dve.scalar_tensor_tensor(m.hT[:, c, :], m.xT[:, c, :], m.v("norm2_gain", c), rstd[:, :],
                                         ALU.mult, ALU.mult).then_inc(h_done, 1)


def routing_part(nc, m, a):
    NL = 4 + N_EXP
    with ExitStack() as ctx:
        def sem(n):
            return ctx.enter_context(nc.semaphore(n))

        def sb(n, s):
            return ctx.enter_context(nc.sbuf_tensor(n, s, F32))
        router_w = sb("router_w", [P, KC, NL])
        router_b = sb("router_b", [P, NL])
        logits = sb("logits", [P, TT, NL])
        group_max = sb("group_max", [P, TT, 1])
        group_exp = sb("group_exp", [P, TT, 4])
        group_p = sb("group_p", [P, TT, 1])
        value = sb("pick_value", [P, TT, N_EXP])
        value_max = sb("pick_max", [P, TT, 1])
        group_hot = sb("group_hot", [P, TT, 4])
        masked = sb("masked", [P, TT, N_EXP])
        top = sb("top", [P, 2, TT, 1])
        ratio = sb("ratio", [P, TT, 1])
        ratio_inv = sb("ratio_inv", [P, TT, 1])
        hot = sb("hot", [P, 2, TT, N_EXP])
        assign = sb("assign", [P, TT, N_EXP])
        gates = sb("gates", [P, TT, N_EXP])
        slot = sb("slot", [P, TT, N_EXP])
        past = sb("past", [P, TT, N_EXP])
        scratch = sb("route_scratch", [P, TT, N_EXP])
        blocks = sb("over_blocks", [P, N_EXP])
        blocks_col = sb("over_blocks_col", [N_EXP, 1])
        blocks_wide = sb("over_blocks_wide", [N_EXP, P])
        count_col = sb("count_col", [N_EXP, 1])
        ends = sb("ends", [P, N_EXP])
        before_end = sb("before_end", [P, OVER, N_EXP])
        weighted = sb("weighted", [P, TT, N_EXP, SLOTS])
        over_f = sb("over_f", [P, OVER + 1])

        filled, drained = m.filled, m.drained
        router_in, group_in, group_out, ratio_in, ratio_out, assigned, wide_done, weights_done = (
            sem("router_in"), sem("group_in"), sem("group_out"), sem("ratio_in"), sem("ratio_out"),
            sem("assigned"), sem("blocks_wide"), sem("weights_done"))
        U_LOG, U_RANK, U_START, U_GT = 0, 1, 2, 3

        block = ctx.enter_context(nc.Block())

        @block.sync
        def _(sp):
            for k, name, c0, c1 in ((0, "group", 0, 4), (1, "expert", 4, NL)):
                sp.dma_start(router_w[:, :, c0:c1], a[f"w_{name}_router"][0].rearrange("(c p) n -> p c n", p=P)
                             ).then_inc(router_in, 16)
                sp.dma_start(router_b[:, c0:c1], a[f"b_{name}_router"].to_broadcast([P, c1 - c0])
                             ).then_inc(router_in, 16)
            m.load_pair(sp, 0)

        @block.scalar
        def _(act):
            act.wait_ge(group_in, 1)
            act.activation(group_exp[:, :, :], group_exp[:, :, :], ACT.Exp).then_inc(group_out, 1)
            act.wait_ge(ratio_in, 1)
            act.activation(ratio[:, :, :], ratio[:, :, :], ACT.Exp).then_inc(ratio_out, 1)
            for n in range(8):
                q = U_GT + n
                act.wait_ge(filled[q % BANKS], q // BANKS + 1)
                act.activation(m.gate_T[:, 2 * n:2 * n + 2, :], m.ps[:, q % BANKS, :].rearrange("p (i t) -> p i t", i=2),
                               ACT.Copy).then_inc(drained[q % BANKS], 1)

        @block.tensor
        def _(pe):
            pe.wait_ge(router_in, 64)
            for t in range(TT):
                for k in range(KC):
                    mm = pe.matmul(m.ps[:, U_LOG, t * NL:(t + 1) * NL], m.hT[:, k, t * P:(t + 1) * P], router_w[:, k, :],
                                   start=(k == 0), stop=(k == KC - 1))
            mm.then_inc(filled[U_LOG], 1)
            pe.wait_ge(assigned, 1)
            out = m.ps[:, U_RANK, :]
            pe.matmul(out[:, 0:32], m.c("before"), assign[:, 0, :], start=True, stop=True)
            pe.matmul(out[:, 32:64], m.c("before"), assign[:, 1, :], start=True, stop=False)
            pe.matmul(out[:, 32:64], m.c("ones"), assign[:, 0, :], start=False, stop=True)
            pe.matmul(out[:, 64:96], m.c("ones"), assign[:, 0, :], start=True, stop=False)
            pe.matmul(out[:, 64:96], m.c("ones"), assign[:, 1, :], start=False, stop=True)
            pe.matmul(out[0:32, 96:97], assign[:, 0, :], m.c("ones")[:, 0:1], start=True, stop=False)
            pe.matmul(out[0:32, 96:97], assign[:, 1, :], m.c("ones")[:, 0:1], start=False, stop=True
                      ).then_inc(filled[U_RANK], 1)
            pe.wait_ge(wide_done, 1)
            pe.matmul(m.ps[:, U_START, 0:N_EXP], blocks_wide[:, :], m.c("before")[0:N_EXP, 0:N_EXP], start=True, stop=True
                      ).then_inc(filled[U_START], 1)
            pe.wait_ge(weights_done, 1)
            for n in range(8):
                q = U_GT + n
                if q >= BANKS:
                    pe.wait_ge(drained[q % BANKS], q // BANKS)
                for i in range(2):
                    pair = 2 * n + i
                    for t in range(TT):
                        mm = pe.transpose(m.ps[:, q % BANKS, i * SEQ + t * P:i * SEQ + (t + 1) * P],
                                          weighted[:, t, 2 * pair:2 * pair + 2, :], m.c("ident"))
                mm.then_inc(filled[q % BANKS], 1)

        @block.vector
        def _(dve):
            def op(ins):
                dve.drain()
                return ins

            def wide(x, n):
                return x.to_broadcast([P, TT, n])

            def const_rows(name, n):
                return m.c(name)[:, 0:n].rearrange("p (o n) -> p o n", o=1).to_broadcast([P, TT, n])

            def first_of_largest(dst, src, largest, n):
                v = value[:, :, 0:n]
                op(dve.tensor_reduce(largest, src, AX, ALU.max))
                op(dve.tensor_tensor(v, src, wide(largest, n), ALU.is_equal))
                op(dve.tensor_tensor(v, v, const_rows("first_pick", n), ALU.mult))
                op(dve.tensor_reduce(value_max[:, :, :], v, AX, ALU.max))
                op(dve.tensor_tensor(dst, v, wide(value_max[:, :, :], n), ALU.is_equal))

            dve.wait_ge(router_in, 64)
            dve.wait_ge(filled[U_LOG], 1)
            op(dve.tensor_tensor(logits[:, :, :], m.ps[:, U_LOG, 0:TT * NL].rearrange("p (t n) -> p t n", t=TT),
                                 router_b[:, :].rearrange("p (o n) -> p o n", o=1).to_broadcast([P, TT, NL]), ALU.add
                                 ).then_inc(drained[U_LOG], 1))
            group = logits[:, :, 0:4]
            first_of_largest(group_hot[:, :, :], group, group_max[:, :, :], 4)
            op(dve.tensor_tensor(group_exp[:, :, :], group, wide(group_max[:, :, :], 4), ALU.subtract
                                 ).then_inc(group_in, 1))
            op(dve.tensor_scalar(scratch[:, :, 0:4], group_hot[:, :, :], -NEG, NEG, ALU.mult, ALU.add))
            for t in range(TT):
                dve.tensor_tensor(masked[:, t, :].rearrange("p (g e) -> p g e", g=4),
                                  logits[:, t, 4:NL].rearrange("p (g e) -> p g e", g=4),
                                  scratch[:, t, 0:4].rearrange("p (g o) -> p g o", o=1).to_broadcast([P, 4, 8]), ALU.add)
            dve.drain()
            first_of_largest(hot[:, 0, :, :], masked[:, :, :], top[:, 0, :, :], N_EXP)
            op(dve.scalar_tensor_tensor(masked[:, :, :], hot[:, 0, :, :], NEG, masked[:, :, :], ALU.mult, ALU.add))
            first_of_largest(hot[:, 1, :, :], masked[:, :, :], top[:, 1, :, :], N_EXP)
            op(dve.tensor_tensor(assign[:, :, :], hot[:, 0, :, :], hot[:, 1, :, :], ALU.add).then_inc(assigned, 1))
            op(dve.tensor_tensor(ratio[:, :, :], top[:, 1, :, :], top[:, 0, :, :], ALU.subtract).then_inc(ratio_in, 1))
            dve.wait_ge(group_out, 1)
            op(dve.tensor_reduce(group_p[:, :, :], group_exp[:, :, :], AX, ALU.add))
            op(dve.reciprocal(group_p[:, :, :], group_p[:, :, :]))
            dve.wait_ge(ratio_out, 1)
            op(dve.tensor_scalar(ratio_inv[:, :, :], ratio[:, :, :], 1.0, None, ALU.add))
            op(dve.reciprocal(ratio_inv[:, :, :], ratio_inv[:, :, :]))
            op(dve.tensor_tensor(m.gate[:, 0, :, :], group_p[:, :, :], ratio_inv[:, :, :], ALU.mult))
            op(dve.tensor_tensor(m.gate[:, 1, :, :], m.gate[:, 0, :, :], ratio[:, :, :], ALU.mult))
            op(dve.tensor_tensor(gates[:, :, :], hot[:, 0, :, :], wide(m.gate[:, 0, :, :], N_EXP), ALU.mult))
            op(dve.tensor_tensor(scratch[:, :, :], hot[:, 1, :, :], wide(m.gate[:, 1, :, :], N_EXP), ALU.mult))
            op(dve.tensor_tensor(gates[:, :, :], gates[:, :, :], scratch[:, :, :], ALU.add))
            dve.wait_ge(filled[U_RANK], 1)
            rank = m.ps[:, U_RANK, 0:64].rearrange("p (t e) -> p t e", t=TT)
            count = m.ps[:, U_RANK, 64:96]
            op(dve.scalar_tensor_tensor(slot[:, :, :], rank, 1.0, assign[:, :, :], ALU.add, ALU.mult))
            dve.tensor_scalar(past[:, :, :], slot[:, :, :], float(SLOTS), None, ALU.is_gt)
            dve.tensor_copy(count_col[:, :], m.ps[0:N_EXP, U_RANK, 96:97])
            dve.tensor_scalar(blocks[:, :], count, float(SLOTS), None, ALU.is_gt)
            dve.drain()
            dve.tensor_scalar(blocks_col[:, :], count_col[:, :], float(SLOTS), None, ALU.is_gt)
            dve.drain()
            for k in (2, 3):
                dve.scalar_tensor_tensor(blocks[:, :], count, float(k * SLOTS), blocks[:, :], ALU.is_gt, ALU.add)
                dve.scalar_tensor_tensor(blocks_col[:, :], count_col[:, :], float(k * SLOTS), blocks_col[:, :],
                                         ALU.is_gt, ALU.add)
                dve.drain()
            dve.drain().then_inc(drained[U_RANK], 1)
            dve.tensor_copy(blocks_wide[:, :], blocks_col[:, :].to_broadcast([N_EXP, P])).then_inc(wide_done, 1)
            op(dve.tensor_scalar(slot[:, :, :], slot[:, :, :], -1.0, None, ALU.add))
            pairs = [P, TT * N_EXP, SLOTS]
            iota = m.c("slot_iota").rearrange("p (o n) -> p o n", o=1).to_broadcast(pairs)
            flat = "p t (e o) -> p (t e) o"
            op(dve.tensor_tensor(m.pick[:, :, :, :].rearrange("p t e n -> p (t e) n"), iota,
                                 slot[:, :, :].rearrange(flat, o=1).to_broadcast(pairs), ALU.is_equal))
            dve.tensor_tensor(weighted[:, :, :, :].rearrange("p t e n -> p (t e) n"),
                              m.pick[:, :, :, :].rearrange("p t e n -> p (t e) n"),
                              gates[:, :, :].rearrange(flat, o=1).to_broadcast(pairs), ALU.mult).then_inc(weights_done, 1)
            dve.wait_ge(filled[U_START], 1)
            start = m.ps[:, U_START, 0:N_EXP]
            op(dve.tensor_tensor(ends[:, :], start, blocks[:, :], ALU.add))
            for t in range(TT):
                dve.scalar_tensor_tensor(scratch[:, t, :], start, float(SLOTS), slot[:, t, :], ALU.mult, ALU.add)
            dve.drain().then_inc(drained[U_START], 1)
            op(dve.tensor_scalar(scratch[:, :, :], scratch[:, :, :], 1.0 - SLOTS, None, ALU.add))
            op(dve.tensor_tensor(scratch[:, :, :], scratch[:, :, :], past[:, :, :], ALU.mult))
            for k in range(2):
                op(dve.tensor_tensor(hot[:, k, :, :], hot[:, k, :, :], scratch[:, :, :], ALU.mult))
                op(dve.tensor_reduce(m.over_slot[:, k, :, :], hot[:, k, :, :], AX, ALU.add))
            op(dve.tensor_scalar(m.over_slot[:, :, :, :], m.over_slot[:, :, :, :], -1.0, None, ALU.add))
            op(dve.tensor_tensor(before_end[:, :, :],
                                 ends[:, :].rearrange("p (o n) -> p o n", o=1).to_broadcast([P, OVER, N_EXP]),
                                 m.c("over_iota").rearrange("p (j o) -> p j o", o=1).to_broadcast([P, OVER, N_EXP]),
                                 ALU.is_le))
            op(dve.tensor_reduce(over_f[:, 0:OVER], before_end[:, :, :], AX, ALU.add))
            op(dve.tensor_scalar(over_f[:, 0:OVER], over_f[:, 0:OVER], float(N_EXP - 1), None, ALU.min))
            op(dve.tensor_copy(over_f[:, OVER:OVER + 1], ends[:, N_EXP - 1:N_EXP]))
            op(dve.tensor_copy(m.over_int[:, :], over_f[:, :]))


def expert_part(nc, m, a):
    PAIRS = N_EXP // 2
    FC = D_EXP // P
    with ExitStack() as ctx:
        def sem(n):
            return ctx.enter_context(nc.semaphore(n))

        def sb(n, s):
            return ctx.enter_context(nc.sbuf_tensor(n, s, F32))
        x_pair = sb("x_pair", [P, KC, 2 * SLOTS])
        silu = sb("silu", [P, 2, FC, SLOTS])
        hidden = sb("hidden", [P, 2, FC, SLOTS])
        y_pair = sb("y_pair", [P, D])

        GATHER, GATE_UP, DOWN, SCATTER = 0, 2, 4, 6

        def started(n):
            return not (isinstance(n, int) and n == 0)

        def gather(pe, filled, drained, i, n):
            for j in range(2):
                b = GATHER + j
                if started(n):
                    pe.wait_ge(drained[b], n)
                for c in range(4):
                    for t in range(TT):
                        mm = pe.matmul(m.ps[:, b, c * P:(c + 1) * P], m.h_tok[:, t, (4 * j + c) * P:(4 * j + c + 1) * P],
                                       m.pick[:, t, :, :].rearrange("p e n -> p (e n)")[:, bass.ts(i, 2 * SLOTS)],
                                       start=(t == 0), stop=(t == TT - 1))
                mm.then_inc(filled[b], 1)

        def gate_up(pe, filled, drained, landed, e, n):
            b = GATE_UP + e
            if started(n):
                pe.wait_ge(drained[b], n)
            if e == 0:
                for j in range(2):
                    pe.wait_ge(drained[GATHER + j], n + 1)
            for k, (w, name) in enumerate(((m.gate_w, "gate"), (m.up_w, "up"))):
                pe.wait_ge(landed[name, e], 16 * n + 16)
                for f in range(FC):
                    at = (k * FC + f) * SLOTS
                    for c in range(KC):
                        mm = pe.matmul(m.ps[:, b, at:at + SLOTS], w[:, e, c, f * P:(f + 1) * P],
                                       x_pair[:, c, e * SLOTS:(e + 1) * SLOTS], start=(c == 0), stop=(c == KC - 1))
            mm.then_inc(filled[b], 1)

        def down(pe, filled, drained, landed, e, n):
            if e == 0 and started(n):
                for j in range(2):
                    pe.wait_ge(drained[DOWN + j], n)
            pe.wait_ge(drained[GATE_UP + e], n + 1)
            pe.wait_ge(landed["down", e], 16 * n + 16)
            for j in range(2):
                for f in range(FC):
                    mm = pe.matmul(m.ps[e * SLOTS:(e + 1) * SLOTS, DOWN + j, :], hidden[:, e, f, :],
                                   m.down_w[:, e, f, j * 512:(j + 1) * 512], start=(f == 0), stop=(f == FC - 1))
                mm.then_inc(filled[DOWN + j], 1)

        def scatter(pe, filled, drained, i, n):
            for q in range(4):
                b = SCATTER + q % 2
                if started(n) or q >= 2:
                    pe.wait_ge(drained[b], 2 * n + q // 2)
                if q == 0:
                    for j in range(2):
                        pe.wait_ge(drained[DOWN + j], n + 1)
                for c in range(2):
                    d = 2 * q + c
                    mm = pe.matmul(m.ps[:, b, c * SEQ:(c + 1) * SEQ], y_pair[:, d * P:(d + 1) * P],
                                   m.gate_T[:, :, :].rearrange("p i t -> p (i t)")[:, bass.ts(i, SEQ)],
                                   start=True, stop=True)
                mm.then_inc(filled[b], 1)

        def act_pair(act, filled, drained, silu_done, hidden_done, n):
            for e in range(2):
                act.wait_ge(filled[GATE_UP + e], n + 1)
                act.activation(silu[:, e, :, :], m.ps[:, GATE_UP + e, 0:FC * SLOTS].rearrange("p (f n) -> p f n", f=FC),
                               ACT.Silu).then_inc(silu_done, 1)
            for j in range(2):
                act.wait_ge(filled[DOWN + j], 2 * n + 2)
                act.activation(y_pair[:, j * 512:(j + 1) * 512], m.ps[:, DOWN + j, :], ACT.Copy
                               ).then_inc(drained[DOWN + j], 1)

        def dve_gather(dve, filled, drained, n):
            for j in range(2):
                b = GATHER + j
                dve.wait_ge(filled[b], n + 1)
                dve.tensor_copy(x_pair[:, 4 * j:4 * j + 4, :], m.ps[:, b, :].rearrange("p (c n) -> p c n", c=4)
                                ).then_inc(drained[b], 1)

        def dve_hidden(dve, filled, drained, silu_done, n):
            for e in range(2):
                b = GATE_UP + e
                dve.wait_ge(silu_done, 2 * n + e + 1)
                dve.tensor_tensor(hidden[:, e, :, :], m.ps[:, b, FC * SLOTS:2 * FC * SLOTS].rearrange(
                    "p (f n) -> p f n", f=FC), silu[:, e, :, :], ALU.mult).then_inc(drained[b], 1)

        def dve_scatter(dve, filled, drained, n):
            for q in range(4):
                b = SCATTER + q % 2
                dve.wait_ge(filled[b], 2 * n + q // 2 + 1)
                x = m.xT[:, 2 * q:2 * q + 2, :]
                dve.tensor_tensor(x, m.ps[:, b, :].rearrange("p (c t) -> p c t", c=2), x, ALU.add
                                  ).then_inc(drained[b], 1)
            dve.drain()

        filled, drained = m.filled, m.drained
        silu_done = sem("silu_done")
        with nc.Block() as block:
            @block.sync
            def _(sp):
                with sp.Fori(1, PAIRS) as i:
                    for e in range(2):
                        sp.wait_ge(filled[GATE_UP + e], i)
                        m.load_gate_up(sp, e, 2 * i + e)
                    for e in range(2):
                        sp.wait_ge(filled[DOWN + 1], 2 * i - 1 + e)
                        m.load_down(sp, e, 2 * i + e)

            @block.tensor
            def _(pe):
                gather(pe, filled, drained, 0, 0)

                def pair(i, first=False, last=False):
                    for e in range(2):
                        gate_up(pe, filled, drained, m.landed, e, i)
                    if not first:
                        scatter(pe, filled, drained, i - 1, i - 1)
                    if not last:
                        gather(pe, filled, drained, i + 1, i + 1)
                    for e in range(2):
                        down(pe, filled, drained, m.landed, e, i)
                pair(0, first=True)
                with pe.Fori(1, PAIRS - 1) as i:
                    pair(i)
                pair(PAIRS - 1, last=True)
                scatter(pe, filled, drained, PAIRS - 1, PAIRS - 1)

            @block.scalar
            def _(act):
                with act.Fori(0, PAIRS) as i:
                    act_pair(act, filled, drained, silu_done, None, i)

            @block.vector
            def _(dve):
                dve_gather(dve, filled, drained, 0)

                def pair(i, first=False, last=False):
                    dve_hidden(dve, filled, drained, silu_done, i)
                    if not first:
                        dve_scatter(dve, filled, drained, i - 1)
                    if not last:
                        dve_gather(dve, filled, drained, i + 1)
                pair(0, first=True)
                with dve.Fori(1, PAIRS - 1) as i:
                    pair(i)
                pair(PAIRS - 1, last=True)
                dve_scatter(dve, filled, drained, PAIRS - 1)

        m.clear_banks()
        over_filled, over_drained = filled, drained
        over_silu, over_pick = sem("over_silu"), sem("over_pick")
        over_landed = {(n, e): sem(f"over_{n}{e}") for n in ("gate", "up", "down") for e in range(2)}
        equal = ctx.enter_context(nc.sbuf_tensor("over_equal", [P, 2, OVER * SLOTS], F32))
        over_weighted = ctx.enter_context(nc.sbuf_tensor("over_weighted", [P, TT, OVER * SLOTS], F32))
        turn_filled, turn_drained = sem("turn_filled"), sem("turn_drained")
        with nc.Block() as block:
            def blocks(eng):
                return eng.value_load(m.over_int[0:1, OVER:OVER + 1], min_val=0, max_val=OVER)

            @block.sync
            def _(sp):
                with sp.If(blocks(sp) > 0):
                    for i in range(OVER // 2):
                        for e in range(2):
                            j = 2 * i + e
                            expert = sp.value_load(m.over_int[0:1, j:j + 1], min_val=0, max_val=N_EXP - 1)
                            if i > 0:
                                sp.wait_ge(over_filled[GATE_UP + e], i)
                            m.load_gate_up(sp, e, expert, over_landed)
                            if i > 0:
                                sp.wait_ge(over_filled[DOWN + 1], 2 * i - 1 + e)
                            m.load_down(sp, e, expert, over_landed)

            @block.tensor
            def _(pe):
                with pe.If(blocks(pe) > 0):
                    pe.wait_ge(over_pick, 1)
                    for i in range(OVER // 2):
                        if i >= 2:
                            pe.wait_ge(turn_drained, i - 1)
                        for t in range(TT):
                            mm = pe.transpose(m.ps[:, GATE_UP + i % 2, t * P:(t + 1) * P],
                                              over_weighted[:, t, i * P:(i + 1) * P], m.c("ident"))
                        mm.then_inc(turn_filled, 1)
                    pe.wait_ge(turn_drained, OVER // 2)

                    def pair(i):
                        gather(pe, over_filled, over_drained, i, i)
                        for e in range(2):
                            gate_up(pe, over_filled, over_drained, over_landed, e, i)
                        for e in range(2):
                            down(pe, over_filled, over_drained, over_landed, e, i)
                        scatter(pe, over_filled, over_drained, i, i)
                    pair(0)
                    with pe.Fori(1, OVER // 2) as i:
                        pair(i)

            @block.scalar
            def _(act):
                with act.If(blocks(act) > 0):
                    for i in range(OVER // 2):
                        act.wait_ge(turn_filled, i + 1)
                        act.activation(m.gate_T[:, i, :], m.ps[:, GATE_UP + i % 2, 0:SEQ], ACT.Copy
                                       ).then_inc(turn_drained, 1)
                    with act.Fori(0, OVER // 2) as i:
                        act_pair(act, over_filled, over_drained, over_silu, None, i)

            @block.vector
            def _(dve):
                with dve.If(blocks(dve) > 0):
                    n = OVER * SLOTS
                    for t in range(TT):
                        for k in range(2):
                            dve.tensor_scalar(equal[:, k, :], m.c("over_slots"), m.over_slot[:, k, t, :], None, ALU.is_equal)
                        dve.drain()
                        dve.tensor_tensor(m.pick[:, t, 0:OVER, :].rearrange("p e n -> p (e n)"), equal[:, 0, :],
                                          equal[:, 1, :], ALU.add)
                        dve.tensor_scalar(over_weighted[:, t, :], equal[:, 0, :], m.gate[:, 0, t, :], None, ALU.mult)
                        dve.drain()
                        dve.scalar_tensor_tensor(over_weighted[:, t, :], equal[:, 1, :], m.gate[:, 1, t, :],
                                                 over_weighted[:, t, :], ALU.mult, ALU.add)
                        dve.drain()
                    dve.drain().then_inc(over_pick, 1)
                    with dve.Fori(0, OVER // 2) as i:
                        dve_gather(dve, over_filled, over_drained, i)
                        dve_hidden(dve, over_filled, over_drained, over_silu, i)
                        dve_scatter(dve, over_filled, over_drained, i)


def expert_loads(nc, m, a):
    def load_gate_up(sp, e, expert, landed=None):
        landed = landed or m.landed
        for w, name in ((m.gate_w, "gate"), (m.up_w, "up")):
            src = a[f"w_expert_{name}"][0].rearrange("e (c p) n -> e p c n", p=P)
            sp.dma_start(w[:, e, :, :], src[bass.ds(expert, 1), :, :, :].rearrange("o p c n -> (o p) c n")
                         ).then_inc(landed[name, e], 16)

    def load_down(sp, e, expert, landed=None):
        landed = landed or m.landed
        src = a["w_expert_down"][0].rearrange("e (c p) n -> e p c n", p=P)
        sp.dma_start(m.down_w[:, e, :, :], src[bass.ds(expert, 1), :, :, :].rearrange("o p c n -> (o p) c n")
                     ).then_inc(landed["down", e], 16)

    def load_pair(sp, i):
        for e in range(2):
            load_gate_up(sp, e, 2 * i + e)
        for e in range(2):
            load_down(sp, e, 2 * i + e)
    m.load_gate_up, m.load_down, m.load_pair = load_gate_up, load_down, load_pair


def _units():
    at, n = {}, 0
    for name, count in (("vec", 1), ("ss_mix", 1), ("proj", 12), ("swap", 2), ("conf_mean", 1), ("sb_score", 4),
                        ("conf_var", 1), ("tail", 4), ("ret_score", 4), ("sb_out", 2), ("ret_out", 2),
                        ("ret_mean", 1), ("ret_var", 1), ("out", 4), ("ss_post", 1), ("ss_ffn", 1), ("up", 22),
                        ("down", 8), ("ss_ffn_post", 1)):
        at[name] = n
        n += count
    return at, n


UNIT, UNITS2 = _units()
SLICES = ("conf_a", "conf_gate", "sc_b", "sc_c", "sc_h", "sb_q", "sb_k", "sb_v", "ret_q", "ret_k", "ret_v", "ret_g")
SLICE_COL = {"conf_a": 0, "conf_gate": 1, "sb_q": 2, "sb_k": 3, "sb_v": 4, "ret_q": 5, "ret_k": 6, "ret_v": 7,
             "ret_g": 8, "sc_b": 9, "sc_c": 10, "sc_h": 11}
FF = DFF // P
PIECES = 12 + 4 + FF + 8
SLOTS2 = 6
TAPS = 31


def layers_part(nc, m, a):
    with ExitStack() as ctx:
        def sem(n):
            return ctx.enter_context(nc.semaphore(n))

        def sb(n, s):
            return ctx.enter_context(nc.sbuf_tensor(n, s, F32))
        ring = sb("ring2", [P, SLOTS2, DFF])
        rows1 = sb("rows1", [P, P])
        rows2 = sb("rows2", [FF * 2, 3, P])
        vec = sb("vec2", [P, P])
        ff_taps = sb("ff_taps", [P, 3, 2 * FF])
        square = sb("square2", [P, KC, SEQ])
        log_ms = sb("log2", [P, SEQ])
        rstd = sb("rstd2", [P, SEQ])
        slices = sb("slices", [P, 12, 2, SEQ])
        s_ = {n: slices[:, i, :, :] for i, n in enumerate(SLICES)}
        padded = sb("conf_pad", [P, 2, SEQ + TAPS - 1])
        conf = sb("conf_acc", [P, 2, SEQ])
        conf_sq = sb("conf_sq", [P, 2, SEQ])
        conf_rs = sb("conf_rs", [P, SEQ])
        sc_pad = sb("sc_pad", [P, 2, SEQ + 2])
        W3 = 3 * P
        sb_z = sb("sb_z", [P, 4, W3])
        sb_l = sb("sb_l", [P, 4, W3])
        sb_pos = sb("sb_pos", [P, 4, W3])
        ret_p = sb("ret_p", [P, 4, W3])
        turned = sb("ret_turned", [P, 2, 2, SEQ])
        turn_tmp = sb("turn_tmp", [P, 2, SEQ])
        ret_o = sb("ret_o", [P, 2, SEQ])
        ret_sq = sb("ret_sq", [P, 2, SEQ])
        ret_rs = sb("ret_rs", [P, 2, SEQ])
        y = sb("y_mix", [P, KC, SEQ])
        branch = sb("branch", [P, KC, SEQ])
        hid = slices[:, :, :, :].rearrange("p s c t -> p (s c) t")[:, 0:FF, :]
        ff = sb("ff", [P, 2, 2, SEQ])
        silu = sb("silu2", [P, 2, SEQ])

        landed = [sem(f"landed2_{i}") for i in range(SLOTS2)]
        filled, drained = m.filled, m.drained
        total = {"rows_in": 16 * 13, "squared": 16, "norm_done": 4, "h_done": 16, "conf_done": 1, "conf_centred": 1,
                 "conf_squared": 1, "conf_rstd": 1, "conf_out": 1, "sc_out": 1, "turned": 2, "soft_in": 4,
                 "soft_ln": 4, "sb_masked": 4, "sb_arg": 4, "sb_exp": 4, "ret_masked": 4, "ret_centred": 1,
                 "ret_squared": 1, "ret_rstd": 1, "ret_done": 1, "tap_scaled": FF, "conv_done": FF, "silu_done": FF,
                 "hid_done": FF, "conf_normed": 1, "x_done": 2}
        S = {n: sem(n) for n in total}
        
        def turns(b):
            return (UNITS2 - b + BANKS - 1) // BANKS

        def upto(l, n):
            return l * turns(n % BANKS) + n // BANKS + 2

        def before(l, n):
            return l * turns(n % BANKS) + n // BANKS + 1

        def await_filled(eng, l, n):
            eng.wait_ge(filled[n % BANKS], upto(l, n))
            return n % BANKS

        def await_drained(eng, l, n):
            eng.wait_ge(drained[n % BANKS], upto(l, n))

        def signalled(eng, l, name, k):
            eng.wait_ge(S[name], l * total[name] + k)

        def v(name, i):
            return vec[:, VEC2[name] + i:VEC2[name] + i + 1]

        def two(x):
            return x.rearrange("p (c t) -> p c t", c=2)

        def piece_unit(i):
            if i < 12:
                return UNIT["proj"] + i
            if i < 16:
                return UNIT["out"] + i - 12
            if i < 16 + FF:
                return UNIT["up"] + i - 16
            return UNIT["down"] + i - 16 - FF

        def slot_uses(s):
            return (PIECES - s + SLOTS2 - 1) // SLOTS2

        def await_piece(pe, l, i):
            s = i % SLOTS2
            pe.wait_ge(landed[s], (l * slot_uses(s) + i // SLOTS2 + 1) * 16)
            return s

        with nc.Block() as block:
            @block.gpsimd
            def _(pool):
                pool.memset(padded[:, :, 0:TAPS - 1], 0.0)
                pool.memset(sc_pad[:, :, 0:2], 0.0)
                pool.memset(rows1[:, :], 0.0)
                for b in range(BANKS):
                    pool.sem_inc(filled[b], 1)
                    pool.sem_inc(drained[b], 1)


        def load_piece(sp, l, i):
            s = i % SLOTS2

            def of_layer(name):
                return a[name][bass.ds(l, 1)].rearrange("o (c p) n -> (o p) c n", p=P)
            dst = ring[:, s, 0:KC * 256]
            if i < 16:
                name, c = ("w_in_2", SLICE_COL[SLICES[i]]) if i < 12 else ("w_out_2", i - 12)
                dst = dst.rearrange("p (c n) -> p c n", c=KC)
                src = of_layer(name)[:, :, c * 256:(c + 1) * 256]
            elif i < 16 + FF:
                dst = dst.rearrange("p (h c n) -> p h c n", h=2, c=KC)
                src = a["ffn_up_2"][bass.ds(l, 1)].rearrange("o (c p) (h j n) -> (o p) h c j n", p=P, h=2, n=P
                                                             )[:, :, :, i - 16, :]
            else:
                dst = ring[:, s, :].rearrange("p (c n) -> p c n", c=FF)
                c = (i - 16 - FF) * P
                src = of_layer("ffn_down_2")[:, :, c:c + P]
            sp.dma_start(dst, src).then_inc(landed[s], 16)

        def load_rows(pool, l):
            n = 0
            for name in ("norm_mix_pre_2", "norm_mix_post_2", "norm_ffn_pre_2", "norm_ffn_post_2", "conf_dw_b_2",
                         "conf_ln_g_2", "conf_ln_b_2", "ret_norm_g_2"):
                src = a[name][l:l + 1, :].rearrange("o (c p) -> (o c) p", p=P)
                pool.dma_start(rows1[VEC2[name]:VEC2[name] + src.shape[0], :], src).then_inc(S["rows_in"], 16)
                n += 1
            for name in ("sc_conv_w_2", "conf_dw_w_2"):
                src = a[name][l].rearrange("k (c p) -> (k c) p", p=P)
                pool.dma_start(rows1[VEC2[name]:VEC2[name] + src.shape[0], :], src).then_inc(S["rows_in"], 16)
                n += 1
            for k in range(3):
                pool.dma_start(rows2[:, k, :], a["ffn_conv_w_2"][l, k, :].rearrange("(c p) -> c p", p=P)
                               ).then_inc(S["rows_in"], 16)
                n += 1
            assert 16 * n == total["rows_in"]

        block = ctx.enter_context(nc.Block())

        @block.sync
        def _(sp):
            for i in range(SLOTS2):
                load_piece(sp, 0, i)
            with sp.Fori(0, 2) as l:
                for i in range(SLOTS2, PIECES):
                    n = piece_unit(i - SLOTS2)
                    sp.wait_ge(filled[n % BANKS], upto(l, n))
                    load_piece(sp, l, i)
                with sp.If(l < 1):
                    for i in range(SLOTS2):
                        last = max(j for j in range(PIECES) if j % SLOTS2 == i)
                        n = piece_unit(last)
                        sp.wait_ge(filled[n % BANKS], upto(0, n))
                        load_piece(sp, 1, i)

        @block.gpsimd
        def _(pool):
            load_rows(pool, 0)
            n = UNIT["vec"]
            pool.wait_ge(filled[n % BANKS], upto(0, n))
            load_rows(pool, 1)

        @block.tensor
        def _(pe):
            with pe.Fori(0, 2) as l:
                def free(n):
                    pe.wait_ge(drained[n % BANKS], before(l, n))
                    return n % BANKS

                def ss(unit, first):
                    b = free(UNIT[unit])
                    for c in range(KC):
                        signalled(pe, l, "squared", first + c // 2 + 1)
                        mm = pe.matmul(m.ps[:, b, 0:SEQ], m.c("ones"), square[:, c, :], start=(c == 0), stop=(c == KC - 1))
                    mm.then_inc(filled[b], 1)

                def masked_scores(unit, k_src, q_src):
                    for h in range(4):
                        b = free(UNIT[unit] + h)
                        r, c = slice((h % 2) * HEAD, (h % 2 + 1) * HEAD), h // 2
                        pe.matmul(m.ps[:, b, 0:SEQ], k_src[r, c, 0:P], q_src[r, c, :], start=True, stop=True)
                        pe.matmul(m.ps[:, b, SEQ:W3], k_src[r, c, P:SEQ], q_src[r, c, P:SEQ], start=True, stop=True
                                  ).then_inc(filled[b], 1)

                def outputs(unit, values, probs, ready):
                    for c in range(2):
                        b = free(UNIT[unit] + c)
                        for h in (2 * c, 2 * c + 1):
                            signalled(pe, l, ready, h + 1)
                            out = m.ps[(h % 2) * HEAD:(h % 2 + 1) * HEAD, b, :]
                            cols = slice(h * HEAD, (h + 1) * HEAD)
                            pe.matmul(out[:, 0:SEQ], values[:, 0, cols], probs[:, h, 0:SEQ], start=True, stop=False)
                            mm = pe.matmul(out[:, P:SEQ], values[:, 1, cols], probs[:, h, SEQ:W3], start=False, stop=True)
                        mm.then_inc(filled[b], 1)

                def product(unit, w, x, order):
                    b = free(unit)
                    for j in range(2):
                        for n, k in enumerate(order):
                            mm = pe.matmul(m.ps[:, b, j * SEQ:(j + 1) * SEQ], w(k, j), x[:, k, :],
                                           start=(n == 0), stop=(n == len(order) - 1))
                    mm.then_inc(filled[b], 1)

                b = free(UNIT["vec"])
                pe.wait_ge(S["rows_in"], l * total["rows_in"] + total["rows_in"])
                pe.transpose(m.ps[:, b, 0:P], rows1[:, :], m.c("ident"))
                for k in range(3):
                    mm = pe.transpose(m.ps[:, b, P + 2 * FF * k:P + 2 * FF * (k + 1)], rows2[:, k, :],
                                      m.c("ident")[0:2 * FF, 0:2 * FF])
                mm.then_inc(filled[b], 1)
                ss("ss_mix", 0)
                for i, name in enumerate(SLICES):
                    s = await_piece(pe, l, i)
                    w = ring[:, s, 0:KC * 256].rearrange("p (c n) -> p c n", c=KC)
                    if i == 0:
                        signalled(pe, l, "h_done", KC)
                    if name in ("sb_v", "ret_v"):
                        b = free(UNIT["proj"] + i)
                        for t in range(TT):
                            for k in range(KC):
                                mm = pe.matmul(m.ps[:, b, t * 256:(t + 1) * 256], m.hT[:, k, t * P:(t + 1) * P], w[:, k, :],
                                               start=(k == 0), stop=(k == KC - 1))
                        mm.then_inc(filled[b], 1)
                    else:
                        product(UNIT["proj"] + i, lambda k, j: w[:, k, j * P:(j + 1) * P], m.hT, range(KC))
                for i, name in enumerate(("ret_q", "ret_k")):
                    await_drained(pe, l, UNIT["proj"] + SLICES.index(name))
                    b = free(UNIT["swap"] + i)
                    pe.matmul(m.ps[:, b, :], m.c("swap"), s_[name], start=True, stop=True).then_inc(filled[b], 1)
                signalled(pe, l, "conf_done", 1)
                b = free(UNIT["conf_mean"])
                for c in range(2):
                    mm = pe.matmul(m.ps[:, b, 0:SEQ], m.c("ones"), conf[:, c, :], start=(c == 0), stop=(c == 1))
                mm.then_inc(filled[b], 1)
                for name in ("sb_q", "sb_k"):
                    await_drained(pe, l, UNIT["proj"] + SLICES.index(name))
                masked_scores("sb_score", s_["sb_k"], s_["sb_q"])
                signalled(pe, l, "conf_squared", 1)
                b = free(UNIT["conf_var"])
                for c in range(2):
                    mm = pe.matmul(m.ps[:, b, 0:SEQ], m.c("ones"), conf_sq[:, c, :], start=(c == 0), stop=(c == 1))
                mm.then_inc(filled[b], 1)
                for h in range(4):
                    signalled(pe, l, "sb_masked", h + 1)
                    b = free(UNIT["tail"] + h)
                    pe.matmul(m.ps[:, b, 0:SEQ], m.c("down"), sb_l[:, h, 0:SEQ], start=True, stop=False)
                    pe.matmul(m.ps[:, b, P:SEQ], m.c("ones"), sb_l[:, h, SEQ:W3], start=False, stop=True)
                    pe.matmul(m.ps[:, b, SEQ:W3], m.c("down"), sb_l[:, h, SEQ:W3], start=True, stop=True
                              ).then_inc(filled[b], 1)
                signalled(pe, l, "turned", 2)
                masked_scores("ret_score", turned[:, 1, :, :], turned[:, 0, :, :])
                await_drained(pe, l, UNIT["proj"] + SLICES.index("sb_v"))
                outputs("sb_out", s_["sb_v"], sb_z, "sb_exp")
                await_drained(pe, l, UNIT["proj"] + SLICES.index("ret_v"))
                outputs("ret_out", s_["ret_v"], ret_p, "ret_masked")
                for c in range(2):
                    await_drained(pe, l, UNIT["ret_out"] + c)
                b = free(UNIT["ret_mean"])
                pe.matmul(m.ps[:, b, :], m.c("pair_ones"), ret_o[:, :, :], start=True, stop=True).then_inc(filled[b], 1)
                signalled(pe, l, "ret_squared", 1)
                b = free(UNIT["ret_var"])
                pe.matmul(m.ps[:, b, :], m.c("pair_ones"), ret_sq[:, :, :], start=True, stop=True).then_inc(filled[b], 1)
                signalled(pe, l, "conf_out", 1)
                signalled(pe, l, "sc_out", 1)
                for c in range(2):
                    await_drained(pe, l, UNIT["sb_out"] + c)
                signalled(pe, l, "ret_done", 1)
                for i in range(4):
                    s = await_piece(pe, l, 12 + i)
                    w = ring[:, s, 0:KC * 256].rearrange("p (c n) -> p c n", c=KC)
                    product(UNIT["out"] + i, lambda k, j: w[:, k, j * P:(j + 1) * P], y, range(KC))
                ss("ss_post", 4)
                ss("ss_ffn", 8)
                signalled(pe, l, "h_done", 2 * KC)
                for i in range(FF):
                    s = await_piece(pe, l, 16 + i)
                    w = ring[:, s, 0:KC * 256].rearrange("p (h c n) -> p h c n", h=2, c=KC)
                    product(UNIT["up"] + i, lambda k, j: w[:, j, k, :], m.hT, range(KC))
                for i in range(KC):
                    s = await_piece(pe, l, 16 + FF + i)
                    w = ring[:, s, :].rearrange("p (c n) -> p c n", c=FF)
                    b = free(UNIT["down"] + i)
                    for k in range(FF):
                        if i == 0:
                            signalled(pe, l, "hid_done", k + 1)
                        mm = pe.matmul(m.ps[:, b, 0:SEQ], w[:, k, :], hid[:, k, :], start=(k == 0), stop=(k == FF - 1))
                    mm.then_inc(filled[b], 1)
                ss("ss_ffn_post", 12)

        @block.scalar
        def _(act):
            with act.Fori(0, 2) as l:
                def norm(unit, n):
                    b = await_filled(act, l, UNIT[unit])
                    act.activation(log_ms[:, :], m.ps[:, b, 0:SEQ], ACT.Ln, bias=m.c("eps"), scale=1.0 / D
                                   ).then_inc(drained[b], 1)
                    act.drain()
                    act.activation(rstd[:, :], log_ms[:, :], ACT.Exp, scale=-0.5).then_inc(S["norm_done"], 1)

                def squares(src, when):
                    for j in range(4):
                        when(j)
                        act.activation(square[:, 2 * j:2 * j + 2, :], src[:, 2 * j:2 * j + 2, :], ACT.Square
                                       ).then_inc(S["squared"], 1)

                def copy(dst, n, func=ACT.Copy):
                    b = await_filled(act, l, n)
                    act.activation(dst, two(m.ps[:, b, :]), func).then_inc(drained[b], 1)

                act.wait_ge(S["x_done"], l * 2 + 1)
                squares(m.xT, lambda j: None)
                norm("ss_mix", 0)
                for i, name in enumerate(SLICES):
                    copy(s_[name], UNIT["proj"] + i,
                         {"conf_gate": ACT.Sigmoid, "ret_g": ACT.Silu}.get(name, ACT.Copy))
                for h in range(4):
                    signalled(act, l, "soft_in", h + 1)
                    act.activation(sb_l[:, h, :], sb_l[:, h, :], ACT.Exp, scale=-1.0)
                    act.drain()
                    act.activation(sb_l[:, h, :], sb_l[:, h, :], ACT.Ln, bias=1.0).then_inc(S["soft_ln"], 1)
                    if h == 1:
                        signalled(act, l, "conf_centred", 1)
                        act.activation(conf_sq[:, :, :], conf[:, :, :], ACT.Square).then_inc(S["conf_squared"], 1)
                b = await_filled(act, l, UNIT["conf_var"])
                act.activation(conf_rs[:, :], m.ps[:, b, 0:SEQ], ACT.Ln, bias=m.c("eps"), scale=1.0 / 256
                               ).then_inc(drained[b], 1)
                act.drain()
                act.activation(conf_rs[:, :], conf_rs[:, :], ACT.Exp, scale=-0.5).then_inc(S["conf_rstd"], 1)
                for h in range(4):
                    signalled(act, l, "sb_arg", h + 1)
                    act.activation(sb_z[:, h, :], sb_z[:, h, :], ACT.Exp).then_inc(S["sb_exp"], 1)
                for c in range(2):
                    b = await_filled(act, l, UNIT["sb_out"] + c)
                    act.activation(y[:, 2 + c, :], m.ps[:, b, 0:SEQ], ACT.Copy).then_inc(drained[b], 1)
                for c in range(2):
                    b = await_filled(act, l, UNIT["ret_out"] + c)
                    act.activation(ret_o[:, c, :], m.ps[:, b, 0:SEQ], ACT.Copy).then_inc(drained[b], 1)
                signalled(act, l, "ret_centred", 1)
                act.activation(ret_sq[:, :, :], ret_o[:, :, :], ACT.Square).then_inc(S["ret_squared"], 1)
                b = await_filled(act, l, UNIT["ret_var"])
                act.activation(ret_rs[:, :, :], two(m.ps[:, b, :]), ACT.Ln, bias=m.c("eps"), scale=1.0 / HEAD
                               ).then_inc(drained[b], 1)
                act.drain()
                act.activation(ret_rs[:, :, :], ret_rs[:, :, :], ACT.Exp, scale=-0.5).then_inc(S["ret_rstd"], 1)
                signalled(act, l, "conf_normed", 1)
                for c in range(2):
                    ins = act.activation(y[:, c, :], conf[:, c, :], ACT.Silu, bias=v("conf_ln_b_2", c),
                                         scale=v("conf_ln_g_2", c))
                ins.then_inc(S["conf_out"], 1)
                for i in range(4):
                    copy(branch[:, 2 * i:2 * i + 2, :], UNIT["out"] + i)
                squares(branch, lambda j: await_drained(act, l, UNIT["out"] + j))
                norm("ss_post", 1)
                act.wait_ge(S["x_done"], l * 2 + 2)
                squares(m.xT, lambda j: None)
                norm("ss_ffn", 2)
                for i in range(FF):
                    b = await_filled(act, l, UNIT["up"] + i)
                    if i >= 2:
                        signalled(act, l, "hid_done", i - 1)
                    for j in range(2):
                        ins = act.activation(ff[:, i % 2, j, :], m.ps[:, b, j * SEQ:(j + 1) * SEQ], ACT.Copy,
                                             scale=ff_taps[:, 2, j * FF + i:j * FF + i + 1])
                    ins.then_inc(S["tap_scaled"], 1)
                    if i >= 1:
                        signalled(act, l, "conv_done", i)
                        act.activation(silu[:, (i - 1) % 2, :], ff[:, (i - 1) % 2, 0, :], ACT.Silu).then_inc(S["silu_done"], 1)
                signalled(act, l, "conv_done", FF)
                act.activation(silu[:, (FF - 1) % 2, :], ff[:, (FF - 1) % 2, 0, :], ACT.Silu).then_inc(S["silu_done"], 1)
                for i in range(KC):
                    b = await_filled(act, l, UNIT["down"] + i)
                    act.activation(branch[:, i, :], m.ps[:, b, 0:SEQ], ACT.Copy).then_inc(drained[b], 1)
                squares(branch, lambda j: await_drained(act, l, UNIT["down"] + 2 * j + 1))
                norm("ss_ffn_post", 3)

        @block.vector
        def _(dve):
            dve.drain().then_inc(S["x_done"], 1)
            with dve.Fori(0, 2) as l:
                def scaled(dst, src, gain, n):
                    signalled(dve, l, "norm_done", n + 1)
                    for c in range(KC):
                        ins = dve.scalar_tensor_tensor(dst[:, c, :], src[:, c, :], v(gain, c), rstd[:, :], ALU.mult, ALU.mult)
                        yield ins

                def residual(gain, n):
                    for _ in scaled(branch, branch, gain, n):
                        pass
                    dve.drain()
                    dve.tensor_tensor(m.xT[:, :, :], m.xT[:, :, :], branch[:, :, :], ALU.add)
                    dve.drain().then_inc(S["x_done"], 1)

                b = await_filled(dve, l, UNIT["vec"])
                dve.tensor_copy(vec[:, :], m.ps[:, b, 0:P])
                dve.tensor_copy(ff_taps[:, :, :], m.ps[:, b, P:P + 6 * FF].rearrange("p (k c) -> p k c", k=3)
                                ).then_inc(drained[b], 1)
                dve.drain()
                for ins in scaled(m.hT, m.xT, "norm_mix_pre_2", 0):
                    ins.then_inc(S["h_done"], 1)
                for name in ("conf_a", "conf_gate"):
                    await_drained(dve, l, UNIT["proj"] + SLICES.index(name))
                dve.tensor_tensor(padded[:, :, TAPS - 1:], s_["conf_a"], s_["conf_gate"], ALU.mult)
                dve.drain()
                for k in range(TAPS):
                    for c in range(2):
                        src = padded[:, c, k:k + SEQ]
                        tap = v("conf_dw_w_2", 2 * k + c)
                        if k == 0:
                            dve.tensor_scalar(conf[:, c, :], src, tap, v("conf_dw_b_2", c), ALU.mult, ALU.add)
                        else:
                            dve.scalar_tensor_tensor(conf[:, c, :], src, tap, conf[:, c, :], ALU.mult, ALU.add)
                    dve.drain()
                dve.drain().then_inc(S["conf_done"], 1)
                for name in ("sc_b", "sc_c", "sc_h"):
                    await_drained(dve, l, UNIT["proj"] + SLICES.index(name))
                dve.tensor_tensor(sc_pad[:, :, 2:], s_["sc_c"], s_["sc_h"], ALU.mult)
                dve.drain()
                for k in range(3):
                    for c in range(2):
                        src = sc_pad[:, c, k:k + SEQ]
                        tap = v("sc_conv_w_2", 2 * k + c)
                        if k == 0:
                            dve.tensor_scalar(y[:, 6 + c, :], src, tap, None, ALU.mult)
                        else:
                            dve.scalar_tensor_tensor(y[:, 6 + c, :], src, tap, y[:, 6 + c, :], ALU.mult, ALU.add)
                    dve.drain()
                dve.tensor_tensor(y[:, 6:8, :], y[:, 6:8, :], s_["sc_b"], ALU.mult).then_inc(S["sc_out"], 1)
                cos, sin = (m.c(n).rearrange("p (o t) -> p o t", o=1).to_broadcast([P, 2, SEQ]) for n in ("cos", "sin"))
                for i, name in enumerate(("ret_q", "ret_k")):
                    b = await_filled(dve, l, UNIT["swap"] + i)
                    dve.tensor_tensor(turn_tmp[:, :, :], two(m.ps[:, b, :]), sin, ALU.mult).then_inc(drained[b], 1)
                    dve.tensor_tensor(turned[:, i, :, :], s_[name], cos, ALU.mult)
                    dve.drain()
                    dve.tensor_tensor(turned[:, i, :, :], turned[:, i, :, :], turn_tmp[:, :, :], ALU.add)
                    dve.drain().then_inc(S["turned"], 1)
                b = await_filled(dve, l, UNIT["conf_mean"])
                for c in range(2):
                    ins = dve.scalar_tensor_tensor(conf[:, c, :], m.ps[:, b, 0:SEQ], -1.0 / 256, conf[:, c, :],
                                                   ALU.mult, ALU.add)
                ins.then_inc(drained[b], 1)
                dve.drain().then_inc(S["conf_centred"], 1)
                for h in range(4):
                    b = await_filled(dve, l, UNIT["sb_score"] + h)
                    z = m.ps[:, b, 0:W3]
                    dve.tensor_scalar(sb_l[:, h, :], z, HEAD ** -0.5, None, ALU.mult)
                    dve.scalar_tensor_tensor(sb_z[:, h, :], z, HEAD ** -0.5, m.c("past_neg"), ALU.mult, ALU.add)
                    dve.tensor_scalar(sb_pos[:, h, :], z, HEAD ** -0.5, 0.0, ALU.mult, ALU.max).then_inc(drained[b], 1)
                    dve.drain()
                    dve.scalar_tensor_tensor(sb_l[:, h, :], sb_pos[:, h, :], 2.0, sb_l[:, h, :], ALU.mult, ALU.subtract
                                             ).then_inc(S["soft_in"], 1)
                for h in range(4):
                    signalled(dve, l, "soft_ln", h + 1)
                    dve.tensor_tensor(sb_l[:, h, :], sb_l[:, h, :], sb_pos[:, h, :], ALU.add)
                    dve.drain()
                    dve.tensor_tensor(sb_l[:, h, :], sb_l[:, h, :], m.c("past"), ALU.mult).then_inc(S["sb_masked"], 1)
                for h in range(4):
                    b = await_filled(dve, l, UNIT["tail"] + h)
                    dve.scalar_tensor_tensor(sb_z[:, h, :], m.ps[:, b, 0:W3], -1.0, sb_z[:, h, :], ALU.mult, ALU.add
                                             ).then_inc(drained[b], 1)
                    dve.drain().then_inc(S["sb_arg"], 1)
                for h in range(4):
                    b = await_filled(dve, l, UNIT["ret_score"] + h)
                    keep = m.c("retain")[:, h * SEQ:(h + 1) * SEQ]
                    dve.tensor_tensor(ret_p[:, h, 0:SEQ], m.ps[:, b, 0:SEQ], keep, ALU.mult)
                    dve.tensor_tensor(ret_p[:, h, SEQ:W3], m.ps[:, b, SEQ:W3], keep[:, 0:P], ALU.mult
                                      ).then_inc(drained[b], 1)
                    dve.drain().then_inc(S["ret_masked"], 1)
                signalled(dve, l, "conf_rstd", 1)
                for c in range(2):
                    dve.tensor_tensor(conf[:, c, :], conf[:, c, :], conf_rs[:, :], ALU.mult)
                dve.drain().then_inc(S["conf_normed"], 1)
                b = await_filled(dve, l, UNIT["ret_mean"])
                for c in range(2):
                    await_drained(dve, l, UNIT["ret_out"] + c)
                dve.scalar_tensor_tensor(ret_o[:, :, :], two(m.ps[:, b, :]), -1.0 / HEAD, ret_o[:, :, :], ALU.mult, ALU.add
                                         ).then_inc(drained[b], 1)
                dve.drain().then_inc(S["ret_centred"], 1)
                signalled(dve, l, "ret_rstd", 1)
                for c in range(2):
                    dve.scalar_tensor_tensor(ret_o[:, c, :], ret_o[:, c, :], v("ret_norm_g_2", c), ret_rs[:, c, :],
                                             ALU.mult, ALU.mult)
                dve.drain()
                await_drained(dve, l, UNIT["proj"] + SLICES.index("ret_g"))
                dve.tensor_tensor(y[:, 4:6, :], ret_o[:, :, :], s_["ret_g"], ALU.mult).then_inc(S["ret_done"], 1)
                for i in range(4):
                    await_drained(dve, l, UNIT["out"] + i)
                residual("norm_mix_post_2", 1)
                for ins in scaled(m.hT, m.xT, "norm_ffn_pre_2", 2):
                    ins.then_inc(S["h_done"], 1)
                for i in range(FF + 1):
                    if i < FF:
                        b = UNIT["up"] + i
                        signalled(dve, l, "tap_scaled", i + 1)
                        for back in (1, 2):
                            for j in range(2):
                                x = ff[:, i % 2, j, back:]
                                ins = dve.scalar_tensor_tensor(
                                    x, m.ps[:, b % BANKS, j * SEQ:(j + 1) * SEQ - back],
                                    ff_taps[:, 2 - back, j * FF + i:j * FF + i + 1], x, ALU.mult, ALU.add)
                            if back == 2:
                                ins.then_inc(drained[b % BANKS], 1)
                            dve.drain()
                        dve.drain().then_inc(S["conv_done"], 1)
                    if i >= 1:
                        signalled(dve, l, "silu_done", i)
                        dve.tensor_tensor(hid[:, i - 1, :], silu[:, (i - 1) % 2, :], ff[:, (i - 1) % 2, 1, :], ALU.mult
                                          ).then_inc(S["hid_done"], 1)
                for i in range(KC):
                    await_drained(dve, l, UNIT["down"] + i)
                residual("norm_ffn_post_2", 3)


def output_part(nc, m, out):
    with ExitStack() as ctx:
        x_out = ctx.enter_context(nc.sbuf_tensor("x_out", [P, TT, D], F32))
        turned, copied, stored = (ctx.enter_context(nc.semaphore(n)) for n in ("out_turned", "out_copied", "out_stored"))
        with nc.Block() as block:
            @block.tensor
            def _(pe):
                for n in range(4):
                    t, c0 = n // 2, 4 * (n % 2)
                    for c in range(4):
                        mm = pe.transpose(m.ps[:, n, c * P:(c + 1) * P], m.xT[:, c0 + c, t * P:(t + 1) * P], m.c("ident"))
                    mm.then_inc(turned, 1)

            @block.vector
            def _(dve):
                for n in range(4):
                    dve.wait_ge(turned, n + 1)
                    dve.tensor_copy(x_out[:, n // 2, (n % 2) * 512:(n % 2 + 1) * 512], m.ps[:, n, :]).then_inc(copied, 1)

            @block.sync
            def _(sp):
                for t in range(TT):
                    sp.wait_ge(copied, 2 * t + 2)
                    sp.dma_start(out[0, t * P:(t + 1) * P, :], x_out[:, t, :]).then_inc(stored, 16)
                sp.wait_ge(stored, 32)


def program(nc, a, out):
    with ExitStack() as ctx:
        def sb(n, s):
            return ctx.enter_context(nc.sbuf_tensor(n, s, F32))
        m = Shared()
        m.ps = ctx.enter_context(nc.psum_tensor("ps", [P, BANKS, 512], F32))
        m.filled = [ctx.enter_context(nc.semaphore(f"bank_filled{b}")) for b in range(BANKS)]
        m.drained = [ctx.enter_context(nc.semaphore(f"bank_drained{b}")) for b in range(BANKS)]
        m.clear_banks = lambda: clear_bank_semaphores(nc, m)
        m.const = sb("const", [P, CONST.shape[1]])
        m.vec = sb("vec", [P, P])
        m.xT = sb("xT", [P, KC, SEQ])
        m.hT = sb("hT", [P, KC, SEQ])
        m.c = lambda n: m.const[:, CONST_AT[n][0]:CONST_AT[n][0] + CONST_AT[n][1]]
        m.v = lambda n, i: m.vec[:, VEC[n] + i:VEC[n] + i + 1]
        m.strip_dram = nc.dram_tensor("strip_dram", [P, ATT_HEADS, BIAS_W], F32, kind="Internal")
        m.n_vec = 14
        m.lora_in = ctx.enter_context(nc.semaphore("lora_in"))
        with ExitStack() as one:
            m.h_tok = one.enter_context(nc.sbuf_tensor("h_tok", [P, TT, D], F32))
            m.att_T = one.enter_context(nc.sbuf_tensor("att_T", [P, 2, SEQ], F32))
            m.o_T = one.enter_context(nc.sbuf_tensor("o_T", [P, 4, SEQ], F32))
            with ExitStack() as rec:
                m.w_up = rec.enter_context(nc.sbuf_tensor("w_up", [P, RW], F32))
                m.a_up = rec.enter_context(nc.sbuf_tensor("a_up", [P, RW], F32))
                m.g_up = rec.enter_context(nc.sbuf_tensor("g_up", [P, 2, RW], F32))
                m.p_rwkv = rec.enter_context(nc.sbuf_tensor("p_rwkv", [P, 15, SEQ + 1], F32))
                with ExitStack() as att:
                    m.qk = att.enter_context(nc.sbuf_tensor("qk", [P, 12, SEQ], F32))
                    m.v_att = att.enter_context(nc.sbuf_tensor("v_att", [P, TT, 768], F32))
                    m.bias = att.enter_context(nc.sbuf_tensor("bias", [P, ATT_HEADS, SEQ], F32))
                    project_part(nc, m, a)
                    m.clear_banks()
                    attention_part(nc, m, a)
                m.clear_banks()
                recurrence_part(nc, m, a)
            m.clear_banks()
            mix_part(nc, m, a)
            with ExitStack() as moe:
                def sbm(n, s, d=F32):
                    return moe.enter_context(nc.sbuf_tensor(n, s, d))
                m.gate_w = sbm("exp_gate_w", [P, 2, KC, D_EXP])
                m.up_w = sbm("exp_up_w", [P, 2, KC, D_EXP])
                m.down_w = sbm("exp_down_w", [P, 2, D_EXP // P, D])
                m.pick = sbm("pick", [P, TT, N_EXP, SLOTS])
                m.gate_T = sbm("gate_T", [P, N_EXP // 2, SEQ])
                m.gate = sbm("gate12", [P, 2, TT, 1])
                m.over_slot = sbm("over_slot", [P, 2, TT, 1])
                m.over_int = sbm("over_int", [P, OVER + 1], I32)
                m.landed = {(n, e): moe.enter_context(nc.semaphore(f"landed_{n}{e}")) for n in ("gate", "up", "down") for e in range(2)}
                expert_loads(nc, m, a)
                m.clear_banks()
                routing_part(nc, m, a)
                m.clear_banks()
                expert_part(nc, m, a)
        m.clear_banks()
        layers_part(nc, m, a)
        output_part(nc, m, out)


def kernel(**inputs):
    import numpy as _np
    import concourse.bacc as _bacc
    from concourse import mybir as _mybir
    from concourse.bass_utils import run_bass_kernel_spmd as _run
    nc = _bacc.Bacc("TRN2", target_bir_lowering=False, num_devices=1)
    arrays, aps = {}, {}
    for name, x in (*inputs.items(), ("const", CONST), ("bias_rows", BIAS_ROWS)):
        x = _np.ascontiguousarray(x)
        arrays[f"in_{name}"] = x
        aps[name] = nc.dram_tensor(f"in_{name}", x.shape, _mybir.dt.from_np(x.dtype), kind="ExternalInput").ap()
    out = nc.dram_tensor("out", (1, SEQ, D), F32, kind="ExternalOutput").ap()
    program(nc, aps, out)
    r = _run(nc, [arrays], core_ids=[0])
    return r.results[0]["out"]
```

```python
import math
from contextlib import ExitStack


import numpy as np

import concourse.bass as bass
from concourse import mybir



class Shared:
    pass


ALU = mybir.AluOpType
ACT = mybir.ActivationFunctionType
AX = mybir.AxisListType.X
F32 = mybir.dt.float32
F32R = mybir.dt.float32r
I32 = mybir.dt.int32

P = 128
SEQ = 256
TT = SEQ // P
D = 1024
KC = D // P
NEG = -1e30
EPS = 1e-6
GN_EPS = 64e-5
HEAD = 64
ATT_HEADS = 12
DILATIONS = (1, 4, 16)
WINDOW = 128
LORA_CHUNK = 12
RW = 512
N_EXP = 32
D_EXP = 512
SLOTS = 64
OVER = 8
SUB = 64
LEAF = 8
BIAS_W = 384
DFF = 2816
GATE_COL = 3 * 768 + 1824
BANKS = 8



def bucket_of(dist):
    d = np.maximum(dist.astype(np.float32), np.float32(1.0))
    large = 16 + (np.log(d / np.float32(16)) / np.float32(math.log(2048 / 16)) * np.float32(16)).astype(np.int32)
    return np.where(dist < 16, dist, np.minimum(large, 31))


def constants():
    s, t = np.arange(P)[:, None], np.arange(P)[None, :]
    same = s // SUB == t // SUB
    leaf = s // LEAF == t // LEAF
    f = {}
    f["ident"] = (s == t)
    f["ones"] = np.ones((P, P))
    f["pair_ones"] = (s // HEAD == t // HEAD)
    strict, incl = same & (s < t), same & (s <= t)
    f["quad_mask"] = np.concatenate([leaf & (s < t), incl, strict, incl], axis=1)
    f["leaf_low"] = leaf & (s > t)
    f["rest_low"] = same & ~leaf & (s > t)
    decay = -math.exp(-0.5)
    f["cumulate"] = decay * np.concatenate([incl, strict], axis=1)
    f["half_rows"] = np.concatenate([s < SUB, s >= SUB], axis=1)
    f["before"] = (s < t)
    f["slot_iota"] = np.broadcast_to(np.arange(SLOTS)[None, :], (P, SLOTS))
    f["first_pick"] = np.broadcast_to(N_EXP - np.arange(N_EXP)[None, :], (P, N_EXP))
    f["over_iota"] = np.broadcast_to(np.arange(OVER)[None, :], (P, OVER))
    f["over_slots"] = np.broadcast_to(np.arange(OVER * SLOTS)[None, :], (P, OVER * SLOTS))
    f["eps"] = np.full((P, 1), EPS)
    f["gn_eps"] = np.full((P, 1), GN_EPS)
    swap = np.zeros((P, P))
    for m in range(P):
        r = m % HEAD
        if r < 32:
            swap[m + 32, m] = -1.0
        else:
            swap[m - 32, m] = 1.0
    f["swap"] = swap
    inv = (10000.0 ** (-np.arange(0, HEAD, 2, dtype=np.float32) / np.float32(HEAD))).astype(np.float32)
    ang = (np.arange(SEQ, dtype=np.float32)[None, :] * inv[np.arange(P) % 32][:, None]).astype(np.float32)
    f["cos"] = np.cos(ang)
    f["sin"] = np.sin(ang)
    j, i = np.arange(P)[:, None], np.arange(SEQ)[None, :]
    ret = []
    for h in range(4):
        lg = math.log1p(-(2.0 ** (-5.0 - h)))
        ret.append(np.where(i >= j, np.exp(np.where(i >= j, i - j, 0) * lg), 0.0) * HEAD ** -0.5)
    f["retain"] = np.concatenate(ret, axis=1)
    f["past"] = np.concatenate([j < i, (j < i)[:, 0:P]], axis=1)
    f["past_neg"] = np.where(f["past"], 0.0, NEG)
    f["down"] = (s >= t)
    at, cols, w = {}, [], 0
    for name, a in f.items():
        at[name] = (w, a.shape[1])
        cols.append(np.asarray(a, np.float32))
        w += a.shape[1]
    return np.ascontiguousarray(np.concatenate(cols, axis=1)), at


def bias_rows():
    out = np.zeros((35, BIAS_W + ATT_HEADS), np.float32)
    u = np.arange(BIAS_W)
    dist = 255 - u
    b = bucket_of(np.maximum(dist, 0))
    for row in range(32):
        out[row, :BIAS_W] = (b == row) & (dist >= 0)
    for g, dil in enumerate(DILATIONS):
        ok = (dist >= 0) & (dist % dil == 0) & (dist // dil <= WINDOW)
        out[32 + g, :BIAS_W] = np.where(ok, 0.0, NEG)
        out[32 + g, BIAS_W + 4 * g:BIAS_W + 4 * g + 4] = 1.0
    return out


CONST, CONST_AT = constants()
BIAS_ROWS = bias_rows()

VEC = {}
_row = 0
for _name, _n in (("norm1_gain", 8), ("norm2_gain", 8), ("rwkv_shift_mu", 15), ("rwkv_a0", 4), ("rwkv_k_k", 4),
                  ("rwkv_k_a", 4), ("rwkv_r_k", 4), ("rwkv_ln_w", 4), ("rwkv_ln_b", 4),
                  ("q_norm_gain", 3), ("k_norm_gain", 3)):
    VEC[_name] = _row
    _row += _n
VEC_ROWS = _row
VEC2 = {}
_row = 0
for _name, _n in (("norm_mix_pre_2", 8), ("norm_mix_post_2", 8), ("norm_ffn_pre_2", 8), ("norm_ffn_post_2", 8),
                  ("conf_dw_b_2", 2), ("conf_ln_g_2", 2), ("conf_ln_b_2", 2), ("ret_norm_g_2", 2),
                  ("sc_conv_w_2", 6), ("conf_dw_w_2", 62)):
    VEC2[_name] = _row
    _row += _n
VEC2_ROWS = _row


def clear_bank_semaphores(nc, m):
    ids = sorted(s.num for s in m.filled + m.drained)
    assert ids == list(range(ids[0], ids[0] + len(ids)))
    with nc.Block() as block:
        @block.gpsimd
        def _(pool):
            pool.sem_clear(range(ids[0], ids[-1] + 1))


def project_part(nc, m, a):
    UNITS = 17
    RING = 6
    with ExitStack() as ctx:
        def sem(n):
            return ctx.enter_context(nc.semaphore(n))
        w_ring = ctx.enter_context(nc.sbuf_tensor("w_ring", [P, RING, KC, 256], F32))
        x_tok = ctx.enter_context(nc.sbuf_tensor("x_tok", [P, TT, D], F32))
        square = ctx.enter_context(nc.sbuf_tensor("square", [P, KC, SEQ], F32))
        log_ms = ctx.enter_context(nc.sbuf_tensor("log_ms", [P, SEQ], F32))
        rstd = ctx.enter_context(nc.sbuf_tensor("rstd", [P, SEQ], F32))
        vec_rows = ctx.enter_context(nc.sbuf_tensor("vec_rows", [P, P], F32))
        table = ctx.enter_context(nc.sbuf_tensor("table", [35, ATT_HEADS], F32))
        bucket_rows = ctx.enter_context(nc.sbuf_tensor("bucket_rows", [35, BIAS_W], F32))
        table_wide = ctx.enter_context(nc.sbuf_tensor("table_wide", [35, ATT_HEADS, P], F32))
        strip = ctx.enter_context(nc.sbuf_tensor("strip", [P, ATT_HEADS, BIAS_W], F32))

        x_in, const_in, vec_in, table_in = sem("x_in"), sem("const_in"), sem("vec_in"), sem("table_in")
        w_landed = [sem(f"w_landed{i}") for i in range(RING)]
        filled, drained = m.filled, m.drained
        rows_zero, square_done, norm_log, rstd_done, h_done = (
            sem("rows_zero"), sem("square_done"), sem("norm_log"), sem("rstd_done"), sem("h_done"))
        pads_zero, wide_done, strip_out, bias_in = sem("pads_zero"), sem("wide_done"), sem("strip_out"), sem("bias_in")

        U_VEC, U_X, U_SS, U_W = 0, 1, 5, 6
        U_B = U_W + UNITS
        block = ctx.enter_context(nc.Block())

        @block.sync
        def _(sp):
            sp.dma_start(m.const[:, :], a["const"]).then_inc(const_in, 16)
            for t in range(TT):
                sp.dma_start(x_tok[:, t, :], a["x"][0, t * P:(t + 1) * P, :]).then_inc(x_in, 16)
            sp.dma_start(table[0:32, :], a["rel_bias_table"]).then_inc(table_in, 16)
            sp.dma_start(table[32:35, :], a["bias_rows"][32:35, BIAS_W:]).then_inc(table_in, 16)
            sp.dma_start(bucket_rows[:, :], a["bias_rows"][:, 0:BIAS_W]).then_inc(table_in, 16)
            for u in range(UNITS):
                n = 256 if u < 16 else 32
                if u >= RING:
                    q = U_W + u - RING
                    sp.wait_ge(filled[q % BANKS], q // BANKS + 1)
                sp.dma_start(w_ring[:, u % RING, :, 0:n],
                             a["w_in"][0].rearrange("(c p) n -> p c n", p=P)[:, :, 256 * u:256 * u + n]
                             ).then_inc(w_landed[u % RING], 16)
            for h in range(ATT_HEADS):
                q = U_B + h
                sp.wait_ge(drained[q % BANKS], q // BANKS + 1)
            sp.dma_start(m.strip_dram[:, :, :], strip[:, :, :]).then_inc(strip_out, 16)
            sp.wait_ge(strip_out, 16)
            sp.dma_start(m.bias[:, :, :], bass.AP(m.strip_dram, P - 1, [[ATT_HEADS * BIAS_W - 1, P],
                                                                        [BIAS_W, ATT_HEADS], [1, SEQ]])
                         ).then_inc(bias_in, 16)
            sp.wait_ge(bias_in, 16)

        @block.gpsimd
        def _(pool):
            pool.memset(m.w_up[:, :], 0.0)
            pool.memset(m.a_up[:, :], 0.0)
            pool.memset(m.g_up[:, :, :], 0.0)
            pool.memset(m.p_rwkv[:, 0:14, 0:1], 0.0)
            pool.memset(m.p_rwkv[:, 14, :], 0.0).then_inc(pads_zero, 1)

        @block.scalar
        def _(act):
            act.wait_ge(rows_zero, 1)
            n_vec = 0
            def row(name, dst_row, src, c0=0, c1=P):
                act.dma_start(vec_rows[dst_row:dst_row + src.shape[0], c0:c1], src).then_inc(vec_in, 16)
                return 1
            for name in ("norm1_gain", "norm2_gain", "rwkv_a0", "rwkv_k_k", "rwkv_k_a", "rwkv_ln_w", "rwkv_ln_b"):
                n_vec += row(name, VEC[name], a[name][0].rearrange("(c p) -> c p", p=P))
            n_vec += row("", VEC["rwkv_r_k"], a["rwkv_r_k"][0].rearrange("(c h) n -> c (h n)", h=2))
            mu = a["rwkv_shift_mu"]
            n_vec += row("", VEC["rwkv_shift_mu"], mu[0, 0:14 * P].rearrange("(c p) -> c p", p=P))
            n_vec += row("", VEC["rwkv_shift_mu"] + 14, mu[:, 14 * P:1824], 0, 32)
            for name in ("q_norm_gain", "k_norm_gain"):
                for half in range(2):
                    n_vec += row("", VEC[name], a[name][0], half * HEAD, half * HEAD + HEAD)
            assert n_vec == m.n_vec
            act.wait_ge(pads_zero, 1)
            act.dma_start(m.w_up[0:64, :], a["rwkv_w_up"][0]).then_inc(m.lora_in, 16)
            act.dma_start(m.w_up[64:65, :], a["rwkv_w0"]).then_inc(m.lora_in, 16)
            act.dma_start(m.a_up[64:128, :], a["rwkv_a_up"][0]).then_inc(m.lora_in, 16)
            act.dma_start(m.g_up[:, 0, :], a["rwkv_g_up"][0, 0:P, :]).then_inc(m.lora_in, 16)
            act.dma_start(m.g_up[0:32, 1, :], a["rwkv_g_up"][0, P:160, :]).then_inc(m.lora_in, 16)
            for b in range(4):
                act.wait_ge(drained[(U_X + b) % BANKS], (U_X + b) // BANKS + 1)
                act.activation(square[:, 2 * b:2 * b + 2, :], m.xT[:, 2 * b:2 * b + 2, :], ACT.Square
                               ).then_inc(square_done, 1)
            act.wait_ge(filled[U_SS], 1)
            act.activation(log_ms[:, :], m.ps[:, U_SS, 0:SEQ], ACT.Ln, bias=m.c("eps"), scale=1.0 / D
                           ).then_inc(drained[U_SS], 1)
            act.drain()
            act.activation(rstd[:, :], log_ms[:, :], ACT.Exp, scale=-0.5).then_inc(rstd_done, 1)
            for h in range(ATT_HEADS):
                q = U_B + h
                act.wait_ge(filled[q % BANKS], q // BANKS + 1)
                act.activation(strip[:, h, :], m.ps[:, q % BANKS, 0:BIAS_W], ACT.Copy).then_inc(drained[q % BANKS], 1)
            act.wait_ge(m.lora_in, 5 * 16)

        @block.tensor
        def _(pe):
            pe.wait_ge(const_in, 16)
            pe.wait_ge(vec_in, 16 * m.n_vec)
            pe.transpose(m.ps[:, U_VEC, 0:P], vec_rows[:, :], m.c("ident")).then_inc(filled[U_VEC], 1)
            pe.wait_ge(x_in, 32)
            for b in range(4):
                for c in (2 * b, 2 * b + 1):
                    for t in range(TT):
                        at = (c % 2) * SEQ + t * P
                        mm = pe.transpose(m.ps[:, U_X + b, at:at + P], x_tok[:, t, c * P:(c + 1) * P], m.c("ident"))
                mm.then_inc(filled[U_X + b], 1)
            for c in range(KC):
                if c % 2 == 0:
                    pe.wait_ge(square_done, c // 2 + 1)
                mm = pe.matmul(m.ps[:, U_SS, 0:SEQ], m.c("ones"), square[:, c, :], start=(c == 0), stop=(c == KC - 1))
            mm.then_inc(filled[U_SS], 1)
            for u in range(UNITS):
                q = U_W + u
                b = q % BANKS
                if q >= BANKS:
                    pe.wait_ge(drained[b], q // BANKS)
                pe.wait_ge(w_landed[u % RING], 16 * (u // RING + 1))
                w = w_ring[:, u % RING, :, :]
                if 6 <= u < 9:
                    for t in range(TT):
                        for k in range(KC):
                            if u == 6:
                                pe.wait_ge(h_done, KC)
                            mm = pe.matmul(m.ps[:, b, t * 256:t * 256 + 256], m.hT[:, k, t * P:(t + 1) * P],
                                           w[:, k, :], start=(k == 0), stop=(k == KC - 1))
                else:
                    halves = ((0, P), (P, P)) if u < 16 else ((0, 32),)
                    for j, (c0, n) in enumerate(halves):
                        for k in range(KC):
                            if u == 0 and j == 0:
                                pe.wait_ge(h_done, k + 1)
                            mm = pe.matmul(m.ps[0:n, b, j * SEQ:(j + 1) * SEQ], w[:, k, c0:c0 + n],
                                           m.hT[:, k, :], start=(k == 0), stop=(k == KC - 1))
                mm.then_inc(filled[b], 1)
            pe.wait_ge(wide_done, 1)
            for h in range(ATT_HEADS):
                q = U_B + h
                pe.wait_ge(drained[q % BANKS], q // BANKS)
                pe.matmul(m.ps[:, q % BANKS, 0:BIAS_W], table_wide[:, h, :], bucket_rows[:, :],
                          start=True, stop=True).then_inc(filled[q % BANKS], 1)

        @block.vector
        def _(dve):
            dve.memset(vec_rows[:, :], 0.0).then_inc(rows_zero, 1)
            dve.wait_ge(table_in, 48)
            dve.tensor_copy(table_wide[:, :, :],
                            table[:, :].rearrange("p (h o) -> p h o", o=1).to_broadcast([35, ATT_HEADS, P])
                            ).then_inc(wide_done, 1)
            dve.wait_ge(filled[U_VEC], 1)
            dve.tensor_copy(m.vec[:, :], m.ps[:, U_VEC, 0:P]).then_inc(drained[U_VEC], 1)
            for b in range(4):
                dve.wait_ge(filled[U_X + b], 1)
                dve.tensor_copy(m.xT[:, 2 * b:2 * b + 2, :],
                                m.ps[:, U_X + b, :].rearrange("p (c t) -> p c t", c=2)).then_inc(drained[U_X + b], 1)
            dve.wait_ge(rstd_done, 1)
            dve.wait_ge(drained[U_VEC], 1)
            dve.wait_ge(drained[U_X + 3], 1)
            for c in range(KC):
                dve.scalar_tensor_tensor(m.hT[:, c, :], m.xT[:, c, :], m.v("norm1_gain", c), rstd[:, :],
                                         ALU.mult, ALU.mult).then_inc(h_done, 1)
            dve.wait_ge(pads_zero, 1)
            for u in range(UNITS):
                q = U_W + u
                b = q % BANKS
                dve.wait_ge(filled[b], q // BANKS + 1)
                src = m.ps[:, b, :].rearrange("p (c t) -> p c t", c=2)
                if u < 6:
                    ins = dve.tensor_copy(m.qk[:, 2 * u:2 * u + 2, :], src)
                elif u < 9:
                    ins = dve.tensor_copy(m.v_att[:, :, (u - 6) * 256:(u - 5) * 256], src)
                elif u < 16:
                    c = 2 * (u - 9)
                    ins = dve.tensor_copy(m.p_rwkv[:, c:c + 2, 1:SEQ + 1], src)
                else:
                    ins = dve.tensor_copy(m.p_rwkv[0:32, 14, 1:SEQ + 1], m.ps[0:32, b, 0:SEQ])
                ins.then_inc(drained[b], 1)


def attention_part(nc, m, a):
    H = 4
    with ExitStack() as ctx:
        def sem(n):
            return ctx.enter_context(nc.semaphore(n))

        def sb(n, s):
            return ctx.enter_context(nc.sbuf_tensor(n, s, F32))
        square = sb("att_square", [P, 12, SEQ])
        log_ms = sb("att_log", [P, 12, SEQ])
        rstd = sb("att_rstd", [P, 12, SEQ])
        prob = sb("prob", [P, 2, 9 * P])
        neg_max = sb("neg_max", [P, 8])
        row_sum = sb("row_sum", [P, 8])
        row_inv = sb("row_inv", [P, 8])
        prob_T = sb("prob_T", [P, 2, 9 * P])
        filled, drained = m.filled, m.drained
        square_done, log_done, rstd_done, normed = sem("a_square"), sem("a_log"), sem("a_rstd"), sem("a_normed")
        scored, maxed, exped, inv_done, probs_done = (
            sem("a_scored"), sem("a_maxed"), sem("a_exped"), sem("a_inv"), sem("a_probs"))
        U_SS, U_H = 0, 6

        def score_unit(h, j):
            return U_H + (0 if h == 0 else 3 + 8 * (h - 1)) + j

        def turn_unit(h, j):
            return U_H + 3 + 8 * h + (3 if h < H - 1 else 0) + j

        block = ctx.enter_context(nc.Block())

        @block.scalar
        def _(act):
            for u in range(6):
                act.activation(square[:, 2 * u:2 * u + 2, :], m.qk[:, 2 * u:2 * u + 2, :], ACT.Square
                               ).then_inc(square_done, 1)
            for u in range(6):
                act.wait_ge(filled[u], 1)
                act.activation(log_ms[:, 2 * u:2 * u + 2, :], m.ps[:, u, :].rearrange("p (c t) -> p c t", c=2),
                               ACT.Ln, bias=m.c("eps"), scale=1.0 / HEAD).then_inc(drained[u], 1)
            for u in range(6):
                act.wait_ge(drained[u], 1)
                act.activation(rstd[:, 2 * u:2 * u + 2, :], log_ms[:, 2 * u:2 * u + 2, :], ACT.Exp, scale=-0.5
                               ).then_inc(rstd_done, 1)
            for h in range(H):
                for t, (c0, n) in enumerate(((0, 3 * P), (3 * P, 6 * P))):
                    i = 2 * h + t
                    act.wait_ge(maxed, i + 1)
                    act.activation(prob[:, h % 2, c0:c0 + n], prob[:, h % 2, c0:c0 + n], ACT.Exp,
                                   bias=neg_max[:, i:i + 1], accum_out=row_sum[:, i:i + 1]).then_inc(exped, 1)
                for j in range(3):
                    q = turn_unit(h, j)
                    act.wait_ge(filled[q % BANKS], q // BANKS + 1)
                    at, n = ((0, 3 * P), (3 * P, 4 * P), (7 * P, 2 * P))[j]
                    act.activation(prob_T[:, h % 2, at:at + n], m.ps[:, q % BANKS, 0:n], ACT.Copy
                                   ).then_inc(drained[q % BANKS], 1)
                for t in range(2):
                    q = turn_unit(h, 3 + t)
                    r = (h % 2) * HEAD
                    act.wait_ge(filled[q % BANKS], q // BANKS + 1)
                    act.activation(m.att_T[r:r + HEAD, h // 2, t * P:(t + 1) * P], m.ps[r:r + HEAD, q % BANKS, 0:P],
                                   ACT.Copy).then_inc(drained[q % BANKS], 1)

        @block.tensor
        def _(pe):
            for u in range(6):
                pe.wait_ge(square_done, u + 1)
                pe.matmul(m.ps[:, u, :], m.c("pair_ones"), square[:, 2 * u:2 * u + 2, :], start=True, stop=True
                          ).then_inc(filled[u], 1)
            pe.wait_ge(normed, 12)

            def scores(h):
                r = (h % 2) * HEAD
                for j, (t, groups, keys) in enumerate(((0, (0, 1, 2), P), (1, (0, 1), SEQ), (1, (2,), SEQ))):
                    q = score_unit(h, j)
                    if q >= BANKS:
                        pe.wait_ge(drained[q % BANKS], q // BANKS)
                    for g in groups:
                        c = 2 * g + h // 2
                        at = (g - groups[0]) * keys
                        mm = pe.matmul(m.ps[:, q % BANKS, at:at + keys], m.qk[r:r + HEAD, c, t * P:(t + 1) * P],
                                       m.qk[r:r + HEAD, 6 + c, 0:keys], start=True, stop=True)
                    mm.then_inc(filled[q % BANKS], 1)

            def outputs(h):
                for j, (first, n) in enumerate(((0, 3), (3, 4), (7, 2))):
                    q = turn_unit(h, j)
                    pe.wait_ge(probs_done, 2 * h + (1 if j == 0 else 2))
                    pe.wait_ge(drained[q % BANKS], q // BANKS)
                    for i in range(n):
                        c = (first + i) * P
                        mm = pe.transpose(m.ps[:, q % BANKS, i * P:(i + 1) * P], prob[:, h % 2, c:c + P], m.c("ident"))
                    mm.then_inc(filled[q % BANKS], 1)
                r = (h % 2) * HEAD
                for t in range(2):
                    q = turn_unit(h, 3 + t)
                    for j in ((0,), (1, 2))[t]:
                        w = turn_unit(h, j)
                        pe.wait_ge(drained[w % BANKS], w // BANKS + 1)
                    pe.wait_ge(drained[q % BANKS], q // BANKS)
                    tiles = [(g, 0, g) for g in range(3)] if t == 0 else [(3 + 2 * g + k, k, g) for g in range(3) for k in range(2)]
                    for n, (tile, k, g) in enumerate(tiles):
                        col = (4 * g + h) * HEAD
                        mm = pe.matmul(m.ps[r:r + HEAD, q % BANKS, 0:P], m.v_att[:, k, col:col + HEAD],
                                       prob_T[:, h % 2, tile * P:(tile + 1) * P],
                                       start=(n == 0), stop=(n == len(tiles) - 1))
                    mm.then_inc(filled[q % BANKS], 1)

            scores(0)
            for h in range(H):
                if h + 1 < H:
                    scores(h + 1)
                outputs(h)

        @block.vector
        def _(dve):
            for c in range(12):
                dve.wait_ge(rstd_done, c // 2 + 1)
                gain = m.v("q_norm_gain", c // 2) if c < 6 else m.v("k_norm_gain", (c - 6) // 2)
                dve.scalar_tensor_tensor(m.qk[:, c, :], m.qk[:, c, :], gain, rstd[:, c, :], ALU.mult, ALU.mult
                                         ).then_inc(normed, 1)
            bias = m.bias[:, :, :].rearrange("p (g h) k -> p g h k", g=3)
            for h in range(H):
                for t in range(2):
                    i = 2 * h + t
                    c0, n = ((0, 3 * P), (3 * P, 6 * P))[t]
                    if h >= 2 and t == 0:
                        w = turn_unit(h - 2, 2)
                        dve.wait_ge(filled[w % BANKS], w // BANKS + 1)
                    for j in ((0,), (1, 2))[t]:
                        q = score_unit(h, j)
                        g0, ng = ((0, 3), (0, 2), (2, 1))[j]
                        keys = P if t == 0 else SEQ
                        at = (0, 3 * P, 7 * P)[j]
                        dve.wait_ge(filled[q % BANKS], q // BANKS + 1)
                        dve.scalar_tensor_tensor(
                            prob[:, h % 2, at:at + ng * keys].rearrange("p (g k) -> p g k", g=ng),
                            m.ps[:, q % BANKS, 0:ng * keys].rearrange("p (g k) -> p g k", g=ng), HEAD ** -0.5,
                            bias[:, g0:g0 + ng, h, SEQ - keys:SEQ], ALU.mult, ALU.add
                        ).then_inc(drained[q % BANKS], 1)
                    dve.drain()
                    dve.tensor_reduce(neg_max[:, i:i + 1], prob[:, h % 2, c0:c0 + n], AX, ALU.max, negate=True
                                      ).then_inc(maxed, 1)
                for t in range(2):
                    i = 2 * h + t
                    c0, n = ((0, 3 * P), (3 * P, 6 * P))[t]
                    dve.wait_ge(exped, i + 1)
                    dve.reciprocal(row_inv[:, i:i + 1], row_sum[:, i:i + 1])
                    dve.drain()
                    dve.tensor_scalar(prob[:, h % 2, c0:c0 + n], prob[:, h % 2, c0:c0 + n], row_inv[:, i:i + 1],
                                      None, ALU.mult).then_inc(probs_done, 1)


def recurrence_part(nc, m, a):
    PAIRS = 4
    with ExitStack() as ctx:
        def sem(n):
            return ctx.enter_context(nc.semaphore(n))

        def sb(n, s):
            return ctx.enter_context(nc.sbuf_tensor(n, s, F32))

        w_upto = sb("w_upto", [P, 8, P])
        rate = sb("rate", [P, 8, P])
        gate = sb("gate", [P, 8, P])
        alpha_rho = sb("alpha_rho", [P, 8, 2, P])
        beta = sb("beta", [P, 8, P])
        kappa = sb("kappa", [P, 8, P])
        key = sb("key", [P, 8, P])
        quad = sb("quad", [P, 16, 4 * P])
        work = [sb(f"work{i}", [P, 16, P]) for i in range(8)]
        LEAF_, REST, SQ, SQ_T, Q4_T, X, X_T, N = work

        shift = [work[0], work[1]]
        w_before, w_inv = work[7][:, 0:8, :], work[7][:, 8:16, :]
        kk, kk_sq = work[6][:, 0:8, :], work[6][:, 8:16, :]
        kk_inv = work[5][:, 0:8, :]
        sig_w = work[5][:, 8:16, :].rearrange("p (t f) n -> p t (f n)", t=TT)
        tanh_w = work[4][:, 0:2, :].rearrange("p a b -> p (a b)")
        sig_g = work[4][:, 2:6, :].rearrange("p (c t) n -> p c (t n)", c=2)
        beta_z = work[0][:, :, :].rearrange("p (t c f) n -> p t c (f n)", t=TT, c=2)
        kappa_z = work[1][:, :, :].rearrange("p (t c f) n -> p t c (f n)", t=TT, c=2)
        mu_tok = work[2][:, :, :].rearrange("p (t k f) n -> p t k (f n)", t=TT, k=2)
        q_T = work[3][:, 0:8, :].rearrange("p (t f) n -> p t f n", t=TT)
        v_tok = work[3][:, 8:16, :].rearrange("p (t f) n -> p t (f n)", t=TT)
        g_bd = work[4][:, 0:8, :].rearrange("p (c f) n -> p c f n", c=2)
        state = work[5][:, 0:8, :].rearrange("p (c f) n -> p c f n", c=2)
        o_raw = work[5][:, 8:16, :]
        ab_tok = work[7][:, :, :].rearrange("p (t k f) n -> p t k (f n)", t=TT, k=2)
        M_T = X_T

        def rows(c0, c1):
            return m.p_rwkv[:, c0:c1, 1:SEQ + 1]

        def by_chunk(x):
            return x.rearrange("p (c t) n -> p c (t n)", t=TT)

        filled, drained = m.filled, m.drained
        ones_set, mixed, lora_act, kk_raw, kk_squared = (
            sem("ones_set"), sem("mixed"), sem("lora_act"), sem("kk_raw"), sem("kk_squared"))
        clamped, rooted, operands, start_x, start_n = (
            sem("clamped"), sem("rooted"), sem("operands"), sem("start_x"), sem("start_n"))
        centred, o_squared, o_log, o_rstd, bonus_in = (
            sem("centred"), sem("o_squared"), sem("o_log"), sem("o_rstd"), sem("bonus_in"))

        U_Z, U_RATE, U_GATE, U_CUM, U_KK = 0, 2, 4, 6, 10
        U_QUAD, U_LOW, U_INV = 12, 28, 32
        STEPS = 15
        U_TOK = U_INV + 4 * STEPS
        U_BV, U_MU, U_Q, U_O, U_G = U_TOK + 8, U_TOK + 10, U_TOK + 14, U_TOK + 16, U_TOK + 18
        U_S = U_G + 2
        U_MEAN, U_BONUS, U_VAR = U_S + 6, U_S + 8, U_S + 10

        DT = quad
        steps = [
            (DT, LEAF_, SQ, False, ()),
            (LEAF_, DT, SQ_T, False, ()),
            (SQ, SQ_T, Q4_T, False, (0, 1)),
            (SQ_T, X, X, True, (1,)),
            (SQ, X_T, X_T, True, (0,)),
            (X, Q4_T, X_T, True, (2, 3, 4)),
            (Q4_T, X, X, True, (2, 3)),
            (X_T, REST, LEAF_, False, (5,)),
            (REST, X_T, SQ, False, (5,)),
            (SQ, LEAF_, SQ_T, False, (7, 8)),
            (LEAF_, SQ, Q4_T, False, (7, 8)),
            (Q4_T, SQ_T, REST, False, (9, 10)),
            (SQ_T, N, N, True, (9,)),
            (REST, N, N, True, (11, 12)),
            (X, N, M_T, False, (6, 13)),
        ]
        instances = [(tt, par, f) for tt in range(TT) for par in range(2) for f in range(PAIRS)]
        block = ctx.enter_context(nc.Block())

        @block.gpsimd
        def _(pool):
            pool.memset(tanh_w[:, :], 1.0).then_inc(ones_set, 1)

        @block.scalar
        def _(act):
            act.wait_ge(mixed, 3)
            act.wait_ge(ones_set, 1)
            act.activation(tanh_w[0:64, :], m.p_rwkv[0:64, LORA_CHUNK, 1:SEQ + 1], ACT.Tanh).then_inc(lora_act, 1)
            act.activation(sig_g[:, :, :], rows(13, 15), ACT.Sigmoid).then_inc(lora_act, 1)
            for t in range(TT):
                act.wait_ge(filled[U_Z + t], 1)
                act.activation(sig_w[:, t, :], m.ps[:, U_Z + t, :], ACT.Sigmoid).then_inc(drained[U_Z + t], 1)
            for f in range(PAIRS):
                b = U_RATE + f // 2
                act.wait_ge(filled[b], 1)
                ins = act.activation(by_chunk(rate[:, :, :])[:, f, :], m.ps[:, b, (f % 2) * SEQ:(f % 2 + 1) * SEQ],
                                     ACT.Sigmoid, bias=m.v("rwkv_a0", f))
                if f % 2:
                    ins.then_inc(drained[b], 1)
            for f in range(PAIRS):
                act.wait_ge(kk_raw, f + 1)
                act.activation(kk_sq[:, 2 * f:2 * f + 2, :], kk[:, 2 * f:2 * f + 2, :], ACT.Square).then_inc(kk_squared, 1)
            for f in range(PAIRS):
                q = U_CUM + f
                act.wait_ge(filled[q % BANKS], q // BANKS + 1)
                src = m.ps[:, q % BANKS, :].rearrange("p (t k n) -> p t k n", t=TT, k=2)
                act.activation(w_upto[:, 2 * f:2 * f + 2, :], src[:, :, 0, :], ACT.Exp)
                act.activation(w_before[:, 2 * f:2 * f + 2, :], src[:, :, 1, :], ACT.Exp)
                act.activation(w_inv[:, 2 * f:2 * f + 2, :], src[:, :, 0, :], ACT.Exp, scale=-1.0
                               ).then_inc(drained[q % BANKS], 1)
            act.wait_ge(clamped, 2)
            act.activation(kk_inv, kk_inv, ACT.Sqrt).then_inc(rooted, 1)
            for s, (_, _, out, adds, _) in enumerate(steps):
                if adds:
                    continue
                for g in range(4):
                    q = U_INV + 4 * s + g
                    act.wait_ge(filled[q % BANKS], q // BANKS + 1)
                    act.activation(out[:, 4 * g:4 * g + 4, :], m.ps[:, q % BANKS, :].rearrange("p (i n) -> p i n", i=4),
                                   ACT.Copy).then_inc(drained[q % BANKS], 1)
            for q, dst in ((U_TOK, v_tok[:, 0, :]), (U_TOK + 1, v_tok[:, 1, :]),
                           (U_TOK + 6, ab_tok[:, 0, 0, :]), (U_TOK + 7, ab_tok[:, 1, 0, :]),
                           (U_BV, ab_tok[:, 0, 1, :]), (U_BV + 1, ab_tok[:, 1, 1, :])):
                act.wait_ge(filled[q % BANKS], q // BANKS + 1)
                act.activation(dst, m.ps[:, q % BANKS, :], ACT.Copy).then_inc(drained[q % BANKS], 1)
            for n in range(4):
                q = U_MU + n
                t, hq = n // 2, n % 2
                act.wait_ge(filled[q % BANKS], q // BANKS + 1)
                for k in range(2):
                    ins = act.activation(
                        mu_tok[:, t, k, hq * 256:hq * 256 + 256].rearrange("p (h d) -> p h d", h=4),
                        m.ps[:, q % BANKS, :].rearrange("p (h k d) -> p h k d", h=4, k=2)[:, :, k, :], ACT.Copy)
                ins.then_inc(drained[q % BANKS], 1)
            for t in range(TT):
                q = U_O + t
                act.wait_ge(filled[q % BANKS], q // BANKS + 1)
                act.activation(o_raw.rearrange("p (f t) n -> p f t n", t=TT)[:, :, t, :],
                               m.ps[:, q % BANKS, :].rearrange("p (f n) -> p f n", f=PAIRS), ACT.Copy
                               ).then_inc(drained[q % BANKS], 1)
            for j in range(2):
                act.wait_ge(centred, j + 1)
                act.activation(work[0][:, 4 * j:4 * j + 4, :], o_raw[:, 4 * j:4 * j + 4, :], ACT.Square
                               ).then_inc(o_squared, 1)
            for j in range(2):
                q = U_VAR + j
                act.wait_ge(filled[q % BANKS], q // BANKS + 1)
                act.activation(work[1][:, 4 * j:4 * j + 4, :], m.ps[:, q % BANKS, :].rearrange("p (c n) -> p c n", c=4),
                               ACT.Ln, bias=m.c("gn_eps"), scale=1.0 / HEAD).then_inc(drained[q % BANKS], 1)
                act.drain()
                act.activation(work[1][:, 4 * j:4 * j + 4, :], work[1][:, 4 * j:4 * j + 4, :], ACT.Exp, scale=-0.5
                               ).then_inc(o_rstd, 1)

        @block.tensor
        def _(pe):
            def free(q):
                if q >= BANKS:
                    pe.wait_ge(drained[q % BANKS], q // BANKS)
                return q % BANKS

            def drained_of(q):
                pe.wait_ge(drained[q % BANKS], q // BANKS + 1)

            pe.wait_ge(mixed, 3)
            for f in range(PAIRS):
                b = free(U_RATE + f // 2)
                mm = pe.matmul(m.ps[:, b, (f % 2) * SEQ:(f % 2 + 1) * SEQ], m.a_up[:, f * P:(f + 1) * P],
                               m.p_rwkv[:, LORA_CHUNK, 1:SEQ + 1], start=True, stop=True)
                if f % 2:
                    mm.then_inc(filled[b], 1)
            pe.wait_ge(lora_act, 1)
            for t in range(TT):
                b = free(U_Z + t)
                pe.matmul(m.ps[:, b, :], tanh_w[:, t * P:(t + 1) * P], m.w_up[:, :], start=True, stop=True
                          ).then_inc(filled[b], 1)
            pe.wait_ge(lora_act, 2)
            for f in range(PAIRS):
                b = free(U_GATE + f // 2)
                for k in range(2):
                    mm = pe.matmul(m.ps[:, b, (f % 2) * SEQ:(f % 2 + 1) * SEQ], m.g_up[:, k, f * P:(f + 1) * P],
                                   sig_g[:, k, :], start=(k == 0), stop=(k == 1))
                if f % 2:
                    mm.then_inc(filled[b], 1)
            for t in range(TT):
                drained_of(U_Z + t)
            for f in range(PAIRS):
                b = free(U_CUM + f)
                for t in range(TT):
                    mm = pe.matmul(m.ps[:, b, t * 256:(t + 1) * 256], sig_w[:, t, f * P:(f + 1) * P], m.c("cumulate"),
                                   start=True, stop=True)
                mm.then_inc(filled[b], 1)
            for j in range(2):
                pe.wait_ge(kk_squared, 2 * j + 2)
                b = free(U_KK + j)
                pe.matmul(m.ps[:, b, :], m.c("pair_ones"), kk_sq[:, 4 * j:4 * j + 4, :], start=True, stop=True
                          ).then_inc(filled[b], 1)
            pe.wait_ge(operands, 4)
            for i, (tt, par, f) in enumerate(instances):
                b = free(U_QUAD + i)
                r = slice(par * HEAD, par * HEAD + HEAD)
                both = alpha_rho[r, 2 * f + tt, :, :]
                pe.matmul(m.ps[:, b, 0:256], beta[r, 2 * f + tt, :], both, start=True, stop=True)
                pe.matmul(m.ps[:, b, 256:512], kappa[r, 2 * f + tt, :], both, start=True, stop=True
                          ).then_inc(filled[b], 1)
            for g in range(4):
                b = free(U_LOW + g)
                for f in range(PAIRS):
                    tt, par, _ = instances[4 * g]
                    r = slice(par * HEAD, par * HEAD + HEAD)
                    mm = pe.matmul(m.ps[:, b, f * P:(f + 1) * P], alpha_rho[r, 2 * f + tt, 0, :],
                                   beta[r, 2 * f + tt, :], start=True, stop=True)
                mm.then_inc(filled[b], 1)
            for s, (lhs, rhs, _, _, needs) in enumerate(steps):
                for g in range(4):
                    b = free(U_INV + 4 * s + g)
                    if s <= 1:
                        drained_of(U_LOW + g)
                        drained_of(U_QUAD + 4 * g + 3)
                    if s in (3, 4):
                        pe.wait_ge(start_x, g + 1)
                    if s == 12:
                        pe.wait_ge(start_n, g + 1)
                    for n in needs:
                        drained_of(U_INV + 4 * n + g)
                    for i in range(4 * g, 4 * g + 4):
                        mm = pe.matmul(m.ps[:, b, (i % 4) * P:(i % 4 + 1) * P], lhs[:, i, 0:P], rhs[:, i, 0:P],
                                       start=True, stop=True)
                    mm.then_inc(filled[b], 1)
            for n, src in enumerate((rows(8, 12), beta, kappa, None)):
                for t in range(TT):
                    b = free(U_TOK + 2 * n + t)
                    for f in range(PAIRS):
                        if n == 0:
                            x = m.p_rwkv[:, 8 + f, 1 + t * P:1 + (t + 1) * P]
                        elif n == 3:
                            x = alpha_rho[:, 2 * f + t, 0, :]
                        else:
                            x = src[:, 2 * f + t, :]
                        mm = pe.transpose(m.ps[:, b, f * P:(f + 1) * P], x, m.c("ident"))
                    mm.then_inc(filled[b], 1)
            for t in range(TT):
                drained_of(U_TOK + t)
                b = free(U_BV + t)
                for h in range(8):
                    i = (2 * t + h % 2) * 4 + h // 2
                    mm = pe.matmul(m.ps[:, b, h * HEAD:(h + 1) * HEAD], quad[:, i, 256:384],
                                   v_tok[:, t, h * HEAD:(h + 1) * HEAD], start=True, stop=True)
                mm.then_inc(filled[b], 1)
            for g in range(4):
                drained_of(U_INV + 4 * (STEPS - 1) + g)
            for n in range(4):
                t, hq = n // 2, n % 2
                drained_of(U_TOK + 6 + t)
                drained_of(U_BV + t)
                b = free(U_MU + n)
                for h in range(4 * hq, 4 * hq + 4):
                    i = (2 * t + h % 2) * 4 + h // 2
                    mm = pe.matmul(m.ps[:, b, (h % 4) * P:(h % 4 + 1) * P], M_T[:, i, :],
                                   ab_tok[:, t, :, h * HEAD:(h + 1) * HEAD], start=True, stop=True)
                mm.then_inc(filled[b], 1)
            for t in range(TT):
                for n in range(2):
                    drained_of(U_MU + 2 * t + n)
                b = free(U_Q + t)
                for f in range(PAIRS):
                    for par in range(2):
                        h, i = 2 * f + par, (2 * t + par) * 4 + f
                        mm = pe.matmul(m.ps[par * HEAD:par * HEAD + HEAD, b, f * P:(f + 1) * P],
                                       mu_tok[:, t, 0, h * HEAD:(h + 1) * HEAD], quad[:, i, P:2 * P],
                                       start=True, stop=True)
                mm.then_inc(filled[b], 1)
            for t in range(TT):
                b = free(U_O + t)
                for f in range(PAIRS):
                    for par in range(2):
                        h, i = 2 * f + par, (2 * t + par) * 4 + f
                        out = m.ps[par * HEAD:par * HEAD + HEAD, b, f * P:(f + 1) * P]
                        pe.matmul(out, mu_tok[:, t, 1, h * HEAD:(h + 1) * HEAD], quad[:, i, P:2 * P],
                                  start=True, stop=False)
                        mm = pe.matmul(out, v_tok[:, t, h * HEAD:(h + 1) * HEAD], quad[:, i, 3 * P:4 * P],
                                       start=False, stop=True)
                mm.then_inc(filled[b], 1)
            for c in (1, 2):
                t, cb = c // 2, c % 2
                drained_of(U_TOK + 2 + t)
                b = free(U_G + c - 1)
                for f in range(PAIRS):
                    mm = pe.matmul(m.ps[:, b, f * P:(f + 1) * P], mu_tok[:, t, 0, f * P:(f + 1) * P],
                                   beta_z[:, t, cb, f * P:(f + 1) * P], start=True, stop=True)
                mm.then_inc(filled[b], 1)
            for t in range(TT):
                drained_of(U_TOK + 4 + t)
                drained_of(U_Q + t)
            for c in range(4):
                t, cb = c // 2, c % 2
                if c > 0:
                    drained_of(U_S + 2 * (c - 1))
                    b = free(U_S + 2 * c - 1)
                    for f in range(PAIRS):
                        mm = pe.matmul(m.ps[:, b, f * SUB:(f + 1) * SUB], state[:, (c - 1) % 2, f, :],
                                       q_T[:, t, f, cb * SUB:(cb + 1) * SUB], start=True, stop=True)
                    mm.then_inc(filled[b], 1)
                if c < 3:
                    b = free(U_S + 2 * c)
                    if c > 0:
                        drained_of(U_G + c - 1)
                    for f in range(PAIRS):
                        out = m.ps[:, b, f * P:(f + 1) * P]
                        cols = slice(f * P, (f + 1) * P)
                        pe.matmul(out, beta_z[:, t, cb, cols], mu_tok[:, t, 1, cols], start=True, stop=False)
                        mm = pe.matmul(out, kappa_z[:, t, cb, cols], v_tok[:, t, cols], start=False, stop=(c == 0))
                        if c > 0:
                            mm = pe.matmul(out, g_bd[:, c - 1, f, :], state[:, (c - 1) % 2, f, :],
                                           start=False, stop=True)
                    mm.then_inc(filled[b], 1)
            drained_of(U_S + 5)
            for t in range(TT):
                drained_of(U_O + t)
            for j in range(2):
                b = free(U_MEAN + j)
                pe.matmul(m.ps[:, b, :], m.c("pair_ones"), o_raw[:, 4 * j:4 * j + 4, :], start=True, stop=True
                          ).then_inc(filled[b], 1)
            for j in range(2):
                pe.wait_ge(bonus_in, 4)
                b = free(U_BONUS + j)
                pe.matmul(m.ps[:, b, :], m.c("pair_ones"), work[6][:, 4 * j:4 * j + 4, :], start=True, stop=True
                          ).then_inc(filled[b], 1)
            for j in range(2):
                pe.wait_ge(o_squared, j + 1)
                b = free(U_VAR + j)
                pe.matmul(m.ps[:, b, :], m.c("pair_ones"), work[0][:, 4 * j:4 * j + 4, :], start=True, stop=True
                          ).then_inc(filled[b], 1)

        @block.vector
        def _(dve):
            def await_filled(q):
                dve.wait_ge(filled[q % BANKS], q // BANKS + 1)
                return q % BANKS

            for c0, c1, dst in ((12, 15, work[3]), (0, 8, work[0]), (8, 12, work[1])):
                d = by_chunk(dst[:, 0:2 * (c1 - c0), :])
                dve.tensor_tensor(d, m.p_rwkv[:, c0:c1, 0:SEQ], rows(c0, c1), ALU.subtract)
                dve.drain()
                for c in range(c0, c1):
                    dve.scalar_tensor_tensor(m.p_rwkv[:, c, 1:SEQ + 1], d[:, c - c0, :], m.v("rwkv_shift_mu", c),
                                             m.p_rwkv[:, c, 1:SEQ + 1], ALU.mult, ALU.add).then_inc(mixed, 1)
            dve.drain()
            for f in range(PAIRS):
                dve.tensor_scalar(by_chunk(kk)[:, f, :], m.p_rwkv[:, 4 + f, 1:SEQ + 1], m.v("rwkv_k_k", f), None,
                                  ALU.mult).then_inc(kk_raw, 1)
            for j in range(2):
                b = await_filled(U_GATE + j)
                dve.tensor_copy(gate[:, 4 * j:4 * j + 4, :], m.ps[:, b, :].rearrange("p (c n) -> p c n", c=4)
                                ).then_inc(drained[b], 1)
            for j in range(2):
                q = U_RATE + j
                dve.wait_ge(drained[q % BANKS], q // BANKS + 1)
            for f in range(PAIRS):
                dve.tensor_scalar(by_chunk(key[:, :, :])[:, f, :], by_chunk(rate[:, :, :])[:, f, :], -1.0,
                                  m.v("rwkv_k_a", f), ALU.add, ALU.mult)
            dve.drain()
            dve.scalar_tensor_tensor(by_chunk(key[:, :, :]), by_chunk(key[:, :, :]), 1.0, rows(4, 8),
                                     ALU.add, ALU.mult)
            for j in range(2):
                b = await_filled(U_KK + j)
                dve.tensor_scalar(kk_inv[:, 4 * j:4 * j + 4, :], m.ps[:, b, :].rearrange("p (c n) -> p c n", c=4),
                                  1e-24, None, ALU.max).then_inc(drained[b], 1)
                dve.drain().then_inc(clamped, 1)
            for f in range(PAIRS):
                q = U_CUM + f
                dve.wait_ge(drained[q % BANKS], q // BANKS + 1)
            dve.tensor_tensor(kappa[:, :, :], key[:, :, :], w_inv, ALU.mult).then_inc(operands, 1)
            dve.tensor_tensor(alpha_rho[:, :, 1, :], m.p_rwkv[:, 0:4, 1:SEQ + 1].rearrange("p c (t n) -> p c t n", t=2),
                              w_upto[:, :, :].rearrange("p (c t) n -> p c t n", t=2), ALU.mult).then_inc(operands, 1)
            dve.wait_ge(rooted, 1)
            dve.reciprocal(kk_inv, kk_inv)
            dve.drain()
            dve.tensor_tensor(kk, kk, kk_inv, ALU.mult)
            dve.drain()
            dve.scalar_tensor_tensor(alpha_rho[:, :, 0, :], w_before, -1.0, kk, ALU.mult, ALU.mult
                                     ).then_inc(operands, 1)
            dve.tensor_tensor(beta[:, :, :], kk, rate[:, :, :], ALU.mult)
            dve.drain()
            dve.tensor_tensor(beta[:, :, :], beta[:, :, :], w_inv, ALU.mult).then_inc(operands, 1)
            for i in range(16):
                b = await_filled(U_QUAD + i)
                dve.tensor_tensor(quad[:, i, :], m.ps[:, b, :], m.c("quad_mask"), ALU.mult).then_inc(drained[b], 1)

            def wide(name):
                return m.c(name).rearrange("p (o n) -> p o n", o=1).to_broadcast([P, 4, P])
            for g in range(4):
                b = await_filled(U_LOW + g)
                i = slice(4 * g, 4 * g + 4)
                src = m.ps[:, b, :].rearrange("p (i n) -> p i n", i=4)
                dve.tensor_tensor(LEAF_[:, i, :], src, wide("leaf_low"), ALU.mult)
                dve.tensor_tensor(REST[:, i, :], src, wide("rest_low"), ALU.mult).then_inc(drained[b], 1)
                dve.drain()
                dve.tensor_tensor(X[:, i, :], LEAF_[:, i, :], wide("ident"), ALU.add)
                dve.tensor_tensor(X_T[:, i, :], quad[:, i, 0:P], wide("ident"), ALU.add)
                dve.drain().then_inc(start_x, 1)
            for s, (_, _, out, adds, needs) in enumerate(steps):
                if s == 12:
                    for g in range(4):
                        i = slice(4 * g, 4 * g + 4)
                        q = U_INV + 4 * 8 + g
                        dve.wait_ge(drained[q % BANKS], q // BANKS + 1)
                        dve.tensor_tensor(N[:, i, :], SQ[:, i, :], wide("ident"), ALU.add)
                        dve.drain().then_inc(start_n, 1)
                if not adds:
                    continue
                for g in range(4):
                    i = slice(4 * g, 4 * g + 4)
                    b = await_filled(U_INV + 4 * s + g)
                    dve.tensor_tensor(out[:, i, :], m.ps[:, b, :].rearrange("p (i n) -> p i n", i=4), out[:, i, :],
                                      ALU.add).then_inc(drained[b], 1)
                dve.drain()
            for n, dst in ((1, beta_z), (2, kappa_z)):
                for t in range(TT):
                    b = await_filled(U_TOK + 2 * n + t)
                    dve.tensor_scalar(dst[:, t, 0, :], m.ps[:, b, :], m.c("half_rows")[:, 0:1], None, ALU.mult)
                    dve.tensor_scalar(dst[:, t, 1, :], m.ps[:, b, :], m.c("half_rows")[:, 1:2], None, ALU.mult
                                      ).then_inc(drained[b], 1)
            for f in range(PAIRS):
                if f == 0:
                    for n in range(4):
                        q = U_MU + n
                        dve.wait_ge(drained[q % BANKS], q // BANKS + 1)
                dve.scalar_tensor_tensor(by_chunk(work[6][:, 0:8, :])[:, f, :], m.p_rwkv[:, f, 1:SEQ + 1],
                                         m.v("rwkv_r_k", f), by_chunk(key[:, :, :])[:, f, :], ALU.mult, ALU.mult
                                         ).then_inc(bonus_in, 1)
            for t in range(TT):
                b = await_filled(U_Q + t)
                rho = alpha_rho[:, :, 1, :].rearrange("p (f t) n -> p f t n", t=TT)[:, :, t, :]
                dve.tensor_tensor(q_T[:, t, :, :], m.ps[:, b, :].rearrange("p (f n) -> p f n", f=PAIRS), rho, ALU.add
                                  ).then_inc(drained[b], 1)
            for c in (1, 2):
                b = await_filled(U_G + c - 1)
                g = g_bd[:, c - 1, :, :]
                dve.tensor_tensor(g, m.ps[:, b, :].rearrange("p (f n) -> p f n", f=PAIRS), wide("pair_ones"), ALU.mult)
                dve.drain()
                dve.tensor_tensor(g, g, wide("ident"), ALU.add).then_inc(drained[b], 1)
            for t in range(TT):
                q = U_O + t
                dve.wait_ge(drained[q % BANKS], q // BANKS + 1)
            o_rows = by_chunk(o_raw)
            for c in range(4):
                t, cb = c // 2, c % 2
                if c > 0:
                    b = await_filled(U_S + 2 * c - 1)
                    o = o_rows[:, :, c * SUB:(c + 1) * SUB]
                    dve.tensor_tensor(o, m.ps[:, b, 0:256].rearrange("p (f n) -> p f n", f=PAIRS), o, ALU.add
                                      ).then_inc(drained[b], 1)
                if c < 3:
                    b = await_filled(U_S + 2 * c)
                    for f in range(PAIRS):
                        end = cb * SUB + SUB - 1
                        ins = dve.scalar_tensor_tensor(
                            state[:, c % 2, f, :], m.ps[:, b, f * P:(f + 1) * P], w_upto[:, 2 * f + t, end:end + 1],
                            m.c("pair_ones"), ALU.mult, ALU.mult)
                    ins.then_inc(drained[b], 1)
            dve.drain()
            for j in range(2):
                b = await_filled(U_MEAN + j)
                o = o_raw[:, 4 * j:4 * j + 4, :]
                dve.scalar_tensor_tensor(o, m.ps[:, b, :].rearrange("p (c n) -> p c n", c=4), -1.0 / HEAD, o,
                                         ALU.mult, ALU.add).then_inc(drained[b], 1)
                dve.drain().then_inc(centred, 1)
            bonus = by_chunk(work[6][:, 8:16, :])
            for j in range(2):
                b = await_filled(U_BONUS + j)
                dve.tensor_tensor(bonus[:, 2 * j:2 * j + 2, :], m.ps[:, b, :].rearrange("p (c n) -> p c n", c=2),
                                  rows(8 + 2 * j, 10 + 2 * j), ALU.mult).then_inc(drained[b], 1)
            for j in range(2):
                o = o_raw[:, 4 * j:4 * j + 4, :]
                dve.wait_ge(o_rstd, j + 1)
                dve.tensor_tensor(o, o, work[1][:, 4 * j:4 * j + 4, :], ALU.mult)
            dve.drain()
            for f in range(PAIRS):
                dve.tensor_scalar(o_rows[:, f, :], o_rows[:, f, :], m.v("rwkv_ln_w", f), m.v("rwkv_ln_b", f),
                                  ALU.mult, ALU.add)
            dve.drain()
            dve.tensor_tensor(o_rows, o_rows, bonus, ALU.add)
            dve.drain()
            dve.tensor_tensor(m.o_T[:, :, :], o_rows, by_chunk(gate[:, :, :]), ALU.mult)


def mix_part(nc, m, a):
    with ExitStack() as ctx:
        def sem(n):
            return ctx.enter_context(nc.semaphore(n))

        def sb(n, s):
            return ctx.enter_context(nc.sbuf_tensor(n, s, F32))
        gate_w = sb("gate_w", [P, 8, KC, 256])
        att_w = sb("att_w", [P, 2, D])
        rec_w = sb("rec_w", [P, 4, D])
        out_w = sb("out_w", [P, KC, D])
        sig = sb("gate_sig", [P, 2, 2, SEQ])
        part = sb("gate_part", [P, 2, SEQ])
        mixed = sb("gate_mixed", [P, KC, SEQ])
        square = sb("mix_square", [P, KC, SEQ])
        log_ms = sb("mix_log", [P, SEQ])
        rstd = sb("mix_rstd", [P, SEQ])
        gate_landed = [sem(f"gate_landed{i}") for i in range(8)]
        att_landed, rec_landed, out_landed = sem("att_landed"), sem("rec_landed"), sem("out_landed")
        filled, drained = m.filled, m.drained
        gated, squared, rstd_done, h_done = sem("gated"), sem("m_squared"), sem("m_rstd"), sem("m_h")
        U_OUT, U_SS, U_TOK = 16, 20, 21
        block = ctx.enter_context(nc.Block())

        @block.sync
        def _(sp):
            w_in = a["w_in"][0].rearrange("(c p) n -> p c n", p=P)
            sp.dma_start(att_w[:, :, :], a["w_att_out"][0].rearrange("(c p) n -> p c n", p=P)).then_inc(att_landed, 16)
            sp.dma_start(rec_w[:, :, :], a["w_rwkv_out"][0].rearrange("(c p) n -> p c n", p=P)).then_inc(rec_landed, 16)
            for j in range(4):
                for k in range(2):
                    col = GATE_COL + k * D + 256 * j
                    sp.dma_start(gate_w[:, 4 * k + j, :, :], w_in[:, :, col:col + 256]).then_inc(gate_landed[4 * k + j], 16)
            sp.dma_start(out_w[:, :, :], a["w_out"][0].rearrange("(c p) n -> p c n", p=P)).then_inc(out_landed, 16)

        @block.tensor
        def _(pe):
            def free(q):
                if q >= BANKS:
                    pe.wait_ge(drained[q % BANKS], q // BANKS)
                return q % BANKS

            for j in range(4):
                for k, (w, x, n, landed) in enumerate(((att_w, m.att_T, 2, att_landed), (rec_w, m.o_T, 4, rec_landed))):
                    b = free(4 * j + k)
                    pe.wait_ge(landed, 16)
                    for c in range(2):
                        for f in range(n):
                            col = (2 * j + c) * P
                            mm = pe.matmul(m.ps[:, b, c * SEQ:(c + 1) * SEQ], w[:, f, col:col + P], x[:, f, :],
                                           start=(f == 0), stop=(f == n - 1))
                    mm.then_inc(filled[b], 1)
                for k in range(2):
                    b = free(4 * j + 2 + k)
                    pe.wait_ge(gate_landed[4 * k + j], 16)
                    for c in range(2):
                        for f in range(KC):
                            mm = pe.matmul(m.ps[:, b, c * SEQ:(c + 1) * SEQ], gate_w[:, 4 * k + j, f, c * P:(c + 1) * P],
                                           m.hT[:, f, :], start=(f == 0), stop=(f == KC - 1))
                    mm.then_inc(filled[b], 1)
            pe.wait_ge(out_landed, 16)
            for j in range(4):
                b = free(U_OUT + j)
                for c in range(2):
                    for f in range(KC):
                        if j == 0 and c == 0:
                            pe.wait_ge(gated, f // 2 + 1)
                        col = (2 * j + c) * P
                        mm = pe.matmul(m.ps[:, b, c * SEQ:(c + 1) * SEQ], out_w[:, f, col:col + P], mixed[:, f, :],
                                       start=(f == 0), stop=(f == KC - 1))
                mm.then_inc(filled[b], 1)
            b = free(U_SS)
            for c in range(KC):
                pe.wait_ge(squared, c // 2 + 1)
                mm = pe.matmul(m.ps[:, b, 0:SEQ], m.c("ones"), square[:, c, :], start=(c == 0), stop=(c == KC - 1))
            mm.then_inc(filled[b], 1)
            for n in range(4):
                t, c0 = n // 2, 4 * (n % 2)
                b = free(U_TOK + n)
                for c in range(c0, c0 + 4):
                    pe.wait_ge(h_done, KC)
                    mm = pe.transpose(m.ps[:, b, (c - c0) * P:(c - c0 + 1) * P], m.hT[:, c, t * P:(t + 1) * P], m.c("ident"))
                mm.then_inc(filled[b], 1)

        @block.scalar
        def _(act):
            for j in range(4):
                for k in range(2):
                    q = 4 * j + 2 + k
                    act.wait_ge(filled[q % BANKS], q // BANKS + 1)
                    if j >= 1:
                        act.wait_ge(gated, j)
                    act.activation(sig[:, k, :, :], m.ps[:, q % BANKS, :].rearrange("p (c t) -> p c t", c=2), ACT.Sigmoid
                                   ).then_inc(drained[q % BANKS], 1)
            for j in range(4):
                q = U_OUT + j
                act.wait_ge(drained[q % BANKS], q // BANKS + 1)
                act.activation(square[:, 2 * j:2 * j + 2, :], m.xT[:, 2 * j:2 * j + 2, :], ACT.Square).then_inc(squared, 1)
            q = U_SS
            act.wait_ge(filled[q % BANKS], q // BANKS + 1)
            act.activation(log_ms[:, :], m.ps[:, q % BANKS, 0:SEQ], ACT.Ln, bias=m.c("eps"), scale=1.0 / D
                           ).then_inc(drained[q % BANKS], 1)
            act.drain()
            act.activation(rstd[:, :], log_ms[:, :], ACT.Exp, scale=-0.5).then_inc(rstd_done, 1)
            for n in range(4):
                q = U_TOK + n
                act.wait_ge(filled[q % BANKS], q // BANKS + 1)
                act.activation(m.h_tok[:, n // 2, (n % 2) * 512:(n % 2 + 1) * 512], m.ps[:, q % BANKS, :], ACT.Copy
                               ).then_inc(drained[q % BANKS], 1)

        @block.vector
        def _(dve):
            for j in range(4):
                for k, dst in enumerate((mixed[:, 2 * j:2 * j + 2, :], part[:, :, :])):
                    q, s = 4 * j + k, 4 * j + 2 + k
                    dve.wait_ge(filled[q % BANKS], q // BANKS + 1)
                    dve.wait_ge(drained[s % BANKS], s // BANKS + 1)
                    dve.tensor_tensor(dst, m.ps[:, q % BANKS, :].rearrange("p (c t) -> p c t", c=2), sig[:, k, :, :],
                                      ALU.mult).then_inc(drained[q % BANKS], 1)
                dve.drain()
                dve.tensor_tensor(mixed[:, 2 * j:2 * j + 2, :], mixed[:, 2 * j:2 * j + 2, :], part[:, :, :], ALU.add)
                dve.drain().then_inc(gated, 1)
            for j in range(4):
                q = U_OUT + j
                dve.wait_ge(filled[q % BANKS], q // BANKS + 1)
                x = m.xT[:, 2 * j:2 * j + 2, :]
                dve.tensor_tensor(x, m.ps[:, q % BANKS, :].rearrange("p (c t) -> p c t", c=2), x, ALU.add
                                  ).then_inc(drained[q % BANKS], 1)
            dve.wait_ge(rstd_done, 1)
            for c in range(KC):
                dve.scalar_tensor_tensor(m.hT[:, c, :], m.xT[:, c, :], m.v("norm2_gain", c), rstd[:, :],
                                         ALU.mult, ALU.mult).then_inc(h_done, 1)


def routing_part(nc, m, a):
    NL = 4 + N_EXP
    with ExitStack() as ctx:
        def sem(n):
            return ctx.enter_context(nc.semaphore(n))

        def sb(n, s):
            return ctx.enter_context(nc.sbuf_tensor(n, s, F32))
        router_w = sb("router_w", [P, KC, NL])
        router_b = sb("router_b", [P, NL])
        logits = sb("logits", [P, TT, NL])
        group_max = sb("group_max", [P, TT, 1])
        group_exp = sb("group_exp", [P, TT, 4])
        group_p = sb("group_p", [P, TT, 1])
        value = sb("pick_value", [P, TT, N_EXP])
        value_max = sb("pick_max", [P, TT, 1])
        group_hot = sb("group_hot", [P, TT, 4])
        masked = sb("masked", [P, TT, N_EXP])
        top = sb("top", [P, 2, TT, 1])
        ratio = sb("ratio", [P, TT, 1])
        ratio_inv = sb("ratio_inv", [P, TT, 1])
        hot = sb("hot", [P, 2, TT, N_EXP])
        assign = sb("assign", [P, TT, N_EXP])
        gates = sb("gates", [P, TT, N_EXP])
        slot = sb("slot", [P, TT, N_EXP])
        past = sb("past", [P, TT, N_EXP])
        scratch = sb("route_scratch", [P, TT, N_EXP])
        blocks = sb("over_blocks", [P, N_EXP])
        blocks_col = sb("over_blocks_col", [N_EXP, 1])
        blocks_wide = sb("over_blocks_wide", [N_EXP, P])
        count_col = sb("count_col", [N_EXP, 1])
        ends = sb("ends", [P, N_EXP])
        before_end = sb("before_end", [P, OVER, N_EXP])
        weighted = sb("weighted", [P, TT, N_EXP, SLOTS])
        over_f = sb("over_f", [P, OVER + 1])

        filled, drained = m.filled, m.drained
        router_in, group_in, group_out, ratio_in, ratio_out, assigned, wide_done, weights_done = (
            sem("router_in"), sem("group_in"), sem("group_out"), sem("ratio_in"), sem("ratio_out"),
            sem("assigned"), sem("blocks_wide"), sem("weights_done"))
        U_LOG, U_RANK, U_START, U_GT = 0, 1, 2, 3

        block = ctx.enter_context(nc.Block())

        @block.sync
        def _(sp):
            for k, name, c0, c1 in ((0, "group", 0, 4), (1, "expert", 4, NL)):
                sp.dma_start(router_w[:, :, c0:c1], a[f"w_{name}_router"][0].rearrange("(c p) n -> p c n", p=P)
                             ).then_inc(router_in, 16)
                sp.dma_start(router_b[:, c0:c1], a[f"b_{name}_router"].to_broadcast([P, c1 - c0])
                             ).then_inc(router_in, 16)
            m.load_pair(sp, 0)

        @block.scalar
        def _(act):
            act.wait_ge(group_in, 1)
            act.activation(group_exp[:, :, :], group_exp[:, :, :], ACT.Exp).then_inc(group_out, 1)
            act.wait_ge(ratio_in, 1)
            act.activation(ratio[:, :, :], ratio[:, :, :], ACT.Exp).then_inc(ratio_out, 1)
            for n in range(8):
                q = U_GT + n
                act.wait_ge(filled[q % BANKS], q // BANKS + 1)
                act.activation(m.gate_T[:, 2 * n:2 * n + 2, :], m.ps[:, q % BANKS, :].rearrange("p (i t) -> p i t", i=2),
                               ACT.Copy).then_inc(drained[q % BANKS], 1)

        @block.tensor
        def _(pe):
            pe.wait_ge(router_in, 64)
            for t in range(TT):
                for k in range(KC):
                    mm = pe.matmul(m.ps[:, U_LOG, t * NL:(t + 1) * NL], m.hT[:, k, t * P:(t + 1) * P], router_w[:, k, :],
                                   start=(k == 0), stop=(k == KC - 1))
            mm.then_inc(filled[U_LOG], 1)
            pe.wait_ge(assigned, 1)
            out = m.ps[:, U_RANK, :]
            pe.matmul(out[:, 0:32], m.c("before"), assign[:, 0, :], start=True, stop=True)
            pe.matmul(out[:, 32:64], m.c("before"), assign[:, 1, :], start=True, stop=False)
            pe.matmul(out[:, 32:64], m.c("ones"), assign[:, 0, :], start=False, stop=True)
            pe.matmul(out[:, 64:96], m.c("ones"), assign[:, 0, :], start=True, stop=False)
            pe.matmul(out[:, 64:96], m.c("ones"), assign[:, 1, :], start=False, stop=True)
            pe.matmul(out[0:32, 96:97], assign[:, 0, :], m.c("ones")[:, 0:1], start=True, stop=False)
            pe.matmul(out[0:32, 96:97], assign[:, 1, :], m.c("ones")[:, 0:1], start=False, stop=True
                      ).then_inc(filled[U_RANK], 1)
            pe.wait_ge(wide_done, 1)
            pe.matmul(m.ps[:, U_START, 0:N_EXP], blocks_wide[:, :], m.c("before")[0:N_EXP, 0:N_EXP], start=True, stop=True
                      ).then_inc(filled[U_START], 1)
            pe.wait_ge(weights_done, 1)
            for n in range(8):
                q = U_GT + n
                if q >= BANKS:
                    pe.wait_ge(drained[q % BANKS], q // BANKS)
                for i in range(2):
                    pair = 2 * n + i
                    for t in range(TT):
                        mm = pe.transpose(m.ps[:, q % BANKS, i * SEQ + t * P:i * SEQ + (t + 1) * P],
                                          weighted[:, t, 2 * pair:2 * pair + 2, :], m.c("ident"))
                mm.then_inc(filled[q % BANKS], 1)

        @block.vector
        def _(dve):
            def op(ins):
                dve.drain()
                return ins

            def wide(x, n):
                return x.to_broadcast([P, TT, n])

            def const_rows(name, n):
                return m.c(name)[:, 0:n].rearrange("p (o n) -> p o n", o=1).to_broadcast([P, TT, n])

            def first_of_largest(dst, src, largest, n):
                v = value[:, :, 0:n]
                op(dve.tensor_reduce(largest, src, AX, ALU.max))
                op(dve.tensor_tensor(v, src, wide(largest, n), ALU.is_equal))
                op(dve.tensor_tensor(v, v, const_rows("first_pick", n), ALU.mult))
                op(dve.tensor_reduce(value_max[:, :, :], v, AX, ALU.max))
                op(dve.tensor_tensor(dst, v, wide(value_max[:, :, :], n), ALU.is_equal))

            dve.wait_ge(router_in, 64)
            dve.wait_ge(filled[U_LOG], 1)
            op(dve.tensor_tensor(logits[:, :, :], m.ps[:, U_LOG, 0:TT * NL].rearrange("p (t n) -> p t n", t=TT),
                                 router_b[:, :].rearrange("p (o n) -> p o n", o=1).to_broadcast([P, TT, NL]), ALU.add
                                 ).then_inc(drained[U_LOG], 1))
            group = logits[:, :, 0:4]
            first_of_largest(group_hot[:, :, :], group, group_max[:, :, :], 4)
            op(dve.tensor_tensor(group_exp[:, :, :], group, wide(group_max[:, :, :], 4), ALU.subtract
                                 ).then_inc(group_in, 1))
            op(dve.tensor_scalar(scratch[:, :, 0:4], group_hot[:, :, :], -NEG, NEG, ALU.mult, ALU.add))
            for t in range(TT):
                dve.tensor_tensor(masked[:, t, :].rearrange("p (g e) -> p g e", g=4),
                                  logits[:, t, 4:NL].rearrange("p (g e) -> p g e", g=4),
                                  scratch[:, t, 0:4].rearrange("p (g o) -> p g o", o=1).to_broadcast([P, 4, 8]), ALU.add)
            dve.drain()
            first_of_largest(hot[:, 0, :, :], masked[:, :, :], top[:, 0, :, :], N_EXP)
            op(dve.scalar_tensor_tensor(masked[:, :, :], hot[:, 0, :, :], NEG, masked[:, :, :], ALU.mult, ALU.add))
            first_of_largest(hot[:, 1, :, :], masked[:, :, :], top[:, 1, :, :], N_EXP)
            op(dve.tensor_tensor(assign[:, :, :], hot[:, 0, :, :], hot[:, 1, :, :], ALU.add).then_inc(assigned, 1))
            op(dve.tensor_tensor(ratio[:, :, :], top[:, 1, :, :], top[:, 0, :, :], ALU.subtract).then_inc(ratio_in, 1))
            dve.wait_ge(group_out, 1)
            op(dve.tensor_reduce(group_p[:, :, :], group_exp[:, :, :], AX, ALU.add))
            op(dve.reciprocal(group_p[:, :, :], group_p[:, :, :]))
            dve.wait_ge(ratio_out, 1)
            op(dve.tensor_scalar(ratio_inv[:, :, :], ratio[:, :, :], 1.0, None, ALU.add))
            op(dve.reciprocal(ratio_inv[:, :, :], ratio_inv[:, :, :]))
            op(dve.tensor_tensor(m.gate[:, 0, :, :], group_p[:, :, :], ratio_inv[:, :, :], ALU.mult))
            op(dve.tensor_tensor(m.gate[:, 1, :, :], m.gate[:, 0, :, :], ratio[:, :, :], ALU.mult))
            op(dve.tensor_tensor(gates[:, :, :], hot[:, 0, :, :], wide(m.gate[:, 0, :, :], N_EXP), ALU.mult))
            op(dve.tensor_tensor(scratch[:, :, :], hot[:, 1, :, :], wide(m.gate[:, 1, :, :], N_EXP), ALU.mult))
            op(dve.tensor_tensor(gates[:, :, :], gates[:, :, :], scratch[:, :, :], ALU.add))
            dve.wait_ge(filled[U_RANK], 1)
            rank = m.ps[:, U_RANK, 0:64].rearrange("p (t e) -> p t e", t=TT)
            count = m.ps[:, U_RANK, 64:96]
            op(dve.scalar_tensor_tensor(slot[:, :, :], rank, 1.0, assign[:, :, :], ALU.add, ALU.mult))
            dve.tensor_scalar(past[:, :, :], slot[:, :, :], float(SLOTS), None, ALU.is_gt)
            dve.tensor_copy(count_col[:, :], m.ps[0:N_EXP, U_RANK, 96:97])
            dve.tensor_scalar(blocks[:, :], count, float(SLOTS), None, ALU.is_gt)
            dve.drain()
            dve.tensor_scalar(blocks_col[:, :], count_col[:, :], float(SLOTS), None, ALU.is_gt)
            dve.drain()
            for k in (2, 3):
                dve.scalar_tensor_tensor(blocks[:, :], count, float(k * SLOTS), blocks[:, :], ALU.is_gt, ALU.add)
                dve.scalar_tensor_tensor(blocks_col[:, :], count_col[:, :], float(k * SLOTS), blocks_col[:, :],
                                         ALU.is_gt, ALU.add)
                dve.drain()
            dve.drain().then_inc(drained[U_RANK], 1)
            dve.tensor_copy(blocks_wide[:, :], blocks_col[:, :].to_broadcast([N_EXP, P])).then_inc(wide_done, 1)
            op(dve.tensor_scalar(slot[:, :, :], slot[:, :, :], -1.0, None, ALU.add))
            pairs = [P, TT * N_EXP, SLOTS]
            iota = m.c("slot_iota").rearrange("p (o n) -> p o n", o=1).to_broadcast(pairs)
            flat = "p t (e o) -> p (t e) o"
            op(dve.tensor_tensor(m.pick[:, :, :, :].rearrange("p t e n -> p (t e) n"), iota,
                                 slot[:, :, :].rearrange(flat, o=1).to_broadcast(pairs), ALU.is_equal))
            dve.tensor_tensor(weighted[:, :, :, :].rearrange("p t e n -> p (t e) n"),
                              m.pick[:, :, :, :].rearrange("p t e n -> p (t e) n"),
                              gates[:, :, :].rearrange(flat, o=1).to_broadcast(pairs), ALU.mult).then_inc(weights_done, 1)
            dve.wait_ge(filled[U_START], 1)
            start = m.ps[:, U_START, 0:N_EXP]
            op(dve.tensor_tensor(ends[:, :], start, blocks[:, :], ALU.add))
            for t in range(TT):
                dve.scalar_tensor_tensor(scratch[:, t, :], start, float(SLOTS), slot[:, t, :], ALU.mult, ALU.add)
            dve.drain().then_inc(drained[U_START], 1)
            op(dve.tensor_scalar(scratch[:, :, :], scratch[:, :, :], 1.0 - SLOTS, None, ALU.add))
            op(dve.tensor_tensor(scratch[:, :, :], scratch[:, :, :], past[:, :, :], ALU.mult))
            for k in range(2):
                op(dve.tensor_tensor(hot[:, k, :, :], hot[:, k, :, :], scratch[:, :, :], ALU.mult))
                op(dve.tensor_reduce(m.over_slot[:, k, :, :], hot[:, k, :, :], AX, ALU.add))
            op(dve.tensor_scalar(m.over_slot[:, :, :, :], m.over_slot[:, :, :, :], -1.0, None, ALU.add))
            op(dve.tensor_tensor(before_end[:, :, :],
                                 ends[:, :].rearrange("p (o n) -> p o n", o=1).to_broadcast([P, OVER, N_EXP]),
                                 m.c("over_iota").rearrange("p (j o) -> p j o", o=1).to_broadcast([P, OVER, N_EXP]),
                                 ALU.is_le))
            op(dve.tensor_reduce(over_f[:, 0:OVER], before_end[:, :, :], AX, ALU.add))
            op(dve.tensor_scalar(over_f[:, 0:OVER], over_f[:, 0:OVER], float(N_EXP - 1), None, ALU.min))
            op(dve.tensor_copy(over_f[:, OVER:OVER + 1], ends[:, N_EXP - 1:N_EXP]))
            op(dve.tensor_copy(m.over_int[:, :], over_f[:, :]))


def expert_part(nc, m, a):
    PAIRS = N_EXP // 2
    FC = D_EXP // P
    with ExitStack() as ctx:
        def sem(n):
            return ctx.enter_context(nc.semaphore(n))

        def sb(n, s):
            return ctx.enter_context(nc.sbuf_tensor(n, s, F32))
        x_pair = sb("x_pair", [P, KC, 2 * SLOTS])
        silu = sb("silu", [P, D_EXP])
        hidden = sb("hidden", [P, D_EXP])
        hidden_T = sb("hidden_T", [P, FC, 2 * SLOTS])
        y_pair = sb("y_pair", [P, D])

        GATHER, GATE, UP, DOWN, SCATTER = 0, 2, 3, 4, 6

        def started(n):
            return not (isinstance(n, int) and n == 0)

        def gather(pe, filled, drained, i, n):
            for j in range(2):
                b = GATHER + j
                if started(n):
                    pe.wait_ge(drained[b], n)
                for c in range(4):
                    for t in range(TT):
                        mm = pe.matmul(m.ps[:, b, c * P:(c + 1) * P], m.h_tok[:, t, (4 * j + c) * P:(4 * j + c + 1) * P],
                                       m.pick[:, t, :, :].rearrange("p e n -> p (e n)")[:, bass.ts(i, 2 * SLOTS)],
                                       start=(t == 0), stop=(t == TT - 1))
                mm.then_inc(filled[b], 1)

        def gate_up(pe, filled, drained, landed, e, n):
            if e == 0:
                if started(n):
                    pe.wait_ge(drained[GATE], 2 * n)
                    pe.wait_ge(drained[UP], n)
                for j in range(2):
                    pe.wait_ge(drained[GATHER + j], n + 1)
            for b, w, name in ((GATE, m.gate_w, "gate"), (UP, m.up_w, "up")):
                pe.wait_ge(landed[name, e], 16 * n + 16)
                for c in range(KC):
                    mm = pe.matmul(m.ps[e * SLOTS:(e + 1) * SLOTS, b, :], x_pair[:, c, e * SLOTS:(e + 1) * SLOTS],
                                   w[:, e, c, :], start=(c == 0), stop=(c == KC - 1))
                mm.then_inc(filled[b], 1)

        def turn(pe, filled, drained, n):
            pe.wait_ge(drained[UP], n + 1)
            pe.wait_ge(drained[GATE], 2 * n + 1)
            for f in range(FC):
                mm = pe.transpose(m.ps[:, GATE, f * P:(f + 1) * P], hidden[:, f * P:(f + 1) * P], m.c("ident"))
            mm.then_inc(filled[GATE], 1)

        def down(pe, filled, drained, landed, e, n):
            if e == 0 and started(n):
                for j in range(2):
                    pe.wait_ge(drained[DOWN + j], n)
            pe.wait_ge(drained[GATE], 2 * n + 2)
            pe.wait_ge(landed["down", e], 16 * n + 16)
            for j in range(2):
                for f in range(FC):
                    mm = pe.matmul(m.ps[e * SLOTS:(e + 1) * SLOTS, DOWN + j, :], hidden_T[:, f, e * SLOTS:(e + 1) * SLOTS],
                                   m.down_w[:, e, f, j * 512:(j + 1) * 512], start=(f == 0), stop=(f == FC - 1))
                mm.then_inc(filled[DOWN + j], 1)

        def scatter(pe, filled, drained, i, n):
            for q in range(4):
                b = SCATTER + q % 2
                if started(n) or q >= 2:
                    pe.wait_ge(drained[b], 2 * n + q // 2)
                if q == 0:
                    for j in range(2):
                        pe.wait_ge(drained[DOWN + j], n + 1)
                for c in range(2):
                    d = 2 * q + c
                    mm = pe.matmul(m.ps[:, b, c * SEQ:(c + 1) * SEQ], y_pair[:, d * P:(d + 1) * P],
                                   m.gate_T[:, :, :].rearrange("p i t -> p (i t)")[:, bass.ts(i, SEQ)],
                                   start=True, stop=True)
                mm.then_inc(filled[b], 1)

        def act_pair(act, filled, drained, n):
            act.wait_ge(filled[GATE], 3 * n + 2)
            act.activation(silu[:, :], m.ps[:, GATE, :], ACT.Silu).then_inc(drained[GATE], 1)
            act.wait_ge(filled[GATE], 3 * n + 3)
            act.activation(hidden_T[:, :, :], m.ps[:, GATE, :].rearrange("p (f n) -> p f n", f=FC), ACT.Copy
                           ).then_inc(drained[GATE], 1)
            for j in range(2):
                act.wait_ge(filled[DOWN + j], 2 * n + 2)
                act.activation(y_pair[:, j * 512:(j + 1) * 512], m.ps[:, DOWN + j, :], ACT.Copy
                               ).then_inc(drained[DOWN + j], 1)

        def dve_gather(dve, filled, drained, n):
            for j in range(2):
                b = GATHER + j
                dve.wait_ge(filled[b], n + 1)
                dve.tensor_copy(x_pair[:, 4 * j:4 * j + 4, :], m.ps[:, b, :].rearrange("p (c n) -> p c n", c=4)
                                ).then_inc(drained[b], 1)

        def dve_hidden(dve, filled, drained, n):
            dve.wait_ge(drained[GATE], 2 * n + 1)
            dve.wait_ge(filled[UP], 2 * n + 2)
            dve.tensor_tensor(hidden[:, :], m.ps[:, UP, :], silu[:, :], ALU.mult).then_inc(drained[UP], 1)

        def dve_scatter(dve, filled, drained, n):
            for q in range(4):
                b = SCATTER + q % 2
                dve.wait_ge(filled[b], 2 * n + q // 2 + 1)
                x = m.xT[:, 2 * q:2 * q + 2, :]
                dve.tensor_tensor(x, m.ps[:, b, :].rearrange("p (c t) -> p c t", c=2), x, ALU.add
                                  ).then_inc(drained[b], 1)
            dve.drain()

        filled, drained = m.filled, m.drained
        with nc.Block() as block:
            @block.sync
            def _(sp):
                with sp.Fori(1, PAIRS) as i:
                    for e in range(2):
                        sp.wait_ge(filled[UP], 2 * i - 1 + e)
                        m.load_gate_up(sp, e, 2 * i + e)
                    for e in range(2):
                        sp.wait_ge(filled[DOWN + 1], 2 * i - 1 + e)
                        m.load_down(sp, e, 2 * i + e)

            @block.tensor
            def _(pe):
                gather(pe, filled, drained, 0, 0)

                def pair(i, first=False, last=False):
                    for e in range(2):
                        gate_up(pe, filled, drained, m.landed, e, i)
                    if not first:
                        scatter(pe, filled, drained, i - 1, i - 1)
                    turn(pe, filled, drained, i)
                    if not last:
                        gather(pe, filled, drained, i + 1, i + 1)
                    for e in range(2):
                        down(pe, filled, drained, m.landed, e, i)
                pair(0, first=True)
                with pe.Fori(1, PAIRS - 1) as i:
                    pair(i)
                pair(PAIRS - 1, last=True)
                scatter(pe, filled, drained, PAIRS - 1, PAIRS - 1)

            @block.scalar
            def _(act):
                with act.Fori(0, PAIRS) as i:
                    act_pair(act, filled, drained, i)

            @block.vector
            def _(dve):
                dve_gather(dve, filled, drained, 0)

                def pair(i, first=False, last=False):
                    dve_hidden(dve, filled, drained, i)
                    if not first:
                        dve_scatter(dve, filled, drained, i - 1)
                    if not last:
                        dve_gather(dve, filled, drained, i + 1)
                pair(0, first=True)
                with dve.Fori(1, PAIRS - 1) as i:
                    pair(i)
                pair(PAIRS - 1, last=True)
                dve_scatter(dve, filled, drained, PAIRS - 1)

        m.clear_banks()
        over_filled, over_drained = filled, drained
        over_pick = sem("over_pick")
        over_landed = {(n, e): sem(f"over_{n}{e}") for n in ("gate", "up", "down") for e in range(2)}
        equal = ctx.enter_context(nc.sbuf_tensor("over_equal", [P, 2, OVER * SLOTS], F32))
        over_weighted = ctx.enter_context(nc.sbuf_tensor("over_weighted", [P, TT, OVER * SLOTS], F32))
        turn_filled, turn_drained = sem("turn_filled"), sem("turn_drained")
        with nc.Block() as block:
            def blocks(eng):
                return eng.value_load(m.over_int[0:1, OVER:OVER + 1], min_val=0, max_val=OVER)

            @block.sync
            def _(sp):
                with sp.If(blocks(sp) > 0):
                    for i in range(OVER // 2):
                        for e in range(2):
                            j = 2 * i + e
                            expert = sp.value_load(m.over_int[0:1, j:j + 1], min_val=0, max_val=N_EXP - 1)
                            if i > 0:
                                sp.wait_ge(over_filled[UP], 2 * i - 1 + e)
                            m.load_gate_up(sp, e, expert, over_landed)
                            if i > 0:
                                sp.wait_ge(over_filled[DOWN + 1], 2 * i - 1 + e)
                            m.load_down(sp, e, expert, over_landed)

            @block.tensor
            def _(pe):
                with pe.If(blocks(pe) > 0):
                    pe.wait_ge(over_pick, 1)
                    for i in range(OVER // 2):
                        if i >= 2:
                            pe.wait_ge(turn_drained, i - 1)
                        for t in range(TT):
                            mm = pe.transpose(m.ps[:, GATE + i % 2, t * P:(t + 1) * P],
                                              over_weighted[:, t, i * P:(i + 1) * P], m.c("ident"))
                        mm.then_inc(turn_filled, 1)
                    pe.wait_ge(turn_drained, OVER // 2)

                    def pair(i):
                        gather(pe, over_filled, over_drained, i, i)
                        for e in range(2):
                            gate_up(pe, over_filled, over_drained, over_landed, e, i)
                        turn(pe, over_filled, over_drained, i)
                        for e in range(2):
                            down(pe, over_filled, over_drained, over_landed, e, i)
                        scatter(pe, over_filled, over_drained, i, i)
                    pair(0)
                    with pe.Fori(1, OVER // 2) as i:
                        pair(i)

            @block.scalar
            def _(act):
                with act.If(blocks(act) > 0):
                    for i in range(OVER // 2):
                        act.wait_ge(turn_filled, i + 1)
                        act.activation(m.gate_T[:, i, :], m.ps[:, GATE + i % 2, 0:SEQ], ACT.Copy
                                       ).then_inc(turn_drained, 1)
                    with act.Fori(0, OVER // 2) as i:
                        act_pair(act, over_filled, over_drained, i)

            @block.vector
            def _(dve):
                with dve.If(blocks(dve) > 0):
                    n = OVER * SLOTS
                    for t in range(TT):
                        for k in range(2):
                            dve.tensor_scalar(equal[:, k, :], m.c("over_slots"), m.over_slot[:, k, t, :], None, ALU.is_equal)
                        dve.drain()
                        dve.tensor_tensor(m.pick[:, t, 0:OVER, :].rearrange("p e n -> p (e n)"), equal[:, 0, :],
                                          equal[:, 1, :], ALU.add)
                        dve.tensor_scalar(over_weighted[:, t, :], equal[:, 0, :], m.gate[:, 0, t, :], None, ALU.mult)
                        dve.drain()
                        dve.scalar_tensor_tensor(over_weighted[:, t, :], equal[:, 1, :], m.gate[:, 1, t, :],
                                                 over_weighted[:, t, :], ALU.mult, ALU.add)
                        dve.drain()
                    dve.drain().then_inc(over_pick, 1)
                    with dve.Fori(0, OVER // 2) as i:
                        dve_gather(dve, over_filled, over_drained, i)
                        dve_hidden(dve, over_filled, over_drained, i)
                        dve_scatter(dve, over_filled, over_drained, i)


def expert_loads(nc, m, a):
    def load_gate_up(sp, e, expert, landed=None):
        landed = landed or m.landed
        for w, name in ((m.gate_w, "gate"), (m.up_w, "up")):
            src = a[f"w_expert_{name}"][0].rearrange("e (c p) n -> e p c n", p=P)
            sp.dma_start(w[:, e, :, :], src[bass.ds(expert, 1), :, :, :].rearrange("o p c n -> (o p) c n")
                         ).then_inc(landed[name, e], 16)

    def load_down(sp, e, expert, landed=None):
        landed = landed or m.landed
        src = a["w_expert_down"][0].rearrange("e (c p) n -> e p c n", p=P)
        sp.dma_start(m.down_w[:, e, :, :], src[bass.ds(expert, 1), :, :, :].rearrange("o p c n -> (o p) c n")
                     ).then_inc(landed["down", e], 16)

    def load_pair(sp, i):
        for e in range(2):
            load_gate_up(sp, e, 2 * i + e)
        for e in range(2):
            load_down(sp, e, 2 * i + e)
    m.load_gate_up, m.load_down, m.load_pair = load_gate_up, load_down, load_pair


SLICES = ("sb_q", "sb_k", "sb_v", "conf_a", "conf_gate", "sc_c", "sc_h", "ret_q", "ret_k", "ret_v", "sc_b", "ret_g")
SLICE_COL = {"conf_a": 0, "conf_gate": 1, "sb_q": 2, "sb_k": 3, "sb_v": 4, "ret_q": 5, "ret_k": 6, "ret_v": 7,
             "ret_g": 8, "sc_b": 9, "sc_c": 10, "sc_h": 11}


def _units():
    at, n = {}, 0
    for name, count in (("vec", 1), ("ss_mix", 1), ("sb_q", 1), ("sb_k", 1), ("sb_v", 1), ("conf_a", 1),
                        ("sb_score", 4), ("conf_gate", 1), ("sc_c", 1), ("sc_h", 1), ("tail", 4), ("ret_q", 1),
                        ("ret_k", 1), ("sb_out", 2), ("ret_v", 1), ("swap", 2), ("sc_b", 1), ("conf_mean", 1),
                        ("ret_g", 1), ("ret_score", 4), ("conf_var", 1), ("ret_out", 2), ("ret_mean", 1),
                        ("ret_var", 1), ("out", 4), ("ss_post", 1), ("ss_ffn", 1), ("up", 22), ("down", 8),
                        ("ss_ffn_post", 1)):
        at[name] = n
        n += count
    return at, n


UNIT, UNITS2 = _units()
FF = DFF // P
DOWN_ROWS = (8, 8, 6)
PIECE_OUT, PIECE_UP, PIECE_DOWN = 12, 16, 16 + FF
PIECES = PIECE_DOWN + 4 * len(DOWN_ROWS)
SLOTS2 = 3
TAPS = 31


def layers_part(nc, m, a):
    with ExitStack() as ctx:
        def sem(n):
            return ctx.enter_context(nc.semaphore(n))

        def sb(n, s):
            return ctx.enter_context(nc.sbuf_tensor(n, s, F32))

        def sb_r(n, s):
            return ctx.enter_context(nc.sbuf_tensor(n, s, F32R))
        ring = sb("ring2", [P, SLOTS2, KC * 256])
        w_hi = sb_r("w_hi", [P, SLOTS2, KC * 256])
        w_lo = sb_r("w_lo", [P, SLOTS2, KC * 256])
        x_hi = sb_r("x_hi", [P, KC, SEQ])
        x_lo = sb_r("x_lo", [P, KC, SEQ])
        rows1 = sb("rows1", [P, P])
        rows2 = sb("rows2", [FF * 2, 3, P])
        vec = sb("vec2", [P, P])
        ff_taps = sb("ff_taps", [P, 3, 2 * FF])
        square = sb("square2", [P, KC, SEQ])
        rstd = sb("rstd2", [P, SEQ])
        padded = sb("conf_pad", [P, 2, SEQ + TAPS - 1])
        conf = sb("conf_acc", [P, 2, SEQ])
        conf_sq = sb("conf_sq", [P, 2, SEQ])
        conf_rs = sb("conf_rs", [P, SEQ])
        sc_pad = sb("sc_pad", [P, 2, SEQ + 2])
        W3 = 3 * P
        turned = sb("ret_turned", [P, 2, 2, SEQ])
        ret_rs = sb("ret_rs", [P, 2, SEQ])
        y = sb("y_mix", [P, KC, SEQ])
        branch = y
        ff = sb("ff", [P, 2, 2, SEQ])
        silu = sb("silu2", [P, 2, SEQ])
        turn_tmp = silu
        ret_o, ret_sq = ff[:, 0, :, :], ff[:, 1, :, :]
        with ExitStack() as mixers:
            slices = mixers.enter_context(nc.sbuf_tensor("slices", [P, 12, 2, SEQ], F32))
            sb_z, sb_l, sb_pos, ret_p = (mixers.enter_context(nc.sbuf_tensor(n, [P, 4, W3], F32))
                                         for n in ("sb_z", "sb_l", "sb_pos", "ret_p"))
        s_ = {n: slices[:, i, :, :] for i, n in enumerate(SLICES)}
        hid_hi = sb_r("hid_hi", [P, FF, SEQ])
        hid_lo = sb_r("hid_lo", [P, FF, SEQ])

        landed = [sem(f"landed2_{i}") for i in range(SLOTS2)]
        filled, drained = m.filled, m.drained
        total = {"rows_in": 16 * 13, "squared": 16, "h_done": 16, "h_hi": 16, "h_lo": 16, "w_hi": PIECES,
                 "w_lo": PIECES, "down_used": 8, "y_split": 4, "conf_done": 1, "conf_centred": 1,
                 "conf_squared": 1, "conf_out": 1, "turned": 2, "soft_in": 4,
                 "soft_ln": 4, "sb_masked": 4, "sb_arg": 4, "sb_exp": 4, "ret_masked": 4, "ret_centred": 1,
                 "ret_squared": 1, "tap_scaled": FF, "conv_done": FF, "silu_done": FF,
                 "hid_done": FF, "conf_normed": 1, "x_done": 8, "root": 6}
        S = {n: sem(n) for n in total}
        
        def turns(b):
            return (UNITS2 - b + BANKS - 1) // BANKS

        def upto(l, n):
            return l * turns(n % BANKS) + n // BANKS + 2

        def before(l, n):
            return l * turns(n % BANKS) + n // BANKS + 1

        def await_filled(eng, l, n):
            eng.wait_ge(filled[n % BANKS], upto(l, n))
            return n % BANKS

        def await_drained(eng, l, n):
            eng.wait_ge(drained[n % BANKS], upto(l, n))

        def signalled(eng, l, name, k):
            eng.wait_ge(S[name], l * total[name] + k)

        def v(name, i):
            return vec[:, VEC2[name] + i:VEC2[name] + i + 1]

        def two(x):
            return x.rearrange("p (c t) -> p c t", c=2)

        def slot_uses(s):
            return (PIECES - s + SLOTS2 - 1) // SLOTS2

        def await_landed(eng, l, i):
            s = i % SLOTS2
            eng.wait_ge(landed[s], (l * slot_uses(s) + i // SLOTS2 + 1) * 16)
            return s

        with nc.Block() as block:
            @block.gpsimd
            def _(pool):
                pool.memset(padded[:, :, 0:TAPS - 1], 0.0)
                pool.memset(sc_pad[:, :, 0:2], 0.0)
                pool.memset(rows1[:, :], 0.0)
                for b in range(BANKS):
                    pool.sem_inc(filled[b], 1)
                    pool.sem_inc(drained[b], 1)


        def load_piece(sp, l, i):
            s = i % SLOTS2

            def of_layer(name):
                return a[name][bass.ds(l, 1)].rearrange("o (c p) n -> (o p) c n", p=P)
            dst = ring[:, s, :].rearrange("p (c n) -> p c n", c=KC)
            if i < PIECE_UP:
                name, c = ("w_in_2", SLICE_COL[SLICES[i]]) if i < PIECE_OUT else ("w_out_2", i - PIECE_OUT)
                src = of_layer(name)[:, :, c * 256:(c + 1) * 256]
            elif i < PIECE_DOWN:
                dst = ring[:, s, :].rearrange("p (h c n) -> p h c n", h=2, c=KC)
                src = a["ffn_up_2"][bass.ds(l, 1)].rearrange("o (c p) (h j n) -> (o p) h c j n", p=P, h=2, n=P
                                                             )[:, :, :, i - PIECE_UP, :]
            else:
                c, r = divmod(i - PIECE_DOWN, len(DOWN_ROWS))
                n = DOWN_ROWS[r]
                dst = dst[:, 0:n, :]
                src = of_layer("ffn_down_2")[:, KC * r:KC * r + n, c * 256:(c + 1) * 256]
            sp.dma_start(dst, src).then_inc(landed[s], 16)

        def load_rows(pool, l):
            n = 0
            for name in ("norm_mix_pre_2", "norm_mix_post_2", "norm_ffn_pre_2", "norm_ffn_post_2", "conf_dw_b_2",
                         "conf_ln_g_2", "conf_ln_b_2", "ret_norm_g_2"):
                src = a[name][l:l + 1, :].rearrange("o (c p) -> (o c) p", p=P)
                pool.dma_start(rows1[VEC2[name]:VEC2[name] + src.shape[0], :], src).then_inc(S["rows_in"], 16)
                n += 1
            for name in ("sc_conv_w_2", "conf_dw_w_2"):
                src = a[name][l].rearrange("k (c p) -> (k c) p", p=P)
                pool.dma_start(rows1[VEC2[name]:VEC2[name] + src.shape[0], :], src).then_inc(S["rows_in"], 16)
                n += 1
            for k in range(3):
                pool.dma_start(rows2[:, k, :], a["ffn_conv_w_2"][l, k, :].rearrange("(c p) -> c p", p=P)
                               ).then_inc(S["rows_in"], 16)
                n += 1
            assert 16 * n == total["rows_in"]

        block = ctx.enter_context(nc.Block())

        @block.sync
        def _(sp):
            for i in range(SLOTS2):
                load_piece(sp, 0, i)
            with sp.Fori(0, 2) as l:
                for i in range(SLOTS2, PIECES):
                    signalled(sp, l, "w_lo", i - SLOTS2 + 1)
                    load_piece(sp, l, i)
                with sp.If(l < 1):
                    for i in range(SLOTS2):
                        last = max(j for j in range(PIECES) if j % SLOTS2 == i)
                        signalled(sp, 0, "w_lo", last + 1)
                        load_piece(sp, 1, i)

        @block.gpsimd
        def _(pool):
            load_rows(pool, 0)
            n = UNIT["vec"]
            pool.wait_ge(filled[n % BANKS], upto(0, n))
            load_rows(pool, 1)
            with pool.Fori(0, 2) as l:
                for i in range(PIECES):
                    signalled(pool, l, "w_hi", i + 1)
                    s = i % SLOTS2
                    pool.tensor_tensor(w_lo[:, s, :], ring[:, s, :], w_hi[:, s, :].bitcast(F32), ALU.subtract
                                       ).then_inc(S["w_lo"], 1)

        @block.tensor
        def _(pe):
            with pe.Fori(0, 2) as l:
                def free(n):
                    pe.wait_ge(drained[n % BANKS], before(l, n))
                    return n % BANKS

                def ss(unit, first):
                    b = free(UNIT[unit])
                    for c in range(KC):
                        signalled(pe, l, "squared", first + c // 2 + 1)
                        mm = pe.matmul(m.ps[:, b, 0:SEQ], m.c("ones"), square[:, c, :], start=(c == 0), stop=(c == KC - 1))
                    mm.then_inc(filled[b], 1)

                def masked_scores(unit, k_src, q_src):
                    for h in range(4):
                        b = free(UNIT[unit] + h)
                        r, c = slice((h % 2) * HEAD, (h % 2 + 1) * HEAD), h // 2
                        pe.matmul(m.ps[:, b, 0:SEQ], k_src[r, c, 0:P], q_src[r, c, :], start=True, stop=True)
                        pe.matmul(m.ps[:, b, SEQ:W3], k_src[r, c, P:SEQ], q_src[r, c, P:SEQ], start=True, stop=True
                                  ).then_inc(filled[b], 1)

                def outputs(unit, values, probs, ready):
                    for c in range(2):
                        b = free(UNIT[unit] + c)
                        for h in (2 * c, 2 * c + 1):
                            signalled(pe, l, ready, h + 1)
                            out = m.ps[(h % 2) * HEAD:(h % 2 + 1) * HEAD, b, :]
                            cols = slice(h * HEAD, (h + 1) * HEAD)
                            pe.matmul(out[:, 0:SEQ], values[:, 0, cols], probs[:, h, 0:SEQ], start=True, stop=False)
                            mm = pe.matmul(out[:, P:SEQ], values[:, 1, cols], probs[:, h, SEQ:W3], start=False, stop=True)
                        mm.then_inc(filled[b], 1)

                def split_product(i, groups, sync=None):
                    for g, (out, parts) in enumerate(groups):
                        for part, steps in enumerate(parts):
                            if g == 0:
                                signalled(pe, l, "w_lo" if part == 2 else "w_hi", i + 1)
                            for n, (lhs, rhs) in enumerate(steps):
                                if g == 0 and sync:
                                    sync(part, n)
                                mm = pe.matmul(out, lhs, rhs, start=(part == 0 and n == 0),
                                               stop=(part == 2 and n == len(steps) - 1))
                    return mm

                def parts_of(i, at, hi, lo, order=range(KC)):
                    w = [t[:, i % SLOTS2, :] for t in (w_hi, w_lo)]
                    return [[(w[a_][:, at(k):at(k) + P], x[:, k, :]) for k in order]
                            for a_, x in ((0, hi), (0, lo), (1, hi))]

                def product(unit, i, at, order=range(KC), sync=None):
                    b = free(unit)
                    split_product(i, [(m.ps[:, b, j * SEQ:(j + 1) * SEQ],
                                       parts_of(i, lambda k, j=j: at(k, j), x_hi, x_lo, order)) for j in range(2)], sync
                                  ).then_inc(filled[b], 1)

                def column(k, j):
                    return k * 256 + j * P

                b = free(UNIT["vec"])
                pe.wait_ge(S["rows_in"], l * total["rows_in"] + total["rows_in"])
                pe.transpose(m.ps[:, b, 0:P], rows1[:, :], m.c("ident"))
                for k in range(3):
                    mm = pe.transpose(m.ps[:, b, P + 2 * FF * k:P + 2 * FF * (k + 1)], rows2[:, k, :],
                                      m.c("ident")[0:2 * FF, 0:2 * FF])
                mm.then_inc(filled[b], 1)
                ss("ss_mix", 0)
                def h_ready(first):
                    return lambda part, n: signalled(pe, l, "h_lo" if part == 1 else "h_hi", first + n + 1)

                def project(*names):
                    for name in names:
                        i = SLICES.index(name)
                        if name in ("sb_v", "ret_v"):
                            b = free(UNIT[name])
                            w = [t[:, i % SLOTS2, :] for t in (w_hi, w_lo)]
                            split_product(i, [(m.ps[:, b, t * 256:(t + 1) * 256],
                                               [[(x[:, k, t * P:(t + 1) * P], w[a_][:, k * 256:(k + 1) * 256])
                                                 for k in range(KC)] for a_, x in ((0, x_hi), (0, x_lo), (1, x_hi))])
                                              for t in range(TT)]).then_inc(filled[b], 1)
                        else:
                            product(UNIT[name], i, column, sync=h_ready(0) if i == 0 else None)

                project("sb_q", "sb_k", "sb_v", "conf_a")
                for name in ("sb_q", "sb_k"):
                    await_drained(pe, l, UNIT[name])
                masked_scores("sb_score", s_["sb_k"], s_["sb_q"])
                project("conf_gate", "sc_c", "sc_h")
                for h in range(4):
                    signalled(pe, l, "sb_masked", h + 1)
                    b = free(UNIT["tail"] + h)
                    pe.matmul(m.ps[:, b, 0:SEQ], m.c("down"), sb_l[:, h, 0:SEQ], start=True, stop=False)
                    pe.matmul(m.ps[:, b, P:SEQ], m.c("ones"), sb_l[:, h, SEQ:W3], start=False, stop=True)
                    pe.matmul(m.ps[:, b, SEQ:W3], m.c("down"), sb_l[:, h, SEQ:W3], start=True, stop=True
                              ).then_inc(filled[b], 1)
                project("ret_q", "ret_k")
                await_drained(pe, l, UNIT["sb_v"])
                outputs("sb_out", s_["sb_v"], sb_z, "sb_exp")
                project("ret_v")
                for i, name in enumerate(("ret_q", "ret_k")):
                    await_drained(pe, l, UNIT[name])
                    b = free(UNIT["swap"] + i)
                    pe.matmul(m.ps[:, b, :], m.c("swap"), s_[name], start=True, stop=True).then_inc(filled[b], 1)
                project("sc_b")
                signalled(pe, l, "conf_done", 1)
                b = free(UNIT["conf_mean"])
                for c in range(2):
                    mm = pe.matmul(m.ps[:, b, 0:SEQ], m.c("ones"), conf[:, c, :], start=(c == 0), stop=(c == 1))
                mm.then_inc(filled[b], 1)
                project("ret_g")
                signalled(pe, l, "turned", 2)
                masked_scores("ret_score", turned[:, 1, :, :], turned[:, 0, :, :])
                signalled(pe, l, "conf_squared", 1)
                b = free(UNIT["conf_var"])
                for c in range(2):
                    mm = pe.matmul(m.ps[:, b, 0:SEQ], m.c("ones"), conf_sq[:, c, :], start=(c == 0), stop=(c == 1))
                mm.then_inc(filled[b], 1)
                await_drained(pe, l, UNIT["ret_v"])
                outputs("ret_out", s_["ret_v"], ret_p, "ret_masked")
                for c in range(2):
                    await_drained(pe, l, UNIT["ret_out"] + c)
                b = free(UNIT["ret_mean"])
                pe.matmul(m.ps[:, b, :], m.c("pair_ones"), ret_o[:, :, :], start=True, stop=True).then_inc(filled[b], 1)
                signalled(pe, l, "ret_squared", 1)
                b = free(UNIT["ret_var"])
                pe.matmul(m.ps[:, b, :], m.c("pair_ones"), ret_sq[:, :, :], start=True, stop=True).then_inc(filled[b], 1)
                for i in range(4):
                    product(UNIT["out"] + i, PIECE_OUT + i, column, order=(6, 7, 2, 3, 0, 1, 4, 5),
                            sync=(lambda part, n: signalled(pe, l, "y_split", n // 2 + 1)) if i == 0 else None)
                ss("ss_post", 4)
                ss("ss_ffn", 8)
                for i in range(FF):
                    product(UNIT["up"] + i, PIECE_UP + i, lambda k, j: (j * KC + k) * P,
                            sync=h_ready(KC) if i == 0 else None)
                for c in range(4):
                    banks = [free(UNIT["down"] + 2 * c + j) for j in range(2)]
                    for r, n in enumerate(DOWN_ROWS):
                        i = PIECE_DOWN + len(DOWN_ROWS) * c + r
                        w = [t[:, i % SLOTS2, :] for t in (w_hi, w_lo)]
                        for j in range(2):
                            for part, (a_, x) in enumerate(((0, hid_hi), (0, hid_lo), (1, hid_hi))):
                                if j == 0:
                                    signalled(pe, l, "w_lo" if part == 2 else "w_hi", i + 1)
                                for k in range(n):
                                    if c == 0 and j == 0:
                                        signalled(pe, l, "hid_done", KC * r + k + 1)
                                    mm = pe.matmul(m.ps[:, banks[j], 0:SEQ], w[a_][:, column(k, j):column(k, j) + P],
                                                   x[:, KC * r + k, :], start=(r == 0 and part == 0 and k == 0),
                                                   stop=(r == len(DOWN_ROWS) - 1 and part == 2 and k == n - 1))
                            if r == len(DOWN_ROWS) - 1:
                                mm.then_inc(filled[banks[j]], 1)
                        if r < len(DOWN_ROWS) - 1:
                            mm.then_inc(S["down_used"], 1)
                ss("ss_ffn_post", 12)

        @block.scalar
        def _(act):
            with act.Fori(0, 2) as l:
                def root(dst, unit, n, src=lambda ps: ps[:, 0:SEQ]):
                    b = await_filled(act, l, UNIT[unit])
                    act.activation(dst, src(m.ps[:, b, :]), ACT.Sqrt, bias=m.c("eps"), scale=1.0 / n).then_inc(drained[b], 1)
                    act.drain().then_inc(S["root"], 1)

                def square_pair(src, j):
                    act.activation(square[:, 2 * j:2 * j + 2, :], src[:, 2 * j:2 * j + 2, :], ACT.Square
                                   ).then_inc(S["squared"], 1)

                def squares(src, when):
                    for j in range(4):
                        when(j)
                        square_pair(src, j)

                def copy(dst, n, func=ACT.Copy):
                    b = await_filled(act, l, n)
                    act.activation(dst, two(m.ps[:, b, :]), func).then_inc(drained[b], 1)

                def split_piece(i):
                    if i < PIECES:
                        s = await_landed(act, l, i)
                        act.activation(w_hi[:, s, :], ring[:, s, :], ACT.Copy).then_inc(S["w_hi"], 1)

                def split_h(first):
                    for c in range(KC):
                        signalled(act, l, "h_done", first + c + 1)
                        act.activation(x_hi[:, c, :], square[:, c, :], ACT.Copy).then_inc(S["h_hi"], 1)

                split_piece(0)
                split_piece(1)
                squares(m.xT, lambda j: signalled(act, l, "x_done", j + 1))
                split_piece(2)
                root(rstd[:, :], "ss_mix", D)
                split_h(0)

                def project(*names):
                    for name in names:
                        copy(s_[name], UNIT[name], {"conf_gate": ACT.Sigmoid, "ret_g": ACT.Silu}.get(name, ACT.Copy))
                        split_piece(SLICES.index(name) + SLOTS2)

                project("sb_q", "sb_k", "sb_v", "conf_a")
                for h in range(4):
                    signalled(act, l, "soft_in", h + 1)
                    act.activation(sb_l[:, h, :], sb_l[:, h, :], ACT.Exp, scale=-1.0)
                project("conf_gate")
                act.drain()
                for h in range(4):
                    act.activation(sb_l[:, h, :], sb_l[:, h, :], ACT.Ln, bias=1.0).then_inc(S["soft_ln"], 1)
                project("sc_c", "sc_h", "ret_q")
                for h in range(4):
                    signalled(act, l, "sb_arg", h + 1)
                    act.activation(sb_z[:, h, :], sb_z[:, h, :], ACT.Exp).then_inc(S["sb_exp"], 1)
                project("ret_k")
                for c in range(2):
                    b = await_filled(act, l, UNIT["sb_out"] + c)
                    act.activation(y[:, 2 + c, :], m.ps[:, b, 0:SEQ], ACT.Copy).then_inc(drained[b], 1)
                project("ret_v", "sc_b")
                signalled(act, l, "conf_centred", 1)
                act.activation(conf_sq[:, :, :], conf[:, :, :], ACT.Square).then_inc(S["conf_squared"], 1)
                project("ret_g")
                root(conf_rs[:, :], "conf_var", 256)
                for c in range(2):
                    b = await_filled(act, l, UNIT["ret_out"] + c)
                    act.activation(ret_o[:, c, :], m.ps[:, b, 0:SEQ], ACT.Copy).then_inc(drained[b], 1)
                signalled(act, l, "conf_normed", 1)
                for c in range(2):
                    ins = act.activation(y[:, c, :], conf[:, c, :], ACT.Silu, bias=v("conf_ln_b_2", c),
                                         scale=v("conf_ln_g_2", c))
                ins.then_inc(S["conf_out"], 1)
                signalled(act, l, "ret_centred", 1)
                act.activation(ret_sq[:, :, :], ret_o[:, :, :], ACT.Square).then_inc(S["ret_squared"], 1)
                root(ret_rs[:, :, :], "ret_var", HEAD, two)
                signalled(act, l, "y_split", 4)
                for i in range(4):
                    copy(branch[:, 2 * i:2 * i + 2, :], UNIT["out"] + i)
                    act.drain()
                    square_pair(branch, i)
                    if i < 3:
                        split_piece(PIECE_OUT + i + SLOTS2)
                root(rstd[:, :], "ss_post", D)
                split_piece(PIECE_OUT + 3 + SLOTS2)
                squares(m.xT, lambda j: signalled(act, l, "x_done", 4 + j + 1))
                root(rstd[:, :], "ss_ffn", D)
                split_h(KC)
                for i in range(FF):
                    b = await_filled(act, l, UNIT["up"] + i)
                    if i >= 2:
                        signalled(act, l, "hid_done", i - 1)
                    for j in range(2):
                        ins = act.activation(ff[:, i % 2, j, :], m.ps[:, b, j * SEQ:(j + 1) * SEQ], ACT.Copy,
                                             scale=ff_taps[:, 2, j * FF + i:j * FF + i + 1])
                    ins.then_inc(S["tap_scaled"], 1)
                    split_piece(PIECE_UP + i + SLOTS2)
                    if i >= 1:
                        signalled(act, l, "conv_done", i)
                        act.activation(silu[:, (i - 1) % 2, :], ff[:, (i - 1) % 2, 0, :], ACT.Silu).then_inc(S["silu_done"], 1)
                signalled(act, l, "conv_done", FF)
                act.activation(silu[:, (FF - 1) % 2, :], ff[:, (FF - 1) % 2, 0, :], ACT.Silu).then_inc(S["silu_done"], 1)
                for c in range(4):
                    for r in range(len(DOWN_ROWS)):
                        if r < len(DOWN_ROWS) - 1:
                            signalled(act, l, "down_used", (len(DOWN_ROWS) - 1) * c + r + 1)
                        else:
                            for i in (2 * c, 2 * c + 1):
                                b = await_filled(act, l, UNIT["down"] + i)
                                act.activation(branch[:, i, :], m.ps[:, b, 0:SEQ], ACT.Copy).then_inc(drained[b], 1)
                            act.drain()
                            square_pair(branch, c)
                        split_piece(PIECE_DOWN + len(DOWN_ROWS) * c + r + SLOTS2)
                root(rstd[:, :], "ss_ffn_post", D)

        @block.vector
        def _(dve):
            dve.drain().then_inc(S["x_done"], 4)
            with dve.Fori(0, 2) as l:
                def inverse_root(dst, n):
                    signalled(dve, l, "root", n)
                    dve.reciprocal(dst, dst)
                    dve.drain()

                def scaled(dst, src, gain, root):
                    inverse_root(rstd[:, :], root)
                    for c in range(KC):
                        yield dve.scalar_tensor_tensor(dst[:, c, :], src[:, c, :], v(gain, c), rstd[:, :], ALU.mult, ALU.mult)

                def normed(gain, root, first):
                    for ins in scaled(square, m.xT, gain, root):
                        ins.then_inc(S["h_done"], 1)
                    for c in range(KC):
                        signalled(dve, l, "h_hi", first + c + 1)
                        dve.tensor_tensor(x_lo[:, c, :], square[:, c, :], x_hi[:, c, :].bitcast(F32), ALU.subtract
                                          ).then_inc(S["h_lo"], 1)

                def split_y(c):
                    dve.tensor_copy(x_hi[:, c:c + 2, :], y[:, c:c + 2, :])
                    dve.drain()
                    dve.tensor_tensor(x_lo[:, c:c + 2, :], y[:, c:c + 2, :], x_hi[:, c:c + 2, :].bitcast(F32),
                                      ALU.subtract).then_inc(S["y_split"], 1)

                def residual(gain, root):
                    for c, _ in enumerate(scaled(branch, branch, gain, root)):
                        if c % 2:
                            dve.drain()
                            x = m.xT[:, c - 1:c + 1, :]
                            dve.tensor_tensor(x, x, branch[:, c - 1:c + 1, :], ALU.add).then_inc(S["x_done"], 1)
                    dve.drain()

                b = await_filled(dve, l, UNIT["vec"])
                dve.tensor_copy(vec[:, :], m.ps[:, b, 0:P])
                dve.tensor_copy(ff_taps[:, :, :], m.ps[:, b, P:P + 6 * FF].rearrange("p (k c) -> p k c", k=3)
                                ).then_inc(drained[b], 1)
                dve.drain()
                normed("norm_mix_pre_2", 1, 0)
                for h in range(4):
                    b = await_filled(dve, l, UNIT["sb_score"] + h)
                    z = m.ps[:, b, 0:W3]
                    dve.tensor_scalar(sb_l[:, h, :], z, HEAD ** -0.5, None, ALU.mult)
                    dve.scalar_tensor_tensor(sb_z[:, h, :], z, HEAD ** -0.5, m.c("past_neg"), ALU.mult, ALU.add)
                    dve.tensor_scalar(sb_pos[:, h, :], z, HEAD ** -0.5, 0.0, ALU.mult, ALU.max).then_inc(drained[b], 1)
                    dve.drain()
                    dve.scalar_tensor_tensor(sb_l[:, h, :], sb_pos[:, h, :], 2.0, sb_l[:, h, :], ALU.mult, ALU.subtract
                                             ).then_inc(S["soft_in"], 1)

                def conf_taps(first, last):
                    for k in range(first, last):
                        for c in range(2):
                            src = padded[:, c, k:k + SEQ]
                            tap = v("conf_dw_w_2", 2 * k + c)
                            if k == 0:
                                dve.tensor_scalar(conf[:, c, :], src, tap, v("conf_dw_b_2", c), ALU.mult, ALU.add)
                            else:
                                dve.scalar_tensor_tensor(conf[:, c, :], src, tap, conf[:, c, :], ALU.mult, ALU.add)
                        dve.drain()

                for name in ("conf_a", "conf_gate"):
                    await_drained(dve, l, UNIT[name])
                dve.tensor_tensor(padded[:, :, TAPS - 1:], s_["conf_a"], s_["conf_gate"], ALU.mult)
                dve.drain()
                conf_taps(0, 6)
                for h in range(4):
                    signalled(dve, l, "soft_ln", h + 1)
                    dve.tensor_tensor(sb_l[:, h, :], sb_l[:, h, :], sb_pos[:, h, :], ALU.add)
                    dve.drain()
                    dve.tensor_tensor(sb_l[:, h, :], sb_l[:, h, :], m.c("past"), ALU.mult).then_inc(S["sb_masked"], 1)
                conf_taps(6, 11)
                for h in range(4):
                    b = await_filled(dve, l, UNIT["tail"] + h)
                    dve.scalar_tensor_tensor(sb_z[:, h, :], m.ps[:, b, 0:W3], -1.0, sb_z[:, h, :], ALU.mult, ALU.add
                                             ).then_inc(drained[b], 1)
                    dve.drain().then_inc(S["sb_arg"], 1)
                conf_taps(11, TAPS)
                dve.drain().then_inc(S["conf_done"], 1)
                cos, sin = (m.c(n).rearrange("p (o t) -> p o t", o=1).to_broadcast([P, 2, SEQ]) for n in ("cos", "sin"))
                for i, name in enumerate(("ret_q", "ret_k")):
                    b = await_filled(dve, l, UNIT["swap"] + i)
                    dve.tensor_tensor(turn_tmp[:, :, :], two(m.ps[:, b, :]), sin, ALU.mult).then_inc(drained[b], 1)
                    dve.tensor_tensor(turned[:, i, :, :], s_[name], cos, ALU.mult)
                    dve.drain()
                    dve.tensor_tensor(turned[:, i, :, :], turned[:, i, :, :], turn_tmp[:, :, :], ALU.add)
                    dve.drain().then_inc(S["turned"], 1)
                for name in ("sc_c", "sc_h"):
                    await_drained(dve, l, UNIT[name])
                dve.tensor_tensor(sc_pad[:, :, 2:], s_["sc_c"], s_["sc_h"], ALU.mult)
                dve.drain()
                for k in range(3):
                    for c in range(2):
                        src = sc_pad[:, c, k:k + SEQ]
                        tap = v("sc_conv_w_2", 2 * k + c)
                        if k == 0:
                            dve.tensor_scalar(y[:, 6 + c, :], src, tap, None, ALU.mult)
                        else:
                            dve.scalar_tensor_tensor(y[:, 6 + c, :], src, tap, y[:, 6 + c, :], ALU.mult, ALU.add)
                    dve.drain()
                b = await_filled(dve, l, UNIT["conf_mean"])
                for c in range(2):
                    ins = dve.scalar_tensor_tensor(conf[:, c, :], m.ps[:, b, 0:SEQ], -1.0 / 256, conf[:, c, :],
                                                   ALU.mult, ALU.add)
                ins.then_inc(drained[b], 1)
                dve.drain().then_inc(S["conf_centred"], 1)
                await_drained(dve, l, UNIT["sc_b"])
                dve.tensor_tensor(y[:, 6:8, :], y[:, 6:8, :], s_["sc_b"], ALU.mult)
                for h in range(4):
                    b = await_filled(dve, l, UNIT["ret_score"] + h)
                    keep = m.c("retain")[:, h * SEQ:(h + 1) * SEQ]
                    dve.tensor_tensor(ret_p[:, h, 0:SEQ], m.ps[:, b, 0:SEQ], keep, ALU.mult)
                    dve.tensor_tensor(ret_p[:, h, SEQ:W3], m.ps[:, b, SEQ:W3], keep[:, 0:P], ALU.mult
                                      ).then_inc(drained[b], 1)
                    dve.drain().then_inc(S["ret_masked"], 1)
                inverse_root(conf_rs[:, :], 2)
                for c in range(2):
                    dve.tensor_tensor(conf[:, c, :], conf[:, c, :], conf_rs[:, :], ALU.mult)
                dve.drain().then_inc(S["conf_normed"], 1)
                await_drained(dve, l, UNIT["ret_g"])
                split_y(6)
                b = await_filled(dve, l, UNIT["ret_mean"])
                for c in range(2):
                    await_drained(dve, l, UNIT["ret_out"] + c)
                dve.scalar_tensor_tensor(ret_o[:, :, :], two(m.ps[:, b, :]), -1.0 / HEAD, ret_o[:, :, :], ALU.mult, ALU.add
                                         ).then_inc(drained[b], 1)
                dve.drain().then_inc(S["ret_centred"], 1)
                for c in range(2):
                    await_drained(dve, l, UNIT["sb_out"] + c)
                split_y(2)
                inverse_root(ret_rs[:, :, :], 3)
                for c in range(2):
                    dve.scalar_tensor_tensor(ret_o[:, c, :], ret_o[:, c, :], v("ret_norm_g_2", c), ret_rs[:, c, :],
                                             ALU.mult, ALU.mult)
                dve.drain()
                dve.tensor_tensor(y[:, 4:6, :], ret_o[:, :, :], s_["ret_g"], ALU.mult)
                signalled(dve, l, "conf_out", 1)
                split_y(0)
                dve.drain()
                split_y(4)
                for i in range(4):
                    await_drained(dve, l, UNIT["out"] + i)
                residual("norm_mix_post_2", 4)
                normed("norm_ffn_pre_2", 5, KC)
                for i in range(FF + 1):
                    if i < FF:
                        b = UNIT["up"] + i
                        signalled(dve, l, "tap_scaled", i + 1)
                        for back in (1, 2):
                            for j in range(2):
                                x = ff[:, i % 2, j, back:]
                                ins = dve.scalar_tensor_tensor(
                                    x, m.ps[:, b % BANKS, j * SEQ:(j + 1) * SEQ - back],
                                    ff_taps[:, 2 - back, j * FF + i:j * FF + i + 1], x, ALU.mult, ALU.add)
                            if back == 2:
                                ins.then_inc(drained[b % BANKS], 1)
                            dve.drain()
                        dve.drain().then_inc(S["conv_done"], 1)
                    if i >= 1:
                        signalled(dve, l, "silu_done", i)
                        h = silu[:, (i - 1) % 2, :]
                        dve.tensor_tensor(h, h, ff[:, (i - 1) % 2, 1, :], ALU.mult)
                        dve.drain()
                        dve.tensor_copy(hid_hi[:, i - 1, :], h)
                        dve.drain()
                        dve.tensor_tensor(hid_lo[:, i - 1, :], h, hid_hi[:, i - 1, :].bitcast(F32), ALU.subtract
                                          ).then_inc(S["hid_done"], 1)
                for i in range(KC):
                    await_drained(dve, l, UNIT["down"] + i)
                residual("norm_ffn_post_2", 6)


def output_part(nc, m, out):
    with ExitStack() as ctx:
        x_out = ctx.enter_context(nc.sbuf_tensor("x_out", [P, TT, D], F32))
        turned, copied, stored = (ctx.enter_context(nc.semaphore(n)) for n in ("out_turned", "out_copied", "out_stored"))
        with nc.Block() as block:
            @block.tensor
            def _(pe):
                for n in range(4):
                    t, c0 = n // 2, 4 * (n % 2)
                    for c in range(4):
                        mm = pe.transpose(m.ps[:, n, c * P:(c + 1) * P], m.xT[:, c0 + c, t * P:(t + 1) * P], m.c("ident"))
                    mm.then_inc(turned, 1)

            @block.vector
            def _(dve):
                for n in range(4):
                    dve.wait_ge(turned, n + 1)
                    dve.tensor_copy(x_out[:, n // 2, (n % 2) * 512:(n % 2 + 1) * 512], m.ps[:, n, :]).then_inc(copied, 1)

            @block.sync
            def _(sp):
                for t in range(TT):
                    sp.wait_ge(copied, 2 * t + 2)
                    sp.dma_start(out[0, t * P:(t + 1) * P, :], x_out[:, t, :]).then_inc(stored, 16)
                sp.wait_ge(stored, 32)


def program(nc, a, out):
    with ExitStack() as ctx:
        def sb(n, s):
            return ctx.enter_context(nc.sbuf_tensor(n, s, F32))
        m = Shared()
        m.ps = ctx.enter_context(nc.psum_tensor("ps", [P, BANKS, 512], F32))
        m.filled = [ctx.enter_context(nc.semaphore(f"bank_filled{b}")) for b in range(BANKS)]
        m.drained = [ctx.enter_context(nc.semaphore(f"bank_drained{b}")) for b in range(BANKS)]
        m.clear_banks = lambda: clear_bank_semaphores(nc, m)
        m.const = sb("const", [P, CONST.shape[1]])
        m.vec = sb("vec", [P, P])
        m.xT = sb("xT", [P, KC, SEQ])
        m.c = lambda n: m.const[:, CONST_AT[n][0]:CONST_AT[n][0] + CONST_AT[n][1]]
        m.v = lambda n, i: m.vec[:, VEC[n] + i:VEC[n] + i + 1]
        m.strip_dram = nc.dram_tensor("strip_dram", [P, ATT_HEADS, BIAS_W], F32, kind="Internal")
        m.n_vec = 14
        m.lora_in = ctx.enter_context(nc.semaphore("lora_in"))
        with ExitStack() as one:
            m.hT = one.enter_context(nc.sbuf_tensor("hT", [P, KC, SEQ], F32))
            m.h_tok = one.enter_context(nc.sbuf_tensor("h_tok", [P, TT, D], F32))
            m.att_T = one.enter_context(nc.sbuf_tensor("att_T", [P, 2, SEQ], F32))
            m.o_T = one.enter_context(nc.sbuf_tensor("o_T", [P, 4, SEQ], F32))
            with ExitStack() as rec:
                m.w_up = rec.enter_context(nc.sbuf_tensor("w_up", [P, RW], F32))
                m.a_up = rec.enter_context(nc.sbuf_tensor("a_up", [P, RW], F32))
                m.g_up = rec.enter_context(nc.sbuf_tensor("g_up", [P, 2, RW], F32))
                m.p_rwkv = rec.enter_context(nc.sbuf_tensor("p_rwkv", [P, 15, SEQ + 1], F32))
                with ExitStack() as att:
                    m.qk = att.enter_context(nc.sbuf_tensor("qk", [P, 12, SEQ], F32))
                    m.v_att = att.enter_context(nc.sbuf_tensor("v_att", [P, TT, 768], F32))
                    m.bias = att.enter_context(nc.sbuf_tensor("bias", [P, ATT_HEADS, SEQ], F32))
                    project_part(nc, m, a)
                    m.clear_banks()
                    attention_part(nc, m, a)
                m.clear_banks()
                recurrence_part(nc, m, a)
            m.clear_banks()
            mix_part(nc, m, a)
            with ExitStack() as moe:
                def sbm(n, s, d=F32):
                    return moe.enter_context(nc.sbuf_tensor(n, s, d))
                m.gate_w = sbm("exp_gate_w", [P, 2, KC, D_EXP])
                m.up_w = sbm("exp_up_w", [P, 2, KC, D_EXP])
                m.down_w = sbm("exp_down_w", [P, 2, D_EXP // P, D])
                m.pick = sbm("pick", [P, TT, N_EXP, SLOTS])
                m.gate_T = sbm("gate_T", [P, N_EXP // 2, SEQ])
                m.gate = sbm("gate12", [P, 2, TT, 1])
                m.over_slot = sbm("over_slot", [P, 2, TT, 1])
                m.over_int = sbm("over_int", [P, OVER + 1], I32)
                m.landed = {(n, e): moe.enter_context(nc.semaphore(f"landed_{n}{e}")) for n in ("gate", "up", "down") for e in range(2)}
                expert_loads(nc, m, a)
                m.clear_banks()
                routing_part(nc, m, a)
                m.clear_banks()
                expert_part(nc, m, a)
        m.clear_banks()
        layers_part(nc, m, a)
        output_part(nc, m, out)


def kernel(**inputs):
    import numpy as _np
    import concourse.bacc as _bacc
    from concourse import mybir as _mybir
    from concourse.bass_utils import run_bass_kernel_spmd as _run
    nc = _bacc.Bacc("TRN2", target_bir_lowering=False, num_devices=1)
    arrays, aps = {}, {}
    for name, x in (*inputs.items(), ("const", CONST), ("bias_rows", BIAS_ROWS)):
        x = _np.ascontiguousarray(x)
        arrays[f"in_{name}"] = x
        aps[name] = nc.dram_tensor(f"in_{name}", x.shape, _mybir.dt.from_np(x.dtype), kind="ExternalInput").ap()
    out = nc.dram_tensor("out", (1, SEQ, D), F32, kind="ExternalOutput").ap()
    program(nc, aps, out)
    r = _run(nc, [arrays], core_ids=[0])
    return r.results[0]["out"]
```

```python
import math
from contextlib import ExitStack

import numpy as np

import concourse.bass as bass
from concourse import mybir


class Shared:
    pass


ALU = mybir.AluOpType
ACT = mybir.ActivationFunctionType
AX = mybir.AxisListType.X
F32 = mybir.dt.float32
F32R = mybir.dt.float32r
I32 = mybir.dt.int32

P = 128
SEQ = 256
TT = SEQ // P
D = 1024
KC = D // P
NEG = -1e30
EPS = 1e-6
GN_EPS = 64e-5
HEAD = 64
ATT_HEADS = 12
DILATIONS = (1, 4, 16)
WINDOW = 128
LORA_CHUNK = 12
RW = 512
N_EXP = 32
D_EXP = 512
SLOTS = 64
OVER = 8
SUB = 64
LEAF = 8
BIAS_W = 384
DFF = 2816
GATE_COL = 3 * 768 + 1824
BANKS = 8



def bucket_of(dist):
    d = np.maximum(dist.astype(np.float32), np.float32(1.0))
    large = 16 + (np.log(d / np.float32(16)) / np.float32(math.log(2048 / 16)) * np.float32(16)).astype(np.int32)
    return np.where(dist < 16, dist, np.minimum(large, 31))


def constants():
    s, t = np.arange(P)[:, None], np.arange(P)[None, :]
    same = s // SUB == t // SUB
    leaf = s // LEAF == t // LEAF
    f = {}
    f["ident"] = (s == t)
    f["ones"] = np.ones((P, P))
    f["pair_ones"] = (s // HEAD == t // HEAD)
    strict, incl = same & (s < t), same & (s <= t)
    f["quad_mask"] = np.concatenate([leaf & (s < t), incl, strict, incl], axis=1)
    f["leaf_low"] = leaf & (s > t)
    f["rest_low"] = same & ~leaf & (s > t)
    decay = -math.exp(-0.5)
    f["cumulate"] = decay * np.concatenate([incl, strict], axis=1)
    f["half_rows"] = np.concatenate([s < SUB, s >= SUB], axis=1)
    f["before"] = (s < t)
    f["first_pick"] = np.broadcast_to(N_EXP - np.arange(N_EXP)[None, :], (P, N_EXP))
    f["iota"] = np.broadcast_to(np.arange(OVER * SLOTS)[None, :], (P, OVER * SLOTS))
    f["eps"] = np.full((P, 1), EPS)
    f["gn_eps"] = np.full((P, 1), GN_EPS)
    swap = np.zeros((P, P))
    for m in range(P):
        r = m % HEAD
        if r < 32:
            swap[m + 32, m] = -1.0
        else:
            swap[m - 32, m] = 1.0
    f["swap"] = swap
    inv = (10000.0 ** (-np.arange(0, HEAD, 2, dtype=np.float32) / np.float32(HEAD))).astype(np.float32)
    ang = (np.arange(SEQ, dtype=np.float32)[None, :] * inv[np.arange(P) % 32][:, None]).astype(np.float32)
    f["cos"] = np.cos(ang)
    f["sin"] = np.sin(ang)
    j, i = np.arange(P)[:, None], np.arange(SEQ)[None, :]
    ret = []
    for h in range(4):
        lg = math.log1p(-(2.0 ** (-5.0 - h)))
        ret.append(np.where(i >= j, np.exp(np.where(i >= j, i - j, 0) * lg), 0.0) * HEAD ** -0.5)
    f["retain"] = np.concatenate(ret, axis=1)
    f["past"] = np.concatenate([j < i, (j < i)[:, 0:P]], axis=1)
    f["past_neg"] = np.where(f["past"], 0.0, NEG)
    f["down"] = (s >= t)
    at, cols, w = {}, [], 0
    for name, a in f.items():
        at[name] = (w, a.shape[1])
        cols.append(np.asarray(a, np.float32))
        w += a.shape[1]
    return np.ascontiguousarray(np.concatenate(cols, axis=1)), at


def bias_rows():
    out = np.zeros((35, BIAS_W + ATT_HEADS), np.float32)
    u = np.arange(BIAS_W)
    dist = 255 - u
    b = bucket_of(np.maximum(dist, 0))
    for row in range(32):
        out[row, :BIAS_W] = (b == row) & (dist >= 0)
    for g, dil in enumerate(DILATIONS):
        ok = (dist >= 0) & (dist % dil == 0) & (dist // dil <= WINDOW)
        out[32 + g, :BIAS_W] = np.where(ok, 0.0, NEG)
        out[32 + g, BIAS_W + 4 * g:BIAS_W + 4 * g + 4] = 1.0
    return out


CONST, CONST_AT = constants()
BIAS_ROWS = bias_rows()

VEC = {}
_row = 0
for _name, _n in (("norm1_gain", 8), ("norm2_gain", 8), ("rwkv_shift_mu", 15), ("rwkv_a0", 4), ("rwkv_k_k", 4),
                  ("rwkv_k_a", 4), ("rwkv_r_k", 4), ("rwkv_ln_w", 4), ("rwkv_ln_b", 4),
                  ("q_norm_gain", 3), ("k_norm_gain", 3)):
    VEC[_name] = _row
    _row += _n
assert _row <= P
VEC2 = {}
_row = 0
for _name, _n in (("norm_mix_pre_2", 8), ("norm_mix_post_2", 8), ("norm_ffn_pre_2", 8), ("norm_ffn_post_2", 8),
                  ("conf_dw_b_2", 2), ("conf_ln_g_2", 2), ("conf_ln_b_2", 2), ("ret_norm_g_2", 2),
                  ("sc_conv_w_2", 6), ("conf_dw_w_2", 62)):
    VEC2[_name] = _row
    _row += _n
assert _row <= P


def clear_bank_semaphores(nc, m):
    ids = sorted(s.num for s in m.filled + m.drained)
    assert ids == list(range(ids[0], ids[0] + len(ids)))
    with nc.Block() as block:
        @block.gpsimd
        def _(pool):
            pool.sem_clear(range(ids[0], ids[-1] + 1))


PROJECT_UNITS = 17
RING = 3
MIX_PIECES = 16


def load_mix_piece(sp, m, a, i):
    s = i % RING

    def load(name, k0, n, c0):
        src = a[name][0].rearrange("(c p) n -> p c n", p=P)[:, :, c0:c0 + 256]
        sp.dma_start(m.w_slots[s][:, k0:k0 + n, :], src).then_inc(m.w_landed[s], 16)
    j, part = divmod(i, 3)
    if i >= 12:
        load("w_out", 0, KC, 256 * (i - 12))
    elif part < 2:
        load("w_in", 0, KC, GATE_COL + part * D + 256 * j)
    else:
        load("w_att_out", 0, 2, 256 * j)
        load("w_rwkv_out", 2, 4, 256 * j)


def await_mix_piece(eng, m, i):
    s = i % RING
    loads = len(range(s, PROJECT_UNITS, RING)) + sum(2 if p < 12 and p % 3 == 2 else 1 for p in range(s, i + 1, RING))
    eng.wait_ge(m.w_landed[s], 16 * loads)
    return s


def project_part(nc, m, a):
    UNITS = PROJECT_UNITS
    SPLITS = 2
    with ExitStack() as ctx:
        def sem(n):
            return ctx.enter_context(nc.semaphore(n))
        w_hi = ctx.enter_context(nc.sbuf_tensor("w1_hi", [P, SPLITS, KC, 256], F32R))
        w_lo = ctx.enter_context(nc.sbuf_tensor("w1_lo", [P, SPLITS, KC, 256], F32R))
        x_hi = ctx.enter_context(nc.sbuf_tensor("x1_hi", [P, KC, SEQ], F32R))
        x_lo = ctx.enter_context(nc.sbuf_tensor("x1_lo", [P, KC, SEQ], F32R))
        square, log_ms, rstd = m.bias[:, 0:KC, :], m.bias[:, KC, :], m.bias[:, KC + 1, :]
        x_tok = m.p_rwkv[:, 0:8, 0:256]
        vec_rows = ctx.enter_context(nc.sbuf_tensor("vec_rows", [P, P], F32))
        table = ctx.enter_context(nc.sbuf_tensor("table", [35, ATT_HEADS], F32))
        bucket_rows = ctx.enter_context(nc.sbuf_tensor("bucket_rows", [35, BIAS_W], F32))
        bias_line = ctx.enter_context(nc.sbuf_tensor("bias_line", [ATT_HEADS, BIAS_W], F32))

        x_in, const_in, vec_in, table_in = sem("x_in"), sem("const_in"), sem("vec_in"), sem("table_in")
        m.w_slots[2] = ctx.enter_context(nc.sbuf_tensor("w_slot2", [P, KC, 256], F32))
        w_slots, w_landed = m.w_slots, m.w_landed
        filled, drained = m.filled, m.drained
        rows_zero, square_done, rstd_done, h_done, h_hi, h_lo, split_hi, split_lo = (
            sem("rows_zero"), sem("square_done"), sem("rstd_done"), sem("h_done"), sem("h1_hi"), sem("h1_lo"),
            sem("w1_hi_done"), sem("w1_lo_done"))
        pads_zero, line_out, strip_out, bias_in = sem("pads_zero"), sem("line_out"), sem("strip_out"), sem("bias_in")

        U_VEC, U_X, U_SS, U_B = 0, 1, 5, 6
        U_W = U_B + 1
        block = ctx.enter_context(nc.Block())

        @block.sync
        def _(sp):
            def load(u):
                n = 256 if u < 16 else 32
                sp.dma_start(w_slots[u % RING][:, :, 0:n],
                             a["w_in"][0].rearrange("(c p) n -> p c n", p=P)[:, :, 256 * u:256 * u + n]
                             ).then_inc(w_landed[u % RING], 16)

            for t in range(TT):
                sp.dma_start(x_tok[:, 4 * t:4 * t + 4, :], a["x"][0, t * P:(t + 1) * P, :].rearrange(
                    "p (r n) -> p r n", n=256)).then_inc(x_in, 16)
            sp.dma_start(m.const[:, :], a["const"]).then_inc(const_in, 16)
            sp.dma_start(table[0:32, :], a["rel_bias_table"]).then_inc(table_in, 16)
            sp.dma_start(table[32:35, :], a["bias_rows"][32:35, BIAS_W:]).then_inc(table_in, 16)
            sp.dma_start(bucket_rows[:, :], a["bias_rows"][:, 0:BIAS_W]).then_inc(table_in, 16)
            sp.wait_ge(x_in, 32)
            sp.wait_ge(vec_in, 16 * m.n_vec)
            for u in range(RING):
                load(u)
            for u in range(RING, UNITS):
                sp.wait_ge(split_lo, u - RING + 1)
                load(u)
                if u == 4:
                    sp.wait_ge(drained[U_B], 1)
                    sp.dma_start(m.line_dram[:, :], bias_line[:, :]).then_inc(line_out, 16)
                if u == 6:
                    sp.wait_ge(line_out, 16)
                    n = ATT_HEADS * BIAS_W
                    sp.dma_start(bass.AP(m.strip_dram, 0, [[n, P], [1, n]]), bass.AP(m.line_dram, 0, [[0, P], [1, n]])
                                 ).then_inc(strip_out, 16)
                if u == 9:
                    sp.wait_ge(h_done, KC)
                    sp.wait_ge(strip_out, 16)
                    sp.dma_start(m.bias[:, :, :], bass.AP(m.strip_dram, P - 1, [[ATT_HEADS * BIAS_W - 1, P],
                                                                                [BIAS_W, ATT_HEADS], [1, SEQ]])
                                 ).then_inc(bias_in, 16)
            sp.wait_ge(split_lo, UNITS - 1)
            q = U_W + UNITS - 1
            sp.wait_ge(filled[q % BANKS], q // BANKS + 1)
            for i in range(2):
                load_mix_piece(sp, m, a, i)
            sp.wait_ge(bias_in, 16)

        @block.gpsimd
        def _(pool):
            pool.memset(m.w_up[:, :], 0.0)
            pool.memset(m.a_up[:, :], 0.0)
            pool.memset(m.g_up[:, :, :], 0.0).then_inc(pads_zero, 1)
            pool.wait_ge(filled[U_X + 3], 1)
            pool.memset(m.p_rwkv[:, 0:14, 0:1], 0.0)
            pool.memset(m.p_rwkv[:, 14, :], 0.0).then_inc(pads_zero, 1)
            for u in range(UNITS - 1):
                pool.wait_ge(split_hi, u + 1)
                pool.tensor_tensor(w_lo[:, u % SPLITS, :, :], w_slots[u % RING][:, :, :],
                                   w_hi[:, u % SPLITS, :, :].bitcast(F32), ALU.subtract).then_inc(split_lo, 1)

        @block.scalar
        def _(act):
            act.wait_ge(rows_zero, 1)
            n_vec = 0

            def row(name, dst_row, src, c0=0, c1=P):
                act.dma_start(vec_rows[dst_row:dst_row + src.shape[0], c0:c1], src).then_inc(vec_in, 16)
                return 1
            for name in ("norm1_gain", "norm2_gain", "rwkv_a0", "rwkv_k_k", "rwkv_k_a", "rwkv_ln_w", "rwkv_ln_b"):
                n_vec += row(name, VEC[name], a[name][0].rearrange("(c p) -> c p", p=P))
            n_vec += row("", VEC["rwkv_r_k"], a["rwkv_r_k"][0].rearrange("(c h) n -> c (h n)", h=2))
            mu = a["rwkv_shift_mu"]
            n_vec += row("", VEC["rwkv_shift_mu"], mu[0, 0:14 * P].rearrange("(c p) -> c p", p=P))
            n_vec += row("", VEC["rwkv_shift_mu"] + 14, mu[:, 14 * P:1824], 0, 32)
            for name in ("q_norm_gain", "k_norm_gain"):
                for half in range(2):
                    n_vec += row("", VEC[name], a[name][0], half * HEAD, half * HEAD + HEAD)
            assert n_vec == m.n_vec
            act.wait_ge(pads_zero, 1)
            act.dma_start(m.w_up[0:64, :], a["rwkv_w_up"][0]).then_inc(m.lora_in, 16)
            act.dma_start(m.w_up[64:65, :], a["rwkv_w0"]).then_inc(m.lora_in, 16)
            act.dma_start(m.a_up[64:128, :], a["rwkv_a_up"][0]).then_inc(m.lora_in, 16)
            act.dma_start(m.g_up[:, 0, :], a["rwkv_g_up"][0, 0:P, :]).then_inc(m.lora_in, 16)
            act.dma_start(m.g_up[0:32, 1, :], a["rwkv_g_up"][0, P:160, :]).then_inc(m.lora_in, 16)
            for b in range(4):
                act.wait_ge(drained[(U_X + b) % BANKS], (U_X + b) // BANKS + 1)
                act.activation(square[:, 2 * b:2 * b + 2, :], m.xT[:, 2 * b:2 * b + 2, :], ACT.Square
                               ).then_inc(square_done, 1)
            act.wait_ge(filled[U_SS], 1)
            act.activation(log_ms[:, :], m.ps[:, U_SS, 0:SEQ], ACT.Ln, bias=m.c("eps"), scale=1.0 / D
                           ).then_inc(drained[U_SS], 1)
            act.drain()
            act.activation(rstd[:, :], log_ms[:, :], ACT.Exp, scale=-0.5).then_inc(rstd_done, 1)
            def split(u):
                if u >= SPLITS:
                    q = U_W + u - SPLITS
                    act.wait_ge(filled[q % BANKS], q // BANKS + 1)
                act.wait_ge(w_landed[u % RING], 16 * (u // RING + 1))
                act.activation(w_hi[:, u % SPLITS, :, :], w_slots[u % RING][:, :, :], ACT.Copy).then_inc(split_hi, 1)

            split(0)
            for c in range(KC):
                act.wait_ge(h_done, c + 1)
                act.activation(x_hi[:, c, :], m.hT[:, c, :], ACT.Copy).then_inc(h_hi, 1)
            for u in range(1, UNITS - 1):
                split(u)
            act.wait_ge(m.lora_in, 5 * 16)

        @block.tensor
        def _(pe):
            pe.wait_ge(const_in, 16)
            pe.wait_ge(x_in, 32)
            for b in range(4):
                for c in (2 * b, 2 * b + 1):
                    for t in range(TT):
                        at = (c % 2) * SEQ + t * P
                        src = x_tok[:, 4 * t + c // 2, (c % 2) * P:(c % 2 + 1) * P]
                        mm = pe.transpose(m.ps[:, U_X + b, at:at + P], src, m.c("ident"))
                mm.then_inc(filled[U_X + b], 1)
            for c in range(KC):
                if c % 2 == 0:
                    pe.wait_ge(square_done, c // 2 + 1)
                mm = pe.matmul(m.ps[:, U_SS, 0:SEQ], m.c("ones"), square[:, c, :], start=(c == 0), stop=(c == KC - 1))
            mm.then_inc(filled[U_SS], 1)
            pe.wait_ge(vec_in, 16 * m.n_vec)
            pe.transpose(m.ps[:, U_VEC, 0:P], vec_rows[:, :], m.c("ident")).then_inc(filled[U_VEC], 1)
            pe.wait_ge(table_in, 48)
            pe.matmul(m.ps[0:ATT_HEADS, U_B, 0:BIAS_W], table[:, :], bucket_rows[:, :], start=True, stop=True
                      ).then_inc(filled[U_B], 1)
            for u in range(UNITS):
                q = U_W + u
                b = q % BANKS
                if q >= BANKS:
                    pe.wait_ge(drained[b], q // BANKS)
                if u == 16:
                    pe.wait_ge(w_landed[u % RING], 16 * (u // RING + 1))
                    for k in range(KC):
                        mm = pe.matmul(m.ps[0:32, b, 0:SEQ], w_slots[u % RING][:, k, 0:32], m.hT[:, k, :],
                                       start=(k == 0), stop=(k == KC - 1))
                else:
                    for j in range(2):
                        for part, (w, x) in enumerate(((w_hi, x_hi), (w_hi, x_lo), (w_lo, x_hi))):
                            if j == 0:
                                pe.wait_ge(split_lo if part == 2 else split_hi, u + 1)
                            for k in range(KC):
                                if u == 0 and j == 0:
                                    pe.wait_ge(h_lo if part == 1 else h_hi, k + 1)
                                cut = slice(j * P, (j + 1) * P)
                                if 6 <= u < 9:
                                    lhs, rhs = x[:, k, cut], w[:, u % SPLITS, k, :]
                                else:
                                    lhs, rhs = w[:, u % SPLITS, k, cut], x[:, k, :]
                                mm = pe.matmul(m.ps[:, b, j * SEQ:(j + 1) * SEQ], lhs, rhs, start=(part == 0 and k == 0),
                                               stop=(part == 2 and k == KC - 1))
                mm.then_inc(filled[b], 1)

        @block.vector
        def _(dve):
            dve.memset(vec_rows[:, :], 0.0).then_inc(rows_zero, 1)
            for b in range(4):
                dve.wait_ge(filled[U_X + b], 1)
                dve.tensor_copy(m.xT[:, 2 * b:2 * b + 2, :],
                                m.ps[:, U_X + b, :].rearrange("p (c t) -> p c t", c=2)).then_inc(drained[U_X + b], 1)
            dve.wait_ge(filled[U_VEC], 1)
            dve.tensor_copy(m.vec[:, :], m.ps[:, U_VEC, 0:P]).then_inc(drained[U_VEC], 1)

            dve.wait_ge(filled[U_B], 1)
            dve.tensor_copy(bias_line[:, :], m.ps[0:ATT_HEADS, U_B, 0:BIAS_W]).then_inc(drained[U_B], 1)
            dve.wait_ge(rstd_done, 1)
            dve.wait_ge(drained[U_VEC], 1)
            dve.wait_ge(drained[U_X + 3], 1)
            for c in range(KC):
                dve.scalar_tensor_tensor(m.hT[:, c, :], m.xT[:, c, :], m.v("norm1_gain", c), rstd[:, :],
                                         ALU.mult, ALU.mult).then_inc(h_done, 1)
            for c in range(KC):
                dve.wait_ge(h_hi, c + 1)
                dve.tensor_tensor(x_lo[:, c, :], m.hT[:, c, :], x_hi[:, c, :].bitcast(F32), ALU.subtract).then_inc(h_lo, 1)
            dve.wait_ge(pads_zero, 2)
            for u in range(UNITS):
                q = U_W + u
                b = q % BANKS
                dve.wait_ge(filled[b], q // BANKS + 1)
                src = m.ps[:, b, :].rearrange("p (c t) -> p c t", c=2)
                if u < 6:
                    ins = dve.tensor_copy(m.qk[:, 2 * u:2 * u + 2, :], src)
                elif u < 9:
                    ins = dve.tensor_copy(m.v_att[:, :, (u - 6) * 256:(u - 5) * 256], src)
                elif u < 16:
                    c = 2 * (u - 9)
                    ins = dve.tensor_copy(m.p_rwkv[:, c:c + 2, 1:SEQ + 1], src)
                else:
                    ins = dve.tensor_copy(m.p_rwkv[0:32, 14, 1:SEQ + 1], m.ps[0:32, b, 0:SEQ])
                ins.then_inc(drained[b], 1)


def attention_part(nc, m, a):
    H = 4
    with ExitStack() as ctx:
        def sem(n):
            return ctx.enter_context(nc.semaphore(n))

        def sb(n, s):
            return ctx.enter_context(nc.sbuf_tensor(n, s, F32))
        square = sb("att_square", [P, 12, SEQ])
        log_ms = sb("att_log", [P, 12, SEQ])
        rstd = sb("att_rstd", [P, 12, SEQ])
        prob = sb("prob", [P, 2, 9 * P])
        neg_max = sb("neg_max", [P, 8])
        row_sum = sb("row_sum", [P, 8])
        row_inv = sb("row_inv", [P, 8])
        prob_T = sb("prob_T", [P, 2, 9 * P])
        filled, drained = m.filled, m.drained
        square_done, rstd_done, normed = sem("a_square"), sem("a_rstd"), sem("a_normed")
        maxed, exped, probs_done = sem("a_maxed"), sem("a_exped"), sem("a_probs")
        U_H = 6

        def score_unit(h, j):
            return U_H + (0 if h == 0 else 3 + 8 * (h - 1)) + j

        def turn_unit(h, j):
            return U_H + 3 + 8 * h + (3 if h < H - 1 else 0) + j

        block = ctx.enter_context(nc.Block())

        @block.scalar
        def _(act):
            for u in range(6):
                act.activation(square[:, 2 * u:2 * u + 2, :], m.qk[:, 2 * u:2 * u + 2, :], ACT.Square
                               ).then_inc(square_done, 1)
            for u in range(6):
                act.wait_ge(filled[u], 1)
                act.activation(log_ms[:, 2 * u:2 * u + 2, :], m.ps[:, u, :].rearrange("p (c t) -> p c t", c=2),
                               ACT.Ln, bias=m.c("eps"), scale=1.0 / HEAD).then_inc(drained[u], 1)
            for u in range(6):
                act.wait_ge(drained[u], 1)
                act.activation(rstd[:, 2 * u:2 * u + 2, :], log_ms[:, 2 * u:2 * u + 2, :], ACT.Exp, scale=-0.5
                               ).then_inc(rstd_done, 1)
            def exp_head(h):
                for t, (c0, n) in enumerate(((0, 3 * P), (3 * P, 6 * P))):
                    i = 2 * h + t
                    act.wait_ge(maxed, i + 1)
                    act.activation(prob[:, h % 2, c0:c0 + n], prob[:, h % 2, c0:c0 + n], ACT.Exp,
                                   bias=neg_max[:, i:i + 1], accum_out=row_sum[:, i:i + 1]).then_inc(exped, 1)

            exp_head(0)
            for h in range(H):
                if h + 1 < H:
                    exp_head(h + 1)
                for j in range(3):
                    q = turn_unit(h, j)
                    act.wait_ge(filled[q % BANKS], q // BANKS + 1)
                    at, n = ((0, 3 * P), (3 * P, 4 * P), (7 * P, 2 * P))[j]
                    act.activation(prob_T[:, h % 2, at:at + n], m.ps[:, q % BANKS, 0:n], ACT.Copy
                                   ).then_inc(drained[q % BANKS], 1)
                for t in range(2):
                    q = turn_unit(h, 3 + t)
                    r = (h % 2) * HEAD
                    act.wait_ge(filled[q % BANKS], q // BANKS + 1)
                    act.activation(m.att_T[r:r + HEAD, h // 2, t * P:(t + 1) * P], m.ps[r:r + HEAD, q % BANKS, 0:P],
                                   ACT.Copy).then_inc(drained[q % BANKS], 1)

        @block.tensor
        def _(pe):
            for u in range(6):
                pe.wait_ge(square_done, u + 1)
                pe.matmul(m.ps[:, u, :], m.c("pair_ones"), square[:, 2 * u:2 * u + 2, :], start=True, stop=True
                          ).then_inc(filled[u], 1)
            def scores(h):
                pe.wait_ge(normed, 6 if h < 2 else 12)
                r = (h % 2) * HEAD
                for j, (t, groups, keys) in enumerate(((0, (0, 1, 2), P), (1, (0, 1), SEQ), (1, (2,), SEQ))):
                    q = score_unit(h, j)
                    if q >= BANKS:
                        pe.wait_ge(drained[q % BANKS], q // BANKS)
                    for g in groups:
                        c = 2 * g + h // 2
                        at = (g - groups[0]) * keys
                        mm = pe.matmul(m.ps[:, q % BANKS, at:at + keys], m.qk[r:r + HEAD, c, t * P:(t + 1) * P],
                                       m.qk[r:r + HEAD, 6 + c, 0:keys], start=True, stop=True)
                    mm.then_inc(filled[q % BANKS], 1)

            def outputs(h):
                for j, (first, n) in enumerate(((0, 3), (3, 4), (7, 2))):
                    q = turn_unit(h, j)
                    pe.wait_ge(probs_done, 2 * h + (1 if j == 0 else 2))
                    pe.wait_ge(drained[q % BANKS], q // BANKS)
                    for i in range(n):
                        c = (first + i) * P
                        mm = pe.transpose(m.ps[:, q % BANKS, i * P:(i + 1) * P], prob[:, h % 2, c:c + P], m.c("ident"))
                    mm.then_inc(filled[q % BANKS], 1)
                r = (h % 2) * HEAD
                for t in range(2):
                    q = turn_unit(h, 3 + t)
                    for j in ((0,), (1, 2))[t]:
                        w = turn_unit(h, j)
                        pe.wait_ge(drained[w % BANKS], w // BANKS + 1)
                    pe.wait_ge(drained[q % BANKS], q // BANKS)
                    tiles = [(g, 0, g) for g in range(3)] if t == 0 else [(3 + 2 * g + k, k, g) for g in range(3) for k in range(2)]
                    for n, (tile, k, g) in enumerate(tiles):
                        col = (4 * g + h) * HEAD
                        mm = pe.matmul(m.ps[r:r + HEAD, q % BANKS, 0:P], m.v_att[:, k, col:col + HEAD],
                                       prob_T[:, h % 2, tile * P:(tile + 1) * P],
                                       start=(n == 0), stop=(n == len(tiles) - 1))
                    mm.then_inc(filled[q % BANKS], 1)

            scores(0)
            for h in range(H):
                if h + 1 < H:
                    scores(h + 1)
                outputs(h)

        @block.vector
        def _(dve):
            for c in (*range(0, 12, 2), *range(1, 12, 2)):
                dve.wait_ge(rstd_done, c // 2 + 1)
                gain = m.v("q_norm_gain", c // 2) if c < 6 else m.v("k_norm_gain", (c - 6) // 2)
                dve.scalar_tensor_tensor(m.qk[:, c, :], m.qk[:, c, :], gain, rstd[:, c, :], ALU.mult, ALU.mult
                                         ).then_inc(normed, 1)
            bias = m.bias[:, :, :].rearrange("p (g h) k -> p g h k", g=3)
            def masked_head(h):
                for t in range(2):
                    i = 2 * h + t
                    c0, n = ((0, 3 * P), (3 * P, 6 * P))[t]
                    if h >= 2 and t == 0:
                        w = turn_unit(h - 2, 2)
                        dve.wait_ge(filled[w % BANKS], w // BANKS + 1)
                    for j in ((0,), (1, 2))[t]:
                        q = score_unit(h, j)
                        g0, ng = ((0, 3), (0, 2), (2, 1))[j]
                        keys = P if t == 0 else SEQ
                        at = (0, 3 * P, 7 * P)[j]
                        dve.wait_ge(filled[q % BANKS], q // BANKS + 1)
                        dve.scalar_tensor_tensor(
                            prob[:, h % 2, at:at + ng * keys].rearrange("p (g k) -> p g k", g=ng),
                            m.ps[:, q % BANKS, 0:ng * keys].rearrange("p (g k) -> p g k", g=ng), HEAD ** -0.5,
                            bias[:, g0:g0 + ng, h, SEQ - keys:SEQ], ALU.mult, ALU.add
                        ).then_inc(drained[q % BANKS], 1)
                    dve.drain()
                    dve.tensor_reduce(neg_max[:, i:i + 1], prob[:, h % 2, c0:c0 + n], AX, ALU.max, negate=True
                                      ).then_inc(maxed, 1)

            masked_head(0)
            for h in range(H):
                if h + 1 < H:
                    masked_head(h + 1)
                for t in range(2):
                    i = 2 * h + t
                    c0, n = ((0, 3 * P), (3 * P, 6 * P))[t]
                    dve.wait_ge(exped, i + 1)
                    dve.reciprocal(row_inv[:, i:i + 1], row_sum[:, i:i + 1])
                    dve.drain()
                    dve.tensor_scalar(prob[:, h % 2, c0:c0 + n], prob[:, h % 2, c0:c0 + n], row_inv[:, i:i + 1],
                                      None, ALU.mult).then_inc(probs_done, 1)


def recurrence_part(nc, m, a):
    PAIRS = 4
    with ExitStack() as ctx:
        def sem(n):
            return ctx.enter_context(nc.semaphore(n))

        def sb(n, s):
            return ctx.enter_context(nc.sbuf_tensor(n, s, F32))

        w_upto = sb("w_upto", [P, 8, P])
        rate = sb("rate", [P, 8, P])
        gate = sb("gate", [P, 8, P])
        alpha_rho = sb("alpha_rho", [P, 8, 2, P])
        beta = sb("beta", [P, 8, P])
        kappa = sb("kappa", [P, 8, P])
        key = sb("key", [P, 8, P])
        quad = sb("quad", [P, 16, 4 * P])
        work = [sb(f"work{i}", [P, 16, P]) for i in range(8)]
        LEAF_, REST, SQ, SQ_T, Q4_T, X, X_T, N = work

        w_before, w_inv = work[7][:, 0:8, :], work[7][:, 8:16, :]
        kk, kk_sq = work[6][:, 0:8, :], work[6][:, 8:16, :]
        kk_inv = work[5][:, 0:8, :]
        sig_w = work[5][:, 8:16, :].rearrange("p (t f) n -> p t (f n)", t=TT)
        tanh_w = work[4][:, 0:2, :].rearrange("p a b -> p (a b)")
        sig_g = work[4][:, 2:6, :].rearrange("p (c t) n -> p c (t n)", c=2)
        beta_z = work[0][:, :, :].rearrange("p (t c f) n -> p t c (f n)", t=TT, c=2)
        kappa_z = work[1][:, :, :].rearrange("p (t c f) n -> p t c (f n)", t=TT, c=2)
        mu_tok = work[2][:, :, :].rearrange("p (t k f) n -> p t k (f n)", t=TT, k=2)
        q_T = work[3][:, 0:8, :].rearrange("p (t f) n -> p t f n", t=TT)
        v_tok = work[3][:, 8:16, :].rearrange("p (t f) n -> p t (f n)", t=TT)
        g_bd = work[4][:, 0:8, :].rearrange("p (c f) n -> p c f n", c=2)
        state = work[5][:, 0:8, :].rearrange("p (c f) n -> p c f n", c=2)
        o_raw = work[5][:, 8:16, :]
        ab_tok = work[7][:, :, :].rearrange("p (t k f) n -> p t k (f n)", t=TT, k=2)
        M_T = X_T

        def rows(c0, c1):
            return m.p_rwkv[:, c0:c1, 1:SEQ + 1]

        def by_chunk(x):
            return x.rearrange("p (c t) n -> p c (t n)", t=TT)

        filled, drained = m.filled, m.drained
        ones_set, mixed, lora_act, kk_raw, kk_squared = (
            sem("ones_set"), sem("mixed"), sem("lora_act"), sem("kk_raw"), sem("kk_squared"))
        clamped, rooted, operands, start_x, start_n = (
            sem("clamped"), sem("rooted"), sem("operands"), sem("start_x"), sem("start_n"))
        centred, o_squared, o_rstd, bonus_in = (
            sem("centred"), sem("o_squared"), sem("o_rstd"), sem("bonus_in"))

        U_Z, U_RATE, U_GATE, U_CUM, U_KK = 0, 2, 4, 6, 10
        U_QUAD, U_LOW, U_INV = 12, 28, 32
        STEPS = 15
        U_TOK = U_INV + 4 * STEPS
        U_BV, U_MU, U_Q, U_O, U_G = U_TOK + 8, U_TOK + 10, U_TOK + 14, U_TOK + 16, U_TOK + 18
        U_S = U_G + 2
        U_MEAN, U_BONUS, U_VAR = U_S + 6, U_S + 8, U_S + 10

        DT = quad
        steps = [
            (DT, LEAF_, SQ, False, ()),
            (LEAF_, DT, SQ_T, False, ()),
            (SQ, SQ_T, Q4_T, False, (0, 1)),
            (SQ_T, X, X, True, (1,)),
            (SQ, X_T, X_T, True, (0,)),
            (X, Q4_T, X_T, True, (2, 3, 4)),
            (Q4_T, X, X, True, (2, 3)),
            (X_T, REST, LEAF_, False, (5,)),
            (REST, X_T, SQ, False, (5,)),
            (SQ, LEAF_, SQ_T, False, (7, 8)),
            (LEAF_, SQ, Q4_T, False, (7, 8)),
            (Q4_T, SQ_T, REST, False, (9, 10)),
            (SQ_T, N, N, True, (9,)),
            (REST, N, N, True, (11, 12)),
            (X, N, M_T, False, (6, 13)),
        ]
        instances = [(tt, par, f) for tt in range(TT) for par in range(2) for f in range(PAIRS)]
        block = ctx.enter_context(nc.Block())

        @block.gpsimd
        def _(pool):
            pool.memset(tanh_w[:, :], 1.0).then_inc(ones_set, 1)

        @block.scalar
        def _(act):
            act.wait_ge(mixed, 3)
            act.wait_ge(ones_set, 1)
            act.activation(tanh_w[0:64, :], m.p_rwkv[0:64, LORA_CHUNK, 1:SEQ + 1], ACT.Tanh).then_inc(lora_act, 1)
            act.activation(sig_g[:, :, :], rows(13, 15), ACT.Sigmoid).then_inc(lora_act, 1)
            for t in range(TT):
                act.wait_ge(filled[U_Z + t], 1)
                act.activation(sig_w[:, t, :], m.ps[:, U_Z + t, :], ACT.Sigmoid).then_inc(drained[U_Z + t], 1)
            for f in range(PAIRS):
                b = U_RATE + f // 2
                act.wait_ge(filled[b], 1)
                ins = act.activation(by_chunk(rate[:, :, :])[:, f, :], m.ps[:, b, (f % 2) * SEQ:(f % 2 + 1) * SEQ],
                                     ACT.Sigmoid, bias=m.v("rwkv_a0", f))
                if f % 2:
                    ins.then_inc(drained[b], 1)
            for f in range(PAIRS):
                act.wait_ge(kk_raw, f + 1)
                act.activation(kk_sq[:, 2 * f:2 * f + 2, :], kk[:, 2 * f:2 * f + 2, :], ACT.Square).then_inc(kk_squared, 1)
            for f in range(PAIRS):
                q = U_CUM + f
                act.wait_ge(filled[q % BANKS], q // BANKS + 1)
                src = m.ps[:, q % BANKS, :].rearrange("p (t k n) -> p t k n", t=TT, k=2)
                act.activation(w_upto[:, 2 * f:2 * f + 2, :], src[:, :, 0, :], ACT.Exp)
                act.activation(w_before[:, 2 * f:2 * f + 2, :], src[:, :, 1, :], ACT.Exp)
                act.activation(w_inv[:, 2 * f:2 * f + 2, :], src[:, :, 0, :], ACT.Exp, scale=-1.0
                               ).then_inc(drained[q % BANKS], 1)
            act.wait_ge(clamped, 2)
            act.activation(kk_inv, kk_inv, ACT.Ln)
            act.drain()
            act.activation(kk_inv, kk_inv, ACT.Exp, scale=-0.5).then_inc(rooted, 1)
            for s, (_, _, out, adds, _) in enumerate(steps):
                if adds:
                    continue
                for g in range(4):
                    q = U_INV + 4 * s + g
                    act.wait_ge(filled[q % BANKS], q // BANKS + 1)
                    act.activation(out[:, 4 * g:4 * g + 4, :], m.ps[:, q % BANKS, :].rearrange("p (i n) -> p i n", i=4),
                                   ACT.Copy).then_inc(drained[q % BANKS], 1)
            for q, dst in ((U_TOK, v_tok[:, 0, :]), (U_TOK + 1, v_tok[:, 1, :]),
                           (U_TOK + 6, ab_tok[:, 0, 0, :]), (U_TOK + 7, ab_tok[:, 1, 0, :]),
                           (U_BV, ab_tok[:, 0, 1, :]), (U_BV + 1, ab_tok[:, 1, 1, :])):
                act.wait_ge(filled[q % BANKS], q // BANKS + 1)
                act.activation(dst, m.ps[:, q % BANKS, :], ACT.Copy).then_inc(drained[q % BANKS], 1)
            for n in range(4):
                q = U_MU + n
                t, hq = n // 2, n % 2
                act.wait_ge(filled[q % BANKS], q // BANKS + 1)
                for k in range(2):
                    ins = act.activation(
                        mu_tok[:, t, k, hq * 256:hq * 256 + 256].rearrange("p (h d) -> p h d", h=4),
                        m.ps[:, q % BANKS, :].rearrange("p (h k d) -> p h k d", h=4, k=2)[:, :, k, :], ACT.Copy)
                ins.then_inc(drained[q % BANKS], 1)
            for t in range(TT):
                q = U_O + t
                act.wait_ge(filled[q % BANKS], q // BANKS + 1)
                act.activation(o_raw.rearrange("p (f t) n -> p f t n", t=TT)[:, :, t, :],
                               m.ps[:, q % BANKS, :].rearrange("p (f n) -> p f n", f=PAIRS), ACT.Copy
                               ).then_inc(drained[q % BANKS], 1)
            for j in range(2):
                act.wait_ge(centred, j + 1)
                act.activation(work[0][:, 4 * j:4 * j + 4, :], o_raw[:, 4 * j:4 * j + 4, :], ACT.Square
                               ).then_inc(o_squared, 1)
            for j in range(2):
                q = U_VAR + j
                act.wait_ge(filled[q % BANKS], q // BANKS + 1)
                act.activation(work[1][:, 4 * j:4 * j + 4, :], m.ps[:, q % BANKS, :].rearrange("p (c n) -> p c n", c=4),
                               ACT.Ln, bias=m.c("gn_eps"), scale=1.0 / HEAD).then_inc(drained[q % BANKS], 1)
            act.drain()
            for j in range(2):
                act.activation(work[1][:, 4 * j:4 * j + 4, :], work[1][:, 4 * j:4 * j + 4, :], ACT.Exp, scale=-0.5
                               ).then_inc(o_rstd, 1)

        @block.tensor
        def _(pe):
            def free(q):
                if q >= BANKS:
                    pe.wait_ge(drained[q % BANKS], q // BANKS)
                return q % BANKS

            def drained_of(q):
                pe.wait_ge(drained[q % BANKS], q // BANKS + 1)

            pe.wait_ge(mixed, 3)
            for f in range(PAIRS):
                b = free(U_RATE + f // 2)
                mm = pe.matmul(m.ps[:, b, (f % 2) * SEQ:(f % 2 + 1) * SEQ], m.a_up[:, f * P:(f + 1) * P],
                               m.p_rwkv[:, LORA_CHUNK, 1:SEQ + 1], start=True, stop=True)
                if f % 2:
                    mm.then_inc(filled[b], 1)
            pe.wait_ge(lora_act, 1)
            for t in range(TT):
                b = free(U_Z + t)
                pe.matmul(m.ps[:, b, :], tanh_w[:, t * P:(t + 1) * P], m.w_up[:, :], start=True, stop=True
                          ).then_inc(filled[b], 1)
            pe.wait_ge(lora_act, 2)
            for f in range(PAIRS):
                b = free(U_GATE + f // 2)
                for k in range(2):
                    mm = pe.matmul(m.ps[:, b, (f % 2) * SEQ:(f % 2 + 1) * SEQ], m.g_up[:, k, f * P:(f + 1) * P],
                                   sig_g[:, k, :], start=(k == 0), stop=(k == 1))
                if f % 2:
                    mm.then_inc(filled[b], 1)
            for t in range(TT):
                drained_of(U_Z + t)
            for f in range(PAIRS):
                b = free(U_CUM + f)
                for t in range(TT):
                    mm = pe.matmul(m.ps[:, b, t * 256:(t + 1) * 256], sig_w[:, t, f * P:(f + 1) * P], m.c("cumulate"),
                                   start=True, stop=True)
                mm.then_inc(filled[b], 1)
            for j in range(2):
                pe.wait_ge(kk_squared, 2 * j + 2)
                b = free(U_KK + j)
                pe.matmul(m.ps[:, b, :], m.c("pair_ones"), kk_sq[:, 4 * j:4 * j + 4, :], start=True, stop=True
                          ).then_inc(filled[b], 1)
            pe.wait_ge(operands, 4)
            for i, (tt, par, f) in enumerate(instances):
                b = free(U_QUAD + i)
                r = slice(par * HEAD, par * HEAD + HEAD)
                both = alpha_rho[r, 2 * f + tt, :, :]
                pe.matmul(m.ps[:, b, 0:256], beta[r, 2 * f + tt, :], both, start=True, stop=True)
                pe.matmul(m.ps[:, b, 256:512], kappa[r, 2 * f + tt, :], both, start=True, stop=True
                          ).then_inc(filled[b], 1)
            for g in range(4):
                b = free(U_LOW + g)
                for f in range(PAIRS):
                    tt, par, _ = instances[4 * g]
                    r = slice(par * HEAD, par * HEAD + HEAD)
                    mm = pe.matmul(m.ps[:, b, f * P:(f + 1) * P], alpha_rho[r, 2 * f + tt, 0, :],
                                   beta[r, 2 * f + tt, :], start=True, stop=True)
                mm.then_inc(filled[b], 1)
            for s, (lhs, rhs, _, _, needs) in enumerate(steps):
                for g in range(4):
                    b = free(U_INV + 4 * s + g)
                    if s <= 1:
                        drained_of(U_LOW + g)
                        drained_of(U_QUAD + 4 * g + 3)
                    if s in (3, 4):
                        pe.wait_ge(start_x, g + 1)
                    if s == 12:
                        pe.wait_ge(start_n, g + 1)
                    for n in needs:
                        drained_of(U_INV + 4 * n + g)
                    for i in range(4 * g, 4 * g + 4):
                        mm = pe.matmul(m.ps[:, b, (i % 4) * P:(i % 4 + 1) * P], lhs[:, i, 0:P], rhs[:, i, 0:P],
                                       start=True, stop=True)
                    mm.then_inc(filled[b], 1)
            for n, src in enumerate((rows(8, 12), beta, kappa, None)):
                for t in range(TT):
                    b = free(U_TOK + 2 * n + t)
                    for f in range(PAIRS):
                        if n == 0:
                            x = m.p_rwkv[:, 8 + f, 1 + t * P:1 + (t + 1) * P]
                        elif n == 3:
                            x = alpha_rho[:, 2 * f + t, 0, :]
                        else:
                            x = src[:, 2 * f + t, :]
                        mm = pe.transpose(m.ps[:, b, f * P:(f + 1) * P], x, m.c("ident"))
                    mm.then_inc(filled[b], 1)
            for t in range(TT):
                drained_of(U_TOK + t)
                b = free(U_BV + t)
                for h in range(8):
                    i = (2 * t + h % 2) * 4 + h // 2
                    mm = pe.matmul(m.ps[:, b, h * HEAD:(h + 1) * HEAD], quad[:, i, 256:384],
                                   v_tok[:, t, h * HEAD:(h + 1) * HEAD], start=True, stop=True)
                mm.then_inc(filled[b], 1)
            for g in range(4):
                drained_of(U_INV + 4 * (STEPS - 1) + g)
            for n in range(4):
                t, hq = n // 2, n % 2
                drained_of(U_TOK + 6 + t)
                drained_of(U_BV + t)
                b = free(U_MU + n)
                for h in range(4 * hq, 4 * hq + 4):
                    i = (2 * t + h % 2) * 4 + h // 2
                    mm = pe.matmul(m.ps[:, b, (h % 4) * P:(h % 4 + 1) * P], M_T[:, i, :],
                                   ab_tok[:, t, :, h * HEAD:(h + 1) * HEAD], start=True, stop=True)
                mm.then_inc(filled[b], 1)
            for t in range(TT):
                for n in range(2):
                    drained_of(U_MU + 2 * t + n)
                b = free(U_Q + t)
                for f in range(PAIRS):
                    for par in range(2):
                        h, i = 2 * f + par, (2 * t + par) * 4 + f
                        mm = pe.matmul(m.ps[par * HEAD:par * HEAD + HEAD, b, f * P:(f + 1) * P],
                                       mu_tok[:, t, 0, h * HEAD:(h + 1) * HEAD], quad[:, i, P:2 * P],
                                       start=True, stop=True)
                mm.then_inc(filled[b], 1)
            for t in range(TT):
                b = free(U_O + t)
                for f in range(PAIRS):
                    for par in range(2):
                        h, i = 2 * f + par, (2 * t + par) * 4 + f
                        out = m.ps[par * HEAD:par * HEAD + HEAD, b, f * P:(f + 1) * P]
                        pe.matmul(out, mu_tok[:, t, 1, h * HEAD:(h + 1) * HEAD], quad[:, i, P:2 * P],
                                  start=True, stop=False)
                        mm = pe.matmul(out, v_tok[:, t, h * HEAD:(h + 1) * HEAD], quad[:, i, 3 * P:4 * P],
                                       start=False, stop=True)
                mm.then_inc(filled[b], 1)
            for c in (1, 2):
                t, cb = c // 2, c % 2
                drained_of(U_TOK + 2 + t)
                b = free(U_G + c - 1)
                for f in range(PAIRS):
                    mm = pe.matmul(m.ps[:, b, f * P:(f + 1) * P], mu_tok[:, t, 0, f * P:(f + 1) * P],
                                   beta_z[:, t, cb, f * P:(f + 1) * P], start=True, stop=True)
                mm.then_inc(filled[b], 1)
            for t in range(TT):
                drained_of(U_TOK + 4 + t)
                drained_of(U_Q + t)
            for c in range(4):
                t, cb = c // 2, c % 2
                if c > 0:
                    drained_of(U_S + 2 * (c - 1))
                    b = free(U_S + 2 * c - 1)
                    for f in range(PAIRS):
                        mm = pe.matmul(m.ps[:, b, f * SUB:(f + 1) * SUB], state[:, (c - 1) % 2, f, :],
                                       q_T[:, t, f, cb * SUB:(cb + 1) * SUB], start=True, stop=True)
                    mm.then_inc(filled[b], 1)
                if c < 3:
                    b = free(U_S + 2 * c)
                    if c > 0:
                        drained_of(U_G + c - 1)
                    for f in range(PAIRS):
                        out = m.ps[:, b, f * P:(f + 1) * P]
                        cols = slice(f * P, (f + 1) * P)
                        pe.matmul(out, beta_z[:, t, cb, cols], mu_tok[:, t, 1, cols], start=True, stop=False)
                        mm = pe.matmul(out, kappa_z[:, t, cb, cols], v_tok[:, t, cols], start=False, stop=(c == 0))
                        if c > 0:
                            mm = pe.matmul(out, g_bd[:, c - 1, f, :], state[:, (c - 1) % 2, f, :],
                                           start=False, stop=True)
                    mm.then_inc(filled[b], 1)
            drained_of(U_S + 5)
            for t in range(TT):
                drained_of(U_O + t)
            for j in range(2):
                b = free(U_MEAN + j)
                pe.matmul(m.ps[:, b, :], m.c("pair_ones"), o_raw[:, 4 * j:4 * j + 4, :], start=True, stop=True
                          ).then_inc(filled[b], 1)
            for j in range(2):
                pe.wait_ge(bonus_in, 4)
                b = free(U_BONUS + j)
                pe.matmul(m.ps[:, b, :], m.c("pair_ones"), work[6][:, 4 * j:4 * j + 4, :], start=True, stop=True
                          ).then_inc(filled[b], 1)
            for j in range(2):
                pe.wait_ge(o_squared, j + 1)
                b = free(U_VAR + j)
                pe.matmul(m.ps[:, b, :], m.c("pair_ones"), work[0][:, 4 * j:4 * j + 4, :], start=True, stop=True
                          ).then_inc(filled[b], 1)

        @block.vector
        def _(dve):
            def await_filled(q):
                dve.wait_ge(filled[q % BANKS], q // BANKS + 1)
                return q % BANKS

            for c0, c1, dst in ((12, 15, work[3]), (0, 8, work[0]), (8, 12, work[1])):
                d = by_chunk(dst[:, 0:2 * (c1 - c0), :])
                dve.tensor_tensor(d, m.p_rwkv[:, c0:c1, 0:SEQ], rows(c0, c1), ALU.subtract)
                dve.drain()
                for c in range(c0, c1):
                    dve.scalar_tensor_tensor(m.p_rwkv[:, c, 1:SEQ + 1], d[:, c - c0, :], m.v("rwkv_shift_mu", c),
                                             m.p_rwkv[:, c, 1:SEQ + 1], ALU.mult, ALU.add).then_inc(mixed, 1)
            dve.drain()
            for f in range(PAIRS):
                dve.tensor_scalar(by_chunk(kk)[:, f, :], m.p_rwkv[:, 4 + f, 1:SEQ + 1], m.v("rwkv_k_k", f), None,
                                  ALU.mult).then_inc(kk_raw, 1)
            for j in range(2):
                b = await_filled(U_GATE + j)
                dve.tensor_copy(gate[:, 4 * j:4 * j + 4, :], m.ps[:, b, :].rearrange("p (c n) -> p c n", c=4)
                                ).then_inc(drained[b], 1)
            for j in range(2):
                q = U_RATE + j
                dve.wait_ge(drained[q % BANKS], q // BANKS + 1)
            for f in range(PAIRS):
                dve.tensor_scalar(by_chunk(key[:, :, :])[:, f, :], by_chunk(rate[:, :, :])[:, f, :], -1.0,
                                  m.v("rwkv_k_a", f), ALU.add, ALU.mult)
            dve.drain()
            dve.scalar_tensor_tensor(by_chunk(key[:, :, :]), by_chunk(key[:, :, :]), 1.0, rows(4, 8),
                                     ALU.add, ALU.mult)
            for j in range(2):
                b = await_filled(U_KK + j)
                dve.tensor_scalar(kk_inv[:, 4 * j:4 * j + 4, :], m.ps[:, b, :].rearrange("p (c n) -> p c n", c=4),
                                  1e-24, None, ALU.max).then_inc(drained[b], 1)
                dve.drain().then_inc(clamped, 1)
            for f in range(PAIRS):
                q = U_CUM + f
                dve.wait_ge(drained[q % BANKS], q // BANKS + 1)
            dve.tensor_tensor(kappa[:, :, :], key[:, :, :], w_inv, ALU.mult).then_inc(operands, 1)
            dve.tensor_tensor(alpha_rho[:, :, 1, :], m.p_rwkv[:, 0:4, 1:SEQ + 1].rearrange("p c (t n) -> p c t n", t=2),
                              w_upto[:, :, :].rearrange("p (c t) n -> p c t n", t=2), ALU.mult).then_inc(operands, 1)
            dve.wait_ge(rooted, 1)
            dve.tensor_tensor(kk, kk, kk_inv, ALU.mult)
            dve.drain()
            dve.scalar_tensor_tensor(alpha_rho[:, :, 0, :], w_before, -1.0, kk, ALU.mult, ALU.mult
                                     ).then_inc(operands, 1)
            dve.tensor_tensor(beta[:, :, :], kk, rate[:, :, :], ALU.mult)
            dve.drain()
            dve.tensor_tensor(beta[:, :, :], beta[:, :, :], w_inv, ALU.mult).then_inc(operands, 1)
            for i in range(16):
                b = await_filled(U_QUAD + i)
                dve.tensor_tensor(quad[:, i, :], m.ps[:, b, :], m.c("quad_mask"), ALU.mult).then_inc(drained[b], 1)

            def wide(name):
                return m.c(name).rearrange("p (o n) -> p o n", o=1).to_broadcast([P, 4, P])
            for g in range(4):
                b = await_filled(U_LOW + g)
                i = slice(4 * g, 4 * g + 4)
                src = m.ps[:, b, :].rearrange("p (i n) -> p i n", i=4)
                dve.tensor_tensor(LEAF_[:, i, :], src, wide("leaf_low"), ALU.mult)
                dve.tensor_tensor(REST[:, i, :], src, wide("rest_low"), ALU.mult).then_inc(drained[b], 1)
                dve.drain()
                dve.tensor_tensor(X[:, i, :], LEAF_[:, i, :], wide("ident"), ALU.add)
                dve.tensor_tensor(X_T[:, i, :], quad[:, i, 0:P], wide("ident"), ALU.add)
                dve.drain().then_inc(start_x, 1)
            for s, (_, _, out, adds, needs) in enumerate(steps):
                if s == 12:
                    for g in range(4):
                        i = slice(4 * g, 4 * g + 4)
                        q = U_INV + 4 * 8 + g
                        dve.wait_ge(drained[q % BANKS], q // BANKS + 1)
                        dve.tensor_tensor(N[:, i, :], SQ[:, i, :], wide("ident"), ALU.add)
                        dve.drain().then_inc(start_n, 1)
                if not adds:
                    continue
                for g in range(4):
                    i = slice(4 * g, 4 * g + 4)
                    b = await_filled(U_INV + 4 * s + g)
                    dve.tensor_tensor(out[:, i, :], m.ps[:, b, :].rearrange("p (i n) -> p i n", i=4), out[:, i, :],
                                      ALU.add).then_inc(drained[b], 1)
                dve.drain()
            for n, dst in ((1, beta_z), (2, kappa_z)):
                for t in range(TT):
                    b = await_filled(U_TOK + 2 * n + t)
                    dve.tensor_scalar(dst[:, t, 0, :], m.ps[:, b, :], m.c("half_rows")[:, 0:1], None, ALU.mult)
                    dve.tensor_scalar(dst[:, t, 1, :], m.ps[:, b, :], m.c("half_rows")[:, 1:2], None, ALU.mult
                                      ).then_inc(drained[b], 1)
            for f in range(PAIRS):
                if f == 0:
                    for n in range(4):
                        q = U_MU + n
                        dve.wait_ge(drained[q % BANKS], q // BANKS + 1)
                dve.scalar_tensor_tensor(by_chunk(work[6][:, 0:8, :])[:, f, :], m.p_rwkv[:, f, 1:SEQ + 1],
                                         m.v("rwkv_r_k", f), by_chunk(key[:, :, :])[:, f, :], ALU.mult, ALU.mult
                                         ).then_inc(bonus_in, 1)
            for t in range(TT):
                b = await_filled(U_Q + t)
                rho = alpha_rho[:, :, 1, :].rearrange("p (f t) n -> p f t n", t=TT)[:, :, t, :]
                dve.tensor_tensor(q_T[:, t, :, :], m.ps[:, b, :].rearrange("p (f n) -> p f n", f=PAIRS), rho, ALU.add
                                  ).then_inc(drained[b], 1)
            for c in (1, 2):
                b = await_filled(U_G + c - 1)
                g = g_bd[:, c - 1, :, :]
                dve.tensor_tensor(g, m.ps[:, b, :].rearrange("p (f n) -> p f n", f=PAIRS), wide("pair_ones"), ALU.mult)
                dve.drain()
                dve.tensor_tensor(g, g, wide("ident"), ALU.add).then_inc(drained[b], 1)
            for t in range(TT):
                q = U_O + t
                dve.wait_ge(drained[q % BANKS], q // BANKS + 1)
            o_rows = by_chunk(o_raw)
            for c in range(4):
                t, cb = c // 2, c % 2
                if c > 0:
                    b = await_filled(U_S + 2 * c - 1)
                    o = o_rows[:, :, c * SUB:(c + 1) * SUB]
                    dve.tensor_tensor(o, m.ps[:, b, 0:256].rearrange("p (f n) -> p f n", f=PAIRS), o, ALU.add
                                      ).then_inc(drained[b], 1)
                if c < 3:
                    b = await_filled(U_S + 2 * c)
                    for f in range(PAIRS):
                        end = cb * SUB + SUB - 1
                        ins = dve.scalar_tensor_tensor(
                            state[:, c % 2, f, :], m.ps[:, b, f * P:(f + 1) * P], w_upto[:, 2 * f + t, end:end + 1],
                            m.c("pair_ones"), ALU.mult, ALU.mult)
                    ins.then_inc(drained[b], 1)
            dve.drain()
            for j in range(2):
                b = await_filled(U_MEAN + j)
                o = o_raw[:, 4 * j:4 * j + 4, :]
                dve.scalar_tensor_tensor(o, m.ps[:, b, :].rearrange("p (c n) -> p c n", c=4), -1.0 / HEAD, o,
                                         ALU.mult, ALU.add).then_inc(drained[b], 1)
                dve.drain().then_inc(centred, 1)
            bonus = by_chunk(work[6][:, 8:16, :])
            for j in range(2):
                b = await_filled(U_BONUS + j)
                dve.tensor_tensor(bonus[:, 2 * j:2 * j + 2, :], m.ps[:, b, :].rearrange("p (c n) -> p c n", c=2),
                                  rows(8 + 2 * j, 10 + 2 * j), ALU.mult).then_inc(drained[b], 1)
            for j in range(2):
                o = o_raw[:, 4 * j:4 * j + 4, :]
                dve.wait_ge(o_rstd, j + 1)
                dve.tensor_tensor(o, o, work[1][:, 4 * j:4 * j + 4, :], ALU.mult)
            dve.drain()
            for f in range(PAIRS):
                dve.tensor_scalar(o_rows[:, f, :], o_rows[:, f, :], m.v("rwkv_ln_w", f), m.v("rwkv_ln_b", f),
                                  ALU.mult, ALU.add)
            dve.drain()
            dve.tensor_tensor(o_rows, o_rows, bonus, ALU.add)
            dve.drain()
            dve.tensor_tensor(m.o_T[:, :, :], o_rows, by_chunk(gate[:, :, :]), ALU.mult)


def mix_part(nc, m, a):
    with ExitStack() as ctx:
        def sem(n):
            return ctx.enter_context(nc.semaphore(n))

        def sb(n, s):
            return ctx.enter_context(nc.sbuf_tensor(n, s, F32))
        def sb_r(n, s):
            return ctx.enter_context(nc.sbuf_tensor(n, s, F32R))
        m.w_slots[2] = sb("w3_slot2", [P, KC, 256])
        SPLITS = 3
        w_hi, w_lo = sb_r("w3_hi", [P, SPLITS, KC, 256]), sb_r("w3_lo", [P, SPLITS, KC, 256])
        h_hi, h_lo = sb_r("h3_hi", [P, KC, SEQ]), sb_r("h3_lo", [P, KC, SEQ])
        branch_hi, branch_lo = sb_r("branch_hi", [P, 6, SEQ]), sb_r("branch_lo", [P, 6, SEQ])
        mixed_hi, mixed_lo = sb_r("mixed_hi", [P, KC, SEQ]), sb_r("mixed_lo", [P, KC, SEQ])
        sig = sb("gate_sig", [P, 2, 2, SEQ])
        part = sb("gate_part", [P, 2, SEQ])
        mixed = sb("gate_mixed", [P, KC, SEQ])
        square = mixed
        log_ms = sb("mix_log", [P, SEQ])
        rstd = sb("mix_rstd", [P, SEQ])
        filled, drained = m.filled, m.drained
        gated, squared, rstd_done, h_done = sem("gated"), sem("m_squared"), sem("m_rstd"), sem("m_h")
        h_hi_done, h_lo_done, branch_hi_done, branch_lo_done, split_hi, split_lo = (
            sem("h3_hi_done"), sem("h3_lo_done"), sem("branch_hi_done"), sem("branch_lo_done"), sem("w3_hi_done"),
            sem("w3_lo_done"))
        U_OUT, U_SS, U_TOK = 16, 20, 21

        def unit_of(i):
            return U_OUT + i - 12 if i >= 12 else 4 * (i // 3) + (0, 1, 3)[i % 3]

        block = ctx.enter_context(nc.Block())

        @block.sync
        def _(sp):
            for i in range(2, MIX_PIECES):
                if i >= RING:
                    sp.wait_ge(split_lo, i - RING + 1)
                load_mix_piece(sp, m, a, i)
            for name, c0, c1 in (("group", 0, 4), ("expert", 4, 4 + N_EXP)):
                sp.dma_start(m.router_w[:, :, c0:c1], a[f"w_{name}_router"][0].rearrange("(c p) n -> p c n", p=P)
                             ).then_inc(m.router_in, 16)
                sp.dma_start(m.router_b[:, c0:c1], a[f"b_{name}_router"].to_broadcast([P, c1 - c0])
                             ).then_inc(m.router_in, 16)

        @block.gpsimd
        def _(pool):
            for i in range(MIX_PIECES):
                pool.wait_ge(split_hi, i + 1)
                n = 6 if i < 12 and i % 3 == 2 else KC
                pool.tensor_tensor(w_lo[:, i % SPLITS, 0:n, :], m.w_slots[i % RING][:, 0:n, :],
                                   w_hi[:, i % SPLITS, 0:n, :].bitcast(F32), ALU.subtract).then_inc(split_lo, 1)

        @block.tensor
        def _(pe):
            def free(q):
                if q >= BANKS:
                    pe.wait_ge(drained[q % BANKS], q // BANKS)
                return q % BANKS

            def product(q, i, x, chunks, k0=0, sync=None):
                b = free(q)
                for j in range(2):
                    for p, (w, y) in enumerate(((w_hi, x[0]), (w_hi, x[1]), (w_lo, x[0]))):
                        if j == 0:
                            pe.wait_ge(split_lo if p == 2 else split_hi, i + 1)
                        for k in range(chunks):
                            if j == 0 and sync:
                                sync(p, k)
                            mm = pe.matmul(m.ps[:, b, j * SEQ:(j + 1) * SEQ], w[:, i % SPLITS, k0 + k, j * P:(j + 1) * P],
                                           y[:, k0 + k, :],
                                           start=(p == 0 and k == 0), stop=(p == 2 and k == chunks - 1))
                mm.then_inc(filled[b], 1)

            for j in range(4):
                for k in range(2):
                    product(4 * j + k, 3 * j + k, (h_hi, h_lo), KC, sync=None if j or k else
                            lambda p, k: pe.wait_ge(h_lo_done if p == 1 else h_hi_done, 1))
                for k, (k0, n) in enumerate(((0, 2), (2, 4))):
                    product(4 * j + 2 + k, 3 * j + 2, (branch_hi, branch_lo), n, k0, sync=None if j or k else
                            lambda p, k: pe.wait_ge(branch_lo_done if p == 1 else branch_hi_done, 1))
            for j in range(4):
                product(U_OUT + j, 12 + j, (mixed_hi, mixed_lo), KC, sync=None if j else
                        lambda p, k: pe.wait_ge(gated, k // 2 + 1))
            b = free(U_SS)
            for c in range(KC):
                pe.wait_ge(squared, c // 2 + 1)
                mm = pe.matmul(m.ps[:, b, 0:SEQ], m.c("ones"), square[:, c, :], start=(c == 0), stop=(c == KC - 1))
            mm.then_inc(filled[b], 1)
            for n in range(4):
                t, c0 = n // 2, 4 * (n % 2)
                b = free(U_TOK + n)
                for c in range(c0, c0 + 4):
                    pe.wait_ge(h_done, KC)
                    mm = pe.transpose(m.ps[:, b, (c - c0) * P:(c - c0 + 1) * P], m.hT[:, c, t * P:(t + 1) * P], m.c("ident"))
                mm.then_inc(filled[b], 1)

        @block.scalar
        def _(act):
            def split(i):
                if i >= MIX_PIECES:
                    return
                if i >= SPLITS:
                    q = unit_of(i - SPLITS)
                    act.wait_ge(filled[q % BANKS], q // BANKS + 1)
                s = await_mix_piece(act, m, i)
                n = 6 if i < 12 and i % 3 == 2 else KC
                act.activation(w_hi[:, i % SPLITS, 0:n, :], m.w_slots[s][:, 0:n, :], ACT.Copy).then_inc(split_hi, 1)

            split(0)
            act.activation(h_hi[:, :, :], m.hT[:, :, :], ACT.Copy).then_inc(h_hi_done, 1)
            split(1)
            split(2)
            for j in range(4):
                for k in range(2):
                    q = 4 * j + k
                    act.wait_ge(filled[q % BANKS], q // BANKS + 1)
                    if j >= 1:
                        act.wait_ge(gated, j)
                    act.activation(sig[:, k, :, :], m.ps[:, q % BANKS, :].rearrange("p (c t) -> p c t", c=2), ACT.Sigmoid
                                   ).then_inc(drained[q % BANKS], 1)
                    split(3 * j + k + SPLITS)
                split(3 * j + 2 + SPLITS)
            split(12 + SPLITS)
            for j in range(4):
                q = U_OUT + j
                act.wait_ge(drained[q % BANKS], q // BANKS + 1)
                act.activation(square[:, 2 * j:2 * j + 2, :], m.xT[:, 2 * j:2 * j + 2, :], ACT.Square).then_inc(squared, 1)
            q = U_SS
            act.wait_ge(filled[q % BANKS], q // BANKS + 1)
            act.activation(log_ms[:, :], m.ps[:, q % BANKS, 0:SEQ], ACT.Ln, bias=m.c("eps"), scale=1.0 / D
                           ).then_inc(drained[q % BANKS], 1)
            act.drain()
            act.activation(rstd[:, :], log_ms[:, :], ACT.Exp, scale=-0.5).then_inc(rstd_done, 1)
            for n in range(4):
                q = U_TOK + n
                act.wait_ge(filled[q % BANKS], q // BANKS + 1)
                act.activation(m.h_tok[:, n // 2, (n % 2) * 512:(n % 2 + 1) * 512], m.ps[:, q % BANKS, :], ACT.Copy
                               ).then_inc(drained[q % BANKS], 1)

        @block.vector
        def _(dve):
            for x, c0, n in ((m.att_T, 0, 2), (m.o_T, 2, 4)):
                dve.tensor_copy(branch_hi[:, c0:c0 + n, :], x[:, :, :])
            dve.drain().then_inc(branch_hi_done, 1)
            dve.wait_ge(h_hi_done, 1)
            dve.tensor_tensor(h_lo[:, :, :], m.hT[:, :, :], h_hi[:, :, :].bitcast(F32), ALU.subtract).then_inc(h_lo_done, 1)
            for x, c0, n in ((m.att_T, 0, 2), (m.o_T, 2, 4)):
                dve.tensor_tensor(branch_lo[:, c0:c0 + n, :], x[:, :, :], branch_hi[:, c0:c0 + n, :].bitcast(F32), ALU.subtract)
            dve.drain().then_inc(branch_lo_done, 1)
            for j in range(4):
                for k, dst in enumerate((mixed[:, 2 * j:2 * j + 2, :], part[:, :, :])):
                    q, s = 4 * j + 2 + k, 4 * j + k
                    dve.wait_ge(filled[q % BANKS], q // BANKS + 1)
                    dve.wait_ge(drained[s % BANKS], s // BANKS + 1)
                    dve.tensor_tensor(dst, m.ps[:, q % BANKS, :].rearrange("p (c t) -> p c t", c=2), sig[:, k, :, :],
                                      ALU.mult).then_inc(drained[q % BANKS], 1)
                dve.drain()
                dve.tensor_tensor(mixed[:, 2 * j:2 * j + 2, :], mixed[:, 2 * j:2 * j + 2, :], part[:, :, :], ALU.add)
                dve.drain()
                pair = slice(2 * j, 2 * j + 2)
                dve.tensor_copy(mixed_hi[:, pair, :], mixed[:, pair, :])
                dve.drain()
                dve.tensor_tensor(mixed_lo[:, pair, :], mixed[:, pair, :], mixed_hi[:, pair, :].bitcast(F32), ALU.subtract
                                  ).then_inc(gated, 1)
            for j in range(4):
                q = U_OUT + j
                dve.wait_ge(filled[q % BANKS], q // BANKS + 1)
                x = m.xT[:, 2 * j:2 * j + 2, :]
                dve.tensor_tensor(x, m.ps[:, q % BANKS, :].rearrange("p (c t) -> p c t", c=2), x, ALU.add
                                  ).then_inc(drained[q % BANKS], 1)
            dve.wait_ge(rstd_done, 1)
            for c in range(KC):
                dve.scalar_tensor_tensor(m.hT[:, c, :], m.xT[:, c, :], m.v("norm2_gain", c), rstd[:, :],
                                         ALU.mult, ALU.mult).then_inc(h_done, 1)


def routing_part(nc, m, a):
    NL = 4 + N_EXP
    with ExitStack() as ctx:
        def sem(n):
            return ctx.enter_context(nc.semaphore(n))

        def sb(n, s):
            return ctx.enter_context(nc.sbuf_tensor(n, s, F32))
        router_w, router_b = m.router_w, m.router_b
        logits = sb("logits", [P, TT, NL])
        group_max = sb("group_max", [P, TT, 1])
        group_exp = sb("group_exp", [P, TT, 4])
        group_p = sb("group_p", [P, TT, 1])
        value = sb("pick_value", [P, TT, N_EXP])
        value_max = sb("pick_max", [P, TT, 1])
        group_hot = sb("group_hot", [P, TT, 4])
        masked = sb("masked", [P, TT, N_EXP])
        top = sb("top", [P, 2, TT, 1])
        ratio = sb("ratio", [P, TT, 1])
        ratio_inv = sb("ratio_inv", [P, TT, 1])
        hot = sb("hot", [P, 2, TT, N_EXP])
        assign = sb("assign", [P, TT, N_EXP])
        slot = sb("slot", [P, TT, N_EXP])
        past = sb("past", [P, TT, N_EXP])
        scratch = sb("route_scratch", [P, TT, N_EXP])
        blocks = sb("over_blocks", [P, N_EXP])
        blocks_col = sb("over_blocks_col", [N_EXP, 1])
        blocks_wide = sb("over_blocks_wide", [N_EXP, P])
        count_col = sb("count_col", [N_EXP, 1])
        ends = sb("ends", [P, N_EXP])
        before_end = sb("before_end", [P, OVER, N_EXP])
        over_f = sb("over_f", [P, OVER + 1])

        filled, drained = m.filled, m.drained
        router_in = m.router_in
        group_in, group_out, ratio_in, ratio_out, assigned, wide_done = (
            sem("group_in"), sem("group_out"), sem("ratio_in"), sem("ratio_out"),
            sem("assigned"), sem("blocks_wide"))
        U_LOG, U_RANK, U_START = 0, 1, 2

        block = ctx.enter_context(nc.Block())

        @block.sync
        def _(sp):
            m.load_pair(sp, 0)

        @block.scalar
        def _(act):
            act.wait_ge(group_in, 1)
            act.activation(group_exp[:, :, :], group_exp[:, :, :], ACT.Exp).then_inc(group_out, 1)
            act.wait_ge(ratio_in, 1)
            act.activation(ratio[:, :, :], ratio[:, :, :], ACT.Exp).then_inc(ratio_out, 1)

        @block.tensor
        def _(pe):
            pe.wait_ge(router_in, 64)
            for t in range(TT):
                for k in range(KC):
                    mm = pe.matmul(m.ps[:, U_LOG, t * NL:(t + 1) * NL], m.hT[:, k, t * P:(t + 1) * P], router_w[:, k, :],
                                   start=(k == 0), stop=(k == KC - 1))
            mm.then_inc(filled[U_LOG], 1)
            pe.wait_ge(assigned, 1)
            out = m.ps[:, U_RANK, :]
            pe.matmul(out[:, 0:32], m.c("before"), assign[:, 0, :], start=True, stop=True)
            pe.matmul(out[:, 32:64], m.c("before"), assign[:, 1, :], start=True, stop=False)
            pe.matmul(out[:, 32:64], m.c("ones"), assign[:, 0, :], start=False, stop=True)
            pe.matmul(out[:, 64:96], m.c("ones"), assign[:, 0, :], start=True, stop=False)
            pe.matmul(out[:, 64:96], m.c("ones"), assign[:, 1, :], start=False, stop=True)
            pe.matmul(out[0:32, 96:97], assign[:, 0, :], m.c("ones")[:, 0:1], start=True, stop=False)
            pe.matmul(out[0:32, 96:97], assign[:, 1, :], m.c("ones")[:, 0:1], start=False, stop=True
                      ).then_inc(filled[U_RANK], 1)
            pe.wait_ge(wide_done, 1)
            pe.matmul(m.ps[:, U_START, 0:N_EXP], blocks_wide[:, :], m.c("before")[0:N_EXP, 0:N_EXP], start=True, stop=True
                      ).then_inc(filled[U_START], 1)

        @block.vector
        def _(dve):
            def op(ins):
                dve.drain()
                return ins

            def wide(x, n):
                return x.to_broadcast([P, TT, n])

            def const_rows(name, n):
                return m.c(name)[:, 0:n].rearrange("p (o n) -> p o n", o=1).to_broadcast([P, TT, n])

            def first_of_largest(dst, src, largest, n):
                v = value[:, :, 0:n]
                op(dve.tensor_reduce(largest, src, AX, ALU.max))
                op(dve.tensor_tensor(v, src, wide(largest, n), ALU.is_equal))
                op(dve.tensor_tensor(v, v, const_rows("first_pick", n), ALU.mult))
                op(dve.tensor_reduce(value_max[:, :, :], v, AX, ALU.max))
                op(dve.tensor_tensor(dst, v, wide(value_max[:, :, :], n), ALU.is_equal))

            dve.wait_ge(router_in, 64)
            dve.wait_ge(filled[U_LOG], 1)
            op(dve.tensor_tensor(logits[:, :, :], m.ps[:, U_LOG, 0:TT * NL].rearrange("p (t n) -> p t n", t=TT),
                                 router_b[:, :].rearrange("p (o n) -> p o n", o=1).to_broadcast([P, TT, NL]), ALU.add
                                 ).then_inc(drained[U_LOG], 1))
            group = logits[:, :, 0:4]
            first_of_largest(group_hot[:, :, :], group, group_max[:, :, :], 4)
            op(dve.tensor_tensor(group_exp[:, :, :], group, wide(group_max[:, :, :], 4), ALU.subtract
                                 ).then_inc(group_in, 1))
            op(dve.tensor_scalar(scratch[:, :, 0:4], group_hot[:, :, :], -NEG, NEG, ALU.mult, ALU.add))
            for t in range(TT):
                dve.tensor_tensor(masked[:, t, :].rearrange("p (g e) -> p g e", g=4),
                                  logits[:, t, 4:NL].rearrange("p (g e) -> p g e", g=4),
                                  scratch[:, t, 0:4].rearrange("p (g o) -> p g o", o=1).to_broadcast([P, 4, 8]), ALU.add)
            dve.drain()
            first_of_largest(hot[:, 0, :, :], masked[:, :, :], top[:, 0, :, :], N_EXP)
            op(dve.scalar_tensor_tensor(masked[:, :, :], hot[:, 0, :, :], NEG, masked[:, :, :], ALU.mult, ALU.add))
            first_of_largest(hot[:, 1, :, :], masked[:, :, :], top[:, 1, :, :], N_EXP)
            op(dve.tensor_tensor(assign[:, :, :], hot[:, 0, :, :], hot[:, 1, :, :], ALU.add).then_inc(assigned, 1))
            op(dve.tensor_tensor(ratio[:, :, :], top[:, 1, :, :], top[:, 0, :, :], ALU.subtract).then_inc(ratio_in, 1))
            dve.wait_ge(group_out, 1)
            op(dve.tensor_reduce(group_p[:, :, :], group_exp[:, :, :], AX, ALU.add))
            op(dve.reciprocal(group_p[:, :, :], group_p[:, :, :]))
            dve.wait_ge(ratio_out, 1)
            op(dve.tensor_scalar(ratio_inv[:, :, :], ratio[:, :, :], 1.0, None, ALU.add))
            op(dve.reciprocal(ratio_inv[:, :, :], ratio_inv[:, :, :]))
            op(dve.tensor_tensor(m.gate[:, 0, :, :], group_p[:, :, :], ratio_inv[:, :, :], ALU.mult))
            op(dve.tensor_tensor(m.gate[:, 1, :, :], m.gate[:, 0, :, :], ratio[:, :, :], ALU.mult))
            op(dve.tensor_tensor(m.gates[:, :, :], hot[:, 0, :, :], wide(m.gate[:, 0, :, :], N_EXP), ALU.mult))
            op(dve.tensor_tensor(scratch[:, :, :], hot[:, 1, :, :], wide(m.gate[:, 1, :, :], N_EXP), ALU.mult))
            op(dve.tensor_tensor(m.gates[:, :, :], m.gates[:, :, :], scratch[:, :, :], ALU.add))
            dve.wait_ge(filled[U_RANK], 1)
            rank = m.ps[:, U_RANK, 0:64].rearrange("p (t e) -> p t e", t=TT)
            count = m.ps[:, U_RANK, 64:96]
            op(dve.scalar_tensor_tensor(slot[:, :, :], rank, 1.0, assign[:, :, :], ALU.add, ALU.mult))
            dve.tensor_scalar(past[:, :, :], slot[:, :, :], float(SLOTS), None, ALU.is_gt)
            dve.tensor_copy(count_col[:, :], m.ps[0:N_EXP, U_RANK, 96:97])
            dve.tensor_scalar(blocks[:, :], count, float(SLOTS), None, ALU.is_gt)
            dve.drain()
            dve.tensor_scalar(blocks_col[:, :], count_col[:, :], float(SLOTS), None, ALU.is_gt)
            dve.drain()
            for k in (2, 3):
                dve.scalar_tensor_tensor(blocks[:, :], count, float(k * SLOTS), blocks[:, :], ALU.is_gt, ALU.add)
                dve.scalar_tensor_tensor(blocks_col[:, :], count_col[:, :], float(k * SLOTS), blocks_col[:, :],
                                         ALU.is_gt, ALU.add)
                dve.drain()
            dve.drain().then_inc(drained[U_RANK], 1)
            dve.tensor_copy(blocks_wide[:, :], blocks_col[:, :].to_broadcast([N_EXP, P])).then_inc(wide_done, 1)
            op(dve.tensor_scalar(slot[:, :, :], slot[:, :, :], -1.0, None, ALU.add))
            pairs = [P, TT * N_EXP, SLOTS]
            iota = m.c("iota")[:, 0:SLOTS].rearrange("p (o n) -> p o n", o=1).to_broadcast(pairs)
            flat = "p t (e o) -> p (t e) o"
            op(dve.tensor_tensor(m.pick[:, :, :, :].rearrange("p t e n -> p (t e) n"), iota,
                                 slot[:, :, :].rearrange(flat, o=1).to_broadcast(pairs), ALU.is_equal))
            dve.wait_ge(filled[U_START], 1)
            start = m.ps[:, U_START, 0:N_EXP]
            op(dve.tensor_tensor(ends[:, :], start, blocks[:, :], ALU.add))
            for t in range(TT):
                dve.scalar_tensor_tensor(scratch[:, t, :], start, float(SLOTS), slot[:, t, :], ALU.mult, ALU.add)
            dve.drain().then_inc(drained[U_START], 1)
            op(dve.tensor_scalar(scratch[:, :, :], scratch[:, :, :], 1.0 - SLOTS, None, ALU.add))
            op(dve.tensor_tensor(scratch[:, :, :], scratch[:, :, :], past[:, :, :], ALU.mult))
            for k in range(2):
                op(dve.tensor_tensor(hot[:, k, :, :], hot[:, k, :, :], scratch[:, :, :], ALU.mult))
                op(dve.tensor_reduce(m.over_slot[:, k, :, :], hot[:, k, :, :], AX, ALU.add))
            op(dve.tensor_scalar(m.over_slot[:, :, :, :], m.over_slot[:, :, :, :], -1.0, None, ALU.add))
            op(dve.tensor_tensor(before_end[:, :, :],
                                 ends[:, :].rearrange("p (o n) -> p o n", o=1).to_broadcast([P, OVER, N_EXP]),
                                 m.c("iota")[:, 0:OVER].rearrange("p (j o) -> p j o", o=1).to_broadcast([P, OVER, N_EXP]),
                                 ALU.is_le))
            op(dve.tensor_reduce(over_f[:, 0:OVER], before_end[:, :, :], AX, ALU.add))
            op(dve.tensor_scalar(over_f[:, 0:OVER], over_f[:, 0:OVER], float(N_EXP - 1), None, ALU.min))
            op(dve.tensor_copy(over_f[:, OVER:OVER + 1], ends[:, N_EXP - 1:N_EXP]))
            op(dve.tensor_copy(m.over_int[:, :], over_f[:, :]))


def expert_part(nc, m, a):
    PAIRS = N_EXP // 2
    FC = D_EXP // P
    with ExitStack() as ctx:
        def sem(n):
            return ctx.enter_context(nc.semaphore(n))
        free = m.w_slots[1][:, :, :].rearrange("p c n -> p (c n)")
        x_pair = free[:, 0:D].rearrange("p (c n) -> p c n", c=KC)
        y_pair = free[:, D:2 * D]
        free = m.hT[:, :, :].rearrange("p c n -> p (c n)")
        silu = free[:, 0:D_EXP]
        hidden = free[:, D_EXP:2 * D_EXP]
        hidden_T = free[:, 2 * D_EXP:3 * D_EXP].rearrange("p (f n) -> p f n", f=FC)

        GATHER, GATE, UP, DOWN, SCATTER = 0, 2, 3, 4, 6

        def started(n):
            return not (isinstance(n, int) and n == 0)

        def gather(pe, filled, drained, i, n):
            for j in range(2):
                b = GATHER + j
                if started(n):
                    pe.wait_ge(drained[b], n)
                for c in range(4):
                    for t in range(TT):
                        mm = pe.matmul(m.ps[:, b, c * P:(c + 1) * P], m.h_tok[:, t, (4 * j + c) * P:(4 * j + c + 1) * P],
                                       m.pick[:, t, :, :].rearrange("p e n -> p (e n)")[:, bass.ts(i, 2 * SLOTS)],
                                       start=(t == 0), stop=(t == TT - 1))
                mm.then_inc(filled[b], 1)

        def gate_up(pe, filled, drained, landed, e, n):
            if e == 0:
                if started(n):
                    pe.wait_ge(drained[GATE], 2 * n)
                    pe.wait_ge(drained[UP], n)
                for j in range(2):
                    pe.wait_ge(drained[GATHER + j], n + 1)
            for b, w, name in ((GATE, m.gate_w, "gate"), (UP, m.up_w, "up")):
                pe.wait_ge(landed[name, e], 16 * n + 16)
                for c in range(KC):
                    mm = pe.matmul(m.ps[e * SLOTS:(e + 1) * SLOTS, b, :], x_pair[:, c, e * SLOTS:(e + 1) * SLOTS],
                                   w[:, e, c, :], start=(c == 0), stop=(c == KC - 1))
                mm.then_inc(filled[b], 1)

        def turn(pe, filled, drained, n):
            pe.wait_ge(drained[UP], n + 1)
            pe.wait_ge(drained[GATE], 2 * n + 1)
            for f in range(FC):
                mm = pe.transpose(m.ps[:, GATE, f * P:(f + 1) * P], hidden[:, f * P:(f + 1) * P], m.c("ident"))
            mm.then_inc(filled[GATE], 1)

        def down(pe, filled, drained, landed, e, n):
            if e == 0 and started(n):
                for j in range(2):
                    pe.wait_ge(drained[DOWN + j], n)
            pe.wait_ge(drained[GATE], 2 * n + 2)
            pe.wait_ge(landed["down", e], 16 * n + 16)
            for j in range(2):
                for f in range(FC):
                    mm = pe.matmul(m.ps[e * SLOTS:(e + 1) * SLOTS, DOWN + j, :], hidden_T[:, f, e * SLOTS:(e + 1) * SLOTS],
                                   m.down_w[:, e, f, j * 512:(j + 1) * 512], start=(f == 0), stop=(f == FC - 1))
                mm.then_inc(filled[DOWN + j], 1)

        def scatter(pe, filled, drained, i, n):
            for q in range(4):
                b = SCATTER + q % 2
                if started(n) or q >= 2:
                    pe.wait_ge(drained[b], 2 * n + q // 2)
                if q == 0:
                    for j in range(2):
                        pe.wait_ge(drained[DOWN + j], n + 1)
                for c in range(2):
                    d = 2 * q + c
                    mm = pe.matmul(m.ps[:, b, c * SEQ:(c + 1) * SEQ], y_pair[:, d * P:(d + 1) * P],
                                   m.gate_T[:, :, :].rearrange("p i t -> p (i t)")[:, bass.ts(i, SEQ)],
                                   start=True, stop=True)
                mm.then_inc(filled[b], 1)

        def act_pair(act, filled, drained, n):
            act.wait_ge(filled[GATE], 3 * n + 2)
            act.activation(silu[:, :], m.ps[:, GATE, :], ACT.Silu).then_inc(drained[GATE], 1)
            act.wait_ge(filled[GATE], 3 * n + 3)
            act.activation(hidden_T[:, :, :], m.ps[:, GATE, :].rearrange("p (f n) -> p f n", f=FC), ACT.Copy
                           ).then_inc(drained[GATE], 1)
            for j in range(2):
                act.wait_ge(filled[DOWN + j], 2 * n + 2)
                act.activation(y_pair[:, j * 512:(j + 1) * 512], m.ps[:, DOWN + j, :], ACT.Copy
                               ).then_inc(drained[DOWN + j], 1)

        def dve_gather(dve, filled, drained, n):
            for j in range(2):
                b = GATHER + j
                dve.wait_ge(filled[b], n + 1)
                dve.tensor_copy(x_pair[:, 4 * j:4 * j + 4, :], m.ps[:, b, :].rearrange("p (c n) -> p c n", c=4)
                                ).then_inc(drained[b], 1)

        def dve_hidden(dve, filled, drained, n):
            dve.wait_ge(drained[GATE], 2 * n + 1)
            dve.wait_ge(filled[UP], 2 * n + 2)
            dve.tensor_tensor(hidden[:, :], m.ps[:, UP, :], silu[:, :], ALU.mult).then_inc(drained[UP], 1)

        def dve_scatter(dve, filled, drained, n):
            for q in range(4):
                b = SCATTER + q % 2
                dve.wait_ge(filled[b], 2 * n + q // 2 + 1)
                x = m.xT[:, 2 * q:2 * q + 2, :]
                dve.tensor_tensor(x, m.ps[:, b, :].rearrange("p (c t) -> p c t", c=2), x, ALU.add
                                  ).then_inc(drained[b], 1)
            dve.drain()

        filled, drained = m.filled, m.drained
        weights_done, gates_turned, gates_copied = sem("weights_done"), sem("gates_turned"), sem("gates_copied")
        with nc.Block() as block:
            @block.gpsimd
            def _(pool):
                shape = [P, TT * N_EXP, SLOTS]
                pool.tensor_tensor(m.weighted[:, :, :, :].rearrange("p t e n -> p (t e) n"),
                                   m.pick[:, :, :, :].rearrange("p t e n -> p (t e) n"),
                                   m.gates[:, :, :].rearrange("p t (e o) -> p (t e) o", o=1).to_broadcast(shape),
                                   ALU.mult).then_inc(weights_done, 1)

            @block.sync
            def _(sp):
                with sp.Fori(1, PAIRS) as i:
                    for e in range(2):
                        sp.wait_ge(filled[GATE], 3 * i - 2 + e)
                        m.load_gate_up(sp, e, 2 * i + e, names=("gate",))
                        sp.wait_ge(filled[UP], 2 * i - 1 + e)
                        m.load_gate_up(sp, e, 2 * i + e, names=("up",))
                    for e in range(2):
                        sp.wait_ge(filled[DOWN + 1], 2 * i - 1 + e)
                        m.load_down(sp, e, 2 * i + e)

            @block.tensor
            def _(pe):
                gather(pe, filled, drained, 0, 0)

                def turn_gates():
                    pe.wait_ge(weights_done, 1)
                    for n in range(8):
                        if n >= 2:
                            pe.wait_ge(gates_copied, n - 1)
                        for i in range(2):
                            for t in range(TT):
                                at = i * SEQ + t * P
                                pair = 2 * (2 * n + i)
                                mm = pe.transpose(m.ps[:, SCATTER + n % 2, at:at + P],
                                                  m.weighted[:, t, pair:pair + 2, :], m.c("ident"))
                        mm.then_inc(gates_turned, 1)
                    pe.wait_ge(gates_copied, 8)

                def pair(i, first=False, last=False):
                    for e in range(2):
                        gate_up(pe, filled, drained, m.landed, e, i)
                    if not first:
                        scatter(pe, filled, drained, i - 1, i - 1)
                    turn(pe, filled, drained, i)
                    if not last:
                        gather(pe, filled, drained, i + 1, i + 1)
                    for e in range(2):
                        down(pe, filled, drained, m.landed, e, i)
                pair(0, first=True)
                turn_gates()
                with pe.Fori(1, PAIRS - 1) as i:
                    pair(i)
                pair(PAIRS - 1, last=True)
                scatter(pe, filled, drained, PAIRS - 1, PAIRS - 1)

            @block.scalar
            def _(act):
                act_pair(act, filled, drained, 0)
                for n in range(8):
                    act.wait_ge(gates_turned, n + 1)
                    act.activation(m.gate_T[:, 2 * n:2 * n + 2, :],
                                   m.ps[:, SCATTER + n % 2, :].rearrange("p (i t) -> p i t", i=2), ACT.Copy
                                   ).then_inc(gates_copied, 1)
                with act.Fori(1, PAIRS) as i:
                    act_pair(act, filled, drained, i)

            @block.vector
            def _(dve):
                dve_gather(dve, filled, drained, 0)

                def pair(i, first=False, last=False):
                    dve_hidden(dve, filled, drained, i)
                    if not first:
                        dve_scatter(dve, filled, drained, i - 1)
                    if not last:
                        dve_gather(dve, filled, drained, i + 1)
                pair(0, first=True)
                with dve.Fori(1, PAIRS - 1) as i:
                    pair(i)
                pair(PAIRS - 1, last=True)
                dve_scatter(dve, filled, drained, PAIRS - 1)

        m.clear_banks()
        over_filled, over_drained = filled, drained
        over_pick = sem("over_pick")
        over_landed = {(n, e): sem(f"over_{n}{e}") for n in ("gate", "up", "down") for e in range(2)}
        equal = m.o_T[:, :, :].rearrange("p c n -> p (c n)").rearrange("p (k n) -> p k n", k=2)
        over_weighted = m.weighted[:, :, 0:OVER, :].rearrange("p t e n -> p t (e n)")
        turn_filled, turn_drained = sem("turn_filled"), sem("turn_drained")
        with nc.Block() as block:
            def blocks(eng):
                return eng.value_load(m.over_int[0:1, OVER:OVER + 1], min_val=0, max_val=OVER)

            @block.sync
            def _(sp):
                with sp.If(blocks(sp) > 0):
                    for i in range(OVER // 2):
                        for e in range(2):
                            j = 2 * i + e
                            expert = sp.value_load(m.over_int[0:1, j:j + 1], min_val=0, max_val=N_EXP - 1)
                            if i > 0:
                                sp.wait_ge(over_filled[UP], 2 * i - 1 + e)
                            m.load_gate_up(sp, e, expert, over_landed)
                            if i > 0:
                                sp.wait_ge(over_filled[DOWN + 1], 2 * i - 1 + e)
                            m.load_down(sp, e, expert, over_landed)

            @block.tensor
            def _(pe):
                with pe.If(blocks(pe) > 0):
                    pe.wait_ge(over_pick, 1)
                    for i in range(OVER // 2):
                        if i >= 2:
                            pe.wait_ge(turn_drained, i - 1)
                        for t in range(TT):
                            mm = pe.transpose(m.ps[:, GATE + i % 2, t * P:(t + 1) * P],
                                              over_weighted[:, t, i * P:(i + 1) * P], m.c("ident"))
                        mm.then_inc(turn_filled, 1)
                    pe.wait_ge(turn_drained, OVER // 2)

                    def pair(i):
                        gather(pe, over_filled, over_drained, i, i)
                        for e in range(2):
                            gate_up(pe, over_filled, over_drained, over_landed, e, i)
                        turn(pe, over_filled, over_drained, i)
                        for e in range(2):
                            down(pe, over_filled, over_drained, over_landed, e, i)
                        scatter(pe, over_filled, over_drained, i, i)
                    pair(0)
                    with pe.Fori(1, OVER // 2) as i:
                        pair(i)

            @block.scalar
            def _(act):
                with act.If(blocks(act) > 0):
                    for i in range(OVER // 2):
                        act.wait_ge(turn_filled, i + 1)
                        act.activation(m.gate_T[:, i, :], m.ps[:, GATE + i % 2, 0:SEQ], ACT.Copy
                                       ).then_inc(turn_drained, 1)
                    with act.Fori(0, OVER // 2) as i:
                        act_pair(act, over_filled, over_drained, i)

            @block.vector
            def _(dve):
                with dve.If(blocks(dve) > 0):
                    n = OVER * SLOTS
                    for t in range(TT):
                        for k in range(2):
                            dve.tensor_scalar(equal[:, k, :], m.c("iota"), m.over_slot[:, k, t, :], None, ALU.is_equal)
                        dve.drain()
                        dve.tensor_tensor(m.pick[:, t, 0:OVER, :].rearrange("p e n -> p (e n)"), equal[:, 0, :],
                                          equal[:, 1, :], ALU.add)
                        dve.tensor_scalar(over_weighted[:, t, :], equal[:, 0, :], m.gate[:, 0, t, :], None, ALU.mult)
                        dve.drain()
                        dve.scalar_tensor_tensor(over_weighted[:, t, :], equal[:, 1, :], m.gate[:, 1, t, :],
                                                 over_weighted[:, t, :], ALU.mult, ALU.add)
                        dve.drain()
                    dve.drain().then_inc(over_pick, 1)
                    with dve.Fori(0, OVER // 2) as i:
                        dve_gather(dve, over_filled, over_drained, i)
                        dve_hidden(dve, over_filled, over_drained, i)
                        dve_scatter(dve, over_filled, over_drained, i)


def expert_loads(nc, m, a):
    def load_gate_up(sp, e, expert, landed=None, names=("gate", "up")):
        landed = landed or m.landed
        for name in names:
            w = m.gate_w if name == "gate" else m.up_w
            src = a[f"w_expert_{name}"][0].rearrange("e (c p) n -> e p c n", p=P)
            sp.dma_start(w[:, e, :, :], src[bass.ds(expert, 1), :, :, :].rearrange("o p c n -> (o p) c n")
                         ).then_inc(landed[name, e], 16)

    def load_down(sp, e, expert, landed=None):
        landed = landed or m.landed
        src = a["w_expert_down"][0].rearrange("e (c p) n -> e p c n", p=P)
        sp.dma_start(m.down_w[:, e, :, :], src[bass.ds(expert, 1), :, :, :].rearrange("o p c n -> (o p) c n")
                     ).then_inc(landed["down", e], 16)

    def load_pair(sp, i):
        for e in range(2):
            load_gate_up(sp, e, 2 * i + e)
        for e in range(2):
            load_down(sp, e, 2 * i + e)
    m.load_gate_up, m.load_down, m.load_pair = load_gate_up, load_down, load_pair


SLICES = ("sb_q", "sb_k", "sb_v", "conf_a", "conf_gate", "sc_c", "sc_h", "ret_q", "ret_k", "ret_v", "sc_b", "ret_g")
SLICE_COL = {"conf_a": 0, "conf_gate": 1, "sb_q": 2, "sb_k": 3, "sb_v": 4, "ret_q": 5, "ret_k": 6, "ret_v": 7,
             "ret_g": 8, "sc_b": 9, "sc_c": 10, "sc_h": 11}


def _units():
    at, n = {}, 0
    for name, count in (("vec", 1), ("ss_mix", 1), ("sb_q", 1), ("sb_k", 1), ("sb_v", 1), ("conf_a", 1),
                        ("sb_score", 4), ("conf_gate", 1), ("sc_c", 1), ("sc_h", 1), ("tail", 4), ("ret_q", 1),
                        ("ret_k", 1), ("sb_out", 2), ("ret_v", 1), ("swap", 2), ("sc_b", 1), ("conf_mean", 1),
                        ("ret_g", 1), ("ret_score", 4), ("conf_var", 1), ("ret_out", 2), ("ret_mean", 1),
                        ("ret_var", 1), ("out", 4), ("ss_post", 1), ("ss_ffn", 1), ("up", 22), ("down", 8),
                        ("ss_ffn_post", 1)):
        at[name] = n
        n += count
    return at, n


UNIT, UNITS2 = _units()
FF = DFF // P
DOWN_ROWS = (8, 8, 6)
PIECE_OUT, PIECE_UP, PIECE_DOWN = 12, 16, 16 + FF
PIECES = PIECE_DOWN + 4 * len(DOWN_ROWS)
SLOTS2 = 3
TAPS = 31


def layers_part(nc, m, a):
    with ExitStack() as ctx:
        def sem(n):
            return ctx.enter_context(nc.semaphore(n))

        def sb(n, s):
            return ctx.enter_context(nc.sbuf_tensor(n, s, F32))

        def sb_r(n, s):
            return ctx.enter_context(nc.sbuf_tensor(n, s, F32R))
        ring = sb("ring2", [P, SLOTS2, KC * 256])
        w_hi = sb_r("w_hi", [P, SLOTS2, KC * 256])
        w_lo = sb_r("w_lo", [P, SLOTS2, KC * 256])
        x_hi = sb_r("x_hi", [P, KC, SEQ])
        x_lo = sb_r("x_lo", [P, KC, SEQ])
        rows1 = sb("rows1", [P, P])
        rows2 = sb("rows2", [FF * 2, 3, P])
        vec = sb("vec2", [P, P])
        ff_taps = sb("ff_taps", [P, 3, 2 * FF])
        square = sb("square2", [P, KC, SEQ])
        rstd = sb("rstd2", [P, SEQ])
        padded = sb("conf_pad", [P, 2, SEQ + TAPS - 1])
        conf = sb("conf_acc", [P, 2, SEQ])
        conf_sq = sb("conf_sq", [P, 2, SEQ])
        conf_rs = sb("conf_rs", [P, SEQ])
        sc_pad = sb("sc_pad", [P, 2, SEQ + 2])
        W3 = 3 * P
        turned = sb("ret_turned", [P, 2, 2, SEQ])
        ret_rs = sb("ret_rs", [P, 2, SEQ])
        y = sb("y_mix", [P, KC, SEQ])
        branch = y
        ff = sb("ff", [P, 2, 2, SEQ])
        silu = sb("silu2", [P, 2, SEQ])
        turn_tmp = silu
        ret_o, ret_sq = ff[:, 0, :, :], ff[:, 1, :, :]
        with ExitStack() as mixers:
            slices = mixers.enter_context(nc.sbuf_tensor("slices", [P, 12, 2, SEQ], F32))
            sb_z, sb_l, sb_pos, ret_p = (mixers.enter_context(nc.sbuf_tensor(n, [P, 4, W3], F32))
                                         for n in ("sb_z", "sb_l", "sb_pos", "ret_p"))
        s_ = {n: slices[:, i, :, :] for i, n in enumerate(SLICES)}
        hid_hi = sb_r("hid_hi", [P, FF, SEQ])
        hid_lo = sb_r("hid_lo", [P, FF, SEQ])

        landed = [sem(f"landed2_{i}") for i in range(SLOTS2)]
        filled, drained = m.filled, m.drained
        total = {"rows_in": 16 * 13, "squared": 16, "h_done": 16, "h_hi": 16, "h_lo": 16, "w_hi": PIECES,
                 "w_lo": PIECES, "down_used": 8, "y_split": 4, "conf_done": 1, "conf_centred": 1,
                 "conf_squared": 1, "conf_out": 1, "turned": 2, "soft_in": 4,
                 "soft_ln": 4, "sb_masked": 4, "sb_arg": 4, "sb_exp": 4, "ret_masked": 4, "ret_centred": 1,
                 "ret_squared": 1, "tap_scaled": FF, "conv_done": FF, "silu_done": FF,
                 "hid_done": FF, "conf_normed": 1, "x_done": 8, "root": 6}
        S = {n: sem(n) for n in total}

        def turns(b):
            return (UNITS2 - b + BANKS - 1) // BANKS

        def upto(l, n):
            return l * turns(n % BANKS) + n // BANKS + 2

        def before(l, n):
            return l * turns(n % BANKS) + n // BANKS + 1

        def await_filled(eng, l, n):
            eng.wait_ge(filled[n % BANKS], upto(l, n))
            return n % BANKS

        def await_drained(eng, l, n):
            eng.wait_ge(drained[n % BANKS], upto(l, n))

        def signalled(eng, l, name, k):
            eng.wait_ge(S[name], l * total[name] + k)

        def v(name, i):
            return vec[:, VEC2[name] + i:VEC2[name] + i + 1]

        def two(x):
            return x.rearrange("p (c t) -> p c t", c=2)

        def slot_uses(s):
            return (PIECES - s + SLOTS2 - 1) // SLOTS2

        def await_landed(eng, l, i):
            s = i % SLOTS2
            eng.wait_ge(landed[s], (l * slot_uses(s) + i // SLOTS2 + 1) * 16)
            return s

        with nc.Block() as block:
            @block.gpsimd
            def _(pool):
                pool.memset(padded[:, :, 0:TAPS - 1], 0.0)
                pool.memset(sc_pad[:, :, 0:2], 0.0)
                pool.memset(rows1[:, :], 0.0)
                for b in range(BANKS):
                    pool.sem_inc(filled[b], 1)
                    pool.sem_inc(drained[b], 1)

        def load_piece(sp, l, i):
            s = i % SLOTS2

            def of_layer(name):
                return a[name][bass.ds(l, 1)].rearrange("o (c p) n -> (o p) c n", p=P)
            dst = ring[:, s, :].rearrange("p (c n) -> p c n", c=KC)
            if i < PIECE_UP:
                name, c = ("w_in_2", SLICE_COL[SLICES[i]]) if i < PIECE_OUT else ("w_out_2", i - PIECE_OUT)
                src = of_layer(name)[:, :, c * 256:(c + 1) * 256]
            elif i < PIECE_DOWN:
                dst = ring[:, s, :].rearrange("p (h c n) -> p h c n", h=2, c=KC)
                src = a["ffn_up_2"][bass.ds(l, 1)].rearrange("o (c p) (h j n) -> (o p) h c j n", p=P, h=2, n=P
                                                             )[:, :, :, i - PIECE_UP, :]
            else:
                c, r = divmod(i - PIECE_DOWN, len(DOWN_ROWS))
                n = DOWN_ROWS[r]
                dst = dst[:, 0:n, :]
                src = of_layer("ffn_down_2")[:, KC * r:KC * r + n, c * 256:(c + 1) * 256]
            sp.dma_start(dst, src).then_inc(landed[s], 16)

        def load_rows(sp, l):
            n = 0
            for name in ("norm_mix_pre_2", "norm_mix_post_2", "norm_ffn_pre_2", "norm_ffn_post_2", "conf_dw_b_2",
                         "conf_ln_g_2", "conf_ln_b_2", "ret_norm_g_2"):
                src = a[name][l:l + 1, :].rearrange("o (c p) -> (o c) p", p=P)
                sp.dma_start(rows1[VEC2[name]:VEC2[name] + src.shape[0], :], src).then_inc(S["rows_in"], 16)
                n += 1
            for name in ("sc_conv_w_2", "conf_dw_w_2"):
                src = a[name][l].rearrange("k (c p) -> (k c) p", p=P)
                sp.dma_start(rows1[VEC2[name]:VEC2[name] + src.shape[0], :], src).then_inc(S["rows_in"], 16)
                n += 1
            for k in range(3):
                sp.dma_start(rows2[:, k, :], a["ffn_conv_w_2"][l, k, :].rearrange("(c p) -> c p", p=P)
                               ).then_inc(S["rows_in"], 16)
                n += 1
            assert 16 * n == total["rows_in"]

        block = ctx.enter_context(nc.Block())

        @block.sync
        def _(sp):
            load_piece(sp, 0, 0)
            load_rows(sp, 0)
            for i in range(1, SLOTS2):
                load_piece(sp, 0, i)
            with sp.Fori(0, 2) as l:
                for i in range(SLOTS2, PIECES):
                    signalled(sp, l, "w_lo", i - SLOTS2 + 1)
                    load_piece(sp, l, i)
                with sp.If(l < 1):
                    n = UNIT["vec"]
                    sp.wait_ge(filled[n % BANKS], upto(0, n))
                    load_rows(sp, 1)
                    for i in range(SLOTS2):
                        last = max(j for j in range(PIECES) if j % SLOTS2 == i)
                        signalled(sp, 0, "w_lo", last + 1)
                        load_piece(sp, 1, i)

        @block.gpsimd
        def _(pool):
            with pool.Fori(0, 2) as l:
                for i in range(PIECES):
                    signalled(pool, l, "w_hi", i + 1)
                    s = i % SLOTS2
                    pool.tensor_tensor(w_lo[:, s, :], ring[:, s, :], w_hi[:, s, :].bitcast(F32), ALU.subtract
                                       ).then_inc(S["w_lo"], 1)

        @block.tensor
        def _(pe):
            with pe.Fori(0, 2) as l:
                def free(n):
                    pe.wait_ge(drained[n % BANKS], before(l, n))
                    return n % BANKS

                def ss(unit, first):
                    b = free(UNIT[unit])
                    for c in range(KC):
                        signalled(pe, l, "squared", first + c // 2 + 1)
                        mm = pe.matmul(m.ps[:, b, 0:SEQ], m.c("ones"), square[:, c, :], start=(c == 0), stop=(c == KC - 1))
                    mm.then_inc(filled[b], 1)

                def masked_scores(unit, k_src, q_src):
                    for h in range(4):
                        b = free(UNIT[unit] + h)
                        r, c = slice((h % 2) * HEAD, (h % 2 + 1) * HEAD), h // 2
                        pe.matmul(m.ps[:, b, 0:SEQ], k_src[r, c, 0:P], q_src[r, c, :], start=True, stop=True)
                        pe.matmul(m.ps[:, b, SEQ:W3], k_src[r, c, P:SEQ], q_src[r, c, P:SEQ], start=True, stop=True
                                  ).then_inc(filled[b], 1)

                def outputs(unit, values, probs, ready):
                    for c in range(2):
                        b = free(UNIT[unit] + c)
                        for h in (2 * c, 2 * c + 1):
                            signalled(pe, l, ready, h + 1)
                            out = m.ps[(h % 2) * HEAD:(h % 2 + 1) * HEAD, b, :]
                            cols = slice(h * HEAD, (h + 1) * HEAD)
                            pe.matmul(out[:, 0:SEQ], values[:, 0, cols], probs[:, h, 0:SEQ], start=True, stop=False)
                            mm = pe.matmul(out[:, P:SEQ], values[:, 1, cols], probs[:, h, SEQ:W3], start=False, stop=True)
                        mm.then_inc(filled[b], 1)

                def split_product(i, groups, sync=None):
                    for g, (out, parts) in enumerate(groups):
                        for part, steps in enumerate(parts):
                            if g == 0:
                                signalled(pe, l, "w_lo" if part == 2 else "w_hi", i + 1)
                            for n, (lhs, rhs) in enumerate(steps):
                                if g == 0 and sync:
                                    sync(part, n)
                                mm = pe.matmul(out, lhs, rhs, start=(part == 0 and n == 0),
                                               stop=(part == 2 and n == len(steps) - 1))
                    return mm

                def parts_of(i, at, hi, lo, order=range(KC)):
                    w = [t[:, i % SLOTS2, :] for t in (w_hi, w_lo)]
                    return [[(w[a_][:, at(k):at(k) + P], x[:, k, :]) for k in order]
                            for a_, x in ((0, hi), (0, lo), (1, hi))]

                def product(unit, i, at, order=range(KC), sync=None):
                    b = free(unit)
                    split_product(i, [(m.ps[:, b, j * SEQ:(j + 1) * SEQ],
                                       parts_of(i, lambda k, j=j: at(k, j), x_hi, x_lo, order)) for j in range(2)], sync
                                  ).then_inc(filled[b], 1)

                def column(k, j):
                    return k * 256 + j * P

                b = free(UNIT["vec"])
                pe.wait_ge(S["rows_in"], l * total["rows_in"] + total["rows_in"])
                pe.transpose(m.ps[:, b, 0:P], rows1[:, :], m.c("ident"))
                for k in range(3):
                    mm = pe.transpose(m.ps[:, b, P + 2 * FF * k:P + 2 * FF * (k + 1)], rows2[:, k, :],
                                      m.c("ident")[0:2 * FF, 0:2 * FF])
                mm.then_inc(filled[b], 1)
                ss("ss_mix", 0)
                def h_ready(first):
                    return lambda part, n: signalled(pe, l, "h_lo" if part == 1 else "h_hi", first + n + 1)

                def project(*names):
                    for name in names:
                        i = SLICES.index(name)
                        if name in ("sb_v", "ret_v"):
                            b = free(UNIT[name])
                            w = [t[:, i % SLOTS2, :] for t in (w_hi, w_lo)]
                            split_product(i, [(m.ps[:, b, t * 256:(t + 1) * 256],
                                               [[(x[:, k, t * P:(t + 1) * P], w[a_][:, k * 256:(k + 1) * 256])
                                                 for k in range(KC)] for a_, x in ((0, x_hi), (0, x_lo), (1, x_hi))])
                                              for t in range(TT)]).then_inc(filled[b], 1)
                        else:
                            product(UNIT[name], i, column, sync=h_ready(0) if i == 0 else None)

                project("sb_q", "sb_k", "sb_v", "conf_a")
                for name in ("sb_q", "sb_k"):
                    await_drained(pe, l, UNIT[name])
                masked_scores("sb_score", s_["sb_k"], s_["sb_q"])
                project("conf_gate", "sc_c", "sc_h")
                for h in range(4):
                    signalled(pe, l, "sb_masked", h + 1)
                    b = free(UNIT["tail"] + h)
                    pe.matmul(m.ps[:, b, 0:SEQ], m.c("down"), sb_l[:, h, 0:SEQ], start=True, stop=False)
                    pe.matmul(m.ps[:, b, P:SEQ], m.c("ones"), sb_l[:, h, SEQ:W3], start=False, stop=True)
                    pe.matmul(m.ps[:, b, SEQ:W3], m.c("down"), sb_l[:, h, SEQ:W3], start=True, stop=True
                              ).then_inc(filled[b], 1)
                project("ret_q", "ret_k")
                await_drained(pe, l, UNIT["sb_v"])
                outputs("sb_out", s_["sb_v"], sb_z, "sb_exp")
                project("ret_v")
                for i, name in enumerate(("ret_q", "ret_k")):
                    await_drained(pe, l, UNIT[name])
                    b = free(UNIT["swap"] + i)
                    pe.matmul(m.ps[:, b, :], m.c("swap"), s_[name], start=True, stop=True).then_inc(filled[b], 1)
                project("sc_b")
                signalled(pe, l, "conf_done", 1)
                b = free(UNIT["conf_mean"])
                for c in range(2):
                    mm = pe.matmul(m.ps[:, b, 0:SEQ], m.c("ones"), conf[:, c, :], start=(c == 0), stop=(c == 1))
                mm.then_inc(filled[b], 1)
                project("ret_g")
                signalled(pe, l, "turned", 2)
                masked_scores("ret_score", turned[:, 1, :, :], turned[:, 0, :, :])
                signalled(pe, l, "conf_squared", 1)
                b = free(UNIT["conf_var"])
                for c in range(2):
                    mm = pe.matmul(m.ps[:, b, 0:SEQ], m.c("ones"), conf_sq[:, c, :], start=(c == 0), stop=(c == 1))
                mm.then_inc(filled[b], 1)
                await_drained(pe, l, UNIT["ret_v"])
                outputs("ret_out", s_["ret_v"], ret_p, "ret_masked")
                for c in range(2):
                    await_drained(pe, l, UNIT["ret_out"] + c)
                b = free(UNIT["ret_mean"])
                pe.matmul(m.ps[:, b, :], m.c("pair_ones"), ret_o[:, :, :], start=True, stop=True).then_inc(filled[b], 1)
                signalled(pe, l, "ret_squared", 1)
                b = free(UNIT["ret_var"])
                pe.matmul(m.ps[:, b, :], m.c("pair_ones"), ret_sq[:, :, :], start=True, stop=True).then_inc(filled[b], 1)
                for i in range(4):
                    product(UNIT["out"] + i, PIECE_OUT + i, column, order=(6, 7, 2, 3, 0, 1, 4, 5),
                            sync=(lambda part, n: signalled(pe, l, "y_split", n // 2 + 1)) if i == 0 else None)
                ss("ss_post", 4)
                ss("ss_ffn", 8)
                for i in range(FF):
                    product(UNIT["up"] + i, PIECE_UP + i, lambda k, j: (j * KC + k) * P,
                            sync=h_ready(KC) if i == 0 else None)
                for c in range(4):
                    banks = [free(UNIT["down"] + 2 * c + j) for j in range(2)]
                    for r, n in enumerate(DOWN_ROWS):
                        i = PIECE_DOWN + len(DOWN_ROWS) * c + r
                        w = [t[:, i % SLOTS2, :] for t in (w_hi, w_lo)]
                        for j in range(2):
                            for part, (a_, x) in enumerate(((0, hid_hi), (0, hid_lo), (1, hid_hi))):
                                if j == 0:
                                    signalled(pe, l, "w_lo" if part == 2 else "w_hi", i + 1)
                                for k in range(n):
                                    if c == 0 and j == 0:
                                        signalled(pe, l, "hid_done", KC * r + k + 1)
                                    mm = pe.matmul(m.ps[:, banks[j], 0:SEQ], w[a_][:, column(k, j):column(k, j) + P],
                                                   x[:, KC * r + k, :], start=(r == 0 and part == 0 and k == 0),
                                                   stop=(r == len(DOWN_ROWS) - 1 and part == 2 and k == n - 1))
                            if r == len(DOWN_ROWS) - 1:
                                mm.then_inc(filled[banks[j]], 1)
                        if r < len(DOWN_ROWS) - 1:
                            mm.then_inc(S["down_used"], 1)
                ss("ss_ffn_post", 12)

        @block.scalar
        def _(act):
            with act.Fori(0, 2) as l:
                def root(dst, unit, n):
                    b = await_filled(act, l, UNIT[unit])
                    act.activation(dst, m.ps[:, b, 0:SEQ], ACT.Sqrt, bias=m.c("eps"), scale=1.0 / n).then_inc(drained[b], 1)
                    act.drain().then_inc(S["root"], 1)

                def square_pair(src, j):
                    act.activation(square[:, 2 * j:2 * j + 2, :], src[:, 2 * j:2 * j + 2, :], ACT.Square
                                   ).then_inc(S["squared"], 1)

                def squares(src, when):
                    for j in range(4):
                        when(j)
                        square_pair(src, j)

                def copy(dst, n, func=ACT.Copy):
                    b = await_filled(act, l, n)
                    act.activation(dst, two(m.ps[:, b, :]), func).then_inc(drained[b], 1)

                def split_piece(i):
                    if i < PIECES:
                        s = await_landed(act, l, i)
                        act.activation(w_hi[:, s, :], ring[:, s, :], ACT.Copy).then_inc(S["w_hi"], 1)

                def split_h(first):
                    for c in range(KC):
                        signalled(act, l, "h_done", first + c + 1)
                        act.activation(x_hi[:, c, :], square[:, c, :], ACT.Copy).then_inc(S["h_hi"], 1)

                split_piece(0)
                split_piece(1)
                squares(m.xT, lambda j: signalled(act, l, "x_done", j + 1))
                split_piece(2)
                root(rstd[:, :], "ss_mix", D)
                split_h(0)

                def project(*names):
                    for name in names:
                        copy(s_[name], UNIT[name], {"conf_gate": ACT.Sigmoid, "ret_g": ACT.Silu}.get(name, ACT.Copy))
                        split_piece(SLICES.index(name) + SLOTS2)

                project("sb_q", "sb_k", "sb_v", "conf_a")
                for h in range(4):
                    signalled(act, l, "soft_in", h + 1)
                    act.activation(sb_l[:, h, :], sb_l[:, h, :], ACT.Exp, scale=-1.0)
                project("conf_gate")
                act.drain()
                for h in range(4):
                    act.activation(sb_l[:, h, :], sb_l[:, h, :], ACT.Ln, bias=1.0).then_inc(S["soft_ln"], 1)
                project("sc_c", "sc_h", "ret_q")
                for h in range(4):
                    signalled(act, l, "sb_arg", h + 1)
                    act.activation(sb_z[:, h, :], sb_z[:, h, :], ACT.Exp).then_inc(S["sb_exp"], 1)
                project("ret_k")
                for c in range(2):
                    b = await_filled(act, l, UNIT["sb_out"] + c)
                    act.activation(y[:, 2 + c, :], m.ps[:, b, 0:SEQ], ACT.Copy).then_inc(drained[b], 1)
                project("ret_v", "sc_b")
                signalled(act, l, "conf_centred", 1)
                act.activation(conf_sq[:, :, :], conf[:, :, :], ACT.Square).then_inc(S["conf_squared"], 1)
                project("ret_g")
                root(conf_rs[:, :], "conf_var", 256)
                for c in range(2):
                    b = await_filled(act, l, UNIT["ret_out"] + c)
                    act.activation(ret_o[:, c, :], m.ps[:, b, 0:SEQ], ACT.Copy).then_inc(drained[b], 1)
                signalled(act, l, "conf_normed", 1)
                for c in range(2):
                    ins = act.activation(y[:, c, :], conf[:, c, :], ACT.Silu, bias=v("conf_ln_b_2", c),
                                         scale=v("conf_ln_g_2", c))
                ins.then_inc(S["conf_out"], 1)
                signalled(act, l, "ret_centred", 1)
                act.activation(ret_sq[:, :, :], ret_o[:, :, :], ACT.Square).then_inc(S["ret_squared"], 1)
                b = await_filled(act, l, UNIT["ret_var"])
                act.activation(ret_rs[:, :, :], two(m.ps[:, b, :]), ACT.Ln, bias=m.c("eps"), scale=1.0 / HEAD
                               ).then_inc(drained[b], 1)
                act.drain()
                act.activation(ret_rs[:, :, :], ret_rs[:, :, :], ACT.Exp, scale=-0.5)
                act.drain().then_inc(S["root"], 1)
                signalled(act, l, "y_split", 4)
                for i in range(4):
                    copy(branch[:, 2 * i:2 * i + 2, :], UNIT["out"] + i)
                    act.drain()
                    square_pair(branch, i)
                    if i < 3:
                        split_piece(PIECE_OUT + i + SLOTS2)
                root(rstd[:, :], "ss_post", D)
                split_piece(PIECE_OUT + 3 + SLOTS2)
                squares(m.xT, lambda j: signalled(act, l, "x_done", 4 + j + 1))
                root(rstd[:, :], "ss_ffn", D)
                split_h(KC)
                for i in range(FF):
                    b = await_filled(act, l, UNIT["up"] + i)
                    if i >= 2:
                        signalled(act, l, "hid_done", i - 1)
                    for j in range(2):
                        ins = act.activation(ff[:, i % 2, j, :], m.ps[:, b, j * SEQ:(j + 1) * SEQ], ACT.Copy,
                                             scale=ff_taps[:, 2, j * FF + i:j * FF + i + 1])
                    ins.then_inc(S["tap_scaled"], 1)
                    split_piece(PIECE_UP + i + SLOTS2)
                    if i >= 1:
                        signalled(act, l, "conv_done", i)
                        act.activation(silu[:, (i - 1) % 2, :], ff[:, (i - 1) % 2, 0, :], ACT.Silu).then_inc(S["silu_done"], 1)
                signalled(act, l, "conv_done", FF)
                act.activation(silu[:, (FF - 1) % 2, :], ff[:, (FF - 1) % 2, 0, :], ACT.Silu).then_inc(S["silu_done"], 1)
                for c in range(4):
                    for r in range(len(DOWN_ROWS)):
                        if r < len(DOWN_ROWS) - 1:
                            signalled(act, l, "down_used", (len(DOWN_ROWS) - 1) * c + r + 1)
                        else:
                            for i in (2 * c, 2 * c + 1):
                                b = await_filled(act, l, UNIT["down"] + i)
                                act.activation(branch[:, i, :], m.ps[:, b, 0:SEQ], ACT.Copy).then_inc(drained[b], 1)
                            act.drain()
                            square_pair(branch, c)
                        split_piece(PIECE_DOWN + len(DOWN_ROWS) * c + r + SLOTS2)
                root(rstd[:, :], "ss_ffn_post", D)

        @block.vector
        def _(dve):
            dve.drain().then_inc(S["x_done"], 4)
            with dve.Fori(0, 2) as l:
                def inverse_root(dst, n):
                    signalled(dve, l, "root", n)
                    dve.reciprocal(dst, dst)
                    dve.drain()

                def scaled(dst, src, gain, root):
                    inverse_root(rstd[:, :], root)
                    for c in range(KC):
                        yield dve.scalar_tensor_tensor(dst[:, c, :], src[:, c, :], v(gain, c), rstd[:, :], ALU.mult, ALU.mult)

                def normed(gain, root, first):
                    for ins in scaled(square, m.xT, gain, root):
                        ins.then_inc(S["h_done"], 1)
                    for c in range(KC):
                        signalled(dve, l, "h_hi", first + c + 1)
                        dve.tensor_tensor(x_lo[:, c, :], square[:, c, :], x_hi[:, c, :].bitcast(F32), ALU.subtract
                                          ).then_inc(S["h_lo"], 1)

                def split_y(c):
                    dve.tensor_copy(x_hi[:, c:c + 2, :], y[:, c:c + 2, :])
                    dve.drain()
                    dve.tensor_tensor(x_lo[:, c:c + 2, :], y[:, c:c + 2, :], x_hi[:, c:c + 2, :].bitcast(F32),
                                      ALU.subtract).then_inc(S["y_split"], 1)

                def residual(gain, root):
                    for c, _ in enumerate(scaled(branch, branch, gain, root)):
                        if c % 2:
                            dve.drain()
                            x = m.xT[:, c - 1:c + 1, :]
                            dve.tensor_tensor(x, x, branch[:, c - 1:c + 1, :], ALU.add).then_inc(S["x_done"], 1)
                    dve.drain()

                b = await_filled(dve, l, UNIT["vec"])
                dve.tensor_copy(vec[:, :], m.ps[:, b, 0:P])
                dve.tensor_copy(ff_taps[:, :, :], m.ps[:, b, P:P + 6 * FF].rearrange("p (k c) -> p k c", k=3)
                                ).then_inc(drained[b], 1)
                dve.drain()
                normed("norm_mix_pre_2", 1, 0)
                for h in range(4):
                    b = await_filled(dve, l, UNIT["sb_score"] + h)
                    z = m.ps[:, b, 0:W3]
                    dve.tensor_scalar(sb_l[:, h, :], z, HEAD ** -0.5, None, ALU.mult)
                    dve.scalar_tensor_tensor(sb_z[:, h, :], z, HEAD ** -0.5, m.c("past_neg"), ALU.mult, ALU.add)
                    dve.tensor_scalar(sb_pos[:, h, :], z, HEAD ** -0.5, 0.0, ALU.mult, ALU.max).then_inc(drained[b], 1)
                    dve.drain()
                    dve.scalar_tensor_tensor(sb_l[:, h, :], sb_pos[:, h, :], 2.0, sb_l[:, h, :], ALU.mult, ALU.subtract
                                             ).then_inc(S["soft_in"], 1)

                def conf_taps(first, last):
                    for k in range(first, last):
                        for c in range(2):
                            src = padded[:, c, k:k + SEQ]
                            tap = v("conf_dw_w_2", 2 * k + c)
                            if k == 0:
                                dve.tensor_scalar(conf[:, c, :], src, tap, v("conf_dw_b_2", c), ALU.mult, ALU.add)
                            else:
                                dve.scalar_tensor_tensor(conf[:, c, :], src, tap, conf[:, c, :], ALU.mult, ALU.add)
                        dve.drain()

                for name in ("conf_a", "conf_gate"):
                    await_drained(dve, l, UNIT[name])
                dve.tensor_tensor(padded[:, :, TAPS - 1:], s_["conf_a"], s_["conf_gate"], ALU.mult)
                dve.drain()
                conf_taps(0, 6)
                for h in range(4):
                    signalled(dve, l, "soft_ln", h + 1)
                    dve.tensor_tensor(sb_l[:, h, :], sb_l[:, h, :], sb_pos[:, h, :], ALU.add)
                    dve.drain()
                    dve.tensor_tensor(sb_l[:, h, :], sb_l[:, h, :], m.c("past"), ALU.mult).then_inc(S["sb_masked"], 1)
                conf_taps(6, 11)
                for h in range(4):
                    b = await_filled(dve, l, UNIT["tail"] + h)
                    dve.scalar_tensor_tensor(sb_z[:, h, :], m.ps[:, b, 0:W3], -1.0, sb_z[:, h, :], ALU.mult, ALU.add
                                             ).then_inc(drained[b], 1)
                    dve.drain().then_inc(S["sb_arg"], 1)
                conf_taps(11, TAPS)
                dve.drain().then_inc(S["conf_done"], 1)
                cos, sin = (m.c(n).rearrange("p (o t) -> p o t", o=1).to_broadcast([P, 2, SEQ]) for n in ("cos", "sin"))
                for i, name in enumerate(("ret_q", "ret_k")):
                    b = await_filled(dve, l, UNIT["swap"] + i)
                    dve.tensor_tensor(turn_tmp[:, :, :], two(m.ps[:, b, :]), sin, ALU.mult).then_inc(drained[b], 1)
                    dve.tensor_tensor(turned[:, i, :, :], s_[name], cos, ALU.mult)
                    dve.drain()
                    dve.tensor_tensor(turned[:, i, :, :], turned[:, i, :, :], turn_tmp[:, :, :], ALU.add)
                    dve.drain().then_inc(S["turned"], 1)
                for name in ("sc_c", "sc_h"):
                    await_drained(dve, l, UNIT[name])
                dve.tensor_tensor(sc_pad[:, :, 2:], s_["sc_c"], s_["sc_h"], ALU.mult)
                dve.drain()
                for k in range(3):
                    for c in range(2):
                        src = sc_pad[:, c, k:k + SEQ]
                        tap = v("sc_conv_w_2", 2 * k + c)
                        if k == 0:
                            dve.tensor_scalar(y[:, 6 + c, :], src, tap, None, ALU.mult)
                        else:
                            dve.scalar_tensor_tensor(y[:, 6 + c, :], src, tap, y[:, 6 + c, :], ALU.mult, ALU.add)
                    dve.drain()
                b = await_filled(dve, l, UNIT["conf_mean"])
                for c in range(2):
                    ins = dve.scalar_tensor_tensor(conf[:, c, :], m.ps[:, b, 0:SEQ], -1.0 / 256, conf[:, c, :],
                                                   ALU.mult, ALU.add)
                ins.then_inc(drained[b], 1)
                dve.drain().then_inc(S["conf_centred"], 1)
                await_drained(dve, l, UNIT["sc_b"])
                dve.tensor_tensor(y[:, 6:8, :], y[:, 6:8, :], s_["sc_b"], ALU.mult)
                for h in range(4):
                    b = await_filled(dve, l, UNIT["ret_score"] + h)
                    keep = m.c("retain")[:, h * SEQ:(h + 1) * SEQ]
                    dve.tensor_tensor(ret_p[:, h, 0:SEQ], m.ps[:, b, 0:SEQ], keep, ALU.mult)
                    dve.tensor_tensor(ret_p[:, h, SEQ:W3], m.ps[:, b, SEQ:W3], keep[:, 0:P], ALU.mult
                                      ).then_inc(drained[b], 1)
                    dve.drain().then_inc(S["ret_masked"], 1)
                inverse_root(conf_rs[:, :], 2)
                for c in range(2):
                    dve.tensor_tensor(conf[:, c, :], conf[:, c, :], conf_rs[:, :], ALU.mult)
                dve.drain().then_inc(S["conf_normed"], 1)
                await_drained(dve, l, UNIT["ret_g"])
                split_y(6)
                b = await_filled(dve, l, UNIT["ret_mean"])
                for c in range(2):
                    await_drained(dve, l, UNIT["ret_out"] + c)
                dve.scalar_tensor_tensor(ret_o[:, :, :], two(m.ps[:, b, :]), -1.0 / HEAD, ret_o[:, :, :], ALU.mult, ALU.add
                                         ).then_inc(drained[b], 1)
                dve.drain().then_inc(S["ret_centred"], 1)
                for c in range(2):
                    await_drained(dve, l, UNIT["sb_out"] + c)
                split_y(2)
                signalled(dve, l, "root", 3)
                for c in range(2):
                    dve.scalar_tensor_tensor(ret_o[:, c, :], ret_o[:, c, :], v("ret_norm_g_2", c), ret_rs[:, c, :],
                                             ALU.mult, ALU.mult)
                dve.drain()
                dve.tensor_tensor(y[:, 4:6, :], ret_o[:, :, :], s_["ret_g"], ALU.mult)
                signalled(dve, l, "conf_out", 1)
                split_y(0)
                dve.drain()
                split_y(4)
                for i in range(4):
                    await_drained(dve, l, UNIT["out"] + i)
                residual("norm_mix_post_2", 4)
                normed("norm_ffn_pre_2", 5, KC)
                for i in range(FF + 1):
                    if i < FF:
                        b = UNIT["up"] + i
                        signalled(dve, l, "tap_scaled", i + 1)
                        for back in (1, 2):
                            for j in range(2):
                                x = ff[:, i % 2, j, back:]
                                ins = dve.scalar_tensor_tensor(
                                    x, m.ps[:, b % BANKS, j * SEQ:(j + 1) * SEQ - back],
                                    ff_taps[:, 2 - back, j * FF + i:j * FF + i + 1], x, ALU.mult, ALU.add)
                            if back == 2:
                                ins.then_inc(drained[b % BANKS], 1)
                            dve.drain()
                        dve.drain().then_inc(S["conv_done"], 1)
                    if i >= 1:
                        signalled(dve, l, "silu_done", i)
                        h = silu[:, (i - 1) % 2, :]
                        dve.tensor_tensor(h, h, ff[:, (i - 1) % 2, 1, :], ALU.mult)
                        dve.drain()
                        dve.tensor_copy(hid_hi[:, i - 1, :], h)
                        dve.drain()
                        dve.tensor_tensor(hid_lo[:, i - 1, :], h, hid_hi[:, i - 1, :].bitcast(F32), ALU.subtract
                                          ).then_inc(S["hid_done"], 1)
                for i in range(KC):
                    await_drained(dve, l, UNIT["down"] + i)
                residual("norm_ffn_post_2", 6)


def output_part(nc, m, out):
    with ExitStack() as ctx:
        x_out = ctx.enter_context(nc.sbuf_tensor("x_out", [P, TT, D], F32))
        turned, copied, stored = (ctx.enter_context(nc.semaphore(n)) for n in ("out_turned", "out_copied", "out_stored"))
        with nc.Block() as block:
            @block.tensor
            def _(pe):
                for n in range(4):
                    t, c0 = n // 2, 4 * (n % 2)
                    for c in range(4):
                        mm = pe.transpose(m.ps[:, n, c * P:(c + 1) * P], m.xT[:, c0 + c, t * P:(t + 1) * P], m.c("ident"))
                    mm.then_inc(turned, 1)

            @block.vector
            def _(dve):
                for n in range(4):
                    dve.wait_ge(turned, n + 1)
                    dve.tensor_copy(x_out[:, n // 2, (n % 2) * 512:(n % 2 + 1) * 512], m.ps[:, n, :]).then_inc(copied, 1)

            @block.sync
            def _(sp):
                for t in range(TT):
                    sp.wait_ge(copied, 2 * t + 2)
                    sp.dma_start(out[0, t * P:(t + 1) * P, :], x_out[:, t, :]).then_inc(stored, 16)
                sp.wait_ge(stored, 32)


def program(nc, a, out):
    with ExitStack() as ctx:
        def sb(n, s):
            return ctx.enter_context(nc.sbuf_tensor(n, s, F32))
        m = Shared()
        m.ps = ctx.enter_context(nc.psum_tensor("ps", [P, BANKS, 512], F32))
        m.filled = [ctx.enter_context(nc.semaphore(f"bank_filled{b}")) for b in range(BANKS)]
        m.drained = [ctx.enter_context(nc.semaphore(f"bank_drained{b}")) for b in range(BANKS)]
        m.clear_banks = lambda: clear_bank_semaphores(nc, m)
        m.const = sb("const", [P, CONST.shape[1]])
        m.vec = sb("vec", [P, P])
        m.xT = sb("xT", [P, KC, SEQ])
        m.c = lambda n: m.const[:, CONST_AT[n][0]:CONST_AT[n][0] + CONST_AT[n][1]]
        m.v = lambda n, i: m.vec[:, VEC[n] + i:VEC[n] + i + 1]
        m.strip_dram = nc.dram_tensor("strip_dram", [P, ATT_HEADS, BIAS_W], F32, kind="Internal")
        m.line_dram = nc.dram_tensor("line_dram", [ATT_HEADS, BIAS_W], F32, kind="Internal")
        m.n_vec = 14
        m.lora_in = ctx.enter_context(nc.semaphore("lora_in"))
        with ExitStack() as one:
            m.hT = one.enter_context(nc.sbuf_tensor("hT", [P, KC, SEQ], F32))
            m.w_slots = [one.enter_context(nc.sbuf_tensor(f"w_slot{i}", [P, KC, 256], F32)) for i in range(2)] + [None]
            m.w_landed = [one.enter_context(nc.semaphore(f"w_landed{i}")) for i in range(RING)]
            m.att_T = one.enter_context(nc.sbuf_tensor("att_T", [P, 2, SEQ], F32))
            m.o_T = one.enter_context(nc.sbuf_tensor("o_T", [P, 4, SEQ], F32))
            with ExitStack() as rec:
                m.w_up = rec.enter_context(nc.sbuf_tensor("w_up", [P, RW], F32))
                m.a_up = rec.enter_context(nc.sbuf_tensor("a_up", [P, RW], F32))
                m.g_up = rec.enter_context(nc.sbuf_tensor("g_up", [P, 2, RW], F32))
                m.p_rwkv = rec.enter_context(nc.sbuf_tensor("p_rwkv", [P, 15, SEQ + 1], F32))
                with ExitStack() as att:
                    m.qk = att.enter_context(nc.sbuf_tensor("qk", [P, 12, SEQ], F32))
                    m.v_att = att.enter_context(nc.sbuf_tensor("v_att", [P, TT, 768], F32))
                    m.bias = att.enter_context(nc.sbuf_tensor("bias", [P, ATT_HEADS, SEQ], F32))
                    project_part(nc, m, a)
                    m.clear_banks()
                    attention_part(nc, m, a)
                m.clear_banks()
                recurrence_part(nc, m, a)
            m.clear_banks()
            m.h_tok = m.w_slots[0][:, :, :].rearrange("p c n -> p (c n)").rearrange("p (t d) -> p t d", t=TT)
            m.router_w = one.enter_context(nc.sbuf_tensor("router_w", [P, KC, 4 + N_EXP], F32))
            m.router_b = one.enter_context(nc.sbuf_tensor("router_b", [P, 4 + N_EXP], F32))
            m.router_in = one.enter_context(nc.semaphore("router_in"))
            mix_part(nc, m, a)
            with ExitStack() as moe:
                def sbm(n, s, d=F32):
                    return moe.enter_context(nc.sbuf_tensor(n, s, d))
                m.gate_w = sbm("exp_gate_w", [P, 2, KC, D_EXP])
                m.up_w = sbm("exp_up_w", [P, 2, KC, D_EXP])
                m.down_w = sbm("exp_down_w", [P, 2, D_EXP // P, D])
                m.pick = sbm("pick", [P, TT, N_EXP, SLOTS])
                m.weighted = sbm("weighted", [P, TT, N_EXP, SLOTS])
                m.gates = sbm("gates", [P, TT, N_EXP])
                m.gate_T = sbm("gate_T", [P, N_EXP // 2, SEQ])
                m.gate = sbm("gate12", [P, 2, TT, 1])
                m.over_slot = sbm("over_slot", [P, 2, TT, 1])
                m.over_int = sbm("over_int", [P, OVER + 1], I32)
                m.landed = {(n, e): moe.enter_context(nc.semaphore(f"landed_{n}{e}"))
                            for n in ("gate", "up", "down") for e in range(2)}
                expert_loads(nc, m, a)
                m.clear_banks()
                routing_part(nc, m, a)
                m.clear_banks()
                expert_part(nc, m, a)
        m.clear_banks()
        layers_part(nc, m, a)
        output_part(nc, m, out)


def kernel(**inputs):
    import numpy as _np
    import concourse.bacc as _bacc
    from concourse import mybir as _mybir
    from concourse.bass_utils import run_bass_kernel_spmd as _run
    nc = _bacc.Bacc("TRN2", target_bir_lowering=False, num_devices=1)
    arrays, aps = {}, {}
    for name, x in (*inputs.items(), ("const", CONST), ("bias_rows", BIAS_ROWS)):
        x = _np.ascontiguousarray(x)
        arrays[f"in_{name}"] = x
        aps[name] = nc.dram_tensor(f"in_{name}", x.shape, _mybir.dt.from_np(x.dtype), kind="ExternalInput").ap()
    out = nc.dram_tensor("out", (1, SEQ, D), F32, kind="ExternalOutput").ap()
    program(nc, aps, out)
    r = _run(nc, [arrays], core_ids=[0])
    return r.results[0]["out"]
```
